# Optimizing a Trainium2 kernel written in Bass

```python
import jax
import jax.numpy as jnp
from jax import lax
import numpy as np
import jax, jax.numpy as jnp

D_MODEL = 1024
BATCH = 1
SEQ = 256
DEPTH = 2

GRID_W = 64
CTX_LEN = 256

NA_HEAD_DIM = 64
NA_HEADS = (D_MODEL // 2) // NA_HEAD_DIM
NA_WIDTH = NA_HEADS * NA_HEAD_DIM
NA_KH = 8
NA_KW = 16
ML_HEAD_DIM = 128
ML_HEADS = (D_MODEL // 2) // ML_HEAD_DIM
ML_WIDTH = ML_HEADS * ML_HEAD_DIM
ML_CHUNK = 128
ML_GATE_CAP = 15.0
AB_IN_WIDTH = 3 * NA_WIDTH + 4 * ML_WIDTH + 4 * ML_HEADS
RW_HEAD_DIM = 64
RW_HEADS = D_MODEL // RW_HEAD_DIM
RW_DECAY_LORA = 64
RW_AAA_LORA = 64
RW_GATE_LORA = 160
RW_GN_EPS = 64e-5
D_FF = 4 * D_MODEL
ROPE_BASE = 10000.0
NORM_EPS = 1e-6


def rms_norm(x, eps=NORM_EPS):
    xf = x.astype(jnp.float32)
    return (xf * lax.rsqrt(jnp.mean(xf * xf, axis=-1, keepdims=True) + eps)).astype(x.dtype)

def modulate(x, shift, scale):
    return rms_norm(x) * (1.0 + scale) + shift

def split_heads(t, n_heads, head_dim):
    return t.reshape(*t.shape[:-1], n_heads, head_dim)

def adaln(cond, w, b):
    return jnp.split(jax.nn.silu(cond) @ w + b, 6, axis=-1)

def squared_relu_mlp(h, w1, w2):
    return jnp.square(jax.nn.relu(h @ w1)) @ w2

def axial_rope_angles(n_tokens, head_dim):
    pos = jnp.arange(n_tokens)
    rows = (pos // GRID_W).astype(jnp.float32)
    cols = (pos % GRID_W).astype(jnp.float32)
    n_freq = head_dim // 4
    inv_freq = ROPE_BASE ** (-jnp.arange(n_freq, dtype=jnp.float32) / n_freq)
    return rows[:, None] * inv_freq, cols[:, None] * inv_freq

def rope_rotate(x, ang):
    x1, x2 = jnp.split(x, 2, axis=-1)
    cos = jnp.cos(ang)[:, None, :].astype(x.dtype)
    sin = jnp.sin(ang)[:, None, :].astype(x.dtype)
    return jnp.concatenate([x1 * cos - x2 * sin, x1 * sin + x2 * cos], axis=-1)

def axial_rope(x, ang_r, ang_c):
    x_row, x_col = jnp.split(x, 2, axis=-1)
    return jnp.concatenate([rope_rotate(x_row, ang_r), rope_rotate(x_col, ang_c)], axis=-1)

def context_attention(q, k, v):
    s = jnp.einsum('bqhd,bkhd->bhqk', q, k).astype(jnp.float32) * (q.shape[-1] ** -0.5)
    p = jax.nn.softmax(s, axis=-1).astype(v.dtype)
    return jnp.einsum('bhqk,bkhd->bqhd', p, v)

def neighbourhood_attention(q, k, v, k_ctx, v_ctx, rpb):
    n_b, n_tok, n_h, d_h = q.shape
    rows = n_tok // GRID_W
    kh = min(NA_KH, rows)
    n_win = kh * NA_KW
    scale = d_h ** -0.5
    qg = q.reshape(n_b, rows, GRID_W, n_h, d_h)
    kg = k.reshape(n_b, rows, GRID_W, n_h, d_h)
    vg = v.reshape(n_b, rows, GRID_W, n_h, d_h)
    row_idx = jnp.arange(rows)
    row_start = jnp.clip(row_idx - kh // 2, 0, rows - kh)
    col_idx = jnp.arange(GRID_W)
    col_win = jnp.clip(col_idx - NA_KW // 2, 0, GRID_W - NA_KW)[:, None] + jnp.arange(NA_KW)[None, :]
    rpb_c = rpb[:, :, col_win - col_idx[:, None] + NA_KW - 1]

    def one_row(args):
        r, rs, q_row = args
        k_nb = lax.dynamic_slice_in_dim(kg, rs, kh, axis=1)[:, :, col_win]
        v_nb = lax.dynamic_slice_in_dim(vg, rs, kh, axis=1)[:, :, col_win]
        bias = rpb_c[:, rs + jnp.arange(kh) - r + NA_KH - 1]
        s_nb = jnp.einsum('bchd,bicjhd->bhcij', q_row, k_nb).astype(jnp.float32) * scale + jnp.transpose(bias, (0, 2, 1, 3))
        s_cx = jnp.einsum('bchd,bnhd->bhcn', q_row, k_ctx).astype(jnp.float32) * scale
        p = jax.nn.softmax(jnp.concatenate([s_nb.reshape(n_b, n_h, GRID_W, n_win), s_cx], axis=-1), axis=-1).astype(v.dtype)
        p_nb = p[..., :n_win].reshape(n_b, n_h, GRID_W, kh, NA_KW)
        return jnp.einsum('bhcij,bicjhd->bchd', p_nb, v_nb) + jnp.einsum('bhcn,bnhd->bchd', p[..., n_win:], v_ctx)

    out = lax.map(one_row, (row_idx, row_start, jnp.moveaxis(qg, 1, 0)))
    return jnp.moveaxis(out, 0, 1).reshape(n_b, n_tok, n_h, d_h)

def mlstm_chunked(q, k, v, log_i, log_f, state, with_out):
    n_b, n_h, n_t, _ = q.shape
    n_c = n_t // ML_CHUNK

    def chunks(t):
        return jnp.moveaxis(t.reshape(n_b, n_h, n_c, ML_CHUNK, *t.shape[3:]), 2, 0)

    tril = jnp.tril(jnp.ones((ML_CHUNK, ML_CHUNK), dtype=bool))

    def step(carry, inp):
        c_st, n_st, m_st = carry
        qc, kc, vc, ic, fc = inp
        b = jnp.cumsum(fc, axis=-1)
        log_d = jnp.where(tril, b[..., :, None] - b[..., None, :] + ic[..., None, :], -jnp.inf)
        log_inter = b + m_st[..., None]
        m_t = jnp.maximum(log_inter, jnp.max(log_d, axis=-1))
        m_new = m_t[..., -1]
        w_s = jnp.exp(b[..., -1:] - b + ic - m_new[..., None])
        decay = jnp.exp(b[..., -1] + m_st - m_new)
        c_new = decay[..., None, None] * c_st + jnp.einsum('bhs,bhsd,bhse->bhde', w_s, kc, vc)
        n_new = decay[..., None] * n_st + jnp.einsum('bhs,bhsd->bhd', w_s, kc)
        if not with_out:
            return (c_new, n_new, m_new), None
        d_mat = jnp.exp(log_d - m_t[..., None])
        w_inter = jnp.exp(log_inter - m_t)
        s = jnp.einsum('bhtd,bhsd->bhts', qc, kc) * d_mat
        num = jnp.einsum('bhts,bhse->bhte', s, vc) + w_inter[..., None] * jnp.einsum('bhtd,bhde->bhte', qc, c_st)
        den = jnp.sum(s, axis=-1) + w_inter * jnp.einsum('bhtd,bhd->bht', qc, n_st)
        h = num / jnp.maximum(jnp.abs(den), jnp.exp(-m_t))[..., None]
        return (c_new, n_new, m_new), h

    state, hs = lax.scan(step, state, tuple(chunks(t) for t in (q, k, v, log_i, log_f)))
    if not with_out:
        return None, state
    return jnp.moveaxis(hs, 0, 2).reshape(n_b, n_h, n_t, -1), state

def mlstm_bidir(q_l, k_l, v_l, g_l, q_c, k_c, v_c, g_c, need_ctx):
    def heads_first(t):
        return jnp.swapaxes(t, 1, 2).astype(jnp.float32)

    def gates(g):
        g = ML_GATE_CAP * jnp.tanh(g.astype(jnp.float32) / ML_GATE_CAP)
        i_f, f_f, i_b, f_b = jnp.split(jnp.swapaxes(g, 1, 2), 4, axis=1)
        return i_f, jax.nn.log_sigmoid(f_f), i_b, jax.nn.log_sigmoid(f_b)

    def flip(t):
        return jnp.flip(t, axis=2)

    n_b = q_l.shape[0]
    zero = (jnp.zeros((n_b, ML_HEADS, ML_HEAD_DIM, ML_HEAD_DIM), jnp.float32),
            jnp.zeros((n_b, ML_HEADS, ML_HEAD_DIM), jnp.float32),
            jnp.zeros((n_b, ML_HEADS), jnp.float32))
    qc, kc, vc = heads_first(q_c), heads_first(k_c), heads_first(v_c)
    if_c, lf_c, ib_c, lb_c = gates(g_c)
    hc_f, st_f = mlstm_chunked(qc, kc, vc, if_c, lf_c, zero, need_ctx)
    hc_b, st_b = mlstm_chunked(flip(qc), flip(kc), flip(vc), flip(ib_c), flip(lb_c), zero, need_ctx)
    ql, kl, vl = heads_first(q_l), heads_first(k_l), heads_first(v_l)
    if_l, lf_l, ib_l, lb_l = gates(g_l)
    hl_f, _ = mlstm_chunked(ql, kl, vl, if_l, lf_l, st_f, True)
    hl_b, _ = mlstm_chunked(flip(ql), flip(kl), flip(vl), flip(ib_l), flip(lb_l), st_b, True)
    h_lat = jnp.swapaxes(hl_f + flip(hl_b), 1, 2)
    h_ctx = jnp.swapaxes(hc_f + flip(hc_b), 1, 2) if need_ctx else None
    return h_lat, h_ctx

def ab_mixer(h_l, h_c, w_in, gate_b, q_norm, k_norm, rpb, head_norm, w_out, ang_r, ang_c, need_ctx):
    splits = [NA_WIDTH, 2 * NA_WIDTH, 3 * NA_WIDTH, 3 * NA_WIDTH + ML_WIDTH, 3 * NA_WIDTH + 2 * ML_WIDTH,
              3 * NA_WIDTH + 3 * ML_WIDTH, 3 * NA_WIDTH + 4 * ML_WIDTH]

    def project(h):
        qa, ka, va, qb, kb, vb, ob, g = jnp.split(h @ w_in, splits, axis=-1)
        qa = rms_norm(split_heads(qa, NA_HEADS, NA_HEAD_DIM)) * q_norm
        ka = rms_norm(split_heads(ka, NA_HEADS, NA_HEAD_DIM)) * k_norm
        va = split_heads(va, NA_HEADS, NA_HEAD_DIM)
        qb = split_heads(qb, ML_HEADS, ML_HEAD_DIM)
        kb = split_heads(kb, ML_HEADS, ML_HEAD_DIM) * (ML_HEAD_DIM ** -0.5)
        vb = split_heads(vb, ML_HEADS, ML_HEAD_DIM)
        return qa, ka, va, qb, kb, vb, ob, g + gate_b

    qa_l, ka_l, va_l, qb_l, kb_l, vb_l, ob_l, g_l = project(h_l)
    qa_c, ka_c, va_c, qb_c, kb_c, vb_c, ob_c, g_c = project(h_c)
    qb_l = axial_rope(qb_l, ang_r, ang_c)
    kb_l = axial_rope(kb_l, ang_r, ang_c)
    na_l = neighbourhood_attention(qa_l, ka_l, va_l, ka_c, va_c, rpb)
    ml_l, ml_c = mlstm_bidir(qb_l, kb_l, vb_l, g_l, qb_c, kb_c, vb_c, g_c, need_ctx)

    def merge(na, ml, o):
        ml = (rms_norm(ml) * head_norm).astype(o.dtype) * jax.nn.sigmoid(split_heads(o, ML_HEADS, ML_HEAD_DIM))
        cat = jnp.concatenate([na.reshape(*na.shape[:2], NA_WIDTH), ml.reshape(*ml.shape[:2], ML_WIDTH)], axis=-1)
        return cat @ w_out

    out_l = merge(na_l, ml_l, ob_l)
    out_c = merge(context_attention(qa_c, ka_c, va_c), ml_c, ob_c) if need_ctx else None
    return out_l, out_c

def centred_shift(x):
    xp = jnp.pad(x, ((0, 0), (1, 1), (0, 0)))
    return 0.5 * (xp[:, :-2] + xp[:, 2:])

def rwkv_prepare(h, mu, w_rkv, w0, w1, w2, a0, a1, a2, g1, g2, k_k, k_a):
    xx = centred_shift(h) - h
    xr, xw, xk, xv, xa, xg = h[None] + xx[None] * mu[:, None, None, :]
    r, k, v = jnp.einsum('sbtd,sde->sbte', jnp.stack([xr, xk, xv]), w_rkv)
    w_logit = w0[:, None, None, :] + jnp.einsum('zbtr,zrd->zbtd', jnp.tanh(jnp.einsum('btd,zdr->zbtr', xw, w1)), w2)
    decay = jnp.exp(-jnp.exp(-jax.nn.softplus(-w_logit.astype(jnp.float32)) - 0.5))
    a = jax.nn.sigmoid(a0[:, None, None, :] + jnp.einsum('zbtr,zrd->zbtd', jnp.einsum('btd,zdr->zbtr', xa, a1), a2))
    g = jax.nn.sigmoid(xg @ g1) @ g2
    kk = split_heads((k * k_k).astype(jnp.float32), RW_HEADS, RW_HEAD_DIM)
    kk = (kk / jnp.maximum(jnp.linalg.norm(kk, axis=-1, keepdims=True), 1e-12)).reshape(k.shape)
    k_dir = k[None] * (1.0 + (a - 1.0) * k_a)
    return r, k_dir, v, decay, -kk, kk[None] * a, g

def rwkv7_scan(r, w, k, v, a, b, state, reverse, with_out):
    def time_major(t):
        return jnp.moveaxis(split_heads(t.astype(jnp.float32), RW_HEADS, RW_HEAD_DIM), 1, 0)

    def step(s, inp):
        rt, wt, kt, vt, at, bt = inp
        sa = jnp.einsum('bhij,bhj->bhi', s, at)
        s = s * wt[:, :, None, :] + sa[..., None] * bt[:, :, None, :] + vt[..., None] * kt[:, :, None, :]
        y = jnp.einsum('bhij,bhj->bhi', s, rt) if with_out else None
        return s, y

    state, ys = lax.scan(step, state, tuple(time_major(t) for t in (r, w, k, v, a, b)), reverse=reverse)
    return (jnp.moveaxis(ys, 0, 1) if with_out else None), state

def rwkv_mixer(h_l, h_c, mu, w_rkv, w0, w1, w2, a0, a1, a2, g1, g2, k_k, k_a, r_k, lnx_w, lnx_b, w_o, need_ctx):
    lat = rwkv_prepare(h_l, mu, w_rkv, w0, w1, w2, a0, a1, a2, g1, g2, k_k, k_a)
    cxt = rwkv_prepare(h_c, mu, w_rkv, w0, w1, w2, a0, a1, a2, g1, g2, k_k, k_a)
    s0 = jnp.zeros((h_l.shape[0], RW_HEADS, RW_HEAD_DIM, RW_HEAD_DIM), jnp.float32)

    def bidir(p, s_f, s_b, with_out):
        r, k_dir, v, decay, a, b_dir, _ = p
        y_f, s_f = rwkv7_scan(r, decay[0], k_dir[0], v, a, b_dir[0], s_f, False, with_out)
        y_b, s_b = rwkv7_scan(r, decay[1], k_dir[1], v, a, b_dir[1], s_b, True, with_out)
        return y_f, y_b, s_f, s_b

    yc_f, yc_b, st_f, st_b = bidir(cxt, s0, s0, need_ctx)
    yl_f, yl_b, _, _ = bidir(lat, st_f, st_b, True)

    def readout(p, y_f, y_b):
        r, k_dir, v, _, _, _, g = p
        y = y_f + y_b
        mean = jnp.mean(y, axis=-1, keepdims=True)
        var = jnp.mean(jnp.square(y - mean), axis=-1, keepdims=True)
        y = ((y - mean) * lax.rsqrt(var + RW_GN_EPS)).reshape(r.shape) * lnx_w + lnx_b
        coef = jnp.sum(split_heads(r, RW_HEADS, RW_HEAD_DIM)[None] * split_heads(k_dir, RW_HEADS, RW_HEAD_DIM)
                       * split_heads(r_k, RW_HEADS, RW_HEAD_DIM), axis=(0, -1))[..., None]
        bonus = (coef * split_heads(v, RW_HEADS, RW_HEAD_DIM)).reshape(r.shape)
        return ((y + bonus) * g).astype(h_l.dtype) @ w_o

    out_l = readout(lat, yl_f, yl_b)
    out_c = readout(cxt, yc_f, yc_b) if need_ctx else None
    return out_l, out_c

def first_inputs(seed: int = 0) -> dict:
    key = jax.random.key(seed)
    keys = iter(jax.random.split(key, 48))
    n_even = (DEPTH + 1) // 2
    n_odd = DEPTH // 2
    d = D_MODEL

    def normal(shape, scale):
        return scale * jax.random.normal(next(keys), shape, jnp.float32)

    def uniform(shape, lo, hi):
        return jax.random.uniform(next(keys), shape, jnp.float32, lo, hi)

    ab_gate_b = jnp.concatenate([normal((n_even, ML_HEADS), 0.1), uniform((n_even, ML_HEADS), 3.0, 6.0),
                                 normal((n_even, ML_HEADS), 0.1), uniform((n_even, ML_HEADS), 3.0, 6.0)], axis=-1)
    return {
        'x': normal((BATCH, SEQ, d), 1.0),
        'c': normal((BATCH, d), 1.0),
        'ctx': normal((BATCH, CTX_LEN, d), 1.0),
        'c_ctx': normal((d,), 1.0),
        'ada_w': normal((DEPTH, d, 6 * d), 0.5 * d ** -0.5),
        'ada_b': normal((DEPTH, 6 * d), 0.02),
        'ab_w_in': normal((n_even, d, AB_IN_WIDTH), d ** -0.5),
        'ab_gate_b': ab_gate_b,
        'na_q_norm': 1.0 + normal((n_even, NA_HEAD_DIM), 0.05),
        'na_k_norm': 1.0 + normal((n_even, NA_HEAD_DIM), 0.05),
        'na_rpb': normal((n_even, NA_HEADS, 2 * NA_KH - 1, 2 * NA_KW - 1), 0.1),
        'ml_head_norm': 1.0 + normal((n_even, ML_HEADS, ML_HEAD_DIM), 0.05),
        'ab_w_out': normal((n_even, d, d), d ** -0.5),
        'rw_mu': uniform((n_odd, 6, d), 0.0, 1.0),
        'rw_w_rkv': normal((n_odd, 3, d, d), d ** -0.5),
        'rw_w0': uniform((n_odd, 2, d), -6.0, -1.0),
        'rw_w1': normal((n_odd, 2, d, RW_DECAY_LORA), 0.1 * d ** -0.5),
        'rw_w2': normal((n_odd, 2, RW_DECAY_LORA, d), 0.1 * RW_DECAY_LORA ** -0.5),
        'rw_a0': normal((n_odd, 2, d), 0.1),
        'rw_a1': normal((n_odd, 2, d, RW_AAA_LORA), d ** -0.5),
        'rw_a2': normal((n_odd, 2, RW_AAA_LORA, d), 0.5 * RW_AAA_LORA ** -0.5),
        'rw_g1': normal((n_odd, d, RW_GATE_LORA), d ** -0.5),
        'rw_g2': normal((n_odd, RW_GATE_LORA, d), RW_GATE_LORA ** -0.5),
        'rw_k_k': 0.85 + normal((n_odd, d), 0.05),
        'rw_k_a': 1.0 + normal((n_odd, d), 0.05),
        'rw_r_k': normal((n_odd, d), 0.1),
        'rw_lnx_w': 1.0 + normal((n_odd, d), 0.05),
        'rw_lnx_b': normal((n_odd, d), 0.02),
        'rw_w_o': normal((n_odd, d, d), d ** -0.5),
        'mlp_w1': normal((DEPTH, d, D_FF), d ** -0.5),
        'mlp_w2': normal((DEPTH, D_FF, d), D_FF ** -0.5),
    }

def first_block(x, c, ctx, c_ctx, ada_w, ada_b, ab_w_in, ab_gate_b, na_q_norm, na_k_norm, na_rpb, ml_head_norm,
              ab_w_out, rw_mu, rw_w_rkv, rw_w0, rw_w1, rw_w2, rw_a0, rw_a1, rw_a2, rw_g1, rw_g2, rw_k_k, rw_k_a,
              rw_r_k, rw_lnx_w, rw_lnx_b, rw_w_o, mlp_w1, mlp_w2):
    ang_r, ang_c = axial_rope_angles(x.shape[1], ML_HEAD_DIM)
    for layer in range(DEPTH):
        need_ctx = layer < DEPTH - 1
        j = layer // 2
        sh_a, sc_a, gt_a, sh_m, sc_m, gt_m = adaln(c[:, None, :], ada_w[layer], ada_b[layer])
        csh_a, csc_a, cgt_a, csh_m, csc_m, cgt_m = adaln(c_ctx, ada_w[layer], ada_b[layer])
        h_l = modulate(x, sh_a, sc_a)
        h_c = modulate(ctx, csh_a, csc_a)
        if layer % 2 == 0:
            o_l, o_c = ab_mixer(h_l, h_c, ab_w_in[j], ab_gate_b[j], na_q_norm[j], na_k_norm[j], na_rpb[j],
                                ml_head_norm[j], ab_w_out[j], ang_r, ang_c, need_ctx)
        else:
            o_l, o_c = rwkv_mixer(h_l, h_c, rw_mu[j], rw_w_rkv[j], rw_w0[j], rw_w1[j], rw_w2[j], rw_a0[j],
                                  rw_a1[j], rw_a2[j], rw_g1[j], rw_g2[j], rw_k_k[j], rw_k_a[j], rw_r_k[j],
                                  rw_lnx_w[j], rw_lnx_b[j], rw_w_o[j], need_ctx)
        x = x + gt_a * o_l
        x = x + gt_m * squared_relu_mlp(modulate(x, sh_m, sc_m), mlp_w1[layer], mlp_w2[layer])
        if need_ctx:
            ctx = ctx + cgt_a * o_c
            ctx = ctx + cgt_m * squared_relu_mlp(modulate(ctx, csh_m, csc_m), mlp_w1[layer], mlp_w2[layer])
    return x


N_EVEN = (DEPTH + 1) // 2
N_ODD = DEPTH // 2
BLOCK = 128
D_FF_2 = 2816
EPS = 1e-6
SB_HEADS = 8
SB_HEAD_DIM = 64
SB_WIDTH = SB_HEADS * SB_HEAD_DIM
SG_GROUPS = 8
SG_GROUP_DIM = 64
SG_WIDTH = SG_GROUPS * SG_GROUP_DIM
SG_CHUNK = 128
EVEN_IN = 3 * SB_WIDTH + 2 * SG_WIDTH
EVEN_MIX = SB_WIDTH + SG_WIDTH
MLA_HEADS = 16
MLA_NOPE = 64
MLA_ROPE = 32
MLA_QK = MLA_NOPE + MLA_ROPE
MLA_V = 64
MLA_Q_LORA = 512
MLA_KV_LORA = 256
MLA_IN = MLA_Q_LORA + MLA_KV_LORA + MLA_ROPE
MLA_MIX = MLA_HEADS * MLA_V
ROPE_THETA = 10000.0
MEM_TOKENS = 256
MEM_HEADS = 4
MEM_HEAD_DIM = D_MODEL // MEM_HEADS


def _rmsnorm(x, g):
    xf = x.astype(jnp.float32)
    y = xf * lax.rsqrt(jnp.mean(xf * xf, axis=-1, keepdims=True) + EPS)
    return (y * g.astype(jnp.float32)).astype(x.dtype)

def _layernorm(x, g, b):
    xf = x.astype(jnp.float32)
    mu = jnp.mean(xf, axis=-1, keepdims=True)
    var = jnp.mean(jnp.square(xf - mu), axis=-1, keepdims=True)
    y = (xf - mu) * lax.rsqrt(var + EPS)
    return (y * g.astype(jnp.float32) + b.astype(jnp.float32)).astype(x.dtype)

def _swiglu(h, w_gu, w_down):
    gate, up = jnp.split(h @ w_gu, 2, axis=-1)
    return (jax.nn.silu(gate) * up) @ w_down

def _to_blocks(t):
    b, s, h, d = t.shape
    return t.reshape(b, s // BLOCK, BLOCK, h, d).transpose(1, 0, 2, 3, 4)

def _from_blocks(t):
    nb, b, l, h, d = t.shape
    return t.transpose(1, 0, 2, 3, 4).reshape(b, nb * l, h, d)

def _rope(t, positions):
    half = t.shape[-1] // 2
    inv_freq = ROPE_THETA ** (-jnp.arange(half, dtype=jnp.float32) / half)
    ang = positions.astype(jnp.float32)[:, :, None, None] * inv_freq
    cos, sin = jnp.cos(ang), jnp.sin(ang)
    tf = t.astype(jnp.float32)
    t1, t2 = tf[..., :half], tf[..., half:]
    return jnp.concatenate([t1 * cos - t2 * sin, t1 * sin + t2 * cos], axis=-1).astype(t.dtype)

def _stick_breaking_attention(q, k, v):
    s_len = q.shape[1]
    scale = SB_HEAD_DIM ** -0.5
    k_pos = jnp.arange(s_len)

    def block(args):
        q_blk, i = args
        z = jnp.einsum('bqhd,bkhd->bhqk', q_blk, k).astype(jnp.float32) * scale
        q_pos = i * BLOCK + jnp.arange(BLOCK)
        strict = (k_pos[None, :] < q_pos[:, None])[None, None]
        log_stay = jnp.where(strict, jax.nn.log_sigmoid(-z), 0.0)
        log_rest = lax.cumsum(log_stay, axis=3, reverse=True) - log_stay
        w = jnp.where(strict, jnp.exp(jax.nn.log_sigmoid(z) + log_rest), 0.0)
        return jnp.einsum('bhqk,bkhd->bqhd', w.astype(v.dtype), v)

    out = lax.map(block, (_to_blocks(q), jnp.arange(s_len // BLOCK)))
    return _from_blocks(out)

def _causal_softmax_attention(q, k, v):
    s_len = q.shape[1]
    scale = q.shape[-1] ** -0.5
    k_pos = jnp.arange(s_len)

    def block(args):
        q_blk, i = args
        sc = jnp.einsum('bqhd,bkhd->bhqk', q_blk, k).astype(jnp.float32) * scale
        q_pos = i * BLOCK + jnp.arange(BLOCK)
        causal = (k_pos[None, :] <= q_pos[:, None])[None, None]
        p = jax.nn.softmax(jnp.where(causal, sc, -jnp.inf), axis=-1)
        return jnp.einsum('bhqk,bkhd->bqhd', p.astype(v.dtype), v)

    out = lax.map(block, (_to_blocks(q), jnp.arange(s_len // BLOCK)))
    return _from_blocks(out)

def _even_mixer(h, w_in, ln_g, ln_b, sgu_w, sgu_b, w_out):
    b, s, _ = h.shape
    q, k, v, z = jnp.split(h @ w_in, [SB_WIDTH, 2 * SB_WIDTH, 3 * SB_WIDTH], axis=-1)
    heads = lambda t: t.reshape(b, s, SB_HEADS, SB_HEAD_DIM)
    o_sb = _stick_breaking_attention(heads(q), heads(k), heads(v)).reshape(b, s, SB_WIDTH)
    u, g = jnp.split(jax.nn.gelu(z), 2, axis=-1)
    g = _layernorm(g, ln_g, ln_b).reshape(b, s // SG_CHUNK, SG_CHUNK, SG_GROUPS, SG_GROUP_DIM)
    tri = jnp.tril(jnp.ones((SG_CHUNK, SG_CHUNK), dtype=sgu_w.dtype))
    mixed = jnp.einsum('gts,bcsgd->bctgd', sgu_w * tri, g) + sgu_b.T[None, None, :, :, None]
    o_sg = u * mixed.reshape(b, s, SG_WIDTH)
    return jnp.concatenate([o_sb, o_sg], axis=-1) @ w_out

def _mla_mixer(h, positions, w_in, q_lora_g, kv_lora_g, w_uq, w_ukv, q_g, k_g, w_out):
    b, s, _ = h.shape
    c_q, c_kv, k_r = jnp.split(h @ w_in, [MLA_Q_LORA, MLA_Q_LORA + MLA_KV_LORA], axis=-1)
    q = (_rmsnorm(c_q, q_lora_g) @ w_uq).reshape(b, s, MLA_HEADS, MLA_QK)
    kv = (_rmsnorm(c_kv, kv_lora_g) @ w_ukv).reshape(b, s, MLA_HEADS, MLA_NOPE + MLA_V)
    k_nope, v = kv[..., :MLA_NOPE], kv[..., MLA_NOPE:]
    k_r = jnp.broadcast_to(k_r[:, :, None, :], (b, s, MLA_HEADS, MLA_ROPE))
    k = jnp.concatenate([k_nope, k_r], axis=-1)
    q = _rmsnorm(q, q_g)
    k = _rmsnorm(k, k_g)
    q = jnp.concatenate([q[..., :MLA_NOPE], _rope(q[..., MLA_NOPE:], positions)], axis=-1)
    k = jnp.concatenate([k[..., :MLA_NOPE], _rope(k[..., MLA_NOPE:], positions)], axis=-1)
    o = _causal_softmax_attention(q, k, v).reshape(b, s, MLA_MIX)
    return o @ w_out

def _memory_cross_attention(hq, hm, wq, wkv, q_g, k_g, wo):
    b, s, _ = hq.shape
    m = hm.shape[1]
    q = _rmsnorm((hq @ wq).reshape(b, s, MEM_HEADS, MEM_HEAD_DIM), q_g)
    k, v = jnp.split((hm @ wkv).reshape(b, m, MEM_HEADS, 2 * MEM_HEAD_DIM), 2, axis=-1)
    k = _rmsnorm(k, k_g)
    sc = jnp.einsum('bqhd,bmhd->bhqm', q, k).astype(jnp.float32) * (MEM_HEAD_DIM ** -0.5)
    p = jax.nn.softmax(sc, axis=-1)
    o = jnp.einsum('bhqm,bmhd->bqhd', p.astype(v.dtype), v).reshape(b, s, D_MODEL)
    return o @ wo

def _w(k, shape, fan_in):
    return jax.random.normal(k, shape, jnp.float32) * (fan_in ** -0.5)

def _gain(k, shape):
    return 1.0 + 0.02 * jax.random.normal(k, shape, jnp.float32)

def second_inputs(seed: int = 0) -> dict:
    key = jax.random.key(seed)
    ks = list(jax.random.split(key, 32))
    nk = ks.pop
    inp = {}
    inp['x'] = jax.random.normal(nk(), (BATCH, SEQ, D_MODEL), jnp.float32)
    inp['mem'] = jax.random.normal(nk(), (BATCH, MEM_TOKENS, D_MODEL), jnp.float32)
    inp['positions'] = jnp.broadcast_to(jnp.arange(SEQ, dtype=jnp.int32)[None, :], (BATCH, SEQ))
    inp['ffn_pre_norm'] = _gain(nk(), (DEPTH, D_MODEL))
    inp['ffn_pre_w_gu'] = _w(nk(), (DEPTH, D_MODEL, 2 * D_FF_2), D_MODEL)
    inp['ffn_pre_w_down'] = _w(nk(), (DEPTH, D_FF_2, D_MODEL), D_FF_2)
    inp['mix_norm'] = _gain(nk(), (DEPTH, D_MODEL))
    inp['sbg_w_in'] = _w(nk(), (N_EVEN, D_MODEL, EVEN_IN), D_MODEL)
    inp['sgu_ln_gain'] = _gain(nk(), (N_EVEN, SG_WIDTH))
    inp['sgu_ln_bias'] = 0.02 * jax.random.normal(nk(), (N_EVEN, SG_WIDTH), jnp.float32)
    inp['sgu_w'] = _w(nk(), (N_EVEN, SG_GROUPS, SG_CHUNK, SG_CHUNK), SG_CHUNK)
    inp['sgu_b'] = 1.0 + 0.1 * jax.random.normal(nk(), (N_EVEN, SG_GROUPS, SG_CHUNK), jnp.float32)
    inp['sbg_w_out'] = _w(nk(), (N_EVEN, EVEN_MIX, D_MODEL), EVEN_MIX)
    inp['mla_w_in'] = _w(nk(), (N_ODD, D_MODEL, MLA_IN), D_MODEL)
    inp['mla_q_lora_gain'] = _gain(nk(), (N_ODD, MLA_Q_LORA))
    inp['mla_kv_lora_gain'] = _gain(nk(), (N_ODD, MLA_KV_LORA))
    inp['mla_w_uq'] = _w(nk(), (N_ODD, MLA_Q_LORA, MLA_HEADS * MLA_QK), MLA_Q_LORA)
    inp['mla_w_ukv'] = _w(nk(), (N_ODD, MLA_KV_LORA, MLA_HEADS * (MLA_NOPE + MLA_V)), MLA_KV_LORA)
    inp['mla_q_gain'] = _gain(nk(), (N_ODD, MLA_QK))
    inp['mla_k_gain'] = _gain(nk(), (N_ODD, MLA_QK))
    inp['mla_w_out'] = _w(nk(), (N_ODD, MLA_MIX, D_MODEL), MLA_MIX)
    inp['xmem_norm'] = _gain(nk(), (DEPTH, D_MODEL))
    inp['xmem_mem_norm'] = _gain(nk(), (DEPTH, D_MODEL))
    inp['xmem_wq'] = _w(nk(), (DEPTH, D_MODEL, D_MODEL), D_MODEL)
    inp['xmem_wkv'] = _w(nk(), (DEPTH, D_MODEL, 2 * D_MODEL), D_MODEL)
    inp['xmem_q_gain'] = _gain(nk(), (DEPTH, MEM_HEAD_DIM))
    inp['xmem_k_gain'] = _gain(nk(), (DEPTH, MEM_HEAD_DIM))
    inp['xmem_wo'] = _w(nk(), (DEPTH, D_MODEL, D_MODEL), D_MODEL)
    inp['ffn_post_norm'] = _gain(nk(), (DEPTH, D_MODEL))
    inp['ffn_post_w_gu'] = _w(nk(), (DEPTH, D_MODEL, 2 * D_FF_2), D_MODEL)
    inp['ffn_post_w_down'] = _w(nk(), (DEPTH, D_FF_2, D_MODEL), D_FF_2)
    return inp

def second_block(x, mem, positions,
              ffn_pre_norm, ffn_pre_w_gu, ffn_pre_w_down,
              mix_norm,
              sbg_w_in, sgu_ln_gain, sgu_ln_bias, sgu_w, sgu_b, sbg_w_out,
              mla_w_in, mla_q_lora_gain, mla_kv_lora_gain, mla_w_uq, mla_w_ukv,
              mla_q_gain, mla_k_gain, mla_w_out,
              xmem_norm, xmem_mem_norm, xmem_wq, xmem_wkv, xmem_q_gain, xmem_k_gain, xmem_wo,
              ffn_post_norm, ffn_post_w_gu, ffn_post_w_down):
    for layer in range(DEPTH):
        x = x + 0.5 * _swiglu(_rmsnorm(x, ffn_pre_norm[layer]),
                              ffn_pre_w_gu[layer], ffn_pre_w_down[layer])
        h = _rmsnorm(x, mix_norm[layer])
        if layer % 2 == 0:
            e = layer // 2
            x = x + _even_mixer(h, sbg_w_in[e], sgu_ln_gain[e], sgu_ln_bias[e],
                                sgu_w[e], sgu_b[e], sbg_w_out[e])
        else:
            o = layer // 2
            x = x + _mla_mixer(h, positions, mla_w_in[o], mla_q_lora_gain[o],
                               mla_kv_lora_gain[o], mla_w_uq[o], mla_w_ukv[o],
                               mla_q_gain[o], mla_k_gain[o], mla_w_out[o])
        x = x + _memory_cross_attention(_rmsnorm(x, xmem_norm[layer]),
                                        _rmsnorm(mem, xmem_mem_norm[layer]),
                                        xmem_wq[layer], xmem_wkv[layer],
                                        xmem_q_gain[layer], xmem_k_gain[layer], xmem_wo[layer])
        x = x + 0.5 * _swiglu(_rmsnorm(x, ffn_post_norm[layer]),
                              ffn_post_w_gu[layer], ffn_post_w_down[layer])
    return x


def setup_inputs(seed=0):
    out = dict(first_inputs(seed))
    for name, value in second_inputs(seed + 1).items():
        if name != "x":
            out[name + "_2"] = value
    return out


def reference(
    x, c, ctx, c_ctx, ada_w, ada_b, ab_w_in, ab_gate_b, na_q_norm, na_k_norm, na_rpb,
    ml_head_norm, ab_w_out, rw_mu, rw_w_rkv, rw_w0, rw_w1, rw_w2, rw_a0, rw_a1, rw_a2, rw_g1,
    rw_g2, rw_k_k, rw_k_a, rw_r_k, rw_lnx_w, rw_lnx_b, rw_w_o, mlp_w1, mlp_w2, mem_2,
    positions_2, ffn_pre_norm_2, ffn_pre_w_gu_2, ffn_pre_w_down_2, mix_norm_2, sbg_w_in_2,
    sgu_ln_gain_2, sgu_ln_bias_2, sgu_w_2, sgu_b_2, sbg_w_out_2, mla_w_in_2, mla_q_lora_gain_2,
    mla_kv_lora_gain_2, mla_w_uq_2, mla_w_ukv_2, mla_q_gain_2, mla_k_gain_2, mla_w_out_2,
    xmem_norm_2, xmem_mem_norm_2, xmem_wq_2, xmem_wkv_2, xmem_q_gain_2, xmem_k_gain_2,
    xmem_wo_2, ffn_post_norm_2, ffn_post_w_gu_2, ffn_post_w_down_2,
):
    x = first_block(
        x, c, ctx, c_ctx, ada_w, ada_b, ab_w_in, ab_gate_b, na_q_norm, na_k_norm, na_rpb,
        ml_head_norm, ab_w_out, rw_mu, rw_w_rkv, rw_w0, rw_w1, rw_w2, rw_a0, rw_a1, rw_a2,
        rw_g1, rw_g2, rw_k_k, rw_k_a, rw_r_k, rw_lnx_w, rw_lnx_b, rw_w_o, mlp_w1, mlp_w2,
    )
    return second_block(
        x, mem_2, positions_2, ffn_pre_norm_2, ffn_pre_w_gu_2, ffn_pre_w_down_2, mix_norm_2,
        sbg_w_in_2, sgu_ln_gain_2, sgu_ln_bias_2, sgu_w_2, sgu_b_2, sbg_w_out_2, mla_w_in_2,
        mla_q_lora_gain_2, mla_kv_lora_gain_2, mla_w_uq_2, mla_w_ukv_2, mla_q_gain_2,
        mla_k_gain_2, mla_w_out_2, xmem_norm_2, xmem_mem_norm_2, xmem_wq_2, xmem_wkv_2,
        xmem_q_gain_2, xmem_k_gain_2, xmem_wo_2, ffn_post_norm_2, ffn_post_w_gu_2,
        ffn_post_w_down_2,
    )


_drawn_inputs = setup_inputs


def setup_inputs(seed=0):
    import zlib

    import numpy as np

    out = dict(_drawn_inputs(seed))
    spreads = {}
    factors = {'na_q_norm': 8.0,
     'na_k_norm': 8.0,
     'na_rpb': 8.0,
     'ml_head_norm': 8.0,
     'rw_w1': 8.0,
     'rw_w2': 8.0,
     'rw_a0': 7.715,
     'rw_lnx_w': 6.427,
     'rw_lnx_b': 8.0,
     'ffn_pre_norm_2': 5.851,
     'mix_norm_2': 4.069,
     'sgu_ln_gain_2': 8.0,
     'sgu_ln_bias_2': 8.0,
     'mla_q_lora_gain_2': 8.0,
     'mla_kv_lora_gain_2': 8.0,
     'mla_q_gain_2': 8.0,
     'mla_k_gain_2': 8.0,
     'xmem_norm_2': 8.0,
     'xmem_mem_norm_2': 8.0,
     'xmem_q_gain_2': 8.0,
     'xmem_k_gain_2': 8.0,
     'ffn_post_norm_2': 7.003}
    for name, (base, spread) in spreads.items():
        noise = np.random.default_rng([zlib.crc32(name.encode()), seed]).standard_normal(out[name].shape)
        drawn = base * np.exp(spread * noise) if base else spread * noise
        out[name] = jnp.asarray(drawn.astype(out[name].dtype))
    for name, factor in factors.items():
        out[name] = (out[name] * factor).astype(out[name].dtype)
    return out
```

```python
from contextlib import ExitStack

import numpy as np

import concourse.bass as bass
from concourse import mybir

ALU = mybir.AluOpType
ACT = mybir.ActivationFunctionType
F32 = mybir.dt.float32
I32 = mybir.dt.int32
AX = mybir.AxisListType

P = 128
T = 256
D = 1024
KT = D // P
RING = 3
SLAB = 8 * 512
EPS = 1e-6
NEG = -1e30
GRID_W = 64
D_FF = 4096
D_FF2 = 2816
C = 64
NCH = 2 * T // C


def constant_blocks():
    p = np.arange(P)[:, None]
    f = np.arange(P)[None, :]
    s64, t64 = np.arange(P)[:, None] % C, np.arange(C)[None, :]
    col, key = np.arange(P)[:, None] % GRID_W, np.arange(GRID_W)[None, :]
    start = np.clip(col - 8, 0, GRID_W - 16)
    blocks = {
        "ident": p == f,
        "headones": (p // 64) == (f // 64),
        "causal_add": np.where(f <= p, 0.0, NEG),
        "strict": f < p,
        "strict_add": np.where(f < p, 0.0, NEG),
        "window_add": np.where((key >= start) & (key < start + 16), 0.0, NEG),
        "st_fwd": p <= f,
        "st_bwd": p >= f,
        "eye64": s64 == t64,
        "diag16": s64 // 16 == t64 // 16,
        "off32": (s64 // 32 == t64 // 32) & (s64 // 16 != t64 // 16),
        "off64": s64 // 32 != t64 // 32,
        "ones": np.ones((P, 64)),
        "chunk_start": np.broadcast_to(np.arange(512) % C != 0, (P, 512)),
    }
    one = np.ones((P, C))
    for z, (lt, le, gt) in enumerate([(s64 < t64, s64 <= t64, s64 > t64), (s64 > t64, s64 >= t64, s64 < t64)]):
        blocks[f"gram{z}"] = np.concatenate([lt, one, le, lt, one, le, gt], axis=1)
    sel = np.zeros((P, 4, P))
    for h in range(4):
        sel[h, h] = 1.0
    blocks["select4"] = sel.reshape(P, -1)
    tok = np.arange(T)
    inv = (10000.0 ** (-np.arange(32, dtype=np.float32) / 32)).astype(np.float32)
    ang = np.stack([(tok // GRID_W).astype(np.float32)[:, None] * inv,
                    (tok % GRID_W).astype(np.float32)[:, None] * inv], axis=1)
    for name, fn in (("cos2d", np.cos), ("sin2d", np.sin)):
        blocks[name] = fn(ang).reshape(2, P, 64).transpose(1, 0, 2).reshape(P, P)
    blocks["inv_freq"] = np.broadcast_to(
        (10000.0 ** (-np.arange(16, dtype=np.float32) / 16)).astype(np.float32), (P, 16))
    return {k: np.asarray(v, np.float32) for k, v in blocks.items()}


def constant_columns():
    at, out = 0, {}
    for name, b in constant_blocks().items():
        out[name] = (at, b.shape[1])
        at += b.shape[1]
    return out, at


ROWS_A, ROWS_B = {}, {}
for _rows, _list in ((ROWS_A, [("mu", 48), ("w0", 16), ("a0", 16), ("k_k", 8), ("k_a", 8), ("r_k", 8),
                               ("lnx_w", 8), ("lnx_b", 8), ("head_norm", 4), ("na_q", 1), ("na_k", 1)]),
                     (ROWS_B, [("ffn_pre", 16), ("mix", 16), ("xmem", 16), ("xmem_mem", 16), ("ffn_post", 16),
                               ("ln_gain", 4), ("ln_bias", 4), ("q_lora", 4), ("kv_lora", 2), ("xq", 4),
                               ("xk", 4), ("sgu_b", 8), ("c", 8), ("c_ctx", 8)])):
    _at = 0
    for _name, _n in _list:
        _rows[_name] = _at
        _at += _n
    _rows["rows"] = _at


class Side:

    def __init__(self, eng, name):
        self.eng, self.name, self.passed = eng, name, {}

    def wait_ge(self, sem, value):
        if self.passed.get(sem.name, 0) < value:
            self.eng.wait_ge(sem, value)
            self.passed[sem.name] = value


def bidir_dual_stack(nc, a, out, scratch_mod, scratch_rpb, noted):
    const_at, n_const = constant_columns()

    with ExitStack() as ctx:
        def sb(name, shape, dt=F32):
            return ctx.enter_context(nc.sbuf_tensor(name, shape, dt))

        sems, count, now, stages, own, tiles = {}, {}, {}, {}, {}, {}

        def sem(name):
            if name not in sems:
                sems[name] = ctx.enter_context(nc.semaphore(name))
            return sems[name]

        def stage(side, name):
            stages[side.name] = name

        def add(name, by, event):
            count[name] = count.get(name, 0) + by
            if event is not None:
                now[event] = (name, count[name])
            return sem(name)

        def up(side, event=None):
            name = f"{stages[side.name]}_by_{side.name}"
            own[side.name] = (add(name, 1, event), count[name])
            return own[side.name][0], 1

        def landing(event):
            return add("landed_" + str(event).replace(" ", "_"), 16, ("dma", event))

        def latest(side):
            return own[side.name]

        def when(event):
            if noted is None:
                return sem("uncounted"), 1
            name, value = noted[event]
            return sem(name), value

        def also(event, same):
            now[event] = now[same]

        def bank(b, tile):
            last, tiles[b] = tiles.get(b), tile
            return (sem("setup_by_pe"), 0) if last is None else when(("read", last))

        x = sb("x", [P, 2, D])
        cx = sb("cx", [P, 2, D])
        hT = sb("hT", [P, KT, 2 * T])
        ring = sb("ring", [P, RING, SLAB])
        sc = sb("sc", [P, 6, 512])
        sc2 = sb("sc2", [P, 3, 512])
        const = sb("const", [P, n_const])
        colA = sb("colA", [P, P])
        colB = sb("colB", [P, P])
        modcol = sb("modcol", [P, 2, 96])
        csil = sb("csil", [P, KT, 2])
        stat = sb("stat", [P, 256])
        half = sb("half", [P, 64])
        gbc = sb("gbc", [P, 192])
        epsc = sb("epsc", [P, 2])
        ARENA = 23588
        arena = sb("arena", [P, ARENA])
        psum = ctx.enter_context(nc.psum_tensor("psum", [P, 8, 512], F32))

        def cst(name, n=P):
            at, w = const_at[name]
            return const[0:n, at:at + w]

        def area(at, *shape):
            n = int(np.prod(shape))
            v = arena[:, at:at + n]
            if len(shape) == 1:
                return v
            names = "abcde"[:len(shape)]
            return v.rearrange(f"p ({' '.join(names)}) -> p {' '.join(names)}",
                               **{k: s for k, s in zip(names[1:], shape[1:])})

        ident = cst("ident")

        slabs = []

        def plan(name, w, nk, n0, nn, k0=0, at=0):
            src = w[k0 * P:(k0 + nk) * P, n0:n0 + nn].rearrange("(k p) n -> p k n", p=P)
            if slabs and slabs[-1][0] == name:
                slabs[-1][1].append((nk, at, nn, src))
            else:
                slabs.append((name, [(nk, at, nn, src)]))

        def plan_rows(name, w, nk_total, n_total):
            for n in range(0, n_total, 512):
                for k in range(0, nk_total, 8):
                    plan((name, n // 512, k // 8), w, min(8, nk_total - k), n, min(512, n_total - n), k)

        def plan_ffn(name, gu, down):
            for n in range(0, D_FF2, 256):
                plan((name + "_gu", n // 256, 0), gu, KT, n, 256)
                plan((name + "_gu", n // 256, 0), gu, KT, D_FF2 + n, 256, at=256)
            plan_rows(name + "_down", down, D_FF2 // P, D)

        for layer in range(2):
            plan_rows(f"ada{layer}", a["ada_w"][layer], KT, 6 * D)
        plan_rows("ab_in", a["ab_w_in"][0], KT, 3600)
        plan_rows("ab_out", a["ab_w_out"][0], KT, D)
        plan_rows("mlp0_up", a["mlp_w1"][0], KT, D_FF)
        plan_rows("mlp0_down", a["mlp_w2"][0], D_FF // P, D)
        for w in ("w1", "a1"):
            for z in range(2):
                plan((w, 0, 0), a["rw_" + w][0, z], KT, 0, 64, at=64 * z)
        plan_rows("g1", a["rw_g1"][0], KT, 160)
        for i, w in enumerate("rkv"):
            plan_rows("rw_" + w, a["rw_w_rkv"][0, i], KT, D)
        plan_rows("rw_o", a["rw_w_o"][0], KT, D)
        plan_rows("mlp1_up", a["mlp_w1"][1], KT, D_FF)
        plan_rows("mlp1_down", a["mlp_w2"][1], D_FF // P, D)
        for layer in range(2):
            plan_ffn(f"pre{layer}", a["ffn_pre_w_gu_2"][layer], a["ffn_pre_w_down_2"][layer])
            if layer == 0:
                plan_rows("sbg_in", a["sbg_w_in_2"][0], KT, 2560)
                plan_rows("sbg_out", a["sbg_w_out_2"][0], KT, D)
            else:
                plan_rows("mla_in", a["mla_w_in_2"][0], KT, 800)
                plan_rows("mla_uq", a["mla_w_uq_2"][0], 4, 1536)
                plan_rows("mla_ukv", a["mla_w_ukv_2"][0], 2, 2048)
                plan_rows("mla_out", a["mla_w_out_2"][0], KT, D)
            plan_rows(f"xkv{layer}", a["xmem_wkv_2"][layer], KT, 2 * D)
            plan_rows(f"xq{layer}", a["xmem_wq_2"][layer], KT, D)
            plan_rows(f"xo{layer}", a["xmem_wo_2"][layer], KT, D)
            plan_ffn(f"post{layer}", a["ffn_post_w_gu_2"][layer], a["ffn_post_w_down_2"][layer])
        slab_at = {name: i for i, (name, _) in enumerate(slabs)}

        def slab(pe, name):
            i = slab_at[name]
            pe.wait_ge(*when(("slab", i)))
            return ring[:, i % RING, :].rearrange("p (k n) -> p k n", k=8)

        norms = []

        def norm_stat(who, key):
            if key not in norms:
                norms.append(key)
            i = norms.index(key)
            if who is not None and i >= 2:
                who.wait_ge(*when((norms[i - 2], "normed", 1)))
            return stat[:, 208 + 8 * (i % 2):216 + 8 * (i % 2)]

        def norm_act(act, key, src, needs=()):
            stage(act, "norm")
            for event in needs:
                act.wait_ge(*when(event))
            s = norm_stat(act, key)
            for t in range(2):
                nc.scalar.activation(sc[:, 4:6, :].rearrange("p a b -> p (a b)"), src[:, t, :], ACT.Square,
                                            accum_out=s[:, t:t + 1]).then_inc(*up(act, (key, "squares", t)))
                act.wait_ge(*latest(act))

        def norm_pool(pool, key):
            stage(pool, "norm")
            pool.wait_ge(*when((key, "squares", 1)))
            s = norm_stat(pool, key)
            nc.gpsimd.tensor_scalar(s[:, 2:4], s[:, 0:2], 1.0 / D, EPS, ALU.mult, ALU.add).then_inc(*up(pool))
            pool.wait_ge(*latest(pool))
            nc.gpsimd.tensor_tensor(s[:, 4:6], s[:, 2:4], half[:, 0:2], ALU.pow).then_inc(*up(pool, (key, "rstd")))
            pool.wait_ge(*latest(pool))

        def norm_dve(dve, key, src, off, scale, shift=None, plus1=False):
            stage(dve, "norm")
            dve.wait_ge(*when((key, "rstd")))
            s = norm_stat(None, key)
            for t in range(2):
                xn = sc[:, 2 * t:2 * t + 2, :].rearrange("p a b -> p (a b)")
                nc.vector.tensor_scalar(xn, src[:, t, :], s[:, 4 + t:5 + t], None, ALU.mult).then_inc(*up(dve, (key, "normed", t)))
                dve.wait_ge(*latest(dve))
            if plus1:
                nc.vector.tensor_scalar(stat[:, 8:16], scale, 1.0, None, ALU.add).then_inc(*up(dve, (key, "scale")))
                dve.wait_ge(*latest(dve))
                scale = stat[:, 8:16]
            for b in range(4):
                dve.wait_ge(*when((key, "turned", b)))
                for k in (2 * b, 2 * b + 1):
                    src_ = psum[:, b + 4, 256 * (k % 2):256 * (k % 2) + 256]
                    dst = hT[:, k, off:off + 256]
                    if shift is None:
                        ins = nc.vector.tensor_scalar(dst, src_, scale[:, k:k + 1], None, ALU.mult)
                    else:
                        ins = nc.vector.tensor_scalar(dst, src_, scale[:, k:k + 1], shift[:, k:k + 1],
                                                      ALU.mult, ALU.add)
                    ins.then_inc(*up(dve, ("read", (key, b)) if k % 2 else None))

        def norm_pe(pe, key):
            stage(pe, "norm")
            norm_stat(None, key)
            for b in range(4):
                pe.wait_ge(*bank(b + 4, (key, b)))
                for k in (2 * b, 2 * b + 1):
                    for t in range(2):
                        pe.wait_ge(*when((key, "normed", t)))
                        at = 256 * (k % 2) + 128 * t
                        ins = nc.tensor.transpose(psum[:, b + 4, at:at + 128],
                                                  sc[:, 2 * t + k // 4, 128 * (k % 4):128 * (k % 4) + 128], ident)
                ins.then_inc(*up(pe, (key, "turned", b)))

        def rows_pe(pe, name, lhs, tiles, kt, n_total, banks, needs=(), only=None):
            stage(pe, "rows")
            for event in needs:
                pe.wait_ge(*when(event))
            i = 0
            for n in range(0, n_total, 512):
                if only is not None and n // 512 not in only:
                    continue
                w = min(512, n_total - n)
                where = [banks[(i + t) % len(banks)] for t in range(len(tiles))]
                i += len(tiles)
                for k0 in range(0, kt, 8):
                    s = slab(pe, (name, n // 512, k0 // 8))
                    nk = min(8, kt - k0)
                    for t, tile in enumerate(tiles):
                        if k0 == 0:
                            pe.wait_ge(*bank(where[t], (name, n // 512, tile)))
                        for k in range(nk):
                            ins = nc.tensor.matmul(psum[:, where[t], 0:w], lhs(k0 + k, tile), s[:, k, 0:w],
                                                   start=(k0 + k == 0), stop=(k0 + k == kt - 1))
                        if k0 + nk == kt and t < len(tiles) - 1:
                            ins.then_inc(*up(pe, (name, "full", n // 512, tile)))
                    if k0 + nk == kt:
                        ins.then_inc(*up(pe, (name, "full", n // 512, tiles[-1])))
                        also(("used", slab_at[(name, n // 512, k0 // 8)]), (name, "full", n // 512, tiles[-1]))
                    else:
                        ins.then_inc(*up(pe, ("used", slab_at[(name, n // 512, k0 // 8)])))

        def rows_bank(name, n, i, tiles, banks):
            return banks[(n * len(tiles) + i) % len(banks)]

        HB = 12288
        modrow = area(0, 2, 6 * D)
        pad = arena[0:56, 23000:23127]
        nab = area(18448, 2, 4, 8, 64)

        def setup_sp(sp):
            nc.sync.dma_start(const[:, :], a["const"])\
                .then_inc(landing("const"), 16)
            nc.sync.dma_start(sc[0:ROWS_A["rows"], 0, 0:P], a["vec_a"])\
                .then_inc(landing("vec_a"), 16)
            nc.sync.dma_start(sc[0:ROWS_B["rows"], 1, 0:P], a["vec_b"])\
                .then_inc(landing("vec_b"), 16)

        def setup_pool(pool):
            nc.gpsimd.memset(half[:, :], -0.5).then_inc(*up(pool))
            pool.wait_ge(*latest(pool))
            nc.gpsimd.memset(pad, 0.0).then_inc(*up(pool, "pad zero"))
            pool.wait_ge(*latest(pool))
            nc.gpsimd.memset(epsc[:, 0:1], EPS).then_inc(*up(pool))
            pool.wait_ge(*latest(pool))
            pool.wait_ge(*when("pad zero"))
            nc.gpsimd.dma_start(pad.rearrange("p (a c) -> p a c", a=1)[:, :, 48:79], bass.AP(tensor=a["na_rpb"].tensor, offset=4 * 31,
                              ap=[[31, 7], [15 * 31, 8], [1, 31]]))\
                .then_inc(landing("rpb"), 16)
            nc.gpsimd.dma_start(modrow[0:2, :, :], a["ada_b"].partition_broadcast(2))\
                .then_inc(landing("ada_b"), 16)
            nc.gpsimd.dma_start(x[:, :, :], a["x"][0].rearrange("(t p) d -> p t d", p=P))\
                .then_inc(landing("x"), 16)
            nc.gpsimd.dma_start(cx[:, :, :], a["ctx"][0].rearrange("(t p) d -> p t d", p=P))\
                .then_inc(landing("ctx"), 16)
            nc.gpsimd.dma_start(gbc[:, 0:96], a["mla_q_gain_2"][0].partition_broadcast(P))\
                .then_inc(landing("q_gain"), 16)
            nc.gpsimd.dma_start(gbc[:, 96:192], a["mla_k_gain_2"][0].partition_broadcast(P))\
                .then_inc(landing("k_gain"), 16)
            nc.gpsimd.dma_start(stat[0:4, 200:204], a["ab_gate_b"][0].rearrange("(a b) -> b a", b=4), allow_slow_non_contiguous=True)\
                .then_inc(landing("gate_b"), 16)
            pool.wait_ge(*when(("dma", "rpb")))
            nc.gpsimd.dma_start(scratch_rpb, pad.unsqueeze(1).to_broadcast([56, 64, 127]))\
                .then_inc(landing("rpb rows"), 16)
            pool.wait_ge(*when(("dma", "rpb rows")))
            for r in range(4):
                qt, r2 = divmod(r, 2)
                nc.gpsimd.dma_start(nab[64 * r2:64 * r2 + 64, qt, :, :, :].rearrange("p a b c -> p (a b) c"), bass.AP(tensor=scratch_rpb.tensor, offset=(3 - r) * 8 * 64 * 127 + 63,
                                  ap=[[126, 64], [64 * 127, 32], [1, 64]]))\
                    .then_inc(landing("bias"), 16)
            pool.wait_ge(*when(("dma", "bias")))
            pool.wait_ge(*when(("dma", "const")))
            nc.gpsimd.tensor_tensor(
                nab.rearrange("p a b c d -> p (a b c) d"),
                nab.rearrange("p a b c d -> p (a b c) d"),
                cst("window_add").unsqueeze(1).to_broadcast([P, 64, 64]), ALU.add).then_inc(*up(pool, "bias ready"))
            pool.wait_ge(*latest(pool))

        def setup_pe(pe):
            pe.wait_ge(*when(("dma", "const")))
            for i, (rows, ev) in enumerate(((ROWS_A, "vec_a"), (ROWS_B, "vec_b"))):
                pe.wait_ge(*when(("dma", ev)))
                pe.wait_ge(*bank(i, ("vec", i)))
                n = rows["rows"]
                nc.tensor.transpose(psum[:, i, 0:n], sc[0:n, i, 0:P], ident[0:n, 0:n]).then_inc(*up(pe, ("vec", "turned", i)))

        def setup_dve(dve):
            for i, (col, rows) in enumerate(((colA, ROWS_A), (colB, ROWS_B))):
                dve.wait_ge(*when(("vec", "turned", i)))
                n = rows["rows"]
                nc.vector.tensor_copy(col[:, 0:n], psum[:, i, 0:n]).then_inc(*up(dve, ("read", ("vec", i))))
                dve.wait_ge(*latest(dve))

        def setup_act(act):
            act.wait_ge(*when(("read", ("vec", 1))))
            for i, name in enumerate(("c", "c_ctx")):
                nc.scalar.activation(csil[:, :, i], colB[:, ROWS_B[name]:ROWS_B[name] + 8], ACT.Silu).then_inc(*up(act, "silu c"))
                act.wait_ge(*latest(act))

        def ada_pe(pe):
            stage(pe, "ada")
            pe.wait_ge(*when("silu c"))
            for i in range(24):
                s = slab(pe, (f"ada{i // 12}", i % 12, 0))
                pe.wait_ge(*bank(i % 4, ("ada", i)))
                for k in range(KT):
                    ins = nc.tensor.matmul(psum[0:2, i % 4, :], csil[:, k, :], s[:, k, :], start=(k == 0), stop=(k == 7))
                ins.then_inc(*up(pe, ("ada", "full", i)))
                also(("used", slab_at[(f"ada{i // 12}", i % 12, 0)]), ("ada", "full", i))
            for layer in range(2):
                pe.wait_ge(*when(("dma", f"mod back {layer}")))
                pe.wait_ge(*bank(layer, ("mod", layer)))
                nc.tensor.transpose(psum[:, layer, 0:96], sc[0:96, layer, 0:P], ident[0:96, 0:96]).then_inc(*up(pe, ("mod", "turned", layer)))

        def ada_dve(dve):
            stage(dve, "ada")
            dve.wait_ge(*when(("dma", "ada_b")))
            for i in range(24):
                dve.wait_ge(*when(("ada", "full", i)))
                row = modrow[0:2, i // 12, 512 * (i % 12):512 * (i % 12) + 512]
                nc.vector.tensor_tensor(row, psum[0:2, i % 4, :], row, ALU.add).then_inc(*up(dve, ("read", ("ada", i))))
            for layer in range(2):
                dve.wait_ge(*when(("mod", "turned", layer)))
                nc.vector.tensor_copy(modcol[:, layer, :], psum[:, layer, 0:96]).then_inc(*up(dve, ("read", ("mod", layer))))
                dve.wait_ge(*latest(dve))

        def ada_pool(pool):
            stage(pool, "ada")
            for layer in range(2):
                pool.wait_ge(*when(("read", ("ada", 12 * layer + 11))))
                nc.gpsimd.dma_start(scratch_mod[layer], modrow[0:2, layer, :])\
                    .then_inc(landing(f"mod {layer}"), 16)
                pool.wait_ge(*when(("dma", f"mod {layer}")))
                pool.wait_ge(*when(("read", ("vec", 1))))
                nc.gpsimd.dma_start(sc[0:96, layer, 0:P], scratch_mod[layer].rearrange("v (r p) -> (v r) p", p=P))\
                    .then_inc(landing(f"mod back {layer}"), 16)

        def mcol(layer, vec, kind):
            at = 48 * vec + 8 * kind
            return modcol[:, layer, at:at + 8]

        def gate_load(pool, tag, dst, layer, vec, kind):
            nc.gpsimd.dma_start(dst, scratch_mod[layer, vec, kind * D:(kind + 1) * D].partition_broadcast(P))\
                .then_inc(landing(tag), 16)

        qa = area(0, 4, 512)
        ka = area(2048, 4, 512)
        va = area(4096, 4, 512)
        qb = area(6144, 4, 512)
        kb = area(8192, 4, 512)
        vb = area(10240, 4, 4, 129)
        so = area(12304, 4, 512)
        qaT = area(14352, 4, 512)
        kaT = area(16400, 4, 512)
        gates_a = (area(10240, 1024), area(11264, 1024))
        AB = ("qa", "ka", "va", "qb", "kb", "vb", "so")
        rowg = ("i_f", "f_f", "i_b", "f_b")

        def ab_in_pe(pe):
            for event in [("read", (k, b)) for k in ("L0a", "C0a") for b in range(4)]:
                pe.wait_ge(*when(event))
            rows_pe(pe, "ab_in", lambda k, t: hT[:, k, P * t:P * t + P], range(4), KT, 3584, [0, 1, 2, 3])
            stage(pe, "ab")
            s = slab(pe, ("ab_in", 7, 0))
            for g in range(4):
                pe.wait_ge(*bank(4 + g, ("gates", g)))
                for k in range(KT):
                    ins = nc.tensor.matmul(psum[0:4, 4 + g, :], s[:, k, 4 * g:4 * g + 4], hT[:, k, :],
                                           start=(k == 0), stop=(k == 7))
                ins.then_inc(*up(pe, ("gates", "full", g)))
            also(("used", slab_at[("ab_in", 7, 0)]), ("gates", "full", 3))

        def ab_in_act(act):
            stage(act, "ab_in")
            act.wait_ge(*when(("dma", "mod 1")))
            for n, name in enumerate(AB):
                for t in range(4):
                    act.wait_ge(*when(("ab_in", "full", n, t)))
                    src = psum[:, t, :]
                    event = ("read", ("ab_in", n, t))
                    if name == "so":
                        ins = nc.scalar.activation(so[:, t, :], src, ACT.Sigmoid)
                    elif name == "kb":
                        ins = nc.scalar.activation(kb[:, t, :], src, ACT.Copy, scale=128 ** -0.5)
                    elif name == "vb":
                        ins = nc.scalar.copy(vb[:, t, :, 0:128], src.rearrange("p (h d) -> p h d", h=4))
                    else:
                        ins = nc.scalar.copy({"qa": qa, "ka": ka, "va": va, "qb": qb}[name][:, t, :], src)
                    ins.then_inc(*up(act, event))

        def qk_norm_dve(dve):
            stage(dve, "qk")
            for i in range(8):
                y = (qa, ka)[i % 2][:, i // 2, :].rearrange("p (h d) -> p h d", h=8)
                sq = sc[:, i % 2, :].rearrange("p (h d) -> p h d", h=8)
                dve.wait_ge(*when(("read", ("ab_in", i % 2, i // 2))))
                if i < 2:
                    dve.wait_ge(*when(("C0a", "turned", 3)))
                nc.vector.tensor_tensor(sq, y, y, ALU.mult).then_inc(*up(dve))
                dve.wait_ge(*latest(dve))
                nc.vector.tensor_reduce(stat[:, 16 + 8 * i:24 + 8 * i], sq, AX.X, ALU.add).then_inc(*up(dve, ("qk", "squares", i)))
                dve.wait_ge(*latest(dve))
            for i in range(8):
                y = (qa, ka)[i % 2][:, i // 2, :].rearrange("p (h d) -> p h d", h=8)
                dve.wait_ge(*when(("qk", "rstd", i)))
                nc.vector.tensor_tensor(y, y, stat[:, 16 + 8 * i:24 + 8 * i].unsqueeze(2).to_broadcast([P, 8, 64]),
                                               ALU.mult).then_inc(*up(dve, ("qk", "normed", i)))
                dve.wait_ge(*latest(dve))
                if i >= 2:
                    qk_turn_out(dve, i - 2)
            qk_turn_out(dve, 6)
            qk_turn_out(dve, 7)

        def qk_turn_out(dve, i):
            dve.wait_ge(*when(("qk", "turned", i)))
            at = ROWS_A["na_q"] + i % 2
            nc.vector.tensor_scalar((qaT, kaT)[i % 2][:, :, P * (i // 2):P * (i // 2) + P],
                                           psum[:, 4 + i % 4, :].rearrange("p (f t) -> p f t", f=4),
                                           colA[:, at:at + 1], None, ALU.mult).then_inc(*up(dve, ("read", ("qkT", i))))
            dve.wait_ge(*latest(dve))

        def qk_norm_pool(pool):
            stage(pool, "qk")
            for i in range(8):
                pool.wait_ge(*when(("qk", "squares", i)))
                r = stat[:, 16 + 8 * i:24 + 8 * i]
                nc.gpsimd.tensor_scalar(r, r, 1.0 / 64, EPS, ALU.mult, ALU.add).then_inc(*up(pool))
                pool.wait_ge(*latest(pool))
                nc.gpsimd.tensor_tensor(r, r, half[:, 0:8], ALU.pow).then_inc(*up(pool, ("qk", "rstd", i)))
                pool.wait_ge(*latest(pool))

        def qk_norm_pe(pe):
            stage(pe, "qk")
            for i in range(8):
                pe.wait_ge(*when(("qk", "normed", i)))
                pe.wait_ge(*bank(4 + i % 4, ("qkT", i)))
                for f in range(4):
                    ins = nc.tensor.transpose(psum[:, 4 + i % 4, P * f:P * f + P],
                                              (qa, ka)[i % 2][:, i // 2, P * f:P * f + P], ident)
                ins.then_inc(*up(pe, ("qk", "turned", i)))

        def unit_tick(n, *steps):
            for i in range(n + len(steps) - 1):
                for j, step in enumerate(steps):
                    if 0 <= i - j < n:
                        yield step, i - j

        def att_pe(pe, key, units, needs=()):
            stage(pe, "att")
            for event in needs:
                pe.wait_ge(*when(event))

            def scores(i):
                u = units[i]
                pe.wait_ge(*bank(i % 2, (key, "s", i)))
                n = len(u["qk"])
                for j, (l, r) in enumerate(u["qk"]):
                    ins = nc.tensor.matmul(psum[:, i % 2, 0:u["keys"]], l, r, start=(j == 0), stop=(j == n - 1))
                ins.then_inc(*up(pe, (key, "scores", i)))

            def turn(i):
                u = units[i]
                pe.wait_ge(*when((key, "probs", i)))
                pe.wait_ge(*bank(2 + i % 2, (key, "t", i)))
                for k in range(u["keys"] // P):
                    ins = nc.tensor.transpose(psum[:, 2 + i % 2, P * k:P * k + P], sc2[:, i % 2, P * k:P * k + P], ident)
                ins.then_inc(*up(pe, (key, "turned", i)))

            def values(i):
                u = units[i]
                pe.wait_ge(*when((key, "probsT", i)))
                pe.wait_ge(*bank(4 + i % 2, (key, "o", i)))
                nk = u["keys"] // P
                for j, (vs, part) in enumerate(u["v"]):
                    for k in range(nk):
                        v = vs(k)
                        w = v.shape[-1]
                        ins = nc.tensor.matmul(psum[part:part + w, 4 + i % 2, P * j:P * j + P], v,
                                               sc[:, 4 + i % 2, P * k:P * k + P], start=(k == 0), stop=(k == nk - 1))
                ins.then_inc(*up(pe, (key, "out", i)))

            for step, i in unit_tick(len(units), scores, turn, values):
                step(i)

        def att_dve(dve, key, units, scale, probs=True, after_first=()):
            stage(dve, "att")

            def maximum(i):
                u = units[i]
                n, s, b = u["keys"], sc[:, i % 2, :], psum[:, i % 2, :]
                dve.wait_ge(*when((key, "scores", i)))
                if i == 0:
                    for event in after_first:
                        dve.wait_ge(*when(event))
                m = stat[:, 96 + 2 * (i % 4):97 + 2 * (i % 4)]
                nm = stat[:, 97 + 2 * (i % 4):98 + 2 * (i % 4)]
                if u["bias"] is None:
                    nc.vector.tensor_reduce(m, b[:, 0:n], AX.X, ALU.max, negate=True).then_inc(*up(dve))
                    dve.wait_ge(*latest(dve))
                    nc.vector.tensor_scalar(nm, m, scale, None, ALU.mult).then_inc(*up(dve, (key, "max", i)))
                    dve.wait_ge(*latest(dve))
                else:
                    at = 0
                    if i >= 2:
                        dve.wait_ge(*when((key, "exp", i - 2)))
                    for w, bias in u["bias"]:
                        if bias is None:
                            ins = nc.vector.tensor_scalar(s[:, at:at + w], b[:, at:at + w], scale, None, ALU.mult)
                        else:
                            o, y = s[:, at:at + w], b[:, at:at + w]
                            if len(bias.shape) == 3:
                                o, y = (v.rearrange("p (a b) -> p a b", b=bias.shape[2]) for v in (o, y))
                            ins = nc.vector.scalar_tensor_tensor(o, y, scale, bias, ALU.mult, ALU.add)
                        at += w
                        ins.then_inc(*up(dve, ("read", (key, "s", i)) if at == n else None))
                        dve.wait_ge(*latest(dve))
                    nc.vector.tensor_reduce(nm, s[:, 0:n], AX.X, ALU.max, negate=True).then_inc(*up(dve, (key, "max", i)))
                    dve.wait_ge(*latest(dve))

            def normalise(i):
                u = units[i]
                n = u["keys"]
                dve.wait_ge(*when((key, "exp", i)))
                rs, ri = stat[:, 104 + i % 4:105 + i % 4], stat[:, 108 + i % 4:109 + i % 4]
                nc.vector.reciprocal(ri, rs).then_inc(*up(dve))
                dve.wait_ge(*latest(dve))
                if i >= 2:
                    dve.wait_ge(*when((key, "turned", i - 2)))
                nc.vector.tensor_scalar(sc2[:, i % 2, 0:n], sc[:, 2 + i % 2, 0:n], ri, None, ALU.mult).then_inc(*up(dve, (key, "probs", i)))
                dve.wait_ge(*latest(dve))

            for step, i in unit_tick(len(units), maximum, normalise):
                step(i)

        def att_act(act, key, units, scale, needs=()):
            stage(act, "att")
            for event in needs:
                act.wait_ge(*when(event))

            def exponent(i):
                u = units[i]
                n = u["keys"]
                act.wait_ge(*when((key, "max", i)))
                nm = stat[:, 97 + 2 * (i % 4):98 + 2 * (i % 4)]
                if i >= 2:
                    act.wait_ge(*when((key, "probs", i - 2)))
                src = psum[:, i % 2, 0:n] if u["bias"] is None else sc[:, i % 2, 0:n]
                nc.scalar.activation(sc[:, 2 + i % 2, 0:n], src, ACT.Exp, bias=nm,
                                            scale=scale if u["bias"] is None else 1.0,
                                            accum_out=stat[:, 104 + i % 4:105 + i % 4]).then_inc(*up(act, (key, "exp", i)))
                if u["bias"] is None:
                    also(("read", (key, "s", i)), (key, "exp", i))

            for step, i in unit_tick(len(units), exponent, lambda i: att_probsT(act, key, units, i),
                                     lambda i: att_out(act, key, units, i)):
                step(i)

        def att_probsT(act, key, units, i):
            n = units[i]["keys"]
            act.wait_ge(*when((key, "turned", i)))
            if i >= 2:
                act.wait_ge(*when((key, "out", i - 2)))
            nc.scalar.copy(sc[:, 4 + i % 2, 0:n], psum[:, 2 + i % 2, 0:n]).then_inc(*up(act, (key, "probsT", i)))
            also(("read", (key, "t", i)), (key, "probsT", i))

        def att_out(act, key, units, i):
            u = units[i]
            act.wait_ge(*when((key, "out", i)))
            for j, ((vs, part), dst) in enumerate(zip(u["v"], u["dst"])):
                w = dst.shape[0]
                nc.scalar.copy(dst, psum[part:part + w, 4 + i % 2, P * j:P * j + P]).then_inc(*up(act, ("read", (key, "o", i)) if j == len(u["v"]) - 1 else None))

        def head_rows(h):
            return slice(64 * (h % 2), 64 * (h % 2) + 64)

        def na_units():
            us = []
            for h in range(8):
                for qt in range(2):
                    r, f = head_rows(h), h // 2
                    us.append(dict(keys=512, qk=[(qaT[r, f, P * qt:P * qt + P], kaT[r, f, :])],
                                   bias=[(256, nab[:, qt, :, h, :]), (256, None)],
                                   v=[(lambda k, h=h: va[:, k, 64 * h:64 * h + 64], r.start)],
                                   dst=[hT[r, f, P * qt:P * qt + P]]))
            return us

        def ctx_units():
            us = []
            for h in range(8):
                for qt in range(2):
                    r, f = head_rows(h), h // 2
                    us.append(dict(keys=256, qk=[(qaT[r, f, 256 + P * qt:256 + P * qt + P], kaT[r, f, 256:512])],
                                   bias=None, v=[(lambda k, h=h: va[:, 2 + k, 64 * h:64 * h + 64], r.start)],
                                   dst=[hT[r, f, 256 + P * qt:256 + P * qt + P]]))
            return us

        na, cxa = na_units(), ctx_units()

        R0 = 14352
        gi = area(R0, 2, 512)
        gl = area(R0 + 1024, 2, 512)
        gb = area(R0 + 2048, 2, 512)
        gm = area(R0 + 3072, 2, 512)
        gw = area(R0 + 4096, 2, 512)
        gv = area(R0 + 5120, 2, 512)
        ge = area(R0 + 6144, 2, 512)
        mlD = area(R0 + 7168, 2, 512)
        capped = [v[p:p + 4] for v in (area(22544, 512), sc2[:, 2, :]) for p in (0, 32)]
        mst = stat[:, 112:128].rearrange("p (z s) -> p z s", z=2)
        qbT = area(0, 4, 512)
        kbT = area(2048, 4, 512)
        mlc = sc2[:, 2, 0:128].rearrange("p (q z t h) -> p q z t h", q=4, z=2, t=4)
        dec = sc2[:, 2, 128:160].rearrange("p (h z t) -> p h z t", h=4, z=2)
        hs = area(4096, 4, 4, 128)
        mlW = sc[:, 0:2, :]
        mlK = sc[:, 2:4, :]
        mlX = sc[:, 4, :]
        mlC = sc2[:, 0:2, 0:129]
        mlY = sc2[:, 0:2, 256:385]
        rope_t = sc2
        ORDER = ((2, 3, 0, 1), (3, 2, 1, 0))

        def gates_act(act):
            stage(act, "gates")
            act.wait_ge(*when("gatecol"))
            act.wait_ge(*when(("dma", "rpb rows")))
            for g in range(4):
                act.wait_ge(*when(("gates", "full", g)))
                nc.scalar.activation(capped[g], psum[0:4, 4 + g, :], ACT.Tanh, bias=stat[0:4, 204 + g:205 + g],
                                            scale=1 / 15.0).then_inc(*up(act, ("read", ("gates", g))))
                act.wait_ge(*latest(act))

        def softplus_act(act):
            stage(act, "softplus")
            act.wait_ge(*when(("na", "probs", 15)))
            act.wait_ge(*when(("cx", "probs", 15)))
            act.wait_ge(*when(("cx", "out", 15)))
            for z in range(2):
                nc.scalar.activation(gl[0:4, z, :], capped[2 * z + 1], ACT.Exp, scale=-15.0).then_inc(*up(act))
                act.wait_ge(*latest(act))
            nc.scalar.activation(gl[0:4], gl[0:4], ACT.Ln, bias=1.0).then_inc(*up(act, "softplus f"))
            act.wait_ge(*latest(act))

        def gates_dve(dve):
            stage(dve, "gates")
            dve.wait_ge(*when(("dma", "gate_b")))
            nc.vector.tensor_scalar(stat[0:4, 204:208], stat[0:4, 200:204], 1 / 15.0, None, ALU.mult).then_inc(*up(dve, "gatecol"))
            dve.wait_ge(*latest(dve))

        def scan_view(a_, z):
            return a_ if z == 0 else a_[:, ::-1]

        def decay_dve(dve):
            stage(dve, "decay")
            dve.wait_ge(*when("softplus f"))
            nc.vector.memset(mlD[0:4, 0, 0:128], 0.0).then_inc(*up(dve))
            dve.wait_ge(*latest(dve))
            nc.vector.memset(mst[0:4, :, 0:1], 0.0).then_inc(*up(dve))
            dve.wait_ge(*latest(dve))
            for z in range(2):
                for t in range(4):
                    s = slice(P * t, P * t + P)
                    nc.vector.tensor_tensor_scan(scan_view(gb[0:4, z, s], z), mlD[0:4, 0, 0:128],
                                                        scan_view(gl[0:4, z, s], z), 0.0, ALU.add, ALU.subtract).then_inc(*up(dve))
                    dve.wait_ge(*latest(dve))
            for z in range(2):
                nc.vector.scalar_tensor_tensor(gi[0:4, z, :], capped[2 * z], 15.0, gb[0:4, z, :],
                                                      ALU.mult, ALU.subtract).then_inc(*up(dve))
                dve.wait_ge(*latest(dve))
            for j in range(4):
                for z in range(2):
                    t = ORDER[z][j]
                    s = slice(P * t, P * t + P)
                    last = P * t + (127 if z == 0 else 0)
                    g = scan_view(gi[0:4, z, s], z)
                    m0 = mst[0:4, z, j:j + 1]
                    nc.vector.tensor_tensor_scan(scan_view(gm[0:4, z, s], z), g, g, m0, ALU.max, ALU.max).then_inc(*up(dve))
                    dve.wait_ge(*latest(dve))
                    nc.vector.tensor_tensor(mst[0:4, z, j + 1:j + 2], gb[0:4, z, last:last + 1],
                                                   gm[0:4, z, last:last + 1], ALU.add).then_inc(*up(dve))
                    dve.wait_ge(*latest(dve))
                    nc.vector.tensor_scalar(gw[0:4, z, s], gi[0:4, z, s], gm[0:4, z, last:last + 1], None,
                                                   ALU.subtract).then_inc(*up(dve))
                    dve.wait_ge(*latest(dve))
                    nc.vector.tensor_scalar(gv[0:4, z, s], gm[0:4, z, s], m0, None, ALU.subtract).then_inc(*up(dve))
                    dve.wait_ge(*latest(dve))
            nc.vector.tensor_tensor(ge[0:4], gb[0:4], gm[0:4], ALU.add).then_inc(*up(dve, "exponents"))
            dve.wait_ge(*latest(dve))

        def decay_act(act):
            stage(act, "decay")
            act.wait_ge(*when("exponents"))
            nc.scalar.activation(gw[0:4], gw[0:4], ACT.Exp).then_inc(*up(act))
            act.wait_ge(*latest(act))
            nc.scalar.activation(gv[0:4], gv[0:4], ACT.Exp, scale=-1.0).then_inc(*up(act))
            act.wait_ge(*latest(act))
            nc.scalar.activation(ge[0:4], ge[0:4], ACT.Exp, scale=-1.0).then_inc(*up(act, "gate rows"))
            act.wait_ge(*latest(act))

        def decay_pe(pe):
            stage(pe, "decay")
            pe.wait_ge(*when("gate rows"))
            pe.wait_ge(*bank(0, "gate columns"))
            for q, src in enumerate((gi, gw, gv, ge)):
                for z in range(2):
                    for t in range(4):
                        at = 32 * q + 16 * z + 4 * t
                        nc.tensor.transpose(psum[:, 0, at:at + 4], src[0:4, z, P * t:P * t + P], ident[0:4, 0:4])
            sel = cst("select4").rearrange("p (h m) -> p h m", h=4)
            for h in range(4):
                for z in range(2):
                    rows = gv[0:4, z, :].rearrange("p (t s) -> p t s", s=P)[:, :, (127 if z == 0 else 0)]
                    at = 128 + 8 * h + 4 * z
                    ins = nc.tensor.matmul(psum[:, 0, at:at + 4], sel[0:4, h, :], rows, start=True, stop=True)
            ins.then_inc(*up(pe, "gate columns full"))

        def decay_out_dve(dve):
            dve.wait_ge(*when("gate columns full"))
            nc.vector.tensor_copy(sc2[:, 2, 0:160], psum[:, 0, 0:160]).then_inc(*up(dve, ("read", "gate columns")))
            dve.wait_ge(*latest(dve))

        def rope_dve(dve):
            stage(dve, "rope")
            for event in [("read", ("ab_in", n, t)) for n in (3, 4) for t in range(2)]:
                dve.wait_ge(*when(event))
            dve.wait_ge(*when(("na", "turned", 15)))
            dve.wait_ge(*when(("cx", "turned", 15)))
            dve.wait_ge(*when(("cx", "exp", 15)))
            dve.wait_ge(*when(("cx", "out", 15)))
            for y in (qb, kb):
                for t in range(2):
                    v = y[:, t, :].rearrange("p (h c u f) -> p h c u f", h=4, c=2, u=2)
                    c = cst("cos2d")[:, 64 * t:64 * t + 64].rearrange("p (c f) -> p c f", c=2)
                    s = cst("sin2d")[:, 64 * t:64 * t + 64].rearrange("p (c f) -> p c f", c=2)
                    tmp = [sc[:, j, 0:256].rearrange("p (h c f) -> p h c f", h=4, c=2) for j in range(4)]
                    for c_ in range(2):
                        for j, (half_, w) in enumerate(((0, c), (1, s), (0, s), (1, c))):
                            nc.vector.tensor_tensor(tmp[j][:, :, c_, :], v[:, :, c_, half_, :],
                                                           w[:, c_, :].unsqueeze(1).to_broadcast([P, 4, 32]), ALU.mult).then_inc(*up(dve))
                            dve.wait_ge(*latest(dve))
                        nc.vector.tensor_tensor(v[:, :, c_, 0, :], tmp[0][:, :, c_, :], tmp[1][:, :, c_, :],
                                                       ALU.subtract).then_inc(*up(dve))
                        dve.wait_ge(*latest(dve))
                        nc.vector.tensor_tensor(v[:, :, c_, 1, :], tmp[2][:, :, c_, :], tmp[3][:, :, c_, :],
                                                       ALU.add).then_inc(*up(dve, ("roped", t)))
                        dve.wait_ge(*latest(dve))
            nc.vector.memset(vb[:, :, :, 128:129], 1.0).then_inc(*up(dve, "v ones"))
            dve.wait_ge(*latest(dve))

        def mlT_pe(pe):
            stage(pe, "mlT")
            pe.wait_ge(*when(("roped", 1)))
            for event in [("read", ("ab_in", n, t)) for n in (3, 4) for t in range(4)]:
                pe.wait_ge(*when(event))
            for i in range(8):
                pe.wait_ge(*bank(4 + i % 4, ("mlT", i)))
                for h in range(4):
                    ins = nc.tensor.transpose(psum[:, 4 + i % 4, P * h:P * h + P],
                                              (qb, kb)[i % 2][:, i // 2, P * h:P * h + P], ident)
                ins.then_inc(*up(pe, ("mlT", "full", i)))

        def mlT_act(act):
            stage(act, "mlT")
            act.wait_ge(*when(("qk", "turned", 7)))
            for i in range(8):
                act.wait_ge(*when(("mlT", "full", i)))
                nc.scalar.copy((qbT, kbT)[i % 2][:, :, P * (i // 2):P * (i // 2) + P],
                                      psum[:, 4 + i % 4, :].rearrange("p (f t) -> p f t", f=4)).then_inc(*up(act, ("read", ("mlT", i))))

        def ml_pe(pe):
            stage(pe, "ml")
            pe.wait_ge(*when(("read", ("mlT", 7))))
            pe.wait_ge(*when("v ones"))
            sel = cst("select4").rearrange("p (h m) -> p h m", h=4)
            for h in range(4):
                pe.wait_ge(*bank(1, ("ml", "S", h)))
                for t in range(4):
                    ins = nc.tensor.matmul(psum[:, 1, P * t:P * t + P], kbT[:, h, P * t:P * t + P],
                                           qbT[:, h, P * t:P * t + P], start=True, stop=True)
                ins.then_inc(*up(pe, ("ml", "S full", h)))
                for z in range(2):
                    pe.wait_ge(*bank(2 + z, ("ml", "M", h, z)))
                    nc.tensor.matmul(psum[:, 2 + z, :], sel[0:4, h, :], gm[0:4, z, :], start=True, stop=True).then_inc(*up(pe, ("ml", "M full", h, z)))
                for j in range(4):
                    for z in range(2):
                        t = ORDER[z][j]
                        i = 4 * h + j
                        b = 4 + z + 2 * (j % 2)
                        s = slice(P * t, P * t + P)
                        pe.wait_ge(*bank(b, ("ml", "P", i, z)))
                        if j == 0:
                            pe.wait_ge(*when(("ml", "W", h, z)))
                            pe.wait_ge(*when(("ml", "K", h, z)))
                        nc.tensor.matmul(psum[:, b, 0:129], mlW[:, z, s], vb[:, t, h, :], start=True, stop=True)
                        nc.tensor.matmul(psum[:, b, 258:387], mlK[:, z, s], vb[:, t, h, :], start=True, stop=True)
                        pe.wait_ge(*when(("ml", "state", i, z)))
                        nc.tensor.matmul(psum[:, b, 129:258], qbT[:, h, s], mlC[:, z, :], start=True, stop=True).then_inc(*up(pe, ("ml", "P full", i, z)))

        def ml_act(act):
            stage(act, "ml")
            for h in range(4):
                for z in range(2):
                    act.wait_ge(*when(("ml", "D", h, z)))
                    nc.scalar.activation(mlD[:, z, :], mlD[:, z, :], ACT.Exp, scale=-1.0).then_inc(*up(act, ("ml", "E", h, z)))
                    act.wait_ge(*latest(act))

        def ml_pool(pool):
            stage(pool, "ml")
            pool.wait_ge(*when("v ones"))
            pool.wait_ge(*when(("read", "gate columns")))
            pool.wait_ge(*when(("roped", 1)))
            for h in range(4):
                for z in range(2):
                    if h:
                        pool.wait_ge(*when(("ml", "P full", 4 * h - 1, z)))
                    for t in range(4):
                        nc.gpsimd.tensor_scalar(mlK[:, z, P * t:P * t + P], kb[:, t, P * h:P * h + P],
                                                        mlc[:, 1, z, t, h:h + 1], None, ALU.mult).then_inc(*up(pool, ("ml", "K", h, z)))
                        pool.wait_ge(*latest(pool))

        def ml_dve(dve):
            stage(dve, "ml")
            mask = (cst("st_fwd"), cst("st_bwd"))
            for h in range(4):
                for z in range(2):
                    dve.wait_ge(*when(("ml", "M full", h, z)))
                    for t in range(4):
                        nc.vector.tensor_scalar(mlD[:, z, P * t:P * t + P], psum[:, 2 + z, P * t:P * t + P],
                                                       mlc[:, 0, z, t, h:h + 1], 0.0, ALU.subtract, ALU.max).then_inc(*up(dve, ("ml", "D", h, z)))
                    also(("read", ("ml", "M", h, z)), ("ml", "D", h, z))
                for z in range(2):
                    dve.wait_ge(*when(("ml", "E", h, z)))
                    dve.wait_ge(*when(("ml", "S full", h)))
                    if h:
                        dve.wait_ge(*when(("ml", "P full", 4 * h - 1, z)))
                    nc.vector.tensor_tensor(mlD[:, z, :].rearrange("p (t s) -> p t s", t=4),
                                                   mlD[:, z, :].rearrange("p (t s) -> p t s", t=4),
                                                   mask[z].unsqueeze(1).to_broadcast([P, 4, P]), ALU.mult).then_inc(*up(dve))
                    dve.wait_ge(*latest(dve))
                    nc.vector.tensor_tensor(mlW[:, z, :], psum[:, 1, :], mlD[:, z, :], ALU.mult).then_inc(*up(dve, ("ml", "W", h, z)))
                    dve.wait_ge(*latest(dve))
                    nc.vector.memset(mlC[:, z, :], 0.0).then_inc(*up(dve, ("ml", "state", 4 * h, z)))
                    dve.wait_ge(*latest(dve))
                also(("read", ("ml", "S", h)), ("ml", "W", h, 1))
                for j in range(4):
                    for z in range(2):
                        t = ORDER[z][j]
                        i = 4 * h + j
                        b = 4 + z + 2 * (j % 2)
                        y, den = mlY[:, z, :], stat[:, 128 + z:129 + z]
                        dve.wait_ge(*when(("ml", "P full", i, z)))
                        if j < 3:
                            nc.vector.scalar_tensor_tensor(mlC[:, z, :], mlC[:, z, :], dec[:, h, z, t:t + 1],
                                                                  psum[:, b, 258:387], ALU.mult, ALU.add).then_inc(*up(dve, ("ml", "state", i + 1, z)))
                            dve.wait_ge(*latest(dve))
                        nc.vector.tensor_scalar(y, psum[:, b, 129:258], mlc[:, 2, z, t, h:h + 1], None, ALU.mult).then_inc(*up(dve))
                        dve.wait_ge(*latest(dve))
                        nc.vector.tensor_tensor(y, psum[:, b, 0:129], y, ALU.add).then_inc(*up(dve, ("read", ("ml", "P", i, z))))
                        dve.wait_ge(*latest(dve))
                        nc.vector.tensor_scalar(den, y[:, 128:129], -1.0, mlc[:, 3, z, t, h:h + 1],
                                                       ALU.mult, ALU.max).then_inc(*up(dve))
                        dve.wait_ge(*latest(dve))
                        nc.vector.tensor_tensor(den, den, y[:, 128:129], ALU.max).then_inc(*up(dve))
                        dve.wait_ge(*latest(dve))
                        nc.vector.reciprocal(den, den).then_inc(*up(dve))
                        dve.wait_ge(*latest(dve))
                        seen_first = ORDER[0].index(t) < ORDER[1].index(t) or (ORDER[0].index(t) == ORDER[1].index(t))
                        first = (z == 0) if seen_first else (z == 1)
                        if first:
                            nc.vector.tensor_scalar(hs[:, t, h, :], y[:, 0:128], den, None, ALU.mult).then_inc(*up(dve))
                            dve.wait_ge(*latest(dve))
                        else:
                            nc.vector.scalar_tensor_tensor(hs[:, t, h, :], y[:, 0:128], den, hs[:, t, h, :],
                                                                  ALU.mult, ALU.add).then_inc(*up(dve, ("ml", "h", i, z)))
                            dve.wait_ge(*latest(dve))

        def merge_dve(dve):
            stage(dve, "merge")
            for t in range(4):
                nc.vector.tensor_tensor(sc[:, t % 2, :].rearrange("p (h d) -> p h d", h=4), hs[:, t], hs[:, t],
                                               ALU.mult).then_inc(*up(dve))
                dve.wait_ge(*latest(dve))
                nc.vector.tensor_reduce(stat[:, 16 + 4 * t:20 + 4 * t],
                                               sc[:, t % 2, :].rearrange("p (h d) -> p h d", h=4), AX.X, ALU.add).then_inc(*up(dve, ("merge", "squares")))
                dve.wait_ge(*latest(dve))
            dve.wait_ge(*when(("merge", "rstd")))
            for t in range(4):
                nc.vector.tensor_tensor(hs[:, t], hs[:, t],
                                               stat[:, 16 + 4 * t:20 + 4 * t].unsqueeze(2).to_broadcast([P, 4, P]), ALU.mult).then_inc(*up(dve))
                dve.wait_ge(*latest(dve))
                nc.vector.tensor_tensor(hs[:, t], hs[:, t], so[:, t, :].rearrange("p (h d) -> p h d", h=4),
                                               ALU.mult).then_inc(*up(dve, ("merge", "gated", t)))
                dve.wait_ge(*latest(dve))
            for t in range(4):
                dve.wait_ge(*when(("merge", "turned", t)))
                for h in range(4):
                    at = ROWS_A["head_norm"] + h
                    nc.vector.tensor_scalar(hT[:, 4 + h, P * t:P * t + P], psum[:, 4 + t, P * h:P * h + P],
                                                   colA[:, at:at + 1], None, ALU.mult).then_inc(*up(dve, ("read", ("merge", t))))

        def merge_pool(pool):
            stage(pool, "merge")
            pool.wait_ge(*when(("merge", "squares")))
            nc.gpsimd.tensor_scalar(stat[:, 16:32], stat[:, 16:32], 1.0 / 128, EPS, ALU.mult, ALU.add).then_inc(*up(pool))
            pool.wait_ge(*latest(pool))
            nc.gpsimd.tensor_tensor(stat[:, 16:32], stat[:, 16:32], half[:, 0:16], ALU.pow).then_inc(*up(pool, ("merge", "rstd")))
            pool.wait_ge(*latest(pool))

        def merge_pe(pe):
            stage(pe, "merge")
            for t in range(4):
                pe.wait_ge(*when(("merge", "gated", t)))
                pe.wait_ge(*bank(4 + t, ("merge", t)))
                for h in range(4):
                    ins = nc.tensor.transpose(psum[:, 4 + t, P * h:P * h + P], hs[:, t, h, :], ident)
                ins.then_inc(*up(pe, ("merge", "turned", t)))

        def gated_rows_dve(dve, name, tiles, banks, gates, tags):
            stage(dve, "gated")
            for event in [("dma", tag) for tag in tags]:
                dve.wait_ge(*when(event))
            for n in range(2):
                for i, t in enumerate(tiles):
                    dve.wait_ge(*when((name, "full", n, t)))
                    b = rows_bank(name, n, i, tiles, banks)
                    dst = (x if t < 2 else cx)[:, t % 2, 512 * n:512 * n + 512]
                    tmp = sc2[:, 0, :]
                    nc.vector.tensor_tensor(tmp, psum[:, b, :], gates[t // 2][:, 512 * n:512 * n + 512], ALU.mult).then_inc(*up(dve, ("read", (name, n, t))))
                    dve.wait_ge(*latest(dve))
                    nc.vector.tensor_tensor(dst, dst, tmp, ALU.add).then_inc(*up(dve, (name, "added", n, t)))
                    dve.wait_ge(*latest(dve))

        hid = area(0, 32, 512)
        gates_m = (area(16384, 1024), area(17408, 1024))

        def up_pe(pe, name, ntok, needs=()):
            stage(pe, "up")
            for event in needs:
                pe.wait_ge(*when(event))
            for n in range(8):
                s = slab(pe, (name, n, 0))
                for j in range(4):
                    i = 4 * n + j
                    pe.wait_ge(*bank(i % 4, (name, i)))
                    for k in range(KT):
                        ins = nc.tensor.matmul(psum[:, i % 4, 0:ntok], s[:, k, P * j:P * j + P], hT[:, k, 0:ntok],
                                               start=(k == 0), stop=(k == 7))
                    ins.then_inc(*up(pe, (name, "full", i)))
                also(("used", slab_at[(name, n, 0)]), (name, "full", 4 * n + 3))

        def up_act(act, name, ntok):
            stage(act, "up")
            for i in range(32):
                act.wait_ge(*when((name, "full", i)))
                if i >= 2:
                    act.wait_ge(*when((name, "hidden", i - 2)))
                nc.scalar.activation(sc[:, i % 2, 0:ntok], psum[:, i % 4, 0:ntok], ACT.Relu).then_inc(*up(act, (name, "relu", i)))

        def up_dve(dve, name, ntok):
            stage(dve, "up")
            for i in range(32):
                dve.wait_ge(*when((name, "relu", i)))
                nc.vector.scalar_tensor_tensor(hid[:, i, 0:ntok], psum[:, i % 4, 0:ntok], 0.0,
                                                      sc[:, i % 2, 0:ntok], ALU.max, ALU.mult).then_inc(*up(dve, (name, "hidden", i)))
                also(("read", (name, i)), (name, "hidden", i))
        KAPPA = float(np.exp(-0.5))
        LNS = 65536.0
        shifted = area(0, 16, 256)
        mixed = (area(4096, 8, 512), area(14336, 8, 512))
        v_rows = area(0, 4, 1024)
        rT = area(8192, 8, 256)
        kT = area(10240, 8, 512)
        VS = area(14336, 8, 8, 64)
        gT = area(18432, 8, 256)
        g2_sb = area(20480, 2, 1024)
        Y = area(20480, 4, 8, 64)
        w2_sb = area(22528, 1024)
        cxf = cx[:, :, :].rearrange("p a b -> p (a b)")
        a2_sb, t_w, t_a = cxf[:, 0:1024], cxf[:, 1024:1536], cxf[:, 1536:2048]
        hTf = hT[:, :, :].rearrange("p a b -> p (a b)")
        scf = sc[:, :, :].rearrange("p a b -> p (a b)")
        sc2f = sc2[:, :, :].rearrange("p a b -> p (a b)")

        def chunks(v):
            return v.rearrange("p (c t) -> p c t", c=8)

        G = [area(3584 * z, 8, 448) for z in range(2)]
        ARI = [hTf[:, 1536 * z:1536 * z + 1536].rearrange("p (c n) -> p c n", c=8) for z in range(2)]
        BK = [hTf[:, 3072:4096], area(7168, 1024)]
        Bh, Kh = [b[:, 0:512] for b in BK], [b[:, 512:1024] for b in BK]
        INV = [[chunks(Bh[0]), chunks(Kh[0])] + [chunks(scf[:, 512 * j:512 * j + 512]) for j in range(4)],
               [chunks(Bh[1]), chunks(Kh[1])] + [chunks(v) for v in (scf[:, 2048:2560], scf[:, 2560:3072],
                                                                   sc2f[:, 0:512], sc2f[:, 512:1024])]]
        small = sc2f[:, 1024:1536]
        St = [[small[:, 128 * z + 64 * j:128 * z + 64 * j + 64] for j in range(2)] for z in range(2)]
        Wt = [small[:, 256 + 64 * z:320 + 64 * z] for z in range(2)]
        Ut = [small[:, 384 + 64 * z:448 + 64 * z] for z in range(2)]
        PC = [stat[:, 0:8], stat[:, 8:16]]
        coef = stat[:, 16:48].rearrange("p (c f) -> p c f", c=4)
        one_ka = stat[:, 48:56]
        neg0 = stat[:, 56:88]
        tmp_ = [[area(3584 * z + 512 * j, 512) for j in range(7)] for z in range(2)]
        WALK = ((4, 5, 6, 7, 0, 1, 2, 3), (7, 6, 5, 4, 3, 2, 1, 0))
        MIXES = ("w", "a", "g", "r", "k", "v")
        MU = dict(r=0, w=1, k=2, v=3, a=4, g=5)
        HH = (slice(0, 64), slice(64, 128))

        def colr(name, i):
            at = ROWS_A[name] + i
            return colA[:, at:at + 1]

        def mix_width(m):
            return 256 if m in "rg" else 512

        def rw_pool(pool):
            stage(pool, "rw")
            pool.wait_ge(*when(("mlp0_down", "added", 1, 3)))
            nc.gpsimd.dma_start(w2_sb, a["rw_w2"][0].rearrange("z r d -> (z r) d"))\
                .then_inc(landing("w2"), 16)
            pool.wait_ge(*when(("C1a", "normed", 1)))
            nc.gpsimd.dma_start(a2_sb, a["rw_a2"][0].rearrange("z r d -> (z r) d"))\
                .then_inc(landing("a2"), 16)
            nc.gpsimd.dma_start(g2_sb[:, 0, :], a["rw_g2"][0, 0:128])\
                .then_inc(landing("g2a"), 16)
            nc.gpsimd.dma_start(g2_sb[0:32, 1, :], a["rw_g2"][0, 128:160])\
                .then_inc(landing("g2b"), 16)
            for t in range(4):
                pool.wait_ge(*when(("rw", "mix used", 5)))
                pool.wait_ge(*when(("rw_v", "rows", 1, t)))
                for hh in range(2):
                    for par in range(2):
                        nc.gpsimd.dma_start(VS[HH[hh], 2 * t + par, :, :], v_rows[HH[par], t, :].rearrange("p (f h d) -> p f h d", f=8, h=2)[:, :, hh, :])\
                            .then_inc(landing("VS"), 16)

        def mix_dve(dve):
            dve.wait_ge(*latest(dve))
            stage(dve, "mix")
            h = hTf.rearrange("p (g t) -> p g t", t=256)
            nc.vector.tensor_tensor(shifted[:, :, 1:255], h[:, :, 0:254], h[:, :, 2:256], ALU.add).then_inc(*up(dve))
            dve.wait_ge(*latest(dve))
            nc.vector.tensor_copy(shifted[:, :, 0:1], h[:, :, 1:2]).then_inc(*up(dve))
            dve.wait_ge(*latest(dve))
            nc.vector.tensor_copy(shifted[:, :, 255:256], h[:, :, 254:255]).then_inc(*up(dve))
            dve.wait_ge(*latest(dve))
            nc.vector.scalar_tensor_tensor(area(0, 4096), area(0, 4096), 0.5, hTf, ALU.mult, ALU.subtract).then_inc(*up(dve))
            dve.wait_ge(*latest(dve))
            for i, m in enumerate(MIXES):
                if i >= 2:
                    dve.wait_ge(*when(("rw", "mix used", i - 2)))
                w = mix_width(m)
                for k in range(KT):
                    s = shifted[:, 2 * k:2 * k + 2, :].rearrange("p a b -> p (a b)")
                    nc.vector.scalar_tensor_tensor(mixed[i % 2][:, k, 0:w], s[:, 0:w], colr("mu", 8 * MU[m] + k),
                                                          hT[:, k, 0:w], ALU.mult, ALU.add).then_inc(*up(dve, ("rw", "mixed", i)))
            nc.vector.tensor_scalar(one_ka, colA[:, ROWS_A["k_a"]:ROWS_A["k_a"] + 8], -1.0, 1.0,
                                           ALU.mult, ALU.add).then_inc(*up(dve))
            dve.wait_ge(*latest(dve))
            nc.vector.tensor_scalar(neg0, colA[:, ROWS_A["w0"]:ROWS_A["w0"] + 32], -1.0, None, ALU.mult).then_inc(*up(dve))
            dve.wait_ge(*latest(dve))
            nc.vector.memset(epsc[:, 1:2], 0.5 * float(np.log(LNS))).then_inc(*up(dve, "rw columns"))
            dve.wait_ge(*latest(dve))

        def proj_pe(pe):
            stage(pe, "proj")
            for i, m in enumerate(MIXES):
                pe.wait_ge(*when(("rw", "mixed", i)))
                x_, w = mixed[i % 2], mix_width(m)
                if m in "wag":
                    name = (m + "1", 0, 0)
                    s = slab(pe, name)
                    for j, n in enumerate((128,) if m != "g" else (128, 32)):
                        pe.wait_ge(*bank(j, (name, j)))
                        for k in range(KT):
                            ins = nc.tensor.matmul(psum[0:n, j, 0:w], s[:, k, P * j:P * j + n], x_[:, k, 0:w],
                                                   start=(k == 0), stop=(k == 7))
                        ins.then_inc(*up(pe, (name, "full", j)))
                    also(("used", slab_at[name]), (name, "full", j))
                    also(("rw", "mix used", i), (name, "full", j))
                    if m == "g":
                        pe.wait_ge(*when(("sig g", 1)))
                        pe.wait_ge(*when(("dma", "g2a")))
                        pe.wait_ge(*when(("dma", "g2b")))
                        for f in range(8):
                            b = 2 + f // 2
                            if f % 2 == 0:
                                pe.wait_ge(*bank(b, ("g2", b)))
                            o = psum[:, b, 256 * (f % 2):256 * (f % 2) + 256]
                            nc.tensor.matmul(o, g2_sb[:, 0, P * f:P * f + P], sc2[:, 0, 0:256], start=True, stop=False)
                            ins = nc.tensor.matmul(o, g2_sb[0:32, 1, P * f:P * f + P], sc2[0:32, 0, 256:512],
                                                   start=False, stop=True)
                            if f % 2:
                                ins.then_inc(*up(pe, ("g2", "full", b)))
                elif m in "rk":
                    for n in range(2):
                        s = slab(pe, ("rw_" + m, n, 0))
                        for j in range(4):
                            pe.wait_ge(*bank(j, ("rw_" + m, n, j)))
                            for k in range(KT):
                                ins = nc.tensor.matmul(psum[:, j, 0:w], s[:, k, P * j:P * j + P], x_[:, k, 0:w],
                                                       start=(k == 0), stop=(k == 7))
                            ins.then_inc(*up(pe, ("rw_" + m, "full", n, j)))
                        also(("used", slab_at[("rw_" + m, n, 0)]), ("rw_" + m, "full", n, 3))
                    also(("rw", "mix used", i), ("rw_" + m, "full", 1, 3))
                else:
                    rows_pe(pe, "rw_v", lambda k, t: mixed[1][:, k, P * t:P * t + P], range(4), KT, D, [0, 1, 2, 3])
                    stage(pe, "proj")
                    also(("rw", "mix used", i), ("rw_v", "full", 1, 3))

        def proj_act(act):
            stage(act, "proj")
            for i, m in enumerate(MIXES):
                if m in "wa":
                    act.wait_ge(*when(((m + "1", 0, 0), "full", 0)))
                    act.wait_ge(*when(("C1a", "normed", 1)))
                    nc.scalar.activation({"w": t_w, "a": t_a}[m], psum[:, 0, :],
                                                ACT.Tanh if m == "w" else ACT.Copy).then_inc(*up(act, ("read", ((m + "1", 0, 0), 0))))
                    act.wait_ge(*latest(act))
                elif m == "g":
                    name = ("g1", 0, 0)
                    for j, n in enumerate((128, 32)):
                        act.wait_ge(*when((name, "full", j)))
                        nc.scalar.activation(sc2[0:n, 0, 256 * j:256 * j + 256], psum[0:n, j, 0:256],
                                                    ACT.Sigmoid).then_inc(*up(act, ("read", (name, j))))
                        act.wait_ge(*latest(act))
                        also(("sig g", j), ("read", (name, j)))
                    for b in range(2, 6):
                        act.wait_ge(*when(("g2", "full", b)))
                        nc.scalar.copy(gT[:, 2 * b - 4:2 * b - 2, :].rearrange("p a b -> p (a b)"), psum[:, b, :]).then_inc(*up(act, ("read", ("g2", b))))
                elif m in "rk":
                    w = mix_width(m)
                    for n in range(2):
                        for j in range(4):
                            act.wait_ge(*when(("rw_" + m, "full", n, j)))
                            nc.scalar.copy({"r": rT, "k": kT}[m][:, 4 * n + j, :], psum[:, j, 0:w]).then_inc(*up(act, ("read", ("rw_" + m, n, j))))
                else:
                    act.wait_ge(*when(("rw", "mixed", 5)))
                    for n in range(2):
                        for t in range(4):
                            act.wait_ge(*when(("rw_v", "full", n, t)))
                            nc.scalar.copy(v_rows[:, t, 512 * n:512 * n + 512], psum[:, t, :]).then_inc(*up(act, ("read", ("rw_v", n, t))))
                            also(("rw_v", "rows", n, t), ("read", ("rw_v", n, t)))

        def prep_pe(pe, f):
            stage(pe, "prep")
            if f == 0:
                pe.wait_ge(*when(("dma", "w2")))
                pe.wait_ge(*when(("dma", "a2")))
                pe.wait_ge(*when(("read", (("w1", 0, 0), 0))))
                pe.wait_ge(*when(("read", (("a1", 0, 0), 0))))
            c = slice(P * f, P * f + P)
            for z in range(2):
                pe.wait_ge(*bank(z, ("wl", f, z)))
                nc.tensor.matmul(psum[:, z, :], w2_sb[HH[z], c], t_w[HH[z], :], start=True, stop=True).then_inc(*up(pe, ("wl", "full", f, z)))
                pe.wait_ge(*bank(2 + z, ("al", f, z)))
                nc.tensor.matmul(psum[:, 2 + z, :], a2_sb[HH[z], c], t_a[HH[z], :], start=True, stop=True).then_inc(*up(pe, ("al", "full", f, z)))
            pe.wait_ge(*when(("kk squared", f)))
            pe.wait_ge(*bank(4, ("kk", f)))
            nc.tensor.matmul(psum[:, 4, :], cst("headones"), tmp_[1][6], start=True, stop=True).then_inc(*up(pe, ("kk", "full", f)))
            pe.wait_ge(*when(("coef product", f)))
            pe.wait_ge(*bank(5, ("coef", f)))
            for hh in range(2):
                for c_ in range(4):
                    ins = nc.tensor.matmul(psum[HH[hh], 5, c_:c_ + 1], tmp_[0][4][HH[hh], 64 * c_:64 * c_ + 64],
                                           cst("ones")[HH[hh], 0:1], start=True, stop=True)
            ins.then_inc(*up(pe, ("coef", "full", f)))

        def prep_act(act, f):
            stage(act, "prep")
            act.wait_ge(*when("rw columns"))
            if f == 0:
                act.wait_ge(*when(("dma", "VS")))
            else:
                act.wait_ge(*when(("chains", f - 1)))
            for z in range(2):
                t = tmp_[z]
                act.wait_ge(*when(("wl", "full", f, z)))
                nc.scalar.activation(t[0], psum[:, z, :], ACT.Exp, bias=neg0[:, 8 * z + f:8 * z + f + 1],
                                            scale=-1.0).then_inc(*up(act, ("read", ("wl", f, z))))
                act.wait_ge(*when(("al", "full", f, z)))
                nc.scalar.activation(t[1], psum[:, 2 + z, :], ACT.Exp,
                                            bias=neg0[:, 16 + 8 * z + f:16 + 8 * z + f + 1], scale=-1.0).then_inc(*up(act, ("read", ("al", f, z))))
            act.wait_ge(*when(("kk", "full", f)))
            act.wait_ge(*when(("kk bounded", f)))
            nc.scalar.activation(tmp_[1][6], tmp_[1][6], ACT.Ln, scale=LNS).then_inc(*up(act))
            act.wait_ge(*latest(act))
            nc.scalar.activation(tmp_[1][6], tmp_[1][6], ACT.Exp, scale=-0.5, bias=epsc[:, 1:2]).then_inc(*up(act, ("kk rnorm", f)))
            act.wait_ge(*latest(act))
            for z in range(2):
                t = tmp_[z]
                act.wait_ge(*when(("decay sums", f, z)))
                nc.scalar.activation(t[2], t[2], ACT.Exp, scale=-KAPPA).then_inc(*up(act))
                nc.scalar.activation(t[0], t[3], ACT.Exp, scale=-KAPPA).then_inc(*up(act))
                nc.scalar.activation(t[3], t[3], ACT.Exp, scale=KAPPA).then_inc(*up(act, ("decays", f, z)))
                act.wait_ge(*latest(act))

        def prep_dve(dve, f):
            stage(dve, "prep")
            if f == 0:
                dve.wait_ge(*when(("dma", "VS")))
                dve.wait_ge(*when(("rw", "mix used", 5)))
                for z in range(2):
                    nc.vector.tensor_copy(ARI[z][:, :, 64:128],
                                                 cst("eye64").unsqueeze(1).to_broadcast([P, 8, 64])).then_inc(*up(dve, "eyes"))
                    dve.wait_ge(*latest(dve))
            else:
                dve.wait_ge(*when(("chains", f - 1)))
            kk, sq = tmp_[0][6], tmp_[1][6]
            nc.vector.tensor_scalar(kk, kT[:, f, :], colr("k_k", f), None, ALU.mult).then_inc(*up(dve))
            dve.wait_ge(*latest(dve))
            nc.vector.tensor_tensor(sq, kk, kk, ALU.mult).then_inc(*up(dve, ("kk squared", f)))
            dve.wait_ge(*latest(dve))
            for z in range(2):
                t = tmp_[z]
                dve.wait_ge(*when(("read", ("wl", f, z))))
                dve.wait_ge(*when(("read", ("al", f, z))))
                nc.vector.tensor_scalar(t[0], t[0], 1.0, None, ALU.add).then_inc(*up(dve))
                dve.wait_ge(*latest(dve))
                nc.vector.reciprocal(t[0], t[0]).then_inc(*up(dve))
                dve.wait_ge(*latest(dve))
                v = (lambda q: q) if z == 0 else (lambda q: q[:, ::-1])
                nc.vector.tensor_tensor_scan(v(t[3]), cst("chunk_start"), v(t[0]), 0.0, ALU.mult, ALU.add).then_inc(*up(dve))
                dve.wait_ge(*latest(dve))
                nc.vector.tensor_tensor(t[2], t[3], t[0], ALU.subtract).then_inc(*up(dve, ("decay sums", f, z)))
                dve.wait_ge(*latest(dve))
                nc.vector.tensor_scalar(t[1], t[1], 1.0, None, ALU.add).then_inc(*up(dve))
                dve.wait_ge(*latest(dve))
                nc.vector.reciprocal(t[1], t[1]).then_inc(*up(dve))
                dve.wait_ge(*latest(dve))
                nc.vector.tensor_scalar(t[4], t[1], colr("k_a", f), one_ka[:, f:f + 1], ALU.mult, ALU.add).then_inc(*up(dve))
                dve.wait_ge(*latest(dve))
                nc.vector.tensor_tensor(t[5], t[4], kT[:, f, :], ALU.mult).then_inc(*up(dve))
                dve.wait_ge(*latest(dve))
            dve.wait_ge(*when(("kk", "full", f)))
            nc.vector.tensor_scalar(sq, psum[:, 4, :], 1e-24, None, ALU.max).then_inc(*up(dve, ("kk bounded", f)))
            dve.wait_ge(*latest(dve))
            also(("read", ("kk", f)), ("kk bounded", f))
            c4 = tmp_[0][4][:, 0:256]
            nc.vector.tensor_tensor(c4, tmp_[0][5][:, 0:256], tmp_[1][5][:, 0:256], ALU.add).then_inc(*up(dve))
            dve.wait_ge(*latest(dve))
            nc.vector.scalar_tensor_tensor(c4, c4, colr("r_k", f), rT[:, f, :], ALU.mult, ALU.mult).then_inc(*up(dve, ("coef product", f)))
            dve.wait_ge(*latest(dve))
            dve.wait_ge(*when(("kk rnorm", f)))
            nc.vector.tensor_tensor(kk, kk, sq, ALU.mult).then_inc(*up(dve))
            dve.wait_ge(*latest(dve))
            for z in range(2):
                t = tmp_[z]
                dve.wait_ge(*when(("decays", f, z)))
                last = 63 if z == 0 else 0
                nc.vector.tensor_copy(PC[z].unsqueeze(2), chunks(t[0])[:, :, last:last + 1]).then_inc(*up(dve))
                dve.wait_ge(*latest(dve))
                nc.vector.scalar_tensor_tensor(ARI[z][:, :, 0:64], chunks(kk), -1.0, chunks(t[2]),
                                                      ALU.mult, ALU.mult).then_inc(*up(dve))
                dve.wait_ge(*latest(dve))
                nc.vector.tensor_tensor(ARI[z][:, 0:4, 128:192], rT[:, f, :].rearrange("p (c t) -> p c t", c=4),
                                               chunks(t[0])[:, 0:4, :], ALU.mult).then_inc(*up(dve))
                dve.wait_ge(*latest(dve))
                nc.vector.tensor_tensor(t[1], t[1], kk, ALU.mult).then_inc(*up(dve))
                dve.wait_ge(*latest(dve))
                nc.vector.tensor_tensor(Bh[z], t[1], t[3], ALU.mult).then_inc(*up(dve))
                dve.wait_ge(*latest(dve))
                nc.vector.tensor_tensor(Kh[z], t[5], t[3], ALU.mult).then_inc(*up(dve, ("scaled", f, z)))
                dve.wait_ge(*latest(dve))
            dve.wait_ge(*when(("coef", "full", f)))
            nc.vector.tensor_copy(coef[:, :, f:f + 1], psum[:, 5, 0:4].unsqueeze(2)).then_inc(*up(dve, ("read", ("coef", f))))
            dve.wait_ge(*latest(dve))

        GRAM_BANKS = (0, 1, 2, 3, 6, 7)

        def gram_list(f):
            return [(z, c) for c in range(8) for z in range(2)]

        def gram_pe(pe, f):
            stage(pe, "gram")
            pe.wait_ge(*when("eyes"))
            pe.wait_ge(*when(("scaled", f, 1)))
            pe.wait_ge(*when(("decays", f, 1)))
            for i, (z, c) in enumerate(gram_list(f)):
                b = GRAM_BANKS[i % 6]
                w = 192 if c < 4 else 128
                s = slice(64 * c, 64 * c + 64)
                pe.wait_ge(*bank(b, ("gram", f, z, c)))
                for r in HH:
                    nc.tensor.matmul(psum[r, b, 0:w], Bh[z][r, s], ARI[z][r, c, 0:w], start=True, stop=True)
                    nc.tensor.matmul(psum[r, b, 192:192 + w], Kh[z][r, s], ARI[z][r, c, 0:w], start=True, stop=True)
                    ins = nc.tensor.matmul(psum[r, b, 384:448], ARI[z][r, c, 0:64], Bh[z][r, s], start=True, stop=True)
                ins.then_inc(*up(pe, ("gram", "full", f, z, c)))

        def gram_dve(dve, f):
            stage(dve, "gram")
            for i, (z, c) in enumerate(gram_list(f)):
                b = GRAM_BANKS[i % 6]
                m = cst(f"gram{z}")
                dve.wait_ge(*when(("gram", "full", f, z, c)))
                if i < 2:
                    dve.wait_ge(*when(("coef", "full", f)))
                    dve.wait_ge(*when(("kk", "full", f)))
                if c < 4:
                    ins = nc.vector.tensor_tensor(G[z][:, c, :], psum[:, b, 0:448], m, ALU.mult)
                else:
                    two = lambda q: q.rearrange("p (a n) -> p a n", a=2)[:, :, 0:128]
                    nc.vector.tensor_tensor(two(G[z][:, c, 0:384]), two(psum[:, b, 0:384]), two(m[:, 0:384]),
                                                   ALU.mult).then_inc(*up(dve))
                    ins = nc.vector.tensor_tensor(G[z][:, c, 384:448], psum[:, b, 384:448], m[:, 384:448], ALU.mult)
                ins.then_inc(*up(dve, ("read", ("gram", f, z, c))))
                dve.wait_ge(*latest(dve))

        INV_STEPS = (
            ((1, 0, 2, None), (0, 1, 3, None)),
            ((3, 4, 4, 4), (3, 2, 0, None), (2, 3, 1, None)),
            ((1, 4, 4, 4), (0, 1, 2, None)),
            ((2, 4, 4, 4),),
            ((4, "eye", 5, None),),
            (("off32", 4, 3, None),),
            ((5, 3, 4, 4), (3, 5, 5, 5)),
            (("off64", 4, 3, None),),
            ((5, 3, 4, 4),),
        )

        def inv_tiles(f):
            n = 0
            for r, steps in enumerate(INV_STEPS):
                for z in range(2):
                    for j, step in enumerate(steps):
                        yield r, z, j, step, n % 8
                        n += 1

        def inv_pe(pe, f):
            stage(pe, "inv")
            for r, z, j, (left, right, dst, add), b in inv_tiles(f):
                pe.wait_ge(*when(("inv ready", f, r, z)))
                pe.wait_ge(*bank(b, ("inv", f, r, z, j)))
                for c in range(8):
                    for h in HH:
                        l = INV[z][2 if left in ("off32", "off64") else left][h, c, :]
                        rr = cst("eye64")[h, :] if right == "eye" else INV[z][right][h, c, :]
                        ins = nc.tensor.matmul(psum[h, b, 64 * c:64 * c + 64], l, rr, start=True, stop=True)
                ins.then_inc(*up(pe, ("inv", "full", f, r, z, j)))

        def inv_dve(dve, f):
            stage(dve, "inv")

            def bc(name):
                return cst(name).unsqueeze(1).to_broadcast([P, 8, 64])

            for z in range(2):
                B = INV[z]
                dve.wait_ge(*when(("gram", "full", f, z, 7)))
                nc.vector.tensor_tensor(B[0], G[z][:, :, 0:64], bc("diag16"), ALU.mult).then_inc(*up(dve))
                dve.wait_ge(*latest(dve))
                nc.vector.tensor_tensor(B[1], G[z][:, :, 384:448], bc("diag16"), ALU.mult).then_inc(*up(dve))
                dve.wait_ge(*latest(dve))
                nc.vector.tensor_tensor(B[4], B[0], bc("eye64"), ALU.add).then_inc(*up(dve, ("inv ready", f, 0, z)))
                dve.wait_ge(*latest(dve))
            for r, z, j, (left, right, dst, add), b in inv_tiles(f):
                B = INV[z]
                dve.wait_ge(*when(("inv", "full", f, r, z, len(INV_STEPS[r]) - 1)))
                src = chunks(psum[:, b, :])
                if add is None:
                    ins = nc.vector.tensor_copy(B[dst], src)
                else:
                    ins = nc.vector.tensor_tensor(B[dst], src, B[add], ALU.add)
                ins.then_inc(*up(dve, ("read", ("inv", f, r, z, j))))
                if j == len(INV_STEPS[r]) - 1:
                    if r == 4:
                        ins = nc.vector.tensor_tensor(B[2], G[z][:, :, 384:448], bc("off32"), ALU.mult)
                        ins.then_inc(*up(dve, ("inv ready", f, 5, z)))
                        dve.wait_ge(*latest(dve))
                    elif r == 6:
                        ins = nc.vector.tensor_tensor(B[2], G[z][:, :, 384:448], bc("off64"), ALU.mult)
                        ins.then_inc(*up(dve, ("inv ready", f, 7, z)))
                        dve.wait_ge(*latest(dve))
                    else:
                        also(("inv ready", f, r + 1, z), ("read", ("inv", f, r, z, j)))

        def walk_pe(pe, f):
            stage(pe, "walk")
            pe.wait_ge(*when(("inv ready", f, len(INV_STEPS), 0)))
            pe.wait_ge(*when(("inv ready", f, len(INV_STEPS), 1)))
            pe.wait_ge(*when(("walk zero", f)))
            for i in range(8):
                for z in range(2):
                    c, S, b = WALK[z][i], St[z][i % 2], 4 * z
                    pe.wait_ge(*bank(b, ("W", f, i, z)))
                    pe.wait_ge(*when(("S", f, i, z)))
                    for r in HH:
                        nc.tensor.matmul(psum[r, b, 0:64], ARI[z][r, c, 0:64], S[r, :], start=True, stop=False)
                        ins = nc.tensor.matmul(psum[r, b, 0:64], G[z][r, c, 192:256], VS[r, c, f, :],
                                               start=False, stop=True)
                    ins.then_inc(*up(pe, ("W", "full", f, i, z)))
                for z in range(2):
                    c, b = WALK[z][i], 4 * z + 1
                    pe.wait_ge(*bank(b, ("U", f, i, z)))
                    pe.wait_ge(*when(("W", "out", f, i, z)))
                    for r in HH:
                        ins = nc.tensor.matmul(psum[r, b, 0:64], INV[z][4][r, c, :], Wt[z][r, :], start=True, stop=True)
                    ins.then_inc(*up(pe, ("U", "full", f, i, z)))
                for z in range(2):
                    c, S = WALK[z][i], St[z][i % 2]
                    pe.wait_ge(*when(("U", "out", f, i, z)))
                    if i < 7:
                        b = 4 * z + 2
                        pe.wait_ge(*bank(b, ("S psum", f, i, z)))
                        for r in HH:
                            nc.tensor.matmul(psum[r, b, 0:64], cst("eye64")[r, :], S[r, :], start=True, stop=False)
                            nc.tensor.matmul(psum[r, b, 0:64], G[z][r, c, 256:320], VS[r, c, f, :], start=False, stop=False)
                            ins = nc.tensor.matmul(psum[r, b, 0:64], G[z][r, c, 64:128], Ut[z][r, :],
                                                   start=False, stop=True)
                        ins.then_inc(*up(pe, ("S", "full", f, i, z)))
                    if c < 4:
                        b = 4 * z + 3
                        pe.wait_ge(*bank(b, ("Y", f, i, z)))
                        for r in HH:
                            nc.tensor.matmul(psum[r, b, 0:64], ARI[z][r, c, 128:192], S[r, :], start=True, stop=False)
                            nc.tensor.matmul(psum[r, b, 0:64], G[z][r, c, 320:384], VS[r, c, f, :], start=False, stop=False)
                            ins = nc.tensor.matmul(psum[r, b, 0:64], G[z][r, c, 128:192], Ut[z][r, :],
                                                   start=False, stop=True)
                        ins.then_inc(*up(pe, ("Y", "full", f, i, z)))

        def walk_act(act, f):
            stage(act, "walk")
            z = 1
            for i in range(8):
                act.wait_ge(*when(("W", "full", f, i, z)))
                nc.scalar.copy(Wt[z], psum[:, 4, 0:64]).then_inc(*up(act, ("W", "out", f, i, z)))
                also(("read", ("W", f, i, z)), ("W", "out", f, i, z))
                act.wait_ge(*when(("U", "full", f, i, z)))
                if i:
                    act.wait_ge(*when(("Y", "full", f, i - 1, z) if WALK[z][i - 1] < 4 else ("S", "full", f, i - 1, z)))
                nc.scalar.copy(Ut[z], psum[:, 5, 0:64]).then_inc(*up(act, ("U", "out", f, i, z)))
                also(("read", ("U", f, i, z)), ("U", "out", f, i, z))
                if i < 7:
                    act.wait_ge(*when(("S", "full", f, i, z)))
                    c = WALK[z][i]
                    nc.scalar.activation(St[z][(i + 1) % 2], psum[:, 6, 0:64], ACT.Copy,
                                                scale=PC[z][:, c:c + 1]).then_inc(*up(act, ("S", f, i + 1, z)))
                    also(("read", ("S psum", f, i, z)), ("S", f, i + 1, z))

        def walk_dve(dve, f):
            dve.wait_ge(*latest(dve))
            stage(dve, "walk")
            for z in range(2):
                nc.vector.memset(St[z][0], 0.0).then_inc(*up(dve, ("S", f, 0, z)))
                dve.wait_ge(*latest(dve))
            also(("walk zero", f), ("S", f, 0, 1))
            z = 0
            for i in range(8):
                dve.wait_ge(*when(("W", "full", f, i, z)))
                nc.vector.tensor_copy(Wt[z], psum[:, 0, 0:64]).then_inc(*up(dve, ("W", "out", f, i, z)))
                also(("read", ("W", f, i, z)), ("W", "out", f, i, z))
                dve.wait_ge(*when(("U", "full", f, i, z)))
                if i:
                    dve.wait_ge(*when(("Y", "full", f, i - 1, z) if WALK[z][i - 1] < 4 else ("S", "full", f, i - 1, z)))
                nc.vector.tensor_copy(Ut[z], psum[:, 1, 0:64]).then_inc(*up(dve, ("U", "out", f, i, z)))
                also(("read", ("U", f, i, z)), ("U", "out", f, i, z))
                if i < 7:
                    dve.wait_ge(*when(("S", "full", f, i, z)))
                    c = WALK[z][i]
                    nc.vector.tensor_scalar(St[z][(i + 1) % 2], psum[:, 2, 0:64], PC[z][:, c:c + 1], None,
                                                   ALU.mult).then_inc(*up(dve, ("S", f, i + 1, z)))
                    also(("read", ("S psum", f, i, z)), ("S", f, i + 1, z))
                if i >= 5:
                    walk_y(dve, f, i - 1)
            walk_y(dve, f, 7)
            also(("chains", f), ("read", ("Y", f, 7, 1)))

        def walk_y(dve, f, i):
            for z in range(2):
                c = WALK[z][i]
                first = (z == 0) == (c < 2)
                dve.wait_ge(*when(("Y", "full", f, i, z)))
                src = psum[:, 4 * z + 3, 0:64]
                if first:
                    ins = nc.vector.tensor_copy(Y[:, c, f, :], src)
                else:
                    ins = nc.vector.tensor_tensor(Y[:, c, f, :], src, Y[:, c, f, :], ALU.add)
                ins.then_inc(*up(dve, ("read", ("Y", f, i, z))))
                dve.wait_ge(*latest(dve))

        bonus = area(0, 4, 8, 64)
        ysq = area(2048, 32, 64)
        ystat = stat[:, 88:120]
        gates_r = (area(4096, 1024),)

        def readout_dve(dve):
            stage(dve, "readout")
            Yf = Y.rearrange("p c f d -> p (c f) d")
            bc = lambda v: v.unsqueeze(2).to_broadcast([P, 32, 64])
            nc.vector.tensor_reduce(ystat, Yf, AX.X, ALU.add).then_inc(*up(dve))
            dve.wait_ge(*latest(dve))
            nc.vector.tensor_scalar(ystat, ystat, 1.0 / 64, None, ALU.mult).then_inc(*up(dve))
            dve.wait_ge(*latest(dve))
            nc.vector.tensor_tensor(Yf, Yf, bc(ystat), ALU.subtract).then_inc(*up(dve))
            dve.wait_ge(*latest(dve))
            nc.vector.tensor_tensor(ysq, Yf, Yf, ALU.mult).then_inc(*up(dve))
            dve.wait_ge(*latest(dve))
            nc.vector.tensor_reduce(ystat, ysq, AX.X, ALU.add).then_inc(*up(dve, "y squares"))
            dve.wait_ge(*latest(dve))
            nc.vector.tensor_tensor(bonus.rearrange("p c f d -> p (c f) d"),
                                           VS[:, 0:4, :, :].rearrange("p c f d -> p (c f) d"),
                                           coef.rearrange("p c f -> p (c f)").unsqueeze(2).to_broadcast([P, 32, 64]),
                                           ALU.mult).then_inc(*up(dve))
            dve.wait_ge(*latest(dve))
            dve.wait_ge(*when("y rstd"))
            nc.vector.tensor_tensor(Yf, Yf, bc(ystat), ALU.mult).then_inc(*up(dve, "y normed"))
            dve.wait_ge(*latest(dve))
            for f in range(8):
                dve.wait_ge(*when(("y turned", f)))
                t = sc[:, f % 2, 0:256]
                nc.vector.tensor_scalar(t, psum[:, f % 4, 0:256], colr("lnx_w", f), colr("lnx_b", f),
                                               ALU.mult, ALU.add).then_inc(*up(dve))
                dve.wait_ge(*latest(dve))
                nc.vector.tensor_tensor(t, t, psum[:, f % 4, 256:512], ALU.add).then_inc(*up(dve, ("read", ("y", f))))
                dve.wait_ge(*latest(dve))
                nc.vector.tensor_tensor(hT[:, f, 0:256], t, gT[:, f, :], ALU.mult).then_inc(*up(dve, ("rw gated", f)))
                dve.wait_ge(*latest(dve))

        def readout_pool(pool):
            stage(pool, "readout")
            pool.wait_ge(*when("y squares"))
            nc.gpsimd.tensor_scalar(ystat, ystat, 1.0 / 64, 64e-5, ALU.mult, ALU.add).then_inc(*up(pool))
            pool.wait_ge(*latest(pool))
            nc.gpsimd.tensor_tensor(ystat, ystat, half[:, 0:32], ALU.pow).then_inc(*up(pool, "y rstd"))
            pool.wait_ge(*latest(pool))
            gate_load(pool, "gate r", gates_r[0], 1, 0, 2)

        def readout_pe(pe):
            stage(pe, "readout")
            pe.wait_ge(*when("y normed"))
            for f in range(8):
                pe.wait_ge(*bank(f % 4, ("y", f)))
                for h in HH:
                    for c in range(4):
                        s = slice(64 * c, 64 * c + 64)
                        nc.tensor.matmul(psum[h, f % 4, 64 * c:64 * c + 64], Y[h, c, f, :], cst("eye64")[h, :],
                                         start=True, stop=True)
                        ins = nc.tensor.matmul(psum[h, f % 4, 256 + 64 * c:320 + 64 * c], bonus[h, c, f, :],
                                               cst("eye64")[h, :], start=True, stop=True)
                ins.then_inc(*up(pe, ("y turned", f)))
        def gain(name, layer=0, n=8):
            at = ROWS_B[name] + n * layer
            return colB[:, at:at + n]

        def add_rows_dve(dve, name, banks, scale):
            stage(dve, "add")
            for n in range(2):
                for i in range(2):
                    dve.wait_ge(*when((name, "full", n, i)))
                    b = rows_bank(name, n, i, range(2), banks)
                    dst = x[:, i, 512 * n:512 * n + 512]
                    nc.vector.scalar_tensor_tensor(dst, psum[:, b, :], scale, dst, ALU.mult, ALU.add).then_inc(*up(dve, (name, "added", n, i)))
                    also(("read", (name, n, i)), (name, "added", n, i))
            dve.wait_ge(*latest(dve))

        UP_BANKS = [4, 5, 6, 7]
        hid2 = area(0, 22, 256)

        def swiglu_pe(pe, key):
            stage(pe, "swiglu")
            for event in [("read", (key, b)) for b in range(4)]:
                pe.wait_ge(*when(event))
            for n in range(11):
                s = slab(pe, (key + "_gu", n, 0))
                for part in range(2):
                    b = 2 * (n % 2) + part
                    pe.wait_ge(*bank(b, (key, "gu", n, part)))
                    for j in range(2):
                        at = 256 * part + P * j
                        for k in range(KT):
                            ins = nc.tensor.matmul(psum[:, b, 256 * j:256 * j + 256], s[:, k, at:at + P],
                                                   hT[:, k, 0:256], start=(k == 0), stop=(k == 7))
                    ins.then_inc(*up(pe, (key, "gu full", n, part)))
                also(("used", slab_at[(key + "_gu", n, 0)]), (key, "gu full", n, 1))
            rows_pe(pe, key + "_down", lambda k, t: hid2[:, k, P * t:P * t + P], range(2), 22, D, UP_BANKS,
                    [(key, "hidden", 10)])

        def swiglu_act(act, key):
            stage(act, "swiglu")
            for n in range(11):
                act.wait_ge(*when((key, "gu full", n, 0)))
                if n >= 2:
                    act.wait_ge(*when((key, "hidden", n - 2)))
                nc.scalar.activation(sc[:, n % 2, :], psum[:, 2 * (n % 2), :], ACT.Silu).then_inc(*up(act, ("read", (key, "gu", n, 0))))

        def swiglu_dve(dve, key):
            stage(dve, "swiglu")
            for n in range(11):
                dve.wait_ge(*when(("read", (key, "gu", n, 0))))
                dve.wait_ge(*when((key, "gu full", n, 1)))
                nc.vector.tensor_tensor(hid2[:, 2 * n:2 * n + 2, :].rearrange("p a b -> p (a b)"), sc[:, n % 2, :],
                                               psum[:, 2 * (n % 2) + 1, :], ALU.mult).then_inc(*up(dve, (key, "hidden", n)))
                also(("read", (key, "gu", n, 1)), (key, "hidden", n))
            add_rows_dve(dve, key + "_down", UP_BANKS, 0.5)

        eq = area(0, 4, 256)
        ek = area(1024, 4, 256)
        ev = area(2048, 2, 512)
        eu = area(3072, 2, 512)
        eg = area(4096, 2, 512)
        e_gain, e_bias = area(6144, 512), area(6656, 512)
        ew = area(7168, 8, P)
        ewT = area(8192, 8, P)
        esq = area(9216, 2, 512)

        def even_pool(pool):
            stage(pool, "even")
            pool.wait_ge(*when(("pre0_down", "added", 1, 1)))
            nc.gpsimd.dma_start(e_gain, a["sgu_ln_gain_2"][0].partition_broadcast(P))\
                .then_inc(landing("ln gain"), 16)
            nc.gpsimd.dma_start(e_bias, a["sgu_ln_bias_2"][0].partition_broadcast(P))\
                .then_inc(landing("ln bias"), 16)
            nc.gpsimd.dma_start(ew, a["sgu_w_2"][0].rearrange("g t s -> t g s"))\
                .then_inc(landing("sgu w"), 16)

        def even_pool_rstd(pool):
            stage(pool, "even")
            pool.wait_ge(*when("g squares"))
            nc.gpsimd.tensor_scalar(stat[:, 132:134], stat[:, 132:134], 1.0 / 512, EPS, ALU.mult, ALU.add).then_inc(*up(pool))
            pool.wait_ge(*latest(pool))
            nc.gpsimd.tensor_tensor(stat[:, 132:134], stat[:, 132:134], half[:, 0:2], ALU.pow).then_inc(*up(pool, "g rstd"))
            pool.wait_ge(*latest(pool))

        def even_in_pe(pe):
            stage(pe, "even")
            for event in [("read", ("mix0", b)) for b in range(4)]:
                pe.wait_ge(*when(event))
            for n in range(2):
                s = slab(pe, ("sbg_in", n, 0))
                for j in range(4):
                    pe.wait_ge(*bank(j, ("sbg", n, j)))
                    for k in range(KT):
                        ins = nc.tensor.matmul(psum[:, j, 0:256], s[:, k, P * j:P * j + P], hT[:, k, 0:256],
                                               start=(k == 0), stop=(k == 7))
                    ins.then_inc(*up(pe, ("sbg", "full", n, j)))
                also(("used", slab_at[("sbg_in", n, 0)]), ("sbg", "full", n, 3))
            rows_pe(pe, "sbg_in", lambda k, t: hT[:, k, P * t:P * t + P], range(2), KT, 2560, [4, 5, 6, 7],
                    only=(2, 3, 4))
            stage(pe, "even")
            pe.wait_ge(*when(("dma", "sgu w")))
            for b in range(2):
                pe.wait_ge(*bank(b, ("ewT", b)))
                for g in range(4):
                    ins = nc.tensor.transpose(psum[:, b, P * g:P * g + P], ew[:, 4 * b + g, :], ident)
                ins.then_inc(*up(pe, ("ewT", "full", b)))

        def even_in_act(act):
            stage(act, "even")
            act.wait_ge(*when(("pre0_down", "full", 1, 1)))
            for n in range(2):
                for j in range(4):
                    act.wait_ge(*when(("sbg", "full", n, j)))
                    nc.scalar.copy((eq, ek)[n][:, j, :], psum[:, j, 0:256]).then_inc(*up(act, ("read", ("sbg", n, j))))
            for i, n in enumerate((2, 3, 4)):
                for t in range(2):
                    act.wait_ge(*when(("sbg_in", "full", n, t)))
                    nc.scalar.activation((ev, eu, eg)[i][:, t, :], psum[:, 4 + (2 * i + t) % 4, :],
                                                ACT.Copy if n == 2 else ACT.Gelu_apprx_tanh).then_inc(*up(act, ("read", ("sbg_in", n, t))))

        def even_gate_dve(dve):
            stage(dve, "even")
            for b in range(2):
                dve.wait_ge(*when(("ewT", "full", b)))
                nc.vector.tensor_tensor(ewT[:, 4 * b:4 * b + 4, :],
                                               psum[:, b, :].rearrange("p (g t) -> p g t", g=4),
                                               cst("st_fwd").unsqueeze(1).to_broadcast([P, 4, P]), ALU.mult).then_inc(*up(dve, ("read", ("ewT", b))))
                dve.wait_ge(*latest(dve))
            dve.wait_ge(*when(("read", ("sbg_in", 4, 0))))
            dve.wait_ge(*when(("read", ("sbg_in", 4, 1))))
            dve.wait_ge(*when(("dma", "ln gain")))
            dve.wait_ge(*when(("dma", "ln bias")))
            m = stat[:, 130:132]
            nc.vector.tensor_reduce(m, eg, AX.X, ALU.add).then_inc(*up(dve))
            dve.wait_ge(*latest(dve))
            nc.vector.tensor_scalar(m, m, 1.0 / 512, None, ALU.mult).then_inc(*up(dve))
            dve.wait_ge(*latest(dve))
            for t in range(2):
                nc.vector.tensor_scalar(eg[:, t, :], eg[:, t, :], m[:, t:t + 1], None, ALU.subtract).then_inc(*up(dve))
                dve.wait_ge(*latest(dve))
            nc.vector.tensor_tensor(esq, eg, eg, ALU.mult).then_inc(*up(dve))
            dve.wait_ge(*latest(dve))
            nc.vector.tensor_reduce(stat[:, 132:134], esq, AX.X, ALU.add).then_inc(*up(dve, "g squares"))
            dve.wait_ge(*latest(dve))
            dve.wait_ge(*when("g rstd"))
            for t in range(2):
                nc.vector.scalar_tensor_tensor(eg[:, t, :], eg[:, t, :], stat[:, 132 + t:133 + t], e_gain,
                                                      ALU.mult, ALU.mult).then_inc(*up(dve))
                dve.wait_ge(*latest(dve))
                nc.vector.tensor_tensor(eg[:, t, :], eg[:, t, :], e_bias, ALU.add).then_inc(*up(dve, "g normed"))
                dve.wait_ge(*latest(dve))
            for t in range(2):
                dve.wait_ge(*when(("mixed", "full", t)))
                for g in range(8):
                    c = slice(64 * g, 64 * g + 64)
                    at = ROWS_B["sgu_b"] + g
                    nc.vector.scalar_tensor_tensor(eu[:, t, c], psum[:, 2 + t, c], colB[:, at:at + 1],
                                                          eu[:, t, c], ALU.add, ALU.mult).then_inc(*up(dve, ("gated", t)))
                also(("read", ("mixed", t)), ("gated", t))
            for t in range(2):
                dve.wait_ge(*when(("gated", "turned", t)))
                nc.vector.tensor_copy(hT[:, 4:8, P * t:P * t + P],
                                             psum[:, 6 + t, :].rearrange("p (f t) -> p f t", f=4)).then_inc(*up(dve, ("read", ("gatedT", t))))

        def even_gate_pe(pe):
            stage(pe, "even")
            pe.wait_ge(*when("g normed"))
            pe.wait_ge(*when(("read", ("ewT", 1))))
            for t in range(2):
                pe.wait_ge(*bank(2 + t, ("mixed", t)))
                for g in range(8):
                    c = slice(64 * g, 64 * g + 64)
                    ins = nc.tensor.matmul(psum[:, 2 + t, c], ewT[:, g, :], eg[:, t, c], start=True, stop=True)
                ins.then_inc(*up(pe, ("mixed", "full", t)))
            for t in range(2):
                pe.wait_ge(*when(("gated", t)))
                pe.wait_ge(*bank(6 + t, ("gatedT", t)))
                for f in range(4):
                    ins = nc.tensor.transpose(psum[:, 6 + t, P * f:P * f + P], eu[:, t, P * f:P * f + P], ident)
                ins.then_inc(*up(pe, ("gated", "turned", t)))

        sb_units = []
        for h in range(8):
            for qt in range(2):
                r, f = head_rows(h), h // 2
                sb_units.append(dict(keys=P * (qt + 1), qk=[(eq[r, f, P * qt:P * qt + P], ek[r, f, 0:P * (qt + 1)])],
                                     v=[(lambda k, h=h: ev[:, k, 64 * h:64 * h + 64], r.start)],
                                     dst=[hT[r, f, P * qt:P * qt + P]]))

        def stick_act(act):
            stage(act, "stick")
            act.wait_ge(*when(("sbg_in", "full", 4, 1)))

            def softplus(i):
                n, s = sb_units[i]["keys"], sc[:, i % 2, :]
                act.wait_ge(*when(("sb", "z", i)))
                if i >= 2:
                    act.wait_ge(*when(("sb", "probs", i - 2)))
                nc.scalar.activation(s[:, 0:n], sc[:, 2 + i % 2, 0:n], ACT.Abs).then_inc(*up(act))
                act.wait_ge(*latest(act))
                nc.scalar.activation(s[:, 0:n], s[:, 0:n], ACT.Exp, scale=-1.0).then_inc(*up(act))
                act.wait_ge(*latest(act))
                nc.scalar.activation(s[:, 0:n], s[:, 0:n], ACT.Ln, bias=1.0).then_inc(*up(act, ("sb", "ln", i)))
                act.wait_ge(*latest(act))

            def weights(i):
                n = sb_units[i]["keys"]
                act.wait_ge(*when(("sb", "exponent", i)))
                if i >= 2:
                    act.wait_ge(*when(("sb", "turned", i - 2)))
                nc.scalar.activation(sc2[:, i % 2, 0:n], sc[:, i % 2, 0:n], ACT.Exp).then_inc(*up(act, ("sb", "probs", i)))

            for step, i in unit_tick(16, softplus, weights, lambda i: att_probsT(act, "sb", sb_units, i),
                                     lambda i: att_out(act, "sb", sb_units, i)):
                step(i)

        def stick_dve(dve):
            stage(dve, "stick")

            def scaled(i):
                n, r = sb_units[i]["keys"], sc[:, 2 + i % 2, :]
                dve.wait_ge(*when(("sb", "scores", i)))
                nc.vector.tensor_scalar(r[:, 0:n], psum[:, i % 2, 0:n], 0.125, None, ALU.mult).then_inc(*up(dve, ("sb", "z", i)))
                dve.wait_ge(*latest(dve))
                also(("read", ("sb", "s", i)), ("sb", "z", i))

            def exponent(i):
                n, s, r = sb_units[i]["keys"], sc[:, i % 2, :], sc[:, 2 + i % 2, :]
                d = slice(n - P, n)
                dve.wait_ge(*when(("sb", "ln", i)))
                nc.vector.scalar_tensor_tensor(s[:, 0:n], r[:, 0:n], 0.0, s[:, 0:n], ALU.max, ALU.add).then_inc(*up(dve))
                dve.wait_ge(*latest(dve))
                nc.vector.tensor_tensor(s[:, d], s[:, d], cst("strict"), ALU.mult).then_inc(*up(dve))
                dve.wait_ge(*latest(dve))
                v = s[:, 0:n][:, ::-1]
                nc.vector.tensor_tensor_scan(v, v, v, 0.0, ALU.add, ALU.max).then_inc(*up(dve))
                dve.wait_ge(*latest(dve))
                nc.vector.tensor_tensor(s[:, 0:n], r[:, 0:n], s[:, 0:n], ALU.subtract).then_inc(*up(dve))
                dve.wait_ge(*latest(dve))
                nc.vector.tensor_tensor(s[:, d], s[:, d], cst("strict_add"), ALU.add).then_inc(*up(dve, ("sb", "exponent", i)))
                dve.wait_ge(*latest(dve))

            for step, i in unit_tick(16, scaled, exponent):
                step(i)

        cq = area(0, 2, 512)
        ckv = area(1024, 2, 288)
        cqT = area(1600, 4, 256)
        ckvT = area(2624, 2, 256)
        mq = area(3136, 2, 16, 96)
        mkv = area(6208, 2, 16, 128)
        mk = area(10304, 2, 16, 96)
        mqT = area(13376, 16, 256)
        mkT = area(17472, 16, 256)
        msq = area(21568, 16, 96)
        pos_i = sb("pos_i", [P, 2], I32)
        rot = area(23104, 6, 32)

        def mla_pool(pool):
            stage(pool, "mla")
            nc.gpsimd.dma_start(pos_i[:, :], a["positions_2"][0].rearrange("(t p) -> p t", p=P), allow_slow_non_contiguous=True)\
                .then_inc(landing("positions"), 16)

        def rstd_pool(pool, v, width, before, event):
            pool.wait_ge(*when(before))
            nc.gpsimd.tensor_scalar(v, v, 1.0 / width, EPS, ALU.mult, ALU.add).then_inc(*up(pool))
            pool.wait_ge(*latest(pool))
            nc.gpsimd.tensor_tensor(v, v, half[:, 0:v.shape[1]], ALU.pow).then_inc(*up(pool, event))
            pool.wait_ge(*latest(pool))

        def mla_pool_rstd(pool):
            stage(pool, "mla")
            rstd_pool(pool, stat[:, 134:136], 512, "cq squares", "cq rstd")
            rstd_pool(pool, stat[:, 136:138], 256, "ckv squares", "ckv rstd")
            for y in range(2):
                for t in range(2):
                    at = 144 + 16 * (2 * y + t)
                    rstd_pool(pool, stat[:, at:at + 16], 96, ("mla squares", y, t), ("mla rstd", y, t))

        def angles_dve(dve):
            stage(dve, "angles")
            dve.wait_ge(*when(("dma", "positions")))
            C1, C2 = 6.28125, 0.0019353071795864769
            posf = stat[:, 138:140]
            ang, n, r, c = (rot[:, j, :] for j in range(4))
            nc.vector.tensor_copy(posf, pos_i[:, :]).then_inc(*up(dve))
            dve.wait_ge(*latest(dve))
            for t in range(2):
                nc.vector.tensor_scalar(ang[:, 16 * t:16 * t + 16], cst("inv_freq"), posf[:, t:t + 1], None,
                                               ALU.mult).then_inc(*up(dve))
                dve.wait_ge(*latest(dve))
            nc.vector.tensor_scalar(n, ang, float(1 / (2 * np.pi)), 12582912.0, ALU.mult, ALU.add).then_inc(*up(dve))
            dve.wait_ge(*latest(dve))
            nc.vector.tensor_scalar(n, n, 12582912.0, None, ALU.subtract).then_inc(*up(dve))
            dve.wait_ge(*latest(dve))
            nc.vector.scalar_tensor_tensor(r, n, -C1, ang, ALU.mult, ALU.add).then_inc(*up(dve))
            dve.wait_ge(*latest(dve))
            nc.vector.scalar_tensor_tensor(r, n, -C2, r, ALU.mult, ALU.add).then_inc(*up(dve))
            dve.wait_ge(*latest(dve))
            nc.vector.tensor_scalar(c, r, float(np.pi / 2), float(-2 * np.pi), ALU.is_gt, ALU.mult).then_inc(*up(dve))
            dve.wait_ge(*latest(dve))
            nc.vector.scalar_tensor_tensor(c, r, float(np.pi / 2), c, ALU.add, ALU.add).then_inc(*up(dve))
            dve.wait_ge(*latest(dve))
            for v in (r, c):
                nc.vector.tensor_scalar(v, v, 3.1415925, -3.1415925, ALU.min, ALU.max).then_inc(*up(dve, "angles"))
                dve.wait_ge(*latest(dve))

        def angles_act(act):
            stage(act, "angles")
            act.wait_ge(*when("angles"))
            nc.scalar.activation(rot[:, 4, :], rot[:, 2, :], ACT.Sin).then_inc(*up(act))
            act.wait_ge(*latest(act))
            nc.scalar.activation(rot[:, 5, :], rot[:, 3, :], ACT.Sin).then_inc(*up(act, "sines"))
            act.wait_ge(*latest(act))

        def mla_pe(pe):
            rows_pe(pe, "mla_in", lambda k, t: hT[:, k, P * t:P * t + P], range(2), KT, 800, [0, 1, 2, 3],
                    [("read", ("mix1", b)) for b in range(4)])
            stage(pe, "mla")
            for i, (src, nf) in enumerate(((cq, 4), (ckv, 2))):
                for t in range(2):
                    b = 4 + 2 * i + t
                    pe.wait_ge(*when(("latent normed", i, t)))
                    pe.wait_ge(*bank(b, ("latT", i, t)))
                    for f in range(nf):
                        ins = nc.tensor.transpose(psum[:, b, P * f:P * f + P], src[:, t, P * f:P * f + P], ident)
                    ins.then_inc(*up(pe, ("latT", "full", i, t)))
            rows_pe(pe, "mla_uq", lambda k, t: cqT[:, k, P * t:P * t + P], range(2), 4, 1536, [0, 1, 2, 3],
                    [("read", ("latT", 0, 1))])
            rows_pe(pe, "mla_ukv", lambda k, t: ckvT[:, k, P * t:P * t + P], range(2), 2, 2048, [4, 5, 6, 7],
                    [("read", ("latT", 1, 1))])
            stage(pe, "mla")
            for i, (y, t, g) in enumerate(mla_turns):
                pe.wait_ge(*when(("mla roped", y, t)))
                b = i % 4
                pe.wait_ge(*bank(b, ("mlaT", i)))
                for j in range(4):
                    ins = nc.tensor.transpose(psum[0:96, b, P * j:P * j + P], (mq, mk)[y][:, t, 4 * g + j, :], ident)
                ins.then_inc(*up(pe, ("mlaT", "full", i)))

        mla_turns = [(y, t, g) for y in range(2) for t in range(2) for g in range(4)]

        def mla_act(act):
            stage(act, "mla")
            act.wait_ge(*when(("pre1_down", "full", 1, 1)))
            for n in range(2):
                for t in range(2):
                    act.wait_ge(*when(("mla_in", "full", n, t)))
                    w = 512 if n == 0 else 288
                    nc.scalar.copy((cq, ckv)[n][:, t, :], psum[:, 2 * n + t, 0:w]).then_inc(*up(act, ("read", ("mla_in", n, t))))
            for n in range(3):
                for t in range(2):
                    act.wait_ge(*when(("mla_uq", "full", n, t)))
                    nc.scalar.copy(mq[:, t].rearrange("p h d -> p (h d)")[:, 512 * n:512 * n + 512],
                                          psum[:, (2 * n + t) % 4, :]).then_inc(*up(act, ("read", ("mla_uq", n, t))))
            for n in range(4):
                for t in range(2):
                    act.wait_ge(*when(("mla_ukv", "full", n, t)))
                    nc.scalar.copy(mkv[:, t].rearrange("p h d -> p (h d)")[:, 512 * n:512 * n + 512],
                                          psum[:, 4 + (2 * n + t) % 4, :]).then_inc(*up(act, ("read", ("mla_ukv", n, t))))
            for i, (y, t, g) in enumerate(mla_turns):
                act.wait_ge(*when(("mlaT", "full", i)))
                nc.scalar.copy((mqT, mkT)[y][0:96, 4 * g:4 * g + 4, P * t:P * t + P],
                                      psum[0:96, i % 4, :].rearrange("p (h t) -> p h t", h=4)).then_inc(*up(act, ("read", ("mlaT", i))))

        def mla_dve(dve):
            stage(dve, "mla")
            for i, (y, w, at, name) in enumerate(((cq, 512, 134, "cq"), (ckv, 256, 136, "ckv"))):
                for t in range(2):
                    dve.wait_ge(*when(("read", ("mla_in", i, t))))
                    nc.vector.tensor_tensor(msq.rearrange("p a b -> p (a b)")[:, 0:w], y[:, t, 0:w], y[:, t, 0:w],
                                                   ALU.mult).then_inc(*up(dve))
                    dve.wait_ge(*latest(dve))
                    nc.vector.tensor_reduce(stat[:, at + t:at + t + 1], msq.rearrange("p a b -> p (a b)")[:, 0:w],
                                                   AX.X, ALU.add).then_inc(*up(dve, name + " squares"))
                    dve.wait_ge(*latest(dve))
            for i, (y, w, at, name) in enumerate(((cq, 512, 134, "cq"), (ckv, 256, 136, "ckv"))):
                dve.wait_ge(*when(name + " rstd"))
                for t in range(2):
                    nc.vector.tensor_scalar(y[:, t, 0:w], y[:, t, 0:w], stat[:, at + t:at + t + 1], None, ALU.mult).then_inc(*up(dve, ("latent normed", i, t)))
                    dve.wait_ge(*latest(dve))
            for i, (nf, dst, name) in enumerate(((4, cqT, "q_lora"), (2, ckvT, "kv_lora"))):
                for t in range(2):
                    b = 4 + 2 * i + t
                    dve.wait_ge(*when(("latT", "full", i, t)))
                    for f in range(nf):
                        at = ROWS_B[name] + f
                        nc.vector.tensor_scalar(dst[:, f, P * t:P * t + P], psum[:, b, P * f:P * f + P],
                                                       colB[:, at:at + 1], None, ALU.mult).then_inc(*up(dve, ("read", ("latT", i, t))))
            for y in range(2):
                v = (mq, mk)[y]
                for t in range(2):
                    if y == 0:
                        for event in [("read", ("mla_uq", n, t)) for n in range(3)]:
                            dve.wait_ge(*when(event))
                    else:
                        for event in [("read", ("mla_ukv", n, t)) for n in range(4)]:
                            dve.wait_ge(*when(event))
                        nc.vector.tensor_copy(mk[:, t, :, 0:64], mkv[:, t, :, 0:64]).then_inc(*up(dve))
                        dve.wait_ge(*latest(dve))
                        nc.vector.tensor_copy(mk[:, t, :, 64:96],
                                                     ckv[:, t, 256:288].unsqueeze(1).to_broadcast([P, 16, 32])).then_inc(*up(dve))
                        dve.wait_ge(*latest(dve))
                    at = 144 + 16 * (2 * y + t)
                    nc.vector.tensor_tensor(msq, v[:, t], v[:, t], ALU.mult).then_inc(*up(dve))
                    dve.wait_ge(*latest(dve))
                    nc.vector.tensor_reduce(stat[:, at:at + 16], msq, AX.X, ALU.add).then_inc(*up(dve, ("mla squares", y, t)))
                    dve.wait_ge(*latest(dve))
            dve.wait_ge(*when("sines"))
            dve.wait_ge(*when(("dma", "q_gain")))
            dve.wait_ge(*when(("dma", "k_gain")))
            for y in range(2):
                for t in range(2):
                    v = (mq, mk)[y][:, t]
                    at = 144 + 16 * (2 * y + t)
                    dve.wait_ge(*when(("mla rstd", y, t)))
                    nc.vector.tensor_tensor(v, v, stat[:, at:at + 16].unsqueeze(2).to_broadcast([P, 16, 96]),
                                                   ALU.mult).then_inc(*up(dve))
                    dve.wait_ge(*latest(dve))
                    nc.vector.tensor_tensor(v, v, gbc[:, 96 * y:96 * y + 96].unsqueeze(1).to_broadcast([P, 16, 96]),
                                                   ALU.mult).then_inc(*up(dve))
                    dve.wait_ge(*latest(dve))
                    s = rot[:, 4, 16 * t:16 * t + 16].unsqueeze(1).to_broadcast([P, 16, 16])
                    c = rot[:, 5, 16 * t:16 * t + 16].unsqueeze(1).to_broadcast([P, 16, 16])
                    tmp = [sc2[:, 0, 256 * (j % 2):256 * (j % 2) + 256].rearrange("p (h d) -> p h d", h=16) if j < 2 else
                           sc2[:, 1, 256 * (j % 2):256 * (j % 2) + 256].rearrange("p (h d) -> p h d", h=16)
                           for j in range(4)]
                    x1, x2 = v[:, :, 64:80], v[:, :, 80:96]
                    for j, (u, w) in enumerate(((x1, c), (x2, s), (x1, s), (x2, c))):
                        nc.vector.tensor_tensor(tmp[j], u, w, ALU.mult).then_inc(*up(dve))
                        dve.wait_ge(*latest(dve))
                    nc.vector.tensor_tensor(x1, tmp[0], tmp[1], ALU.subtract).then_inc(*up(dve))
                    dve.wait_ge(*latest(dve))
                    nc.vector.tensor_tensor(x2, tmp[2], tmp[3], ALU.add).then_inc(*up(dve, ("mla roped", y, t)))
                    dve.wait_ge(*latest(dve))

        mla_units = []
        for h in range(16):
            for qt in range(2):
                r, f = head_rows(h), h // 2
                mla_units.append(dict(keys=P * (qt + 1),
                                      qk=[(mqT[0:96, h, P * qt:P * qt + P], mkT[0:96, h, 0:P * (qt + 1)])],
                                      bias=[(P, None)] * qt + [(P, cst("causal_add"))],
                                      v=[(lambda k, h=h: mkv[:, k, h, 64:128], r.start)],
                                      dst=[hT[r, f, P * qt:P * qt + P]]))

        xkm = area(0, 2, 4, 256)
        xvm = area(2048, 2, 4, 256)
        xqr = area(4096, 2, 4, 256)
        xkT = area(6144, 8, 256)
        xqT = area(8192, 8, 256)
        xsq = area(10240, 2, 4, 256)

        def mem_load(pool, layer):
            if layer == 0:
                pool.wait_ge(*when("y normed"))
                pool.wait_ge(*when(("chains", 7)))
                nc.gpsimd.dma_start(cx[:, :, :], a["mem_2"][0].rearrange("(t p) d -> p t d", p=P))\
                    .then_inc(landing("mem"), 16)

        def xmem_pe(pe, l):
            rows_pe(pe, f"xkv{l}", lambda k, t: hT[:, k, P * t:P * t + P], (2, 3), KT, 2 * D, [0, 1, 2, 3],
                    [("read", (f"xm{l}", b)) for b in range(4)])
            rows_pe(pe, f"xq{l}", lambda k, t: hT[:, k, P * t:P * t + P], (0, 1), KT, D, [4, 5, 6, 7],
                    [("read", (f"xx{l}", b)) for b in range(4)])
            stage(pe, "xmem")
            for i in range(8):
                y, t, b2 = i // 4, (i // 2) % 2, i % 2
                pe.wait_ge(*when((f"x normed {l}", y, t)))
                pe.wait_ge(*bank(i % 4, (f"xT{l}", i)))
                for j in range(4):
                    src = (xkm, xqr)[y][:, t].rearrange("p h d -> p (h d)")
                    at = 512 * b2 + P * j
                    ins = nc.tensor.transpose(psum[:, i % 4, P * j:P * j + P], src[:, at:at + P], ident)
                ins.then_inc(*up(pe, (f"xT{l}", "full", i)))

        def xmem_act(act, l):
            stage(act, "xmem")
            act.wait_ge(*when(("sbg_out" if l == 0 else "mla_out", "full", 1, 1)))
            for n in range(4):
                for i, t in enumerate((2, 3)):
                    act.wait_ge(*when((f"xkv{l}", "full", n, t)))
                    b = (2 * n + i) % 4
                    nc.scalar.copy(xkm[:, i, n, :], psum[:, b, 0:256]).then_inc(*up(act))
                    nc.scalar.copy(xvm[:, i, n, :], psum[:, b, 256:512]).then_inc(*up(act, ("read", (f"xkv{l}", n, t))))
            for n in range(2):
                for t in range(2):
                    act.wait_ge(*when((f"xq{l}", "full", n, t)))
                    nc.scalar.copy(xqr[:, t, 2 * n:2 * n + 2, :].rearrange("p a b -> p (a b)"),
                                          psum[:, 4 + (2 * n + t) % 4, :]).then_inc(*up(act, ("read", (f"xq{l}", n, t))))

        def xmem_dve(dve, l):
            stage(dve, "xmem")
            for y in range(2):
                dve.wait_ge(*when(("read", (f"xkv{l}", 3, 3)) if y == 0 else ("read", (f"xq{l}", 1, 1))))
                v = (xkm, xqr)[y]
                at = 176 + 8 * y
                nc.vector.tensor_tensor(xsq, v, v, ALU.mult).then_inc(*up(dve))
                dve.wait_ge(*latest(dve))
                nc.vector.tensor_reduce(stat[:, at:at + 8], xsq.rearrange("p a b c -> p (a b) c"), AX.X, ALU.add).then_inc(*up(dve, (f"x squares {l}", y)))
                dve.wait_ge(*latest(dve))
                dve.wait_ge(*when((f"x rstd {l}", y)))
                for t in range(2):
                    nc.vector.tensor_tensor(v[:, t], v[:, t], stat[:, at + 4 * t:at + 4 * t + 4].unsqueeze(2)
                                                   .to_broadcast([P, 4, 256]), ALU.mult).then_inc(*up(dve, (f"x normed {l}", y, t)))
                    dve.wait_ge(*latest(dve))
            for i in range(8):
                y, t, b2 = i // 4, (i // 2) % 2, i % 2
                dve.wait_ge(*when((f"xT{l}", "full", i)))
                for j in range(2):
                    at = ROWS_B["xk" if y == 0 else "xq"] + 2 * l + j
                    dst = (xkT, xqT)[y].rearrange("p (h j) n -> p h j n", j=2)[:, 2 * b2:2 * b2 + 2, j, P * t:P * t + P]
                    src = psum[:, i % 4, :].rearrange("p (h j n) -> p h j n", h=2, j=2)[:, :, j, :]
                    nc.vector.tensor_scalar(dst, src, colB[:, at:at + 1], None, ALU.mult).then_inc(*up(dve, ("read", (f"xT{l}", i))))

        def xmem_pool(pool, l):
            stage(pool, "xmem")
            for y in range(2):
                rstd_pool(pool, stat[:, 176 + 8 * y:184 + 8 * y], 256, (f"x squares {l}", y), (f"x rstd {l}", y))

        x_units = []
        for h in range(4):
            for qt in range(2):
                x_units.append(dict(keys=256, bias=None,
                                    qk=[(xqT[:, 2 * h + j, P * qt:P * qt + P], xkT[:, 2 * h + j, :]) for j in range(2)],
                                    v=[(lambda k, h=h, j=j: xvm[:, k, h, P * j:P * j + P], 0) for j in range(2)],
                                    dst=[hT[:, 2 * h + j, P * qt:P * qt + P] for j in range(2)]))

        def cat(k, t):
            return hT[:, k, P * t:P * t + P]


        block = ctx.enter_context(nc.Block())

        @block.sync
        def _(eng):
            sp = Side(eng, "sp")
            stage(sp, "setup")
            setup_sp(sp)
            for i, (name, pieces) in enumerate(slabs):
                if i >= RING:
                    sp.wait_ge(*when(("used", i - RING)))
                view = ring[:, i % RING, :].rearrange("p (k n) -> p k n", k=8)
                for nk, at, nn, src in pieces:
                    nc.sync.dma_start(view[:, 0:nk, at:at + nn], src)\
                        .then_inc(add(f"slab_landed_{i % RING}", 16, ("slab", i)), 16)
            sp.wait_ge(*when(("post1_down", "added", 1, 1)))
            nc.sync.dma_start(out[0].rearrange("(t p) d -> p t d", p=P), x[:, :, :])\
                .then_inc(landing("out"), 16)
            eng.wait_ge(sem("landed_out"), 16)

        @block.tensor
        def _(eng):
            pe = Side(eng, "pe")
            stage(pe, "setup")
            setup_pe(pe)
            ada_pe(pe)
            norm_pe(pe, "L0a")
            norm_pe(pe, "C0a")
            ab_in_pe(pe)
            qk_norm_pe(pe)
            att_pe(pe, "na", na, [("read", ("qkT", i)) for i in range(8)])
            att_pe(pe, "cx", cxa)
            decay_pe(pe)
            mlT_pe(pe)
            ml_pe(pe)
            merge_pe(pe)
            rows_pe(pe, "ab_out", lambda k, t: hT[:, k, P * t:P * t + P], range(4), KT, D, [0, 1, 2, 3], [("read", ("merge", 3)), ("read", ("cx", "o", 15))])
            norm_pe(pe, "L0m")
            norm_pe(pe, "C0m")
            up_pe(pe, "mlp0_up", 512, [("read", (k, b)) for k in ("L0m", "C0m") for b in range(4)])
            rows_pe(pe, "mlp0_down", lambda k, t: hid[:, k, P * t:P * t + P], range(4), 32, D, [0, 1, 2, 3], [("mlp0_up", "hidden", 31)])
            norm_pe(pe, "L1a")
            norm_pe(pe, "C1a")
            proj_pe(pe)
            for f in range(8):
                prep_pe(pe, f)
                gram_pe(pe, f)
                inv_pe(pe, f)
                walk_pe(pe, f)
            readout_pe(pe)
            rows_pe(pe, "rw_o", lambda k, t: hT[:, k, P * t:P * t + P], range(2), KT, D, [4, 5, 6, 7], [("rw gated", 7)])
            norm_pe(pe, "L1m")
            up_pe(pe, "mlp1_up", 256, [("read", ("L1m", b)) for b in range(4)])
            rows_pe(pe, "mlp1_down", lambda k, t: hid[:, k, P * t:P * t + P], range(2), 32, D, [4, 5, 6, 7], [("mlp1_up", "hidden", 31)])
            norm_pe(pe, "pre0")
            swiglu_pe(pe, "pre0")
            norm_pe(pe, "mix0")
            even_in_pe(pe)
            even_gate_pe(pe)
            att_pe(pe, "sb", sb_units)
            rows_pe(pe, "sbg_out", cat, range(2), KT, D, [4, 5, 6, 7], [("read", ("sb", "o", 15)), ("read", ("gatedT", 1))])
            norm_pe(pe, "xm0")
            norm_pe(pe, "xx0")
            xmem_pe(pe, 0)
            att_pe(pe, "xa0", x_units, [("read", ("xT0", i)) for i in range(8)])
            rows_pe(pe, "xo0", cat, range(2), KT, D, [4, 5, 6, 7], [("read", ("xa0", "o", 7))])
            norm_pe(pe, "post0")
            swiglu_pe(pe, "post0")
            norm_pe(pe, "pre1")
            swiglu_pe(pe, "pre1")
            norm_pe(pe, "mix1")
            mla_pe(pe)
            att_pe(pe, "mla", mla_units, [("read", ("mlaT", 15))])
            rows_pe(pe, "mla_out", cat, range(2), KT, D, [4, 5, 6, 7], [("read", ("mla", "o", 31))])
            norm_pe(pe, "xm1")
            norm_pe(pe, "xx1")
            xmem_pe(pe, 1)
            att_pe(pe, "xa1", x_units, [("read", ("xT1", i)) for i in range(8)])
            rows_pe(pe, "xo1", cat, range(2), KT, D, [4, 5, 6, 7], [("read", ("xa1", "o", 7))])
            norm_pe(pe, "post1")
            swiglu_pe(pe, "post1")

        @block.scalar
        def _(eng):
            act = Side(eng, "act")
            stage(act, "setup")
            setup_act(act)
            norm_act(act, "L0a", x, [("dma", "x")])
            norm_act(act, "C0a", cx, [("dma", "ctx")])
            ab_in_act(act)
            gates_act(act)
            att_act(act, "na", na, 0.125, [("gates", "full", 3)])
            att_act(act, "cx", cxa, 0.125)
            softplus_act(act)
            decay_act(act)
            mlT_act(act)
            ml_act(act)
            norm_act(act, "L0m", x, [("ab_out", "added", 1, 1)])
            norm_act(act, "C0m", cx, [("ab_out", "added", 1, 3)])
            up_act(act, "mlp0_up", 512)
            norm_act(act, "L1a", x, [("mlp0_down", "added", 1, 1)])
            norm_act(act, "C1a", cx, [("mlp0_down", "added", 1, 3)])
            proj_act(act)
            for f in range(8):
                prep_act(act, f)
                walk_act(act, f)
            norm_act(act, "L1m", x, [("rw_o", "added", 1, 1)])
            up_act(act, "mlp1_up", 256)
            norm_act(act, "pre0", x, [("mlp1_down", "added", 1, 1)])
            swiglu_act(act, "pre0")
            norm_act(act, "mix0", x, [("pre0_down", "added", 1, 1)])
            even_in_act(act)
            stick_act(act)
            norm_act(act, "xm0", cx, [("dma", "mem"), ("sbg_out", "added", 1, 1)])
            norm_act(act, "xx0", x, [("sbg_out", "added", 1, 1)])
            xmem_act(act, 0)
            att_act(act, "xa0", x_units, 0.0625, [("xq0", "full", 1, 1)])
            norm_act(act, "post0", x, [("xo0", "added", 1, 1)])
            swiglu_act(act, "post0")
            norm_act(act, "pre1", x, [("post0_down", "added", 1, 1)])
            swiglu_act(act, "pre1")
            norm_act(act, "mix1", x, [("pre1_down", "added", 1, 1)])
            angles_act(act)
            mla_act(act)
            att_act(act, "mla", mla_units, 96 ** -0.5)
            norm_act(act, "xm1", cx, [("dma", "mem"), ("mla_out", "added", 1, 1)])
            norm_act(act, "xx1", x, [("mla_out", "added", 1, 1)])
            xmem_act(act, 1)
            att_act(act, "xa1", x_units, 0.0625, [("xq1", "full", 1, 1)])
            norm_act(act, "post1", x, [("xo1", "added", 1, 1)])
            swiglu_act(act, "post1")

        @block.vector
        def _(eng):
            dve = Side(eng, "dve")
            stage(dve, "setup")
            setup_dve(dve)
            ada_dve(dve)
            norm_dve(dve, "L0a", x, 0, mcol(0, 0, 1), mcol(0, 0, 0), True)
            norm_dve(dve, "C0a", cx, 256, mcol(0, 1, 1), mcol(0, 1, 0), True)
            gates_dve(dve)
            qk_norm_dve(dve)
            att_dve(dve, "na", na, 0.125, after_first=["bias ready"])
            att_dve(dve, "cx", cxa, 0.125)
            rope_dve(dve)
            decay_dve(dve)
            decay_out_dve(dve)
            ml_dve(dve)
            merge_dve(dve)
            gated_rows_dve(dve, "ab_out", range(4), [0, 1, 2, 3], gates_a, ("gate a0", "gate a1"))
            norm_dve(dve, "L0m", x, 0, mcol(0, 0, 4), mcol(0, 0, 3), True)
            norm_dve(dve, "C0m", cx, 256, mcol(0, 1, 4), mcol(0, 1, 3), True)
            up_dve(dve, "mlp0_up", 512)
            gated_rows_dve(dve, "mlp0_down", range(4), [0, 1, 2, 3], gates_m, ("gate m0", "gate m1"))
            norm_dve(dve, "L1a", x, 0, mcol(1, 0, 1), mcol(1, 0, 0), True)
            norm_dve(dve, "C1a", cx, 256, mcol(1, 1, 1), mcol(1, 1, 0), True)
            mix_dve(dve)
            for f in range(8):
                prep_dve(dve, f)
                gram_dve(dve, f)
                inv_dve(dve, f)
                walk_dve(dve, f)
            readout_dve(dve)
            gated_rows_dve(dve, "rw_o", range(2), [4, 5, 6, 7], gates_r, ("gate r",))
            norm_dve(dve, "L1m", x, 0, mcol(1, 0, 4), mcol(1, 0, 3), True)
            up_dve(dve, "mlp1_up", 256)
            gated_rows_dve(dve, "mlp1_down", range(2), [4, 5, 6, 7], gates_m, ("gate n",))
            norm_dve(dve, "pre0", x, 0, gain("ffn_pre", 0))
            swiglu_dve(dve, "pre0")
            norm_dve(dve, "mix0", x, 0, gain("mix", 0))
            even_gate_dve(dve)
            stick_dve(dve)
            add_rows_dve(dve, "sbg_out", [4, 5, 6, 7], 1.0)
            norm_dve(dve, "xm0", cx, 256, gain("xmem_mem", 0))
            norm_dve(dve, "xx0", x, 0, gain("xmem", 0))
            xmem_dve(dve, 0)
            att_dve(dve, "xa0", x_units, 0.0625)
            add_rows_dve(dve, "xo0", [4, 5, 6, 7], 1.0)
            norm_dve(dve, "post0", x, 0, gain("ffn_post", 0))
            swiglu_dve(dve, "post0")
            norm_dve(dve, "pre1", x, 0, gain("ffn_pre", 1))
            swiglu_dve(dve, "pre1")
            angles_dve(dve)
            norm_dve(dve, "mix1", x, 0, gain("mix", 1))
            mla_dve(dve)
            att_dve(dve, "mla", mla_units, 96 ** -0.5)
            add_rows_dve(dve, "mla_out", [4, 5, 6, 7], 1.0)
            norm_dve(dve, "xm1", cx, 256, gain("xmem_mem", 1))
            norm_dve(dve, "xx1", x, 0, gain("xmem", 1))
            xmem_dve(dve, 1)
            att_dve(dve, "xa1", x_units, 0.0625)
            add_rows_dve(dve, "xo1", [4, 5, 6, 7], 1.0)
            norm_dve(dve, "post1", x, 0, gain("ffn_post", 1))
            swiglu_dve(dve, "post1")

        @block.gpsimd
        def _(eng):
            pool = Side(eng, "pool")
            stage(pool, "setup")
            setup_pool(pool)
            ada_pool(pool)
            norm_pool(pool, "L0a")
            norm_pool(pool, "C0a")
            qk_norm_pool(pool)
            ml_pool(pool)
            merge_pool(pool)
            pool.wait_ge(*when(("merge", "turned", 3)))
            gate_load(pool, "gate a0", gates_a[0], 0, 0, 2)
            gate_load(pool, "gate a1", gates_a[1], 0, 1, 2)
            pool.wait_ge(*when(("merge", "turned", 3)))
            gate_load(pool, "gate m0", gates_m[0], 0, 0, 5)
            gate_load(pool, "gate m1", gates_m[1], 0, 1, 5)
            norm_pool(pool, "L0m")
            norm_pool(pool, "C0m")
            norm_pool(pool, "L1a")
            norm_pool(pool, "C1a")
            rw_pool(pool)
            readout_pool(pool)
            norm_pool(pool, "L1m")
            pool.wait_ge(*when(("L1m", "normed", 0)))
            gate_load(pool, "gate n", gates_m[0], 1, 0, 5)
            norm_pool(pool, "pre0")
            norm_pool(pool, "mix0")
            even_pool(pool)
            even_pool_rstd(pool)
            mem_load(pool, 0)
            norm_pool(pool, "xm0")
            norm_pool(pool, "xx0")
            xmem_pool(pool, 0)
            norm_pool(pool, "post0")
            norm_pool(pool, "pre1")
            norm_pool(pool, "mix1")
            mla_pool(pool)
            mla_pool_rstd(pool)
            mem_load(pool, 1)
            norm_pool(pool, "xm1")
            norm_pool(pool, "xx1")
            xmem_pool(pool, 1)
            norm_pool(pool, "post1")
    return now


_DIRECT = ["x", "ctx", "ada_w", "ada_b", "ab_w_in", "ab_gate_b", "na_rpb", "ab_w_out", "rw_w_rkv", "rw_w1", "rw_w2",
           "rw_a1", "rw_a2", "rw_g1", "rw_g2", "rw_w_o", "mlp_w1", "mlp_w2", "mem_2", "positions_2",
           "ffn_pre_w_gu_2", "ffn_pre_w_down_2", "sbg_w_in_2", "sgu_w_2", "sgu_ln_gain_2", "sgu_ln_bias_2", "sbg_w_out_2", "mla_w_in_2", "mla_w_uq_2",
           "mla_w_ukv_2", "mla_q_gain_2", "mla_k_gain_2", "mla_w_out_2", "xmem_wq_2", "xmem_wkv_2", "xmem_wo_2",
           "ffn_post_w_gu_2", "ffn_post_w_down_2"]
_VEC_A = ["rw_mu", "rw_w0", "rw_a0", "rw_k_k", "rw_k_a", "rw_r_k", "rw_lnx_w", "rw_lnx_b", "ml_head_norm",
          "na_q_norm", "na_q_norm", "na_k_norm", "na_k_norm"]
_VEC_B = ["ffn_pre_norm_2", "mix_norm_2", "xmem_norm_2", "xmem_mem_norm_2", "ffn_post_norm_2", "sgu_ln_gain_2",
          "sgu_ln_bias_2", "mla_q_lora_gain_2", "mla_kv_lora_gain_2", "xmem_q_gain_2", "xmem_k_gain_2", "sgu_b_2",
          "c", "c_ctx"]


def kernel(**inputs):
    import concourse.bacc as _bacc
    from concourse.bass_utils import run_bass_kernel_spmd as _run

    arrays = {name: np.ascontiguousarray(inputs[name]) for name in _DIRECT}
    arrays["vec_a"] = np.concatenate([np.asarray(inputs[n]).reshape(-1) for n in _VEC_A]).reshape(-1, P)
    arrays["vec_b"] = np.concatenate([np.asarray(inputs[n]).reshape(-1) for n in _VEC_B]).reshape(-1, P)
    arrays["const"] = np.ascontiguousarray(np.concatenate(list(constant_blocks().values()), axis=1))

    noted = None
    for _ in range(2):
        nc = _bacc.Bacc("TRN2", target_bir_lowering=False, num_devices=1)
        a = {name: nc.dram_tensor(f"in_{name}", v.shape, mybir.dt.from_np(v.dtype), kind="ExternalInput").ap()
             for name, v in arrays.items()}
        out = nc.dram_tensor("out", (1, T, D), F32, kind="ExternalOutput").ap()
        scratch_mod = nc.dram_tensor("modulation", (2, 2, 6 * D), F32, kind="Internal").ap()
        scratch_rpb = nc.dram_tensor("bias_rows", (56, 64, 127), F32, kind="Internal").ap()
        noted = bidir_dual_stack(nc, a, out, scratch_mod, scratch_rpb, noted)
    r = _run(nc, [{f"in_{name}": v for name, v in arrays.items()}], core_ids=[0])
    return r.results[0]["out"]
```

```python
from contextlib import ExitStack

import numpy as np

import concourse.bass as bass
from concourse import mybir

ALU = mybir.AluOpType
ACT = mybir.ActivationFunctionType
F32 = mybir.dt.float32
F32R = mybir.dt.float32r
I32 = mybir.dt.int32
AX = mybir.AxisListType

P = 128
T = 256
D = 1024
KT = D // P
RING = 3
SLAB = 8 * 512
EPS = 1e-6
NEG = -1e30
GRID_W = 64
D_FF = 4096
D_FF2 = 2816
C = 64
NCH = 2 * T // C


def constant_blocks():
    p = np.arange(P)[:, None]
    f = np.arange(P)[None, :]
    s64, t64 = np.arange(P)[:, None] % C, np.arange(C)[None, :]
    col, key = np.arange(P)[:, None] % GRID_W, np.arange(GRID_W)[None, :]
    start = np.clip(col - 8, 0, GRID_W - 16)
    blocks = {
        "ident": p == f,
        "headones": (p // 64) == (f // 64),
        "causal_add": np.where(f <= p, 0.0, NEG),
        "strict": f < p,
        "strict_add": np.where(f < p, 0.0, NEG),
        "window_add": np.where((key >= start) & (key < start + 16), 0.0, NEG),
        "st_fwd": p <= f,
        "st_bwd": p >= f,
        "eye64": s64 == t64,
        "diag16": s64 // 16 == t64 // 16,
        "off32": (s64 // 32 == t64 // 32) & (s64 // 16 != t64 // 16),
        "off64": s64 // 32 != t64 // 32,
        "ones": np.ones((P, 64)),
        "chunk_start": np.broadcast_to(np.arange(512) % C != 0, (P, 512)),
    }
    one = np.ones((P, C))
    for z, (lt, le, gt) in enumerate([(s64 < t64, s64 <= t64, s64 > t64), (s64 > t64, s64 >= t64, s64 < t64)]):
        blocks[f"gram{z}"] = np.concatenate([lt, one, le, lt, one, le, gt], axis=1)
    sel = np.zeros((P, 4, P))
    for h in range(4):
        sel[h, h] = 1.0
    blocks["select4"] = sel.reshape(P, -1)
    tok = np.arange(T)
    inv = (10000.0 ** (-np.arange(32, dtype=np.float32) / 32)).astype(np.float32)
    ang = np.stack([(tok // GRID_W).astype(np.float32)[:, None] * inv,
                    (tok % GRID_W).astype(np.float32)[:, None] * inv], axis=1)
    for name, fn in (("cos2d", np.cos), ("sin2d", np.sin)):
        blocks[name] = fn(ang).reshape(2, P, 64).transpose(1, 0, 2).reshape(P, P)
    blocks["inv_freq"] = np.broadcast_to(
        (10000.0 ** (-np.arange(16, dtype=np.float32) / 16)).astype(np.float32), (P, 16))
    return {k: np.asarray(v, np.float32) for k, v in blocks.items()}


def constant_columns():
    at, out = 0, {}
    for name, b in constant_blocks().items():
        out[name] = (at, b.shape[1])
        at += b.shape[1]
    return out, at


ROWS_A, ROWS_B = {}, {}
for _rows, _list in ((ROWS_A, [("mu", 48), ("w0", 16), ("a0", 16), ("k_k", 8), ("k_a", 8), ("r_k", 8),
                               ("lnx_w", 8), ("lnx_b", 8), ("head_norm", 4), ("na_q", 1), ("na_k", 1)]),
                     (ROWS_B, [("ffn_pre", 16), ("mix", 16), ("xmem", 16), ("xmem_mem", 16), ("ffn_post", 16),
                               ("ln_gain", 4), ("ln_bias", 4), ("q_lora", 4), ("kv_lora", 2), ("xq", 4),
                               ("xk", 4), ("sgu_b", 8), ("c", 8), ("c_ctx", 8)])):
    _at = 0
    for _name, _n in _list:
        _rows[_name] = _at
        _at += _n
    _rows["rows"] = _at


class Side:

    def __init__(self, eng, name):
        self.eng, self.name, self.passed = eng, name, {}

    def wait_ge(self, sem, value):
        if self.passed.get(sem.name, 0) < value:
            self.eng.wait_ge(sem, value)
            self.passed[sem.name] = value


def bidir_dual_stack(nc, a, out, scratch_mod, scratch_rpb, noted):
    const_at, n_const = constant_columns()

    with ExitStack() as ctx:
        def sb(name, shape, dt=F32):
            return ctx.enter_context(nc.sbuf_tensor(name, shape, dt))

        sems, count, now, stages, own, tiles = {}, {}, {}, {}, {}, {}

        def sem(name):
            if name not in sems:
                sems[name] = ctx.enter_context(nc.semaphore(name))
            return sems[name]

        def stage(side, name):
            stages[side.name] = name

        def add(name, by, event):
            count[name] = count.get(name, 0) + by
            if event is not None:
                now[event] = (name, count[name])
            return sem(name)

        def up(side, event=None):
            name = f"{stages[side.name]}_by_{side.name}"
            own[side.name] = (add(name, 1, event), count[name])
            return own[side.name][0], 1

        def landing(event):
            return add("landed_" + str(event).replace(" ", "_"), 16, ("dma", event))

        def latest(side):
            return own[side.name]

        def when(event):
            if noted is None:
                return sem("uncounted"), 1
            name, value = noted[event]
            return sem(name), value

        def also(event, same):
            now[event] = now[same]

        def bank(b, tile):
            last, tiles[b] = tiles.get(b), tile
            return (sem("setup_by_pe"), 0) if last is None else when(("read", last))

        x = sb("x", [P, 2, D])
        cx = sb("cx", [P, 2, D])
        hT = sb("hT", [P, KT, 2 * T])
        sc = sb("sc", [P, 6, 512])
        sc2 = sb("sc2", [P, 3, 512])
        const = sb("const", [P, n_const])
        colA = sb("colA", [P, P])
        colB = sb("colB", [P, P])
        modcol = sb("modcol", [P, 2, 96])
        csil = sb("csil", [P, KT, 2])
        stat = sb("stat", [P, 256])
        half = sb("half", [P, 64])
        gbc = sb("gbc", [P, 192])
        epsc = sb("epsc", [P, 2])
        ARENA = 23588
        with ExitStack() as same_place:
            ring = same_place.enter_context(nc.sbuf_tensor("ring", [P, RING, SLAB], F32))
            arena = same_place.enter_context(nc.sbuf_tensor("arena", [P, ARENA], F32))
        ring_parts = sb("ring_parts", [P, RING, SLAB], F32R)
        arena_parts = sb("arena_parts", [P, ARENA], F32R)
        psum = ctx.enter_context(nc.psum_tensor("psum", [P, 8, 512], F32))

        def cst(name, n=P):
            at, w = const_at[name]
            return const[0:n, at:at + w]

        def area(at, *shape, rounded=False):
            n = int(np.prod(shape))
            v = (arena_parts if rounded else arena)[:, at:at + n]
            if len(shape) == 1:
                return v
            names = "abcde"[:len(shape)]
            return v.rearrange(f"p ({' '.join(names)}) -> p {' '.join(names)}",
                               **{k: s for k, s in zip(names[1:], shape[1:])})

        ident = cst("ident")

        slabs = []

        def plan(name, w, nk, n0, nn, k0=0, at=0):
            src = w[k0 * P:(k0 + nk) * P, n0:n0 + nn].rearrange("(k p) n -> p k n", p=P)
            if slabs and slabs[-1][0] == name:
                slabs[-1][1].append((nk, at, nn, src))
            else:
                slabs.append((name, [(nk, at, nn, src)]))

        def plan_rows(name, w, nk_total, n_total):
            for n in range(0, n_total, 512):
                for k in range(0, nk_total, 8):
                    plan((name, n // 512, k // 8), w, min(8, nk_total - k), n, min(512, n_total - n), k)

        def plan_ffn(name, gu, down):
            for n in range(0, D_FF2, 256):
                plan((name + "_gu", n // 256, 0), gu, KT, n, 256)
                plan((name + "_gu", n // 256, 0), gu, KT, D_FF2 + n, 256, at=256)
            plan_rows(name + "_down", down, D_FF2 // P, D)

        for layer in range(2):
            plan_rows(f"ada{layer}", a["ada_w"][layer], KT, 6 * D)
        plan_rows("ab_in", a["ab_w_in"][0], KT, 3600)
        plan_rows("ab_out", a["ab_w_out"][0], KT, D)
        plan_rows("mlp0_up", a["mlp_w1"][0], KT, D_FF)
        plan_rows("mlp0_down", a["mlp_w2"][0], D_FF // P, D)
        for w in ("w1", "a1"):
            for z in range(2):
                plan((w, 0, 0), a["rw_" + w][0, z], KT, 0, 64, at=64 * z)
        plan_rows("g1", a["rw_g1"][0], KT, 160)
        for i, w in enumerate("rkv"):
            plan_rows("rw_" + w, a["rw_w_rkv"][0, i], KT, D)
        plan_rows("rw_o", a["rw_w_o"][0], KT, D)
        plan_rows("mlp1_up", a["mlp_w1"][1], KT, D_FF)
        plan_rows("mlp1_down", a["mlp_w2"][1], D_FF // P, D)
        for layer in range(2):
            plan_ffn(f"pre{layer}", a["ffn_pre_w_gu_2"][layer], a["ffn_pre_w_down_2"][layer])
            if layer == 0:
                plan_rows("sbg_in", a["sbg_w_in_2"][0], KT, 2560)
                plan_rows("sbg_out", a["sbg_w_out_2"][0], KT, D)
            else:
                plan_rows("mla_in", a["mla_w_in_2"][0], KT, 800)
                plan_rows("mla_uq", a["mla_w_uq_2"][0], 4, 1536)
                plan_rows("mla_ukv", a["mla_w_ukv_2"][0], 2, 2048)
                plan_rows("mla_out", a["mla_w_out_2"][0], KT, D)
            plan_rows(f"xkv{layer}", a["xmem_wkv_2"][layer], KT, 2 * D)
            plan_rows(f"xq{layer}", a["xmem_wq_2"][layer], KT, D)
            plan_rows(f"xo{layer}", a["xmem_wo_2"][layer], KT, D)
            plan_ffn(f"post{layer}", a["ffn_post_w_gu_2"][layer], a["ffn_post_w_down_2"][layer])
        slab_at = {name: i for i, (name, _) in enumerate(slabs)}

        def slab(pe, name):
            i = slab_at[name]
            pe.wait_ge(*when(("slab", i)))
            return ring[:, i % RING, :].rearrange("p (k n) -> p k n", k=8)

        x_parts = [area(at, 8, 256, rounded=True) for at in (11264, 13312)]
        split_at = {}
        highs = area(15360, 2, 8, 512, rounded=True)

        def ffn_slabs(key):
            return [(key + "_gu", n, 0) for n in range(11)] + [(key + "_down", n, k) for n in range(2) for k in range(3)]

        for key in ("pre0", "post0", "pre1", "post1"):
            for name in ffn_slabs(key):
                split_at[name] = len(split_at)
        split_names = list(split_at)

        def slab_rows(name):
            return sum(piece[0] for piece in slabs[slab_at[name]][1]) if name[0].endswith("_down") else KT

        def raw_view(name):
            return ring[:, slab_at[name] % RING, :].rearrange("p (k n) -> p k n", k=8)

        def low_view(name):
            return ring_parts[:, slab_at[name] % RING, :].rearrange("p (k n) -> p k n", k=8)

        def high_view(name):
            return highs[:, split_at[name] % 2]

        def high_act(act, name):
            stage(act, "split")
            act.wait_ge(*when(("slab", slab_at[name])))
            if split_at[name] >= 2:
                act.wait_ge(*when(("used", slab_at[split_names[split_at[name] - 2]])))
            rows = slab_rows(name)
            for h in range(2):
                k = slice(4 * h, min(4 * h + 4, rows))
                nc.scalar.copy(high_view(name)[:, k, :], raw_view(name)[:, k, :]).then_inc(*up(act, ("high", name, h)))

        def low_dve(dve, name, h):
            stage(dve, "split")
            k = slice(4 * h, min(4 * h + 4, slab_rows(name)))
            dve.wait_ge(*when(("high", name, h)))
            nc.vector.tensor_tensor(low_view(name)[:, k, :], raw_view(name)[:, k, :],
                                    high_view(name).bitcast(F32)[:, k, :], ALU.subtract)\
                .then_inc(*up(dve, ("low", name, h)))

        def parts(name):
            high, low = high_view(name), low_view(name)
            return ((high, 0), (high, 1), (low, 0))

        def rows3_pe(pe, name, lhs, kt, banks, needs=()):
            stage(pe, "rows")
            for event in needs:
                pe.wait_ge(*when(event))
            for n in range(2):
                for k0 in range(0, kt, 8):
                    w = (name, n, k0 // 8)
                    nk = min(8, kt - k0)
                    for t in range(2):
                        b = banks[2 * n + t]
                        if k0 == 0:
                            pe.wait_ge(*bank(b, (name, n, t)))
                        for k in range(nk):
                            if k % 4 == 0:
                                pe.wait_ge(*when(("low", w, k // 4)))
                            for i, (s, q) in enumerate(parts(w)):
                                ins = nc.tensor.matmul(psum[:, b, :], lhs[q][:, k0 + k, P * t:P * t + P], s[:, k, :],
                                                       start=(k0 + k == 0 and i == 0), stop=(k0 + k == kt - 1 and i == 2))
                        if k0 + nk == kt and t == 0:
                            ins.then_inc(*up(pe, (name, "full", n, t)))
                    if k0 + nk == kt:
                        ins.then_inc(*up(pe, (name, "full", n, 1)))
                        also(("used", slab_at[w]), (name, "full", n, 1))
                    else:
                        ins.then_inc(*up(pe, ("used", slab_at[w])))

        norms = []

        def norm_stat(who, key):
            if key not in norms:
                norms.append(key)
            i = norms.index(key)
            if who is not None and i >= 2:
                who.wait_ge(*when((norms[i - 2], "normed", 1)))
            return stat[:, 208 + 8 * (i % 2):216 + 8 * (i % 2)]

        def norm_act(act, key, src, needs=()):
            stage(act, "norm")
            for event in needs:
                act.wait_ge(*when(event))
            s = norm_stat(act, key)
            for t in range(2):
                nc.scalar.activation(sc[:, 4:6, :].rearrange("p a b -> p (a b)"), src[:, t, :], ACT.Square,
                                            accum_out=s[:, t:t + 1]).then_inc(*up(act, (key, "squares", t)))
                act.wait_ge(*latest(act))

        def norm_pool(pool, key):
            stage(pool, "norm")
            pool.wait_ge(*when((key, "squares", 1)))
            s = norm_stat(pool, key)
            nc.gpsimd.tensor_scalar(s[:, 2:4], s[:, 0:2], 1.0 / D, EPS, ALU.mult, ALU.add).then_inc(*up(pool))
            pool.wait_ge(*latest(pool))
            nc.gpsimd.tensor_tensor(s[:, 4:6], s[:, 2:4], half[:, 0:2], ALU.pow).then_inc(*up(pool, (key, "rstd")))
            pool.wait_ge(*latest(pool))

        def norm_dve(dve, key, src, off, scale, shift=None, plus1=False, split=None):
            stage(dve, "norm")
            dve.wait_ge(*when((key, "rstd")))
            s = norm_stat(None, key)
            for t in range(2):
                xn = sc[:, 2 * t:2 * t + 2, :].rearrange("p a b -> p (a b)")
                nc.vector.tensor_scalar(xn, src[:, t, :], s[:, 4 + t:5 + t], None, ALU.mult).then_inc(*up(dve, (key, "normed", t)))
                dve.wait_ge(*latest(dve))
            if plus1:
                nc.vector.tensor_scalar(stat[:, 8:16], scale, 1.0, None, ALU.add).then_inc(*up(dve, (key, "scale")))
                dve.wait_ge(*latest(dve))
                scale = stat[:, 8:16]
            if split is not None:
                low_dve(dve, split, 0)
                stage(dve, "norm")
            for b in range(4):
                dve.wait_ge(*when((key, "turned", b)))
                for k in (2 * b, 2 * b + 1):
                    src_ = psum[:, b + 4, 256 * (k % 2):256 * (k % 2) + 256]
                    dst = hT[:, k, off:off + 256]
                    if split is not None:
                        nc.vector.tensor_scalar(x_parts[0][:, k, :], src_, scale[:, k:k + 1], None, ALU.mult)\
                            .then_inc(*up(dve))
                        dve.wait_ge(*latest(dve))
                        ins = nc.vector.scalar_tensor_tensor(x_parts[1][:, k, :], src_, scale[:, k:k + 1],
                                                             x_parts[0].bitcast(F32)[:, k, :],
                                                             ALU.mult, ALU.subtract)
                    elif shift is None:
                        ins = nc.vector.tensor_scalar(dst, src_, scale[:, k:k + 1], None, ALU.mult)
                    else:
                        ins = nc.vector.tensor_scalar(dst, src_, scale[:, k:k + 1], shift[:, k:k + 1],
                                                      ALU.mult, ALU.add)
                    ins.then_inc(*up(dve, ("read", (key, b)) if k % 2 else None))

        def norm_pe(pe, key):
            stage(pe, "norm")
            norm_stat(None, key)
            for b in range(4):
                pe.wait_ge(*bank(b + 4, (key, b)))
                for k in (2 * b, 2 * b + 1):
                    for t in range(2):
                        pe.wait_ge(*when((key, "normed", t)))
                        at = 256 * (k % 2) + 128 * t
                        ins = nc.tensor.transpose(psum[:, b + 4, at:at + 128],
                                                  sc[:, 2 * t + k // 4, 128 * (k % 4):128 * (k % 4) + 128], ident)
                ins.then_inc(*up(pe, (key, "turned", b)))

        def rows_pe(pe, name, lhs, tiles, kt, n_total, banks, needs=(), only=None):
            stage(pe, "rows")
            for event in needs:
                pe.wait_ge(*when(event))
            i = 0
            for n in range(0, n_total, 512):
                if only is not None and n // 512 not in only:
                    continue
                w = min(512, n_total - n)
                where = [banks[(i + t) % len(banks)] for t in range(len(tiles))]
                i += len(tiles)
                for k0 in range(0, kt, 8):
                    s = slab(pe, (name, n // 512, k0 // 8))
                    nk = min(8, kt - k0)
                    for t, tile in enumerate(tiles):
                        if k0 == 0:
                            pe.wait_ge(*bank(where[t], (name, n // 512, tile)))
                        for k in range(nk):
                            ins = nc.tensor.matmul(psum[:, where[t], 0:w], lhs(k0 + k, tile), s[:, k, 0:w],
                                                   start=(k0 + k == 0), stop=(k0 + k == kt - 1))
                        if k0 + nk == kt and t < len(tiles) - 1:
                            ins.then_inc(*up(pe, (name, "full", n // 512, tile)))
                    if k0 + nk == kt:
                        ins.then_inc(*up(pe, (name, "full", n // 512, tiles[-1])))
                        also(("used", slab_at[(name, n // 512, k0 // 8)]), (name, "full", n // 512, tiles[-1]))
                    else:
                        ins.then_inc(*up(pe, ("used", slab_at[(name, n // 512, k0 // 8)])))

        def rows_bank(name, n, i, tiles, banks):
            return banks[(n * len(tiles) + i) % len(banks)]

        HB = 12288
        modrow = area(0, 2, 6 * D)
        pad = arena[0:56, 23000:23127]
        nab = area(18448, 2, 4, 8, 64)

        def setup_sp(sp):
            nc.sync.dma_start(const[:, :], a["const"])\
                .then_inc(landing("const"), 16)
            nc.sync.dma_start(sc[0:ROWS_A["rows"], 0, 0:P], a["vec_a"])\
                .then_inc(landing("vec_a"), 16)
            nc.sync.dma_start(sc[0:ROWS_B["rows"], 1, 0:P], a["vec_b"])\
                .then_inc(landing("vec_b"), 16)

        def setup_pool(pool):
            nc.gpsimd.memset(half[:, :], -0.5).then_inc(*up(pool))
            pool.wait_ge(*latest(pool))
            nc.gpsimd.memset(pad, 0.0).then_inc(*up(pool, "pad zero"))
            pool.wait_ge(*latest(pool))
            nc.gpsimd.memset(epsc[:, 0:1], EPS).then_inc(*up(pool))
            pool.wait_ge(*latest(pool))
            pool.wait_ge(*when("pad zero"))
            nc.gpsimd.dma_start(pad.rearrange("p (a c) -> p a c", a=1)[:, :, 48:79], bass.AP(tensor=a["na_rpb"].tensor, offset=4 * 31,
                              ap=[[31, 7], [15 * 31, 8], [1, 31]]))\
                .then_inc(landing("rpb"), 16)
            nc.gpsimd.dma_start(modrow[0:2, :, :], a["ada_b"].partition_broadcast(2))\
                .then_inc(landing("ada_b"), 16)
            nc.gpsimd.dma_start(x[:, :, :], a["x"][0].rearrange("(t p) d -> p t d", p=P))\
                .then_inc(landing("x"), 16)
            nc.gpsimd.dma_start(cx[:, :, :], a["ctx"][0].rearrange("(t p) d -> p t d", p=P))\
                .then_inc(landing("ctx"), 16)
            nc.gpsimd.dma_start(gbc[:, 0:96], a["mla_q_gain_2"][0].partition_broadcast(P))\
                .then_inc(landing("q_gain"), 16)
            nc.gpsimd.dma_start(gbc[:, 96:192], a["mla_k_gain_2"][0].partition_broadcast(P))\
                .then_inc(landing("k_gain"), 16)
            nc.gpsimd.dma_start(stat[0:4, 200:204], a["ab_gate_b"][0].rearrange("(a b) -> b a", b=4), allow_slow_non_contiguous=True)\
                .then_inc(landing("gate_b"), 16)
            pool.wait_ge(*when(("dma", "rpb")))
            nc.gpsimd.dma_start(scratch_rpb, pad.unsqueeze(1).to_broadcast([56, 64, 127]))\
                .then_inc(landing("rpb rows"), 16)
            pool.wait_ge(*when(("dma", "rpb rows")))
            for r in range(4):
                qt, r2 = divmod(r, 2)
                nc.gpsimd.dma_start(nab[64 * r2:64 * r2 + 64, qt, :, :, :].rearrange("p a b c -> p (a b) c"), bass.AP(tensor=scratch_rpb.tensor, offset=(3 - r) * 8 * 64 * 127 + 63,
                                  ap=[[126, 64], [64 * 127, 32], [1, 64]]))\
                    .then_inc(landing("bias"), 16)
            pool.wait_ge(*when(("dma", "bias")))
            pool.wait_ge(*when(("dma", "const")))
            nc.gpsimd.tensor_tensor(
                nab.rearrange("p a b c d -> p (a b c) d"),
                nab.rearrange("p a b c d -> p (a b c) d"),
                cst("window_add").unsqueeze(1).to_broadcast([P, 64, 64]), ALU.add).then_inc(*up(pool, "bias ready"))
            pool.wait_ge(*latest(pool))

        def setup_pe(pe):
            pe.wait_ge(*when(("dma", "const")))
            for i, (rows, ev) in enumerate(((ROWS_A, "vec_a"), (ROWS_B, "vec_b"))):
                pe.wait_ge(*when(("dma", ev)))
                pe.wait_ge(*bank(i, ("vec", i)))
                n = rows["rows"]
                nc.tensor.transpose(psum[:, i, 0:n], sc[0:n, i, 0:P], ident[0:n, 0:n]).then_inc(*up(pe, ("vec", "turned", i)))

        def setup_dve(dve):
            for i, (col, rows) in enumerate(((colA, ROWS_A), (colB, ROWS_B))):
                dve.wait_ge(*when(("vec", "turned", i)))
                n = rows["rows"]
                nc.vector.tensor_copy(col[:, 0:n], psum[:, i, 0:n]).then_inc(*up(dve, ("read", ("vec", i))))
                dve.wait_ge(*latest(dve))

        def setup_act(act):
            act.wait_ge(*when(("read", ("vec", 1))))
            for i, name in enumerate(("c", "c_ctx")):
                nc.scalar.activation(csil[:, :, i], colB[:, ROWS_B[name]:ROWS_B[name] + 8], ACT.Silu).then_inc(*up(act, "silu c"))
                act.wait_ge(*latest(act))

        def ada_pe(pe):
            stage(pe, "ada")
            pe.wait_ge(*when("silu c"))
            for i in range(24):
                s = slab(pe, (f"ada{i // 12}", i % 12, 0))
                pe.wait_ge(*bank(i % 4, ("ada", i)))
                for k in range(KT):
                    ins = nc.tensor.matmul(psum[0:2, i % 4, :], csil[:, k, :], s[:, k, :], start=(k == 0), stop=(k == 7))
                ins.then_inc(*up(pe, ("ada", "full", i)))
                also(("used", slab_at[(f"ada{i // 12}", i % 12, 0)]), ("ada", "full", i))
            for layer in range(2):
                pe.wait_ge(*when(("dma", f"mod back {layer}")))
                pe.wait_ge(*bank(layer, ("mod", layer)))
                nc.tensor.transpose(psum[:, layer, 0:96], sc[0:96, layer, 0:P], ident[0:96, 0:96]).then_inc(*up(pe, ("mod", "turned", layer)))

        def ada_dve(dve):
            stage(dve, "ada")
            dve.wait_ge(*when(("dma", "ada_b")))
            for i in range(24):
                dve.wait_ge(*when(("ada", "full", i)))
                row = modrow[0:2, i // 12, 512 * (i % 12):512 * (i % 12) + 512]
                nc.vector.tensor_tensor(row, psum[0:2, i % 4, :], row, ALU.add).then_inc(*up(dve, ("read", ("ada", i))))
            for layer in range(2):
                dve.wait_ge(*when(("mod", "turned", layer)))
                nc.vector.tensor_copy(modcol[:, layer, :], psum[:, layer, 0:96]).then_inc(*up(dve, ("read", ("mod", layer))))
                dve.wait_ge(*latest(dve))

        def ada_pool(pool):
            stage(pool, "ada")
            for layer in range(2):
                pool.wait_ge(*when(("read", ("ada", 12 * layer + 11))))
                nc.gpsimd.dma_start(scratch_mod[layer], modrow[0:2, layer, :])\
                    .then_inc(landing(f"mod {layer}"), 16)
                pool.wait_ge(*when(("dma", f"mod {layer}")))
                pool.wait_ge(*when(("read", ("vec", 1))))
                nc.gpsimd.dma_start(sc[0:96, layer, 0:P], scratch_mod[layer].rearrange("v (r p) -> (v r) p", p=P))\
                    .then_inc(landing(f"mod back {layer}"), 16)

        def mcol(layer, vec, kind):
            at = 48 * vec + 8 * kind
            return modcol[:, layer, at:at + 8]

        def gate_load(pool, tag, dst, layer, vec, kind):
            nc.gpsimd.dma_start(dst, scratch_mod[layer, vec, kind * D:(kind + 1) * D].partition_broadcast(P))\
                .then_inc(landing(tag), 16)

        qa = area(0, 4, 512)
        ka = area(2048, 4, 512)
        va = area(4096, 4, 512)
        qb = area(6144, 4, 512)
        kb = area(8192, 4, 512)
        vb = area(10240, 4, 4, 129)
        so = area(12304, 4, 512)
        qaT = area(14352, 4, 512)
        kaT = area(16400, 4, 512)
        gates_a = (area(10240, 1024), area(11264, 1024))
        AB = ("qa", "ka", "va", "qb", "kb", "vb", "so")
        rowg = ("i_f", "f_f", "i_b", "f_b")

        def ab_in_pe(pe):
            for event in [("read", (k, b)) for k in ("L0a", "C0a") for b in range(4)]:
                pe.wait_ge(*when(event))
            rows_pe(pe, "ab_in", lambda k, t: hT[:, k, P * t:P * t + P], range(4), KT, 3584, [0, 1, 2, 3])
            stage(pe, "ab")
            s = slab(pe, ("ab_in", 7, 0))
            for g in range(4):
                pe.wait_ge(*bank(4 + g, ("gates", g)))
                for k in range(KT):
                    ins = nc.tensor.matmul(psum[0:4, 4 + g, :], s[:, k, 4 * g:4 * g + 4], hT[:, k, :],
                                           start=(k == 0), stop=(k == 7))
                ins.then_inc(*up(pe, ("gates", "full", g)))
            also(("used", slab_at[("ab_in", 7, 0)]), ("gates", "full", 3))

        def ab_in_act(act):
            stage(act, "ab_in")
            act.wait_ge(*when(("dma", "mod 1")))
            for n, name in enumerate(AB):
                for t in range(4):
                    act.wait_ge(*when(("ab_in", "full", n, t)))
                    src = psum[:, t, :]
                    event = ("read", ("ab_in", n, t))
                    if name == "so":
                        ins = nc.scalar.activation(so[:, t, :], src, ACT.Sigmoid)
                    elif name == "kb":
                        ins = nc.scalar.activation(kb[:, t, :], src, ACT.Copy, scale=128 ** -0.5)
                    elif name == "vb":
                        ins = nc.scalar.copy(vb[:, t, :, 0:128], src.rearrange("p (h d) -> p h d", h=4))
                    else:
                        ins = nc.scalar.copy({"qa": qa, "ka": ka, "va": va, "qb": qb}[name][:, t, :], src)
                    ins.then_inc(*up(act, event))

        def qk_norm_dve(dve):
            stage(dve, "qk")
            for i in range(8):
                y = (qa, ka)[i % 2][:, i // 2, :].rearrange("p (h d) -> p h d", h=8)
                sq = sc[:, i % 2, :].rearrange("p (h d) -> p h d", h=8)
                dve.wait_ge(*when(("read", ("ab_in", i % 2, i // 2))))
                if i < 2:
                    dve.wait_ge(*when(("C0a", "turned", 3)))
                nc.vector.tensor_tensor(sq, y, y, ALU.mult).then_inc(*up(dve))
                dve.wait_ge(*latest(dve))
                nc.vector.tensor_reduce(stat[:, 16 + 8 * i:24 + 8 * i], sq, AX.X, ALU.add).then_inc(*up(dve, ("qk", "squares", i)))
                dve.wait_ge(*latest(dve))
            for i in range(8):
                y = (qa, ka)[i % 2][:, i // 2, :].rearrange("p (h d) -> p h d", h=8)
                dve.wait_ge(*when(("qk", "rstd", i)))
                nc.vector.tensor_tensor(y, y, stat[:, 16 + 8 * i:24 + 8 * i].unsqueeze(2).to_broadcast([P, 8, 64]),
                                               ALU.mult).then_inc(*up(dve, ("qk", "normed", i)))
                dve.wait_ge(*latest(dve))
                if i >= 2:
                    qk_turn_out(dve, i - 2)
            qk_turn_out(dve, 6)
            qk_turn_out(dve, 7)

        def qk_turn_out(dve, i):
            dve.wait_ge(*when(("qk", "turned", i)))
            at = ROWS_A["na_q"] + i % 2
            nc.vector.tensor_scalar((qaT, kaT)[i % 2][:, :, P * (i // 2):P * (i // 2) + P],
                                           psum[:, 4 + i % 4, :].rearrange("p (f t) -> p f t", f=4),
                                           colA[:, at:at + 1], None, ALU.mult).then_inc(*up(dve, ("read", ("qkT", i))))
            dve.wait_ge(*latest(dve))

        def qk_norm_pool(pool):
            stage(pool, "qk")
            for i in range(8):
                pool.wait_ge(*when(("qk", "squares", i)))
                r = stat[:, 16 + 8 * i:24 + 8 * i]
                nc.gpsimd.tensor_scalar(r, r, 1.0 / 64, EPS, ALU.mult, ALU.add).then_inc(*up(pool))
                pool.wait_ge(*latest(pool))
                nc.gpsimd.tensor_tensor(r, r, half[:, 0:8], ALU.pow).then_inc(*up(pool, ("qk", "rstd", i)))
                pool.wait_ge(*latest(pool))

        def qk_norm_pe(pe):
            stage(pe, "qk")
            for i in range(8):
                pe.wait_ge(*when(("qk", "normed", i)))
                pe.wait_ge(*bank(4 + i % 4, ("qkT", i)))
                for f in range(4):
                    ins = nc.tensor.transpose(psum[:, 4 + i % 4, P * f:P * f + P],
                                              (qa, ka)[i % 2][:, i // 2, P * f:P * f + P], ident)
                ins.then_inc(*up(pe, ("qk", "turned", i)))

        def unit_tick(n, *steps):
            for i in range(n + len(steps) - 1):
                for j, step in enumerate(steps):
                    if step is not None and 0 <= i - j < n:
                        yield step, i - j

        def att_pe(pe, key, units, needs=()):
            stage(pe, "att")
            for event in needs:
                pe.wait_ge(*when(event))

            def scores(i):
                u = units[i]
                pe.wait_ge(*bank(i % 2, (key, "s", i)))
                n = len(u["qk"])
                for j, (l, r) in enumerate(u["qk"]):
                    ins = nc.tensor.matmul(psum[:, i % 2, 0:u["keys"]], l, r, start=(j == 0), stop=(j == n - 1))
                ins.then_inc(*up(pe, (key, "scores", i)))

            def turn(i):
                u = units[i]
                pe.wait_ge(*when((key, "probs", i)))
                pe.wait_ge(*bank(2 + i % 2, (key, "t", i)))
                for k in range(u["keys"] // P):
                    ins = nc.tensor.transpose(psum[:, 2 + i % 2, P * k:P * k + P], sc2[:, i % 2, P * k:P * k + P], ident)
                ins.then_inc(*up(pe, (key, "turned", i)))

            def values(i):
                u = units[i]
                pe.wait_ge(*when((key, "probsT", i)))
                pe.wait_ge(*bank(4 + i % 2, (key, "o", i)))
                nk = u["keys"] // P
                for j, (vs, part) in enumerate(u["v"]):
                    for k in range(nk):
                        v = vs(k)
                        w = v.shape[-1]
                        ins = nc.tensor.matmul(psum[part:part + w, 4 + i % 2, P * j:P * j + P], v,
                                               sc[:, 4 + i % 2, P * k:P * k + P], start=(k == 0), stop=(k == nk - 1))
                ins.then_inc(*up(pe, (key, "out", i)))

            for step, i in unit_tick(len(units), scores, None, turn, values):
                step(i)

        def att_dve(dve, key, units, scale, probs=True, after_first=()):
            stage(dve, "att")

            def maximum(i):
                u = units[i]
                n, s, b = u["keys"], sc[:, i % 2, :], psum[:, i % 2, :]
                dve.wait_ge(*when((key, "scores", i)))
                if i == 0:
                    for event in after_first:
                        dve.wait_ge(*when(event))
                m = stat[:, 96 + 2 * (i % 4):97 + 2 * (i % 4)]
                nm = stat[:, 97 + 2 * (i % 4):98 + 2 * (i % 4)]
                if u["bias"] is None:
                    nc.vector.tensor_reduce(m, b[:, 0:n], AX.X, ALU.max, negate=True).then_inc(*up(dve))
                    dve.wait_ge(*latest(dve))
                    nc.vector.tensor_scalar(nm, m, scale, None, ALU.mult).then_inc(*up(dve, (key, "max", i)))
                    dve.wait_ge(*latest(dve))
                else:
                    at = 0
                    if i >= 2:
                        dve.wait_ge(*when((key, "exp", i - 2)))
                    for w, bias in u["bias"]:
                        if bias is None:
                            ins = nc.vector.tensor_scalar(s[:, at:at + w], b[:, at:at + w], scale, None, ALU.mult)
                        else:
                            o, y = s[:, at:at + w], b[:, at:at + w]
                            if len(bias.shape) == 3:
                                o, y = (v.rearrange("p (a b) -> p a b", b=bias.shape[2]) for v in (o, y))
                            ins = nc.vector.scalar_tensor_tensor(o, y, scale, bias, ALU.mult, ALU.add)
                        at += w
                        ins.then_inc(*up(dve, ("read", (key, "s", i)) if at == n else None))
                        dve.wait_ge(*latest(dve))
                    nc.vector.tensor_reduce(nm, s[:, 0:n], AX.X, ALU.max, negate=True).then_inc(*up(dve, (key, "max", i)))
                    dve.wait_ge(*latest(dve))

            def normalise(i):
                u = units[i]
                n = u["keys"]
                dve.wait_ge(*when((key, "exp", i)))
                rs, ri = stat[:, 104 + i % 4:105 + i % 4], stat[:, 108 + i % 4:109 + i % 4]
                nc.vector.reciprocal(ri, rs).then_inc(*up(dve))
                dve.wait_ge(*latest(dve))
                if i >= 2:
                    dve.wait_ge(*when((key, "turned", i - 2)))
                nc.vector.tensor_scalar(sc2[:, i % 2, 0:n], sc[:, 2 + i % 2, 0:n], ri, None, ALU.mult).then_inc(*up(dve, (key, "probs", i)))
                dve.wait_ge(*latest(dve))

            for step, i in unit_tick(len(units), maximum, normalise):
                step(i)

        def att_act(act, key, units, scale, needs=()):
            stage(act, "att")
            for event in needs:
                act.wait_ge(*when(event))

            def exponent(i):
                u = units[i]
                n = u["keys"]
                act.wait_ge(*when((key, "max", i)))
                nm = stat[:, 97 + 2 * (i % 4):98 + 2 * (i % 4)]
                if i >= 2:
                    act.wait_ge(*when((key, "probs", i - 2)))
                src = psum[:, i % 2, 0:n] if u["bias"] is None else sc[:, i % 2, 0:n]
                nc.scalar.activation(sc[:, 2 + i % 2, 0:n], src, ACT.Exp, bias=nm,
                                            scale=scale if u["bias"] is None else 1.0,
                                            accum_out=stat[:, 104 + i % 4:105 + i % 4]).then_inc(*up(act, (key, "exp", i)))
                if u["bias"] is None:
                    also(("read", (key, "s", i)), (key, "exp", i))

            for step, i in unit_tick(len(units), exponent, None, lambda i: att_probsT(act, key, units, i),
                                     lambda i: att_out(act, key, units, i)):
                step(i)

        def att_probsT(act, key, units, i):
            n = units[i]["keys"]
            act.wait_ge(*when((key, "turned", i)))
            if i >= 2:
                act.wait_ge(*when((key, "out", i - 2)))
            nc.scalar.copy(sc[:, 4 + i % 2, 0:n], psum[:, 2 + i % 2, 0:n]).then_inc(*up(act, (key, "probsT", i)))
            also(("read", (key, "t", i)), (key, "probsT", i))

        def att_out(act, key, units, i):
            u = units[i]
            act.wait_ge(*when((key, "out", i)))
            for j, ((vs, part), dst) in enumerate(zip(u["v"], u["dst"])):
                w = dst.shape[0]
                nc.scalar.copy(dst, psum[part:part + w, 4 + i % 2, P * j:P * j + P]).then_inc(*up(act, ("read", (key, "o", i)) if j == len(u["v"]) - 1 else None))

        def head_rows(h):
            return slice(64 * (h % 2), 64 * (h % 2) + 64)

        def na_units():
            us = []
            for h in range(8):
                for qt in range(2):
                    r, f = head_rows(h), h // 2
                    us.append(dict(keys=512, qk=[(qaT[r, f, P * qt:P * qt + P], kaT[r, f, :])],
                                   bias=[(256, nab[:, qt, :, h, :]), (256, None)],
                                   v=[(lambda k, h=h: va[:, k, 64 * h:64 * h + 64], r.start)],
                                   dst=[hT[r, f, P * qt:P * qt + P]]))
            return us

        def ctx_units():
            us = []
            for h in range(8):
                for qt in range(2):
                    r, f = head_rows(h), h // 2
                    us.append(dict(keys=256, qk=[(qaT[r, f, 256 + P * qt:256 + P * qt + P], kaT[r, f, 256:512])],
                                   bias=None, v=[(lambda k, h=h: va[:, 2 + k, 64 * h:64 * h + 64], r.start)],
                                   dst=[hT[r, f, 256 + P * qt:256 + P * qt + P]]))
            return us

        na, cxa = na_units(), ctx_units()

        R0 = 14352
        gi = area(R0, 2, 512)
        gl = area(R0 + 1024, 2, 512)
        gb = area(R0 + 2048, 2, 512)
        gm = area(R0 + 3072, 2, 512)
        gw = area(R0 + 4096, 2, 512)
        gv = area(R0 + 5120, 2, 512)
        ge = area(R0 + 6144, 2, 512)
        mlD = area(R0 + 7168, 2, 512)
        capped = [v[p:p + 4] for v in (area(22544, 512), sc2[:, 2, :]) for p in (0, 32)]
        mst = stat[:, 112:128].rearrange("p (z s) -> p z s", z=2)
        qbT = area(0, 4, 512)
        kbT = area(2048, 4, 512)
        mlc = sc2[:, 2, 0:128].rearrange("p (q z t h) -> p q z t h", q=4, z=2, t=4)
        dec = sc2[:, 2, 128:160].rearrange("p (h z t) -> p h z t", h=4, z=2)
        hs = area(4096, 4, 4, 128)
        mlW = sc[:, 0:2, :]
        mlK = sc[:, 2:4, :]
        mlX = sc[:, 4, :]
        mlC = sc2[:, 0:2, 0:129]
        mlY = sc2[:, 0:2, 256:385]
        rope_t = sc2
        ORDER = ((2, 3, 0, 1), (3, 2, 1, 0))

        def gates_act(act):
            stage(act, "gates")
            act.wait_ge(*when("gatecol"))
            act.wait_ge(*when(("dma", "rpb rows")))
            for g in range(4):
                act.wait_ge(*when(("gates", "full", g)))
                nc.scalar.activation(capped[g], psum[0:4, 4 + g, :], ACT.Tanh, bias=stat[0:4, 204 + g:205 + g],
                                            scale=1 / 15.0).then_inc(*up(act, ("read", ("gates", g))))
                act.wait_ge(*latest(act))

        def softplus_act(act):
            stage(act, "softplus")
            act.wait_ge(*when(("na", "probs", 15)))
            act.wait_ge(*when(("cx", "probs", 15)))
            act.wait_ge(*when(("cx", "out", 15)))
            for z in range(2):
                nc.scalar.activation(gl[0:4, z, :], capped[2 * z + 1], ACT.Exp, scale=-15.0).then_inc(*up(act))
                act.wait_ge(*latest(act))
            nc.scalar.activation(gl[0:4], gl[0:4], ACT.Ln, bias=1.0).then_inc(*up(act, "softplus f"))
            act.wait_ge(*latest(act))

        def gates_dve(dve):
            stage(dve, "gates")
            dve.wait_ge(*when(("dma", "gate_b")))
            nc.vector.tensor_scalar(stat[0:4, 204:208], stat[0:4, 200:204], 1 / 15.0, None, ALU.mult).then_inc(*up(dve, "gatecol"))
            dve.wait_ge(*latest(dve))

        def scan_view(a_, z):
            return a_ if z == 0 else a_[:, ::-1]

        def decay_dve(dve):
            stage(dve, "decay")
            dve.wait_ge(*when("softplus f"))
            nc.vector.memset(mlD[0:4, 0, 0:128], 0.0).then_inc(*up(dve))
            dve.wait_ge(*latest(dve))
            nc.vector.memset(mst[0:4, :, 0:1], 0.0).then_inc(*up(dve))
            dve.wait_ge(*latest(dve))
            for z in range(2):
                for t in range(4):
                    s = slice(P * t, P * t + P)
                    nc.vector.tensor_tensor_scan(scan_view(gb[0:4, z, s], z), mlD[0:4, 0, 0:128],
                                                        scan_view(gl[0:4, z, s], z), 0.0, ALU.add, ALU.subtract).then_inc(*up(dve))
                    dve.wait_ge(*latest(dve))
            for z in range(2):
                nc.vector.scalar_tensor_tensor(gi[0:4, z, :], capped[2 * z], 15.0, gb[0:4, z, :],
                                                      ALU.mult, ALU.subtract).then_inc(*up(dve))
                dve.wait_ge(*latest(dve))
            for j in range(4):
                for z in range(2):
                    t = ORDER[z][j]
                    s = slice(P * t, P * t + P)
                    last = P * t + (127 if z == 0 else 0)
                    g = scan_view(gi[0:4, z, s], z)
                    m0 = mst[0:4, z, j:j + 1]
                    nc.vector.tensor_tensor_scan(scan_view(gm[0:4, z, s], z), g, g, m0, ALU.max, ALU.max).then_inc(*up(dve))
                    dve.wait_ge(*latest(dve))
                    nc.vector.tensor_tensor(mst[0:4, z, j + 1:j + 2], gb[0:4, z, last:last + 1],
                                                   gm[0:4, z, last:last + 1], ALU.add).then_inc(*up(dve))
                    dve.wait_ge(*latest(dve))
                    nc.vector.tensor_scalar(gw[0:4, z, s], gi[0:4, z, s], gm[0:4, z, last:last + 1], None,
                                                   ALU.subtract).then_inc(*up(dve))
                    dve.wait_ge(*latest(dve))
                    nc.vector.tensor_scalar(gv[0:4, z, s], gm[0:4, z, s], m0, None, ALU.subtract).then_inc(*up(dve))
                    dve.wait_ge(*latest(dve))
            nc.vector.tensor_tensor(ge[0:4], gb[0:4], gm[0:4], ALU.add).then_inc(*up(dve, "exponents"))
            dve.wait_ge(*latest(dve))

        def decay_act(act):
            stage(act, "decay")
            act.wait_ge(*when("exponents"))
            nc.scalar.activation(gw[0:4], gw[0:4], ACT.Exp).then_inc(*up(act))
            act.wait_ge(*latest(act))
            nc.scalar.activation(gv[0:4], gv[0:4], ACT.Exp, scale=-1.0).then_inc(*up(act))
            act.wait_ge(*latest(act))
            nc.scalar.activation(ge[0:4], ge[0:4], ACT.Exp, scale=-1.0).then_inc(*up(act, "gate rows"))
            act.wait_ge(*latest(act))

        def decay_pe(pe):
            stage(pe, "decay")
            pe.wait_ge(*when("gate rows"))
            pe.wait_ge(*bank(0, "gate columns"))
            for q, src in enumerate((gi, gw, gv, ge)):
                for z in range(2):
                    for t in range(4):
                        at = 32 * q + 16 * z + 4 * t
                        nc.tensor.transpose(psum[:, 0, at:at + 4], src[0:4, z, P * t:P * t + P], ident[0:4, 0:4])
            sel = cst("select4").rearrange("p (h m) -> p h m", h=4)
            for h in range(4):
                for z in range(2):
                    rows = gv[0:4, z, :].rearrange("p (t s) -> p t s", s=P)[:, :, (127 if z == 0 else 0)]
                    at = 128 + 8 * h + 4 * z
                    ins = nc.tensor.matmul(psum[:, 0, at:at + 4], sel[0:4, h, :], rows, start=True, stop=True)
            ins.then_inc(*up(pe, "gate columns full"))

        def decay_out_dve(dve):
            dve.wait_ge(*when("gate columns full"))
            nc.vector.tensor_copy(sc2[:, 2, 0:160], psum[:, 0, 0:160]).then_inc(*up(dve, ("read", "gate columns")))
            dve.wait_ge(*latest(dve))

        def rope_pool(pool):
            stage(pool, "rope")
            for event in [("read", ("ab_in", n, t)) for n in (3, 4) for t in range(2)]:
                pool.wait_ge(*when(event))
            for t in range(4):
                pool.wait_ge(*when(("ab_in", "full", 6, t)))
            pool.wait_ge(*when(("gates", "full", 3)))
            for y in (qb, kb):
                for t in range(2):
                    v = y[:, t, :].rearrange("p (h c u f) -> p h c u f", h=4, c=2, u=2)
                    c = cst("cos2d")[:, 64 * t:64 * t + 64].rearrange("p (c f) -> p c f", c=2)
                    s = cst("sin2d")[:, 64 * t:64 * t + 64].rearrange("p (c f) -> p c f", c=2)
                    tmp = [hT[:, 4 + j, 0:256].rearrange("p (h c f) -> p h c f", h=4, c=2) for j in range(4)]
                    for c_ in range(2):
                        for j, (half_, w) in enumerate(((0, c), (1, s), (0, s), (1, c))):
                            nc.gpsimd.tensor_tensor(tmp[j][:, :, c_, :], v[:, :, c_, half_, :],
                                                           w[:, c_, :].unsqueeze(1).to_broadcast([P, 4, 32]), ALU.mult).then_inc(*up(pool))
                            pool.wait_ge(*latest(pool))
                        nc.gpsimd.tensor_tensor(v[:, :, c_, 0, :], tmp[0][:, :, c_, :], tmp[1][:, :, c_, :],
                                                       ALU.subtract).then_inc(*up(pool))
                        pool.wait_ge(*latest(pool))
                        nc.gpsimd.tensor_tensor(v[:, :, c_, 1, :], tmp[2][:, :, c_, :], tmp[3][:, :, c_, :],
                                                       ALU.add).then_inc(*up(pool, ("roped", t)))
                        pool.wait_ge(*latest(pool))
            nc.gpsimd.memset(vb[:, :, :, 128:129], 1.0).then_inc(*up(pool, "v ones"))
            pool.wait_ge(*latest(pool))

        def mlT_pe(pe):
            stage(pe, "mlT")
            pe.wait_ge(*when(("roped", 1)))
            for event in [("read", ("ab_in", n, t)) for n in (3, 4) for t in range(4)]:
                pe.wait_ge(*when(event))
            for i in range(8):
                pe.wait_ge(*bank(4 + i % 4, ("mlT", i)))
                for h in range(4):
                    ins = nc.tensor.transpose(psum[:, 4 + i % 4, P * h:P * h + P],
                                              (qb, kb)[i % 2][:, i // 2, P * h:P * h + P], ident)
                ins.then_inc(*up(pe, ("mlT", "full", i)))

        def mlT_act(act):
            stage(act, "mlT")
            act.wait_ge(*when(("qk", "turned", 7)))
            for i in range(8):
                act.wait_ge(*when(("mlT", "full", i)))
                nc.scalar.copy((qbT, kbT)[i % 2][:, :, P * (i // 2):P * (i // 2) + P],
                                      psum[:, 4 + i % 4, :].rearrange("p (f t) -> p f t", f=4)).then_inc(*up(act, ("read", ("mlT", i))))

        def ml_pe(pe):
            stage(pe, "ml")
            pe.wait_ge(*when(("read", ("mlT", 7))))
            pe.wait_ge(*when("v ones"))
            sel = cst("select4").rearrange("p (h m) -> p h m", h=4)
            for h in range(4):
                pe.wait_ge(*bank(1, ("ml", "S", h)))
                for t in range(4):
                    ins = nc.tensor.matmul(psum[:, 1, P * t:P * t + P], kbT[:, h, P * t:P * t + P],
                                           qbT[:, h, P * t:P * t + P], start=True, stop=True)
                ins.then_inc(*up(pe, ("ml", "S full", h)))
                for z in range(2):
                    pe.wait_ge(*bank(2 + z, ("ml", "M", h, z)))
                    nc.tensor.matmul(psum[:, 2 + z, :], sel[0:4, h, :], gm[0:4, z, :], start=True, stop=True).then_inc(*up(pe, ("ml", "M full", h, z)))
                for j in range(4):
                    for z in range(2):
                        t = ORDER[z][j]
                        i = 4 * h + j
                        b = 4 + z + 2 * (j % 2)
                        s = slice(P * t, P * t + P)
                        pe.wait_ge(*bank(b, ("ml", "P", i, z)))
                        if j == 0:
                            pe.wait_ge(*when(("ml", "W", h, z)))
                            pe.wait_ge(*when(("ml", "K", h, z)))
                        nc.tensor.matmul(psum[:, b, 0:129], mlW[:, z, s], vb[:, t, h, :], start=True, stop=True)
                        nc.tensor.matmul(psum[:, b, 258:387], mlK[:, z, s], vb[:, t, h, :], start=True, stop=True)
                        pe.wait_ge(*when(("ml", "state", i, z)))
                        nc.tensor.matmul(psum[:, b, 129:258], qbT[:, h, s], mlC[:, z, :], start=True, stop=True).then_inc(*up(pe, ("ml", "P full", i, z)))

        def ml_act(act):
            stage(act, "ml")
            for h in range(4):
                for z in range(2):
                    act.wait_ge(*when(("ml", "D", h, z)))
                    nc.scalar.activation(mlD[:, z, :], mlD[:, z, :], ACT.Exp, scale=-1.0).then_inc(*up(act, ("ml", "E", h, z)))
                    act.wait_ge(*latest(act))

        def ml_pool(pool):
            stage(pool, "ml")
            pool.wait_ge(*when("v ones"))
            pool.wait_ge(*when(("read", "gate columns")))
            pool.wait_ge(*when(("roped", 1)))
            for h in range(4):
                for z in range(2):
                    if h:
                        pool.wait_ge(*when(("ml", "P full", 4 * h - 1, z)))
                    for t in range(4):
                        nc.gpsimd.tensor_scalar(mlK[:, z, P * t:P * t + P], kb[:, t, P * h:P * h + P],
                                                        mlc[:, 1, z, t, h:h + 1], None, ALU.mult).then_inc(*up(pool, ("ml", "K", h, z)))
                        pool.wait_ge(*latest(pool))

        def ml_dve(dve):
            stage(dve, "ml")
            mask = (cst("st_fwd"), cst("st_bwd"))
            for h in range(4):
                for z in range(2):
                    dve.wait_ge(*when(("ml", "M full", h, z)))
                    for t in range(4):
                        nc.vector.tensor_scalar(mlD[:, z, P * t:P * t + P], psum[:, 2 + z, P * t:P * t + P],
                                                       mlc[:, 0, z, t, h:h + 1], 0.0, ALU.subtract, ALU.max).then_inc(*up(dve, ("ml", "D", h, z)))
                    also(("read", ("ml", "M", h, z)), ("ml", "D", h, z))
                for z in range(2):
                    dve.wait_ge(*when(("ml", "E", h, z)))
                    dve.wait_ge(*when(("ml", "S full", h)))
                    if h:
                        dve.wait_ge(*when(("ml", "P full", 4 * h - 1, z)))
                    nc.vector.tensor_tensor(mlD[:, z, :].rearrange("p (t s) -> p t s", t=4),
                                                   mlD[:, z, :].rearrange("p (t s) -> p t s", t=4),
                                                   mask[z].unsqueeze(1).to_broadcast([P, 4, P]), ALU.mult).then_inc(*up(dve))
                    dve.wait_ge(*latest(dve))
                    nc.vector.tensor_tensor(mlW[:, z, :], psum[:, 1, :], mlD[:, z, :], ALU.mult).then_inc(*up(dve, ("ml", "W", h, z)))
                    dve.wait_ge(*latest(dve))
                    nc.vector.memset(mlC[:, z, :], 0.0).then_inc(*up(dve, ("ml", "state", 4 * h, z)))
                    dve.wait_ge(*latest(dve))
                also(("read", ("ml", "S", h)), ("ml", "W", h, 1))
                for j in range(4):
                    for z in range(2):
                        t = ORDER[z][j]
                        i = 4 * h + j
                        b = 4 + z + 2 * (j % 2)
                        y, den = mlY[:, z, :], stat[:, 128 + z:129 + z]
                        dve.wait_ge(*when(("ml", "P full", i, z)))
                        if j < 3:
                            nc.vector.scalar_tensor_tensor(mlC[:, z, :], mlC[:, z, :], dec[:, h, z, t:t + 1],
                                                                  psum[:, b, 258:387], ALU.mult, ALU.add).then_inc(*up(dve, ("ml", "state", i + 1, z)))
                            dve.wait_ge(*latest(dve))
                        nc.vector.tensor_scalar(y, psum[:, b, 129:258], mlc[:, 2, z, t, h:h + 1], None, ALU.mult).then_inc(*up(dve))
                        dve.wait_ge(*latest(dve))
                        nc.vector.tensor_tensor(y, psum[:, b, 0:129], y, ALU.add).then_inc(*up(dve, ("read", ("ml", "P", i, z))))
                        dve.wait_ge(*latest(dve))
                        nc.vector.tensor_scalar(den, y[:, 128:129], -1.0, mlc[:, 3, z, t, h:h + 1],
                                                       ALU.mult, ALU.max).then_inc(*up(dve))
                        dve.wait_ge(*latest(dve))
                        nc.vector.tensor_tensor(den, den, y[:, 128:129], ALU.max).then_inc(*up(dve))
                        dve.wait_ge(*latest(dve))
                        nc.vector.reciprocal(den, den).then_inc(*up(dve))
                        dve.wait_ge(*latest(dve))
                        seen_first = ORDER[0].index(t) < ORDER[1].index(t) or (ORDER[0].index(t) == ORDER[1].index(t))
                        first = (z == 0) if seen_first else (z == 1)
                        if first:
                            nc.vector.tensor_scalar(hs[:, t, h, :], y[:, 0:128], den, None, ALU.mult).then_inc(*up(dve))
                            dve.wait_ge(*latest(dve))
                        else:
                            nc.vector.scalar_tensor_tensor(hs[:, t, h, :], y[:, 0:128], den, hs[:, t, h, :],
                                                                  ALU.mult, ALU.add).then_inc(*up(dve, ("ml", "h", i, z)))
                            dve.wait_ge(*latest(dve))

        def merge_dve(dve):
            stage(dve, "merge")
            for t in range(4):
                nc.vector.tensor_tensor(sc[:, t % 2, :].rearrange("p (h d) -> p h d", h=4), hs[:, t], hs[:, t],
                                               ALU.mult).then_inc(*up(dve))
                dve.wait_ge(*latest(dve))
                nc.vector.tensor_reduce(stat[:, 16 + 4 * t:20 + 4 * t],
                                               sc[:, t % 2, :].rearrange("p (h d) -> p h d", h=4), AX.X, ALU.add).then_inc(*up(dve, ("merge", "squares")))
                dve.wait_ge(*latest(dve))
            dve.wait_ge(*when(("merge", "rstd")))
            for t in range(4):
                nc.vector.tensor_tensor(hs[:, t], hs[:, t],
                                               stat[:, 16 + 4 * t:20 + 4 * t].unsqueeze(2).to_broadcast([P, 4, P]), ALU.mult).then_inc(*up(dve))
                dve.wait_ge(*latest(dve))
                nc.vector.tensor_tensor(hs[:, t], hs[:, t], so[:, t, :].rearrange("p (h d) -> p h d", h=4),
                                               ALU.mult).then_inc(*up(dve, ("merge", "gated", t)))
                dve.wait_ge(*latest(dve))
            for t in range(4):
                dve.wait_ge(*when(("merge", "turned", t)))
                for h in range(4):
                    at = ROWS_A["head_norm"] + h
                    nc.vector.tensor_scalar(hT[:, 4 + h, P * t:P * t + P], psum[:, 4 + t, P * h:P * h + P],
                                                   colA[:, at:at + 1], None, ALU.mult).then_inc(*up(dve, ("read", ("merge", t))))

        def merge_pool(pool):
            stage(pool, "merge")
            pool.wait_ge(*when(("merge", "squares")))
            nc.gpsimd.tensor_scalar(stat[:, 16:32], stat[:, 16:32], 1.0 / 128, EPS, ALU.mult, ALU.add).then_inc(*up(pool))
            pool.wait_ge(*latest(pool))
            nc.gpsimd.tensor_tensor(stat[:, 16:32], stat[:, 16:32], half[:, 0:16], ALU.pow).then_inc(*up(pool, ("merge", "rstd")))
            pool.wait_ge(*latest(pool))

        def merge_pe(pe):
            stage(pe, "merge")
            for t in range(4):
                pe.wait_ge(*when(("merge", "gated", t)))
                pe.wait_ge(*bank(4 + t, ("merge", t)))
                for h in range(4):
                    ins = nc.tensor.transpose(psum[:, 4 + t, P * h:P * h + P], hs[:, t, h, :], ident)
                ins.then_inc(*up(pe, ("merge", "turned", t)))

        def gated_rows_dve(dve, name, tiles, banks, gates, tags):
            stage(dve, "gated")
            for event in [("dma", tag) for tag in tags]:
                dve.wait_ge(*when(event))
            for n in range(2):
                for i, t in enumerate(tiles):
                    dve.wait_ge(*when((name, "full", n, t)))
                    b = rows_bank(name, n, i, tiles, banks)
                    dst = (x if t < 2 else cx)[:, t % 2, 512 * n:512 * n + 512]
                    tmp = sc2[:, 0, :]
                    nc.vector.tensor_tensor(tmp, psum[:, b, :], gates[t // 2][:, 512 * n:512 * n + 512], ALU.mult).then_inc(*up(dve, ("read", (name, n, t))))
                    dve.wait_ge(*latest(dve))
                    nc.vector.tensor_tensor(dst, dst, tmp, ALU.add).then_inc(*up(dve, (name, "added", n, t)))
                    dve.wait_ge(*latest(dve))

        hid = area(0, 32, 512)
        gates_m = (area(16384, 1024), area(17408, 1024))

        def up_pe(pe, name, ntok, needs=()):
            stage(pe, "up")
            for event in needs:
                pe.wait_ge(*when(event))
            for n in range(8):
                s = slab(pe, (name, n, 0))
                for j in range(4):
                    i = 4 * n + j
                    pe.wait_ge(*bank(i % 4, (name, i)))
                    for k in range(KT):
                        ins = nc.tensor.matmul(psum[:, i % 4, 0:ntok], s[:, k, P * j:P * j + P], hT[:, k, 0:ntok],
                                               start=(k == 0), stop=(k == 7))
                    ins.then_inc(*up(pe, (name, "full", i)))
                also(("used", slab_at[(name, n, 0)]), (name, "full", 4 * n + 3))

        def up_act(act, name, ntok):
            stage(act, "up")
            for i in range(32):
                act.wait_ge(*when((name, "full", i)))
                if i >= 2:
                    act.wait_ge(*when((name, "hidden", i - 2)))
                nc.scalar.activation(sc[:, i % 2, 0:ntok], psum[:, i % 4, 0:ntok], ACT.Relu).then_inc(*up(act, (name, "relu", i)))

        def up_dve(dve, name, ntok):
            stage(dve, "up")
            for i in range(32):
                dve.wait_ge(*when((name, "relu", i)))
                nc.vector.scalar_tensor_tensor(hid[:, i, 0:ntok], psum[:, i % 4, 0:ntok], 0.0,
                                                      sc[:, i % 2, 0:ntok], ALU.max, ALU.mult).then_inc(*up(dve, (name, "hidden", i)))
                also(("read", (name, i)), (name, "hidden", i))
        KAPPA = float(np.exp(-0.5))
        LNS = 65536.0
        shifted = area(0, 16, 256)
        mixed = (area(4096, 8, 512), area(14336, 8, 512))
        v_rows = area(0, 4, 1024)
        rT = area(8192, 8, 256)
        kT = area(10240, 8, 512)
        VS = area(14336, 8, 8, 64)
        gT = area(18432, 8, 256)
        g2_sb = area(20480, 2, 1024)
        Y = area(20480, 4, 8, 64)
        w2_sb = area(22528, 1024)
        cxf = cx[:, :, :].rearrange("p a b -> p (a b)")
        a2_sb, t_w, t_a = cxf[:, 0:1024], cxf[:, 1024:1536], cxf[:, 1536:2048]
        hTf = hT[:, :, :].rearrange("p a b -> p (a b)")
        scf = sc[:, :, :].rearrange("p a b -> p (a b)")
        sc2f = sc2[:, :, :].rearrange("p a b -> p (a b)")

        def chunks(v):
            return v.rearrange("p (c t) -> p c t", c=8)

        ringf = ring[:, :, :].rearrange("p a b -> p (a b)")
        small = sc2f[:, 1024:1536]
        SETS = ((ringf[:, 0:7168], ringf[:, 7168:10240], ringf[:, 10240:11264], ringf[:, 11264:12288]),
                (area(0, 7168), hTf[:, 0:3072], hTf[:, 3072:4096], area(7168, 1024)))
        G, ARI, Bh, Kh, INV, PC, tmp_ = [], [], [], [], [], [], []
        for e, (g_, ari_, bk0, bk1) in enumerate(SETS):
            G.append([g_[:, 3584 * z:3584 * z + 3584].rearrange("p (c n) -> p c n", c=8) for z in range(2)])
            tmp_.append([[g_[:, 3584 * z + 512 * j:3584 * z + 512 * j + 512] for j in range(7)] for z in range(2)])
            ARI.append([ari_[:, 1536 * z:1536 * z + 1536].rearrange("p (c n) -> p c n", c=8) for z in range(2)])
            Bh.append([b_[:, 0:512] for b_ in (bk0, bk1)])
            Kh.append([b_[:, 512:1024] for b_ in (bk0, bk1)])
            INV.append([[chunks(Bh[e][0]), chunks(Kh[e][0])] + [chunks(scf[:, 512 * j:512 * j + 512]) for j in range(4)],
                        [chunks(Bh[e][1]), chunks(Kh[e][1])] + [chunks(v) for v in (scf[:, 2048:2560], scf[:, 2560:3072],
                                                                                  sc2f[:, 0:512], sc2f[:, 512:1024])]])
            PC.append([stat[:, 120 + 16 * e:128 + 16 * e], stat[:, 128 + 16 * e:136 + 16 * e]])
        St = [[small[:, 128 * z + 64 * j:128 * z + 64 * j + 64] for j in range(2)] for z in range(2)]
        Wt = [small[:, 256 + 64 * z:320 + 64 * z] for z in range(2)]
        Ut = [small[:, 384 + 64 * z:448 + 64 * z] for z in range(2)]
        coef = stat[:, 16:48].rearrange("p (c f) -> p c f", c=4)
        one_ka = stat[:, 48:56]
        neg0 = stat[:, 56:88]
        WALK = ((4, 5, 6, 7, 0, 1, 2, 3), (7, 6, 5, 4, 3, 2, 1, 0))
        MIXES = ("w", "a", "g", "r", "k", "v")
        MU = dict(r=0, w=1, k=2, v=3, a=4, g=5)
        HH = (slice(0, 64), slice(64, 128))

        def colr(name, i):
            at = ROWS_A[name] + i
            return colA[:, at:at + 1]

        def mix_width(m):
            return 256 if m in "rg" else 512

        def rw_pool(pool):
            stage(pool, "rw")
            pool.wait_ge(*when(("mlp0_down", "added", 1, 3)))
            nc.gpsimd.dma_start(w2_sb, a["rw_w2"][0].rearrange("z r d -> (z r) d"))\
                .then_inc(landing("w2"), 16)
            pool.wait_ge(*when(("C1a", "normed", 1)))
            nc.gpsimd.dma_start(a2_sb, a["rw_a2"][0].rearrange("z r d -> (z r) d"))\
                .then_inc(landing("a2"), 16)
            nc.gpsimd.dma_start(g2_sb[:, 0, :], a["rw_g2"][0, 0:128])\
                .then_inc(landing("g2a"), 16)
            nc.gpsimd.dma_start(g2_sb[0:32, 1, :], a["rw_g2"][0, 128:160])\
                .then_inc(landing("g2b"), 16)
            for t in range(4):
                pool.wait_ge(*when(("rw", "mix used", 5)))
                pool.wait_ge(*when(("rw_v", "rows", 1, t)))
                for hh in range(2):
                    for par in range(2):
                        nc.gpsimd.dma_start(VS[HH[hh], 2 * t + par, :, :], v_rows[HH[par], t, :].rearrange("p (f h d) -> p f h d", f=8, h=2)[:, :, hh, :])\
                            .then_inc(landing("VS"), 16)

        def mix_dve(dve):
            dve.wait_ge(*latest(dve))
            stage(dve, "mix")
            h = hTf.rearrange("p (g t) -> p g t", t=256)
            nc.vector.tensor_tensor(shifted[:, :, 1:255], h[:, :, 0:254], h[:, :, 2:256], ALU.add).then_inc(*up(dve))
            dve.wait_ge(*latest(dve))
            nc.vector.tensor_copy(shifted[:, :, 0:1], h[:, :, 1:2]).then_inc(*up(dve))
            dve.wait_ge(*latest(dve))
            nc.vector.tensor_copy(shifted[:, :, 255:256], h[:, :, 254:255]).then_inc(*up(dve))
            dve.wait_ge(*latest(dve))
            nc.vector.scalar_tensor_tensor(area(0, 4096), area(0, 4096), 0.5, hTf, ALU.mult, ALU.subtract).then_inc(*up(dve))
            dve.wait_ge(*latest(dve))
            for i, m in enumerate(MIXES):
                if i >= 2:
                    dve.wait_ge(*when(("rw", "mix used", i - 2)))
                w = mix_width(m)
                for k in range(KT):
                    s = shifted[:, 2 * k:2 * k + 2, :].rearrange("p a b -> p (a b)")
                    nc.vector.scalar_tensor_tensor(mixed[i % 2][:, k, 0:w], s[:, 0:w], colr("mu", 8 * MU[m] + k),
                                                          hT[:, k, 0:w], ALU.mult, ALU.add).then_inc(*up(dve, ("rw", "mixed", i)))
            nc.vector.tensor_scalar(one_ka, colA[:, ROWS_A["k_a"]:ROWS_A["k_a"] + 8], -1.0, 1.0,
                                           ALU.mult, ALU.add).then_inc(*up(dve))
            dve.wait_ge(*latest(dve))
            nc.vector.tensor_scalar(neg0, colA[:, ROWS_A["w0"]:ROWS_A["w0"] + 32], -1.0, None, ALU.mult).then_inc(*up(dve))
            dve.wait_ge(*latest(dve))
            nc.vector.memset(epsc[:, 1:2], 0.5 * float(np.log(LNS))).then_inc(*up(dve, "rw columns"))
            dve.wait_ge(*latest(dve))

        def proj_pe(pe):
            stage(pe, "proj")
            for i, m in enumerate(MIXES):
                pe.wait_ge(*when(("rw", "mixed", i)))
                x_, w = mixed[i % 2], mix_width(m)
                if m in "wag":
                    name = (m + "1", 0, 0)
                    s = slab(pe, name)
                    for j, n in enumerate((128,) if m != "g" else (128, 32)):
                        pe.wait_ge(*bank(j, (name, j)))
                        for k in range(KT):
                            ins = nc.tensor.matmul(psum[0:n, j, 0:w], s[:, k, P * j:P * j + n], x_[:, k, 0:w],
                                                   start=(k == 0), stop=(k == 7))
                        ins.then_inc(*up(pe, (name, "full", j)))
                    also(("used", slab_at[name]), (name, "full", j))
                    also(("rw", "mix used", i), (name, "full", j))
                    if m == "g":
                        pe.wait_ge(*when(("sig g", 1)))
                        pe.wait_ge(*when(("dma", "g2a")))
                        pe.wait_ge(*when(("dma", "g2b")))
                        for f in range(8):
                            b = 2 + f // 2
                            if f % 2 == 0:
                                pe.wait_ge(*bank(b, ("g2", b)))
                            o = psum[:, b, 256 * (f % 2):256 * (f % 2) + 256]
                            nc.tensor.matmul(o, g2_sb[:, 0, P * f:P * f + P], sc2[:, 0, 0:256], start=True, stop=False)
                            ins = nc.tensor.matmul(o, g2_sb[0:32, 1, P * f:P * f + P], sc2[0:32, 0, 256:512],
                                                   start=False, stop=True)
                            if f % 2:
                                ins.then_inc(*up(pe, ("g2", "full", b)))
                elif m in "rk":
                    for n in range(2):
                        s = slab(pe, ("rw_" + m, n, 0))
                        for j in range(4):
                            pe.wait_ge(*bank(j, ("rw_" + m, n, j)))
                            for k in range(KT):
                                ins = nc.tensor.matmul(psum[:, j, 0:w], s[:, k, P * j:P * j + P], x_[:, k, 0:w],
                                                       start=(k == 0), stop=(k == 7))
                            ins.then_inc(*up(pe, ("rw_" + m, "full", n, j)))
                        also(("used", slab_at[("rw_" + m, n, 0)]), ("rw_" + m, "full", n, 3))
                    also(("rw", "mix used", i), ("rw_" + m, "full", 1, 3))
                else:
                    rows_pe(pe, "rw_v", lambda k, t: mixed[1][:, k, P * t:P * t + P], range(4), KT, D, [0, 1, 2, 3])
                    stage(pe, "proj")
                    also(("rw", "mix used", i), ("rw_v", "full", 1, 3))

        def proj_act(act):
            stage(act, "proj")
            for i, m in enumerate(MIXES):
                if m in "wa":
                    act.wait_ge(*when(((m + "1", 0, 0), "full", 0)))
                    act.wait_ge(*when(("C1a", "normed", 1)))
                    nc.scalar.activation({"w": t_w, "a": t_a}[m], psum[:, 0, :],
                                                ACT.Tanh if m == "w" else ACT.Copy).then_inc(*up(act, ("read", ((m + "1", 0, 0), 0))))
                    act.wait_ge(*latest(act))
                elif m == "g":
                    name = ("g1", 0, 0)
                    for j, n in enumerate((128, 32)):
                        act.wait_ge(*when((name, "full", j)))
                        nc.scalar.activation(sc2[0:n, 0, 256 * j:256 * j + 256], psum[0:n, j, 0:256],
                                                    ACT.Sigmoid).then_inc(*up(act, ("read", (name, j))))
                        act.wait_ge(*latest(act))
                        also(("sig g", j), ("read", (name, j)))
                    for b in range(2, 6):
                        act.wait_ge(*when(("g2", "full", b)))
                        nc.scalar.copy(gT[:, 2 * b - 4:2 * b - 2, :].rearrange("p a b -> p (a b)"), psum[:, b, :]).then_inc(*up(act, ("read", ("g2", b))))
                elif m in "rk":
                    w = mix_width(m)
                    for n in range(2):
                        for j in range(4):
                            act.wait_ge(*when(("rw_" + m, "full", n, j)))
                            nc.scalar.copy({"r": rT, "k": kT}[m][:, 4 * n + j, :], psum[:, j, 0:w]).then_inc(*up(act, ("read", ("rw_" + m, n, j))))
                else:
                    act.wait_ge(*when(("rw", "mixed", 5)))
                    for n in range(2):
                        for t in range(4):
                            act.wait_ge(*when(("rw_v", "full", n, t)))
                            nc.scalar.copy(v_rows[:, t, 512 * n:512 * n + 512], psum[:, t, :]).then_inc(*up(act, ("read", ("rw_v", n, t))))
                            also(("rw_v", "rows", n, t), ("read", ("rw_v", n, t)))

        PREP_PE = {0: 0, 1: 1, 3: 2, 13: 3}
        PREP_PARTS = 17

        def prep_pe(pe, f, part):
            if f > 7:
                return
            stage(pe, "prep")
            if f == 0 and part == 0:
                pe.wait_ge(*when(("dma", "w2")))
                pe.wait_ge(*when(("dma", "a2")))
                pe.wait_ge(*when(("read", (("w1", 0, 0), 0))))
                pe.wait_ge(*when(("read", (("a1", 0, 0), 0))))
            if f >= 2 and part == 0:
                pe.wait_ge(*when(("chains", f - 2)))
            c = slice(P * f, P * f + P)
            if part == 0:
                pe.wait_ge(*bank(5, ("wl", f, 0)))
                nc.tensor.matmul(psum[:, 5, :], w2_sb[HH[0], c], t_w[HH[0], :], start=True, stop=True)\
                    .then_inc(*up(pe, ("wl", "full", f, 0)))
                pe.wait_ge(*bank(6, ("al", f, 0)))
                nc.tensor.matmul(psum[:, 6, :], a2_sb[HH[0], c], t_a[HH[0], :], start=True, stop=True)\
                    .then_inc(*up(pe, ("al", "full", f, 0)))
                pe.wait_ge(*bank(7, ("wl", f, 1)))
                nc.tensor.matmul(psum[:, 7, :], w2_sb[HH[1], c], t_w[HH[1], :], start=True, stop=True)\
                    .then_inc(*up(pe, ("wl", "full", f, 1)))
            if part == 1:
                pe.wait_ge(*bank(5, ("al", f, 1)))
                nc.tensor.matmul(psum[:, 5, :], a2_sb[HH[1], c], t_a[HH[1], :], start=True, stop=True)\
                    .then_inc(*up(pe, ("al", "full", f, 1)))
            if part == 2:
                pe.wait_ge(*when(("kk squared", f)))
                pe.wait_ge(*bank(6, ("kk", f)))
                nc.tensor.matmul(psum[:, 6, :], cst("headones"), tmp_[f % 2][1][6], start=True, stop=True)\
                    .then_inc(*up(pe, ("kk", "full", f)))
            if part == 3:
                pe.wait_ge(*when(("coef product", f)))
                pe.wait_ge(*bank(7, ("coef", f)))
                for hh in range(2):
                    for c_ in range(4):
                        ins = nc.tensor.matmul(psum[HH[hh], 7, c_:c_ + 1],
                                               tmp_[f % 2][0][4][HH[hh], 64 * c_:64 * c_ + 64],
                                               cst("ones")[HH[hh], 0:1], start=True, stop=True)
                ins.then_inc(*up(pe, ("coef", "full", f)))

        def prep_act(act, f):
            stage(act, "prep")
            act.wait_ge(*when("rw columns"))
            if f == 0:
                act.wait_ge(*when(("dma", "VS")))
                act.wait_ge(*when(("used", slab_at[("rw_o", 0, 0)] - 1)))
            elif f >= 2:
                act.wait_ge(*when(("chains", f - 2)))
            for z in range(2):
                t = tmp_[f % 2][z]
                act.wait_ge(*when(("wl", "full", f, z)))
                nc.scalar.activation(t[0], psum[:, (5, 7)[z], :], ACT.Exp, bias=neg0[:, 8 * z + f:8 * z + f + 1],
                                     scale=-1.0).then_inc(*up(act, ("read", ("wl", f, z))))
                act.wait_ge(*when(("al", "full", f, z)))
                nc.scalar.activation(t[1], psum[:, (6, 5)[z], :], ACT.Exp,
                                     bias=neg0[:, 16 + 8 * z + f:16 + 8 * z + f + 1], scale=-1.0)\
                    .then_inc(*up(act, ("read", ("al", f, z))))
            for z in range(2):
                t = tmp_[f % 2][z]
                act.wait_ge(*latest(act))
                for v in (t[0], t[1]):
                    nc.scalar.activation(v, v, ACT.Ln, bias=cst("ones")[:, 0:1]).then_inc(*up(act))
                act.wait_ge(*latest(act))
                nc.scalar.activation(t[0], t[0], ACT.Exp, scale=-1.0).then_inc(*up(act))
                nc.scalar.activation(t[1], t[1], ACT.Exp, scale=-1.0).then_inc(*up(act, ("sigmoids", f, z)))
            for z in range(2):
                t = tmp_[f % 2][z]
                act.wait_ge(*when(("decay sums", f, z)))
                nc.scalar.activation(t[2], t[2], ACT.Exp, scale=-KAPPA).then_inc(*up(act))
                nc.scalar.activation(t[0], t[3], ACT.Exp, scale=-KAPPA).then_inc(*up(act))
                nc.scalar.activation(t[3], t[3], ACT.Exp, scale=KAPPA).then_inc(*up(act, ("decays", f, z)))
            act.wait_ge(*when(("kk", "full", f)))
            act.wait_ge(*when(("kk bounded", f)))
            sq = tmp_[f % 2][1][6]
            nc.scalar.activation(sq, sq, ACT.Ln, scale=LNS).then_inc(*up(act))
            act.wait_ge(*latest(act))
            nc.scalar.activation(sq, sq, ACT.Exp, scale=-0.5, bias=epsc[:, 1:2]).then_inc(*up(act, ("kk rnorm", f)))

        def prep_dve(dve, f, part):
            if f > 7 or part >= PREP_PARTS:
                return
            stage(dve, "prep")
            kk, sq = tmp_[f % 2][0][6], tmp_[f % 2][1][6]
            if part == 0:
                if f == 0:
                    dve.wait_ge(*when(("dma", "VS")))
                    dve.wait_ge(*when(("rw", "mix used", 5)))
                    dve.wait_ge(*when(("used", slab_at[("rw_o", 0, 0)] - 1)))
                    for e, z in ((0, 0), (0, 1), (1, 0), (1, 1)):
                        nc.vector.tensor_copy(ARI[e][z][:, :, 64:128],
                                              cst("eye64").unsqueeze(1).to_broadcast([P, 8, 64]))\
                            .then_inc(*up(dve, "eyes"))
                elif f >= 2:
                    dve.wait_ge(*when(("chains", f - 2)))
                nc.vector.tensor_scalar(kk, kT[:, f, :], colr("k_k", f), None, ALU.mult).then_inc(*up(dve))
                dve.wait_ge(*latest(dve))
                nc.vector.tensor_tensor(sq, kk, kk, ALU.mult).then_inc(*up(dve, ("kk squared", f)))
            z, quarter = divmod(part - 3, 3)
            if 3 <= part <= 8:
                t = tmp_[f % 2][z]
                v = (lambda q: q) if z == 0 else (lambda q: q[:, ::-1])
                if quarter == 0:
                    dve.wait_ge(*when(("sigmoids", f, z)))
                    nc.vector.tensor_tensor_scan(v(t[3]), cst("chunk_start"), v(t[0]), 0.0, ALU.mult, ALU.add)\
                        .then_inc(*up(dve))
                    nc.vector.tensor_scalar(t[4], t[1], colr("k_a", f), one_ka[:, f:f + 1], ALU.mult, ALU.add)\
                        .then_inc(*up(dve))
                if quarter == 1:
                    dve.wait_ge(*latest(dve))
                    nc.vector.tensor_tensor(t[2], t[3], t[0], ALU.subtract).then_inc(*up(dve, ("decay sums", f, z)))
                    nc.vector.tensor_tensor(t[5], t[4], kT[:, f, :], ALU.mult).then_inc(*up(dve))
            c4 = tmp_[f % 2][0][4][:, 0:256]
            if part == 9:
                dve.wait_ge(*when(("kk", "full", f)))
                nc.vector.tensor_scalar(sq, psum[:, 6, :], 1e-24, None, ALU.max).then_inc(*up(dve, ("kk bounded", f)))
                also(("read", ("kk", f)), ("kk bounded", f))
                dve.wait_ge(*latest(dve))
                nc.vector.tensor_tensor(c4, tmp_[f % 2][0][5][:, 0:256], tmp_[f % 2][1][5][:, 0:256], ALU.add)\
                    .then_inc(*up(dve))
            if part == 10:
                dve.wait_ge(*latest(dve))
                nc.vector.scalar_tensor_tensor(c4, c4, colr("r_k", f), rT[:, f, :], ALU.mult, ALU.mult)\
                    .then_inc(*up(dve, ("coef product", f)))
            if part == 11:
                dve.wait_ge(*when(("kk rnorm", f)))
                nc.vector.tensor_tensor(kk, kk, sq, ALU.mult).then_inc(*up(dve))
            z, half_ = divmod(part - 12, 2)
            if 12 <= part <= 15:
                t = tmp_[f % 2][z]
                ari = ARI[f % 2][z]
                last = 63 if z == 0 else 0
                if half_ == 0:
                    dve.wait_ge(*when(("decays", f, z)))
                    nc.vector.tensor_copy(PC[f % 2][z].unsqueeze(2), chunks(t[0])[:, :, last:last + 1])\
                        .then_inc(*up(dve))
                    dve.wait_ge(*latest(dve))
                    nc.vector.scalar_tensor_tensor(ari[:, :, 0:64], chunks(kk), -1.0, chunks(t[2]),
                                                   ALU.mult, ALU.mult).then_inc(*up(dve))
                    nc.vector.tensor_tensor(t[1], t[1], kk, ALU.mult).then_inc(*up(dve))
                if half_ == 1:
                    nc.vector.tensor_tensor(ari[:, 0:4, 128:192], rT[:, f, :].rearrange("p (c t) -> p c t", c=4),
                                            chunks(t[0])[:, 0:4, :], ALU.mult).then_inc(*up(dve))
                    dve.wait_ge(*latest(dve))
                    nc.vector.tensor_tensor(Bh[f % 2][z], t[1], t[3], ALU.mult).then_inc(*up(dve))
                    nc.vector.tensor_tensor(Kh[f % 2][z], t[5], t[3], ALU.mult).then_inc(*up(dve, ("scaled", f, z)))
            if part == 16:
                dve.wait_ge(*when(("coef", "full", f)))
                nc.vector.tensor_copy(coef[:, :, f:f + 1], psum[:, 7, 0:4].unsqueeze(2))\
                    .then_inc(*up(dve, ("read", ("coef", f))))

        Y_AT = (9, 11, 13, 15)
        GRAM_BANKS = (0, 1, 2, 3, 4)

        def gram_list(f):
            return [(z, c) for z in range(2) for c in range(8)]

        def gram_pe(pe, f):
            stage(pe, "gram")
            pe.wait_ge(*when("eyes"))
            pe.wait_ge(*when(("scaled", f, 1)))
            pe.wait_ge(*when(("decays", f, 1)))
            for i, (z, c) in enumerate(gram_list(f)):
                b = GRAM_BANKS[i % 5]
                w = 192 if c < 4 else 128
                s = slice(64 * c, 64 * c + 64)
                pe.wait_ge(*bank(b, ("gram", f, z, c)))
                for n, r in enumerate(HH):
                    nc.tensor.matmul(psum[r, b, 0:w], Bh[f % 2][z][r, s], ARI[f % 2][z][r, c, 0:w], start=True, stop=True)
                    nc.tensor.matmul(psum[r, b, 192:192 + w], Kh[f % 2][z][r, s], ARI[f % 2][z][r, c, 0:w], start=True, stop=True)
                    ins = nc.tensor.matmul(psum[r, b, 384:448], ARI[f % 2][z][r, c, 0:64], Bh[f % 2][z][r, s],
                                           start=True, stop=True)
                    if n == 1:
                        ins.then_inc(*up(pe, ("gram", "full", f, z, c)))
                    at = 2 * i + n
                    for hop in range(HOPS * at // 32, HOPS * (at + 1) // 32):
                        walk_pe(pe, f - 1, hop)
                    stage(pe, "gram")

        def gram_dve(dve, f):
            stage(dve, "gram")
            for i, (z, c) in enumerate(gram_list(f)):
                b = GRAM_BANKS[i % 5]
                m = cst(f"gram{z}")
                dve.wait_ge(*when(("gram", "full", f, z, c)))
                if i == 0:
                    dve.wait_ge(*when(("coef", "full", f)))
                if c < 4:
                    ins = nc.vector.tensor_tensor(G[f % 2][z][:, c, :], psum[:, b, 0:448], m, ALU.mult)
                else:
                    two = lambda q: q.rearrange("p (a n) -> p a n", a=2)[:, :, 0:128]
                    nc.vector.tensor_tensor(two(G[f % 2][z][:, c, 0:384]), two(psum[:, b, 0:384]), two(m[:, 0:384]),
                                                   ALU.mult).then_inc(*up(dve))
                    ins = nc.vector.tensor_tensor(G[f % 2][z][:, c, 384:448], psum[:, b, 384:448], m[:, 384:448], ALU.mult)
                ins.then_inc(*up(dve, ("read", ("gram", f, z, c))))
                dve.wait_ge(*latest(dve))
                for y in range(4, 8):
                    if i == Y_AT[y - 4]:
                        walk_y(dve, f - 1, y)
                        stage(dve, "gram")
                if i in (9, 15):
                    inv_start(dve, f, i // 15)
                    stage(dve, "gram")

        INV_STEPS = (
            ((1, 0, 2, None), (0, 1, 3, None)),
            ((3, 4, 4, 4), (3, 2, 0, None), (2, 3, 1, None)),
            ((1, 4, 4, 4), (0, 1, 2, None)),
            ((2, 4, 4, 4),),
            ((4, "eye", 5, None),),
            (("off32", 4, 3, None),),
            ((5, 3, 4, 4), (3, 5, 5, 5)),
            (("off64", 4, 3, None),),
            ((5, 3, 0, 4),),
        )

        def inv_tiles(f):
            n = 0
            for r, steps in enumerate(INV_STEPS):
                for z in range(2):
                    for j, step in enumerate(steps):
                        yield r, z, j, step, n % 5
                        n += 1

        def inv_pe(pe, f):
            stage(pe, "inv")
            for r, z, j, (left, right, dst, add), b in inv_tiles(f):
                if j == 0 and 2 * r + z in PREP_PE:
                    prep_pe(pe, f + 1, PREP_PE[2 * r + z])
                    stage(pe, "inv")
                pe.wait_ge(*when(("inv ready", f, r, z)))
                pe.wait_ge(*bank(b, ("inv", f, r, z, j)))
                for c in range(8):
                    for h in HH:
                        l = INV[f % 2][z][2 if left in ("off32", "off64") else left][h, c, :]
                        rr = cst("eye64")[h, :] if right == "eye" else INV[f % 2][z][right][h, c, :]
                        ins = nc.tensor.matmul(psum[h, b, 64 * c:64 * c + 64], l, rr, start=True, stop=True)
                ins.then_inc(*up(pe, ("inv", "full", f, r, z, j)))

        def blocks_of(name):
            return cst(name).unsqueeze(1).to_broadcast([P, 8, 64])

        def inv_start(dve, f, z):
            stage(dve, "inv")
            B = INV[f % 2][z]
            dve.wait_ge(*when(("gram", "full", f, z, 7)))
            dve.wait_ge(*latest(dve))
            nc.vector.tensor_tensor(B[0], G[f % 2][z][:, :, 0:64], blocks_of("diag16"), ALU.mult).then_inc(*up(dve))
            nc.vector.tensor_tensor(B[1], G[f % 2][z][:, :, 384:448], blocks_of("diag16"), ALU.mult)\
                .then_inc(*up(dve))
            dve.wait_ge(*latest(dve))
            nc.vector.tensor_tensor(B[4], B[0], blocks_of("eye64"), ALU.add).then_inc(*up(dve, ("inv ready", f, 0, z)))

        def inv_dve(dve, f):
            stage(dve, "inv")
            for r, z, j, (left, right, dst, add), b in inv_tiles(f):
                B = INV[f % 2][z]
                dve.wait_ge(*when(("inv", "full", f, r, z, len(INV_STEPS[r]) - 1)))
                src = chunks(psum[:, b, :])
                if add is None:
                    ins = nc.vector.tensor_copy(B[dst], src)
                else:
                    ins = nc.vector.tensor_tensor(B[dst], src, B[add], ALU.add)
                ins.then_inc(*up(dve, ("read", ("inv", f, r, z, j))))
                if j == len(INV_STEPS[r]) - 1:
                    if r == 4:
                        ins = nc.vector.tensor_tensor(B[2], G[f % 2][z][:, :, 384:448], blocks_of("off32"), ALU.mult)
                        ins.then_inc(*up(dve, ("inv ready", f, 5, z)))
                        dve.wait_ge(*latest(dve))
                    elif r == 6:
                        ins = nc.vector.tensor_tensor(B[2], G[f % 2][z][:, :, 384:448], blocks_of("off64"), ALU.mult)
                        ins.then_inc(*up(dve, ("inv ready", f, 7, z)))
                        dve.wait_ge(*latest(dve))
                    else:
                        also(("inv ready", f, r + 1, z), ("read", ("inv", f, r, z, j)))
                    prep_dve(dve, f + 1, 2 * r + z)
                    stage(dve, "inv")

        HOPS = 24

        def walk_tile(z, j):
            return psum[:, 5, 64 * z:64 * z + 64] if j == 3 else psum[:, 6 + z, 64 * j:64 * j + 64]

        def walk_pe(pe, f, hop):
            if f < 0 or hop >= HOPS:
                return
            stage(pe, "walk")
            i, part = divmod(hop, 3)
            if hop == 0:
                if f < 7:
                    pe.wait_ge(*when(("read", ("coef", f + 1))))
                pe.wait_ge(*when(("inv ready", f, len(INV_STEPS), 0)))
                pe.wait_ge(*when(("inv ready", f, len(INV_STEPS), 1)))
                pe.wait_ge(*when(("walk zero", f)))
            for z in range(2):
                c, S = WALK[z][i], St[z][i % 2]
                ari, g = ARI[f % 2][z], G[f % 2][z]
                if part == 0:
                    t = walk_tile(z, 0)
                    pe.wait_ge(*bank(("W", z), ("W", f, i, z)))
                    pe.wait_ge(*when(("S", f, i, z)))
                    for r in HH:
                        nc.tensor.matmul(t[r], ari[r, c, 0:64], S[r, :], start=True, stop=False)
                        ins = nc.tensor.matmul(t[r], g[r, c, 192:256], VS[r, c, f, :], start=False, stop=True)
                    ins.then_inc(*up(pe, ("W", "full", f, i, z)))
                if part == 1:
                    t = walk_tile(z, 1)
                    pe.wait_ge(*bank(("U", z), ("U", f, i, z)))
                    pe.wait_ge(*when(("W", "out", f, i, z)))
                    for r in HH:
                        ins = nc.tensor.matmul(t[r], INV[f % 2][z][0][r, c, :], Wt[z][r, :], start=True, stop=True)
                    ins.then_inc(*up(pe, ("U", "full", f, i, z)))
                if part == 2:
                    pe.wait_ge(*when(("U", "out", f, i, z)))
                    if i < 7:
                        t = walk_tile(z, 2)
                        pe.wait_ge(*bank(("S", z), ("S psum", f, i, z)))
                        for r in HH:
                            nc.tensor.matmul(t[r], cst("eye64")[r, :], S[r, :], start=True, stop=False)
                            nc.tensor.matmul(t[r], g[r, c, 256:320], VS[r, c, f, :], start=False, stop=False)
                            ins = nc.tensor.matmul(t[r], g[r, c, 64:128], Ut[z][r, :], start=False, stop=True)
                        ins.then_inc(*up(pe, ("S", "full", f, i, z)))
            for z in range(2):
                c, S = WALK[z][i], St[z][i % 2]
                ari, g = ARI[f % 2][z], G[f % 2][z]
                if part == 2 and c < 4:
                    t = walk_tile(z, 3)
                    if z == 0:
                        pe.wait_ge(*bank(5, ("Y", f, i, 1)))
                    for r in HH:
                        nc.tensor.matmul(t[r], ari[r, c, 128:192], S[r, :], start=True, stop=False)
                        nc.tensor.matmul(t[r], g[r, c, 320:384], VS[r, c, f, :], start=False, stop=False)
                        ins = nc.tensor.matmul(t[r], g[r, c, 128:192], Ut[z][r, :], start=False, stop=True)
                    ins.then_inc(*up(pe, ("Y", "full", f, i, z)))

        def walk_act(act, f, hop):
            if f < 0 or hop >= HOPS:
                return
            stage(act, "walk")
            i, part = divmod(hop, 3)
            for z in range(2):
                if part == 0:
                    act.wait_ge(*when(("W", "full", f, i, z)))
                    nc.scalar.copy(Wt[z], walk_tile(z, 0)).then_inc(*up(act, ("W", "out", f, i, z)))
                    also(("read", ("W", f, i, z)), ("W", "out", f, i, z))
                if part == 1:
                    act.wait_ge(*when(("U", "full", f, i, z)))
                    if i:
                        act.wait_ge(*when(("Y", "full", f, i - 1, z) if WALK[z][i - 1] < 4
                                          else ("S", "full", f, i - 1, z)))
                    nc.scalar.copy(Ut[z], walk_tile(z, 1)).then_inc(*up(act, ("U", "out", f, i, z)))
                    also(("read", ("U", f, i, z)), ("U", "out", f, i, z))
                if part == 2 and i < 7:
                    act.wait_ge(*when(("S", "full", f, i, z)))
                    c = WALK[z][i]
                    nc.scalar.activation(St[z][(i + 1) % 2], walk_tile(z, 2), ACT.Copy,
                                         scale=PC[f % 2][z][:, c:c + 1]).then_inc(*up(act, ("S", f, i + 1, z)))
                    also(("read", ("S psum", f, i, z)), ("S", f, i + 1, z))

        def walk_start(dve, f):
            stage(dve, "walk")
            if f:
                dve.wait_ge(*when(("chains", f - 1)))
            for z in range(2):
                nc.vector.memset(St[z][0], 0.0).then_inc(*up(dve, ("S", f, 0, z)))
            also(("walk zero", f), ("S", f, 0, 1))

        def walk_y(dve, f, i):
            if f < 0:
                return
            stage(dve, "walk")
            for z in range(2):
                c = WALK[z][i]
                first = (z == 0) == (c < 2)
                dve.wait_ge(*when(("Y", "full", f, i, 1)))
                src = walk_tile(z, 3)
                if first:
                    ins = nc.vector.tensor_copy(Y[:, c, f, :], src)
                else:
                    ins = nc.vector.tensor_tensor(Y[:, c, f, :], src, Y[:, c, f, :], ALU.add)
                ins.then_inc(*up(dve, ("read", ("Y", f, i, z))))
                dve.wait_ge(*latest(dve))
            if i == 7:
                also(("chains", f), ("read", ("Y", f, 7, 1)))

        bonus = area(0, 4, 8, 64)
        ysq = area(2048, 32, 64)
        ystat = stat[:, 88:120]
        gates_r = (area(4096, 1024),)

        def readout_dve(dve):
            stage(dve, "readout")
            Yf = Y.rearrange("p c f d -> p (c f) d")
            bc = lambda v: v.unsqueeze(2).to_broadcast([P, 32, 64])
            nc.vector.tensor_reduce(ystat, Yf, AX.X, ALU.add).then_inc(*up(dve))
            dve.wait_ge(*latest(dve))
            nc.vector.tensor_scalar(ystat, ystat, 1.0 / 64, None, ALU.mult).then_inc(*up(dve))
            dve.wait_ge(*latest(dve))
            nc.vector.tensor_tensor(Yf, Yf, bc(ystat), ALU.subtract).then_inc(*up(dve))
            dve.wait_ge(*latest(dve))
            nc.vector.tensor_tensor(ysq, Yf, Yf, ALU.mult).then_inc(*up(dve))
            dve.wait_ge(*latest(dve))
            nc.vector.tensor_reduce(ystat, ysq, AX.X, ALU.add).then_inc(*up(dve, "y squares"))
            dve.wait_ge(*latest(dve))
            nc.vector.tensor_tensor(bonus.rearrange("p c f d -> p (c f) d"),
                                           VS[:, 0:4, :, :].rearrange("p c f d -> p (c f) d"),
                                           coef.rearrange("p c f -> p (c f)").unsqueeze(2).to_broadcast([P, 32, 64]),
                                           ALU.mult).then_inc(*up(dve))
            dve.wait_ge(*latest(dve))
            dve.wait_ge(*when("y rstd"))
            nc.vector.tensor_tensor(Yf, Yf, bc(ystat), ALU.mult).then_inc(*up(dve, "y normed"))
            dve.wait_ge(*latest(dve))
            for f in range(8):
                dve.wait_ge(*when(("y turned", f)))
                t = sc[:, f % 2, 0:256]
                nc.vector.tensor_scalar(t, psum[:, f % 4, 0:256], colr("lnx_w", f), colr("lnx_b", f),
                                               ALU.mult, ALU.add).then_inc(*up(dve))
                dve.wait_ge(*latest(dve))
                nc.vector.tensor_tensor(t, t, psum[:, f % 4, 256:512], ALU.add).then_inc(*up(dve, ("read", ("y", f))))
                dve.wait_ge(*latest(dve))
                nc.vector.tensor_tensor(hT[:, f, 0:256], t, gT[:, f, :], ALU.mult).then_inc(*up(dve, ("rw gated", f)))
                dve.wait_ge(*latest(dve))

        def readout_pool(pool):
            stage(pool, "readout")
            pool.wait_ge(*when("y squares"))
            nc.gpsimd.tensor_scalar(ystat, ystat, 1.0 / 64, 64e-5, ALU.mult, ALU.add).then_inc(*up(pool))
            pool.wait_ge(*latest(pool))
            nc.gpsimd.tensor_tensor(ystat, ystat, half[:, 0:32], ALU.pow).then_inc(*up(pool, "y rstd"))
            pool.wait_ge(*latest(pool))
            gate_load(pool, "gate r", gates_r[0], 1, 0, 2)

        def readout_pe(pe):
            stage(pe, "readout")
            pe.wait_ge(*when("y normed"))
            for f in range(8):
                pe.wait_ge(*bank(f % 4, ("y", f)))
                for h in HH:
                    for c in range(4):
                        s = slice(64 * c, 64 * c + 64)
                        nc.tensor.matmul(psum[h, f % 4, 64 * c:64 * c + 64], Y[h, c, f, :], cst("eye64")[h, :],
                                         start=True, stop=True)
                        ins = nc.tensor.matmul(psum[h, f % 4, 256 + 64 * c:320 + 64 * c], bonus[h, c, f, :],
                                               cst("eye64")[h, :], start=True, stop=True)
                ins.then_inc(*up(pe, ("y turned", f)))
        def gain(name, layer=0, n=8):
            at = ROWS_B[name] + n * layer
            return colB[:, at:at + n]

        def add_rows_dve(dve, name, banks, scale, split=()):
            stage(dve, "add")
            for n in range(2):
                for i in range(2):
                    dve.wait_ge(*when((name, "full", n, i)))
                    b = rows_bank(name, n, i, range(2), banks)
                    dst = x[:, i, 512 * n:512 * n + 512]
                    nc.vector.scalar_tensor_tensor(dst, psum[:, b, :], scale, dst, ALU.mult, ALU.add).then_inc(*up(dve, (name, "added", n, i)))
                    also(("read", (name, n, i)), (name, "added", n, i))
                if n == 0:
                    for slab_name in split:
                        for h in range(2):
                            low_dve(dve, slab_name, h)
                    stage(dve, "add")
            dve.wait_ge(*latest(dve))

        UP_BANKS = [4, 5, 6, 7]

        hid_parts = [area(at, 22, 256, rounded=True) for at in (0, 5632)]

        def swiglu_pe(pe, key):
            stage(pe, "swiglu")
            for event in [("read", (key, b)) for b in range(4)]:
                pe.wait_ge(*when(event))
            for n in range(11):
                w = (key + "_gu", n, 0)
                for part in range(2):
                    b = 2 * (n % 2) + part
                    pe.wait_ge(*bank(b, (key, "gu", n, part)))
                    for j in range(2):
                        at = 256 * part + P * j
                        for k in range(KT):
                            if k % 4 == 0:
                                pe.wait_ge(*when(("low", w, k // 4)))
                            for i, (s, q) in enumerate(parts(w)):
                                ins = nc.tensor.matmul(psum[:, b, 256 * j:256 * j + 256], s[:, k, at:at + P],
                                                       x_parts[q][:, k, :], start=(k == 0 and i == 0),
                                                       stop=(k == 7 and i == 2))
                    ins.then_inc(*up(pe, (key, "gu full", n, part)))
                also(("used", slab_at[w]), (key, "gu full", n, 1))
            rows3_pe(pe, key + "_down", hid_parts, 22, UP_BANKS, [(key, "hidden", 10)])

        def swiglu_act(act, key):
            names = ffn_slabs(key)
            for name in names[0:2]:
                high_act(act, name)
            for n in range(11):
                stage(act, "swiglu")
                act.wait_ge(*when((key, "gu full", n, 0)))
                if n >= 2:
                    act.wait_ge(*when((key, "hidden", n - 2)))
                nc.scalar.activation(sc[:, n % 2, :], psum[:, 2 * (n % 2), :], ACT.Silu)\
                    .then_inc(*up(act, ("read", (key, "gu", n, 0))))
                high_act(act, names[n + 2])
            for name in names[13:]:
                high_act(act, name)

        def swiglu_dve(dve, key):
            names = ffn_slabs(key)
            low_dve(dve, names[0], 1)
            for h in range(2):
                low_dve(dve, names[1], h)
            for n in range(11):
                stage(dve, "swiglu")
                dve.wait_ge(*when(("read", (key, "gu", n, 0))))
                dve.wait_ge(*when((key, "gu full", n, 1)))
                t = sc[:, n % 2, :]
                high, low = [v[:, 2 * n:2 * n + 2, :].rearrange("p a b -> p (a b)") for v in hid_parts]
                nc.vector.tensor_tensor(t, t, psum[:, 2 * (n % 2) + 1, :], ALU.mult)\
                    .then_inc(*up(dve, ("read", (key, "gu", n, 1))))
                dve.wait_ge(*latest(dve))
                nc.vector.tensor_copy(high, t).then_inc(*up(dve))
                dve.wait_ge(*latest(dve))
                nc.vector.tensor_tensor(low, t, high.bitcast(F32), ALU.subtract).then_inc(*up(dve, (key, "hidden", n)))
                for h in range(2):
                    low_dve(dve, names[n + 2], h)
            for name in names[13:15]:
                for h in range(2):
                    low_dve(dve, name, h)
            stage(dve, "swiglu")
            add_rows_dve(dve, key + "_down", UP_BANKS, 0.5, names[15:])

        eq = area(0, 4, 256)
        ek = area(1024, 4, 256)
        ev = area(2048, 2, 512)
        eu = area(3072, 2, 512)
        eg = area(4096, 2, 512)
        e_gain, e_bias = area(6144, 512), area(6656, 512)
        ew = area(7168, 8, P)
        ewT = area(8192, 8, P)
        esq = area(9216, 2, 512)

        def even_pool(pool):
            stage(pool, "even")
            pool.wait_ge(*when(("pre0_down", "added", 1, 1)))
            nc.gpsimd.dma_start(e_gain, a["sgu_ln_gain_2"][0].partition_broadcast(P))\
                .then_inc(landing("ln gain"), 16)
            nc.gpsimd.dma_start(e_bias, a["sgu_ln_bias_2"][0].partition_broadcast(P))\
                .then_inc(landing("ln bias"), 16)
            nc.gpsimd.dma_start(ew, a["sgu_w_2"][0].rearrange("g t s -> t g s"))\
                .then_inc(landing("sgu w"), 16)

        def even_pool_rstd(pool):
            stage(pool, "even")
            pool.wait_ge(*when("g squares"))
            nc.gpsimd.tensor_scalar(stat[:, 132:134], stat[:, 132:134], 1.0 / 512, EPS, ALU.mult, ALU.add).then_inc(*up(pool))
            pool.wait_ge(*latest(pool))
            nc.gpsimd.tensor_tensor(stat[:, 132:134], stat[:, 132:134], half[:, 0:2], ALU.pow).then_inc(*up(pool, "g rstd"))
            pool.wait_ge(*latest(pool))

        def even_in_pe(pe):
            stage(pe, "even")
            for event in [("read", ("mix0", b)) for b in range(4)]:
                pe.wait_ge(*when(event))
            for n in range(2):
                s = slab(pe, ("sbg_in", n, 0))
                for j in range(4):
                    pe.wait_ge(*bank(j, ("sbg", n, j)))
                    for k in range(KT):
                        ins = nc.tensor.matmul(psum[:, j, 0:256], s[:, k, P * j:P * j + P], hT[:, k, 0:256],
                                               start=(k == 0), stop=(k == 7))
                    ins.then_inc(*up(pe, ("sbg", "full", n, j)))
                also(("used", slab_at[("sbg_in", n, 0)]), ("sbg", "full", n, 3))
            rows_pe(pe, "sbg_in", lambda k, t: hT[:, k, P * t:P * t + P], range(2), KT, 2560, [4, 5, 6, 7],
                    only=(2, 3, 4))
            stage(pe, "even")
            pe.wait_ge(*when(("dma", "sgu w")))
            for b in range(2):
                pe.wait_ge(*bank(b, ("ewT", b)))
                for g in range(4):
                    ins = nc.tensor.transpose(psum[:, b, P * g:P * g + P], ew[:, 4 * b + g, :], ident)
                ins.then_inc(*up(pe, ("ewT", "full", b)))

        def even_in_act(act):
            stage(act, "even")
            act.wait_ge(*when(("pre0_down", "full", 1, 1)))
            for n in range(2):
                for j in range(4):
                    act.wait_ge(*when(("sbg", "full", n, j)))
                    nc.scalar.copy((eq, ek)[n][:, j, :], psum[:, j, 0:256]).then_inc(*up(act, ("read", ("sbg", n, j))))
            for i, n in enumerate((2, 3, 4)):
                for t in range(2):
                    act.wait_ge(*when(("sbg_in", "full", n, t)))
                    nc.scalar.activation((ev, eu, eg)[i][:, t, :], psum[:, 4 + (2 * i + t) % 4, :],
                                                ACT.Copy if n == 2 else ACT.Gelu_apprx_tanh).then_inc(*up(act, ("read", ("sbg_in", n, t))))

        def even_gate_dve(dve):
            stage(dve, "even")
            for b in range(2):
                dve.wait_ge(*when(("ewT", "full", b)))
                nc.vector.tensor_tensor(ewT[:, 4 * b:4 * b + 4, :],
                                               psum[:, b, :].rearrange("p (g t) -> p g t", g=4),
                                               cst("st_fwd").unsqueeze(1).to_broadcast([P, 4, P]), ALU.mult).then_inc(*up(dve, ("read", ("ewT", b))))
                dve.wait_ge(*latest(dve))
            dve.wait_ge(*when(("read", ("sbg_in", 4, 0))))
            dve.wait_ge(*when(("read", ("sbg_in", 4, 1))))
            dve.wait_ge(*when(("dma", "ln gain")))
            dve.wait_ge(*when(("dma", "ln bias")))
            m = stat[:, 130:132]
            nc.vector.tensor_reduce(m, eg, AX.X, ALU.add).then_inc(*up(dve))
            dve.wait_ge(*latest(dve))
            nc.vector.tensor_scalar(m, m, 1.0 / 512, None, ALU.mult).then_inc(*up(dve))
            dve.wait_ge(*latest(dve))
            for t in range(2):
                nc.vector.tensor_scalar(eg[:, t, :], eg[:, t, :], m[:, t:t + 1], None, ALU.subtract).then_inc(*up(dve))
                dve.wait_ge(*latest(dve))
            nc.vector.tensor_tensor(esq, eg, eg, ALU.mult).then_inc(*up(dve))
            dve.wait_ge(*latest(dve))
            nc.vector.tensor_reduce(stat[:, 132:134], esq, AX.X, ALU.add).then_inc(*up(dve, "g squares"))
            dve.wait_ge(*latest(dve))
            dve.wait_ge(*when("g rstd"))
            for t in range(2):
                nc.vector.scalar_tensor_tensor(eg[:, t, :], eg[:, t, :], stat[:, 132 + t:133 + t], e_gain,
                                                      ALU.mult, ALU.mult).then_inc(*up(dve))
                dve.wait_ge(*latest(dve))
                nc.vector.tensor_tensor(eg[:, t, :], eg[:, t, :], e_bias, ALU.add).then_inc(*up(dve, "g normed"))
                dve.wait_ge(*latest(dve))
            for t in range(2):
                dve.wait_ge(*when(("mixed", "full", t)))
                for g in range(8):
                    c = slice(64 * g, 64 * g + 64)
                    at = ROWS_B["sgu_b"] + g
                    nc.vector.scalar_tensor_tensor(eu[:, t, c], psum[:, 2 + t, c], colB[:, at:at + 1],
                                                          eu[:, t, c], ALU.add, ALU.mult).then_inc(*up(dve, ("gated", t)))
                also(("read", ("mixed", t)), ("gated", t))
            for t in range(2):
                dve.wait_ge(*when(("gated", "turned", t)))
                nc.vector.tensor_copy(hT[:, 4:8, P * t:P * t + P],
                                             psum[:, 6 + t, :].rearrange("p (f t) -> p f t", f=4)).then_inc(*up(dve, ("read", ("gatedT", t))))

        def even_gate_pe(pe):
            stage(pe, "even")
            pe.wait_ge(*when("g normed"))
            pe.wait_ge(*when(("read", ("ewT", 1))))
            for t in range(2):
                pe.wait_ge(*bank(2 + t, ("mixed", t)))
                for g in range(8):
                    c = slice(64 * g, 64 * g + 64)
                    ins = nc.tensor.matmul(psum[:, 2 + t, c], ewT[:, g, :], eg[:, t, c], start=True, stop=True)
                ins.then_inc(*up(pe, ("mixed", "full", t)))
            for t in range(2):
                pe.wait_ge(*when(("gated", t)))
                pe.wait_ge(*bank(6 + t, ("gatedT", t)))
                for f in range(4):
                    ins = nc.tensor.transpose(psum[:, 6 + t, P * f:P * f + P], eu[:, t, P * f:P * f + P], ident)
                ins.then_inc(*up(pe, ("gated", "turned", t)))

        sb_units = []
        for h in range(8):
            for qt in range(2):
                r, f = head_rows(h), h // 2
                sb_units.append(dict(keys=P * (qt + 1), qk=[(eq[r, f, P * qt:P * qt + P], ek[r, f, 0:P * (qt + 1)])],
                                     v=[(lambda k, h=h: ev[:, k, 64 * h:64 * h + 64], r.start)],
                                     dst=[hT[r, f, P * qt:P * qt + P]]))

        def stick_act(act):
            stage(act, "stick")
            act.wait_ge(*when(("sbg_in", "full", 4, 1)))

            def softplus(i):
                n, s = sb_units[i]["keys"], sc[:, i % 2, :]
                act.wait_ge(*when(("sb", "z", i)))
                if i >= 2:
                    act.wait_ge(*when(("sb", "probs", i - 2)))
                nc.scalar.activation(s[:, 0:n], sc[:, 2 + i % 2, 0:n], ACT.Abs).then_inc(*up(act))
                act.wait_ge(*latest(act))
                nc.scalar.activation(s[:, 0:n], s[:, 0:n], ACT.Exp, scale=-1.0).then_inc(*up(act))
                act.wait_ge(*latest(act))
                nc.scalar.activation(s[:, 0:n], s[:, 0:n], ACT.Ln, bias=1.0).then_inc(*up(act, ("sb", "ln", i)))
                act.wait_ge(*latest(act))

            def weights(i):
                n = sb_units[i]["keys"]
                act.wait_ge(*when(("sb", "exponent", i)))
                if i >= 2:
                    act.wait_ge(*when(("sb", "turned", i - 2)))
                nc.scalar.activation(sc2[:, i % 2, 0:n], sc[:, i % 2, 0:n], ACT.Exp).then_inc(*up(act, ("sb", "probs", i)))

            for step, i in unit_tick(16, softplus, weights, lambda i: att_probsT(act, "sb", sb_units, i),
                                     lambda i: att_out(act, "sb", sb_units, i)):
                step(i)

        def stick_dve(dve):
            stage(dve, "stick")

            def scaled(i):
                n, r = sb_units[i]["keys"], sc[:, 2 + i % 2, :]
                dve.wait_ge(*when(("sb", "scores", i)))
                nc.vector.tensor_scalar(r[:, 0:n], psum[:, i % 2, 0:n], 0.125, None, ALU.mult).then_inc(*up(dve, ("sb", "z", i)))
                dve.wait_ge(*latest(dve))
                also(("read", ("sb", "s", i)), ("sb", "z", i))

            def exponent(i):
                n, s, r = sb_units[i]["keys"], sc[:, i % 2, :], sc[:, 2 + i % 2, :]
                d = slice(n - P, n)
                dve.wait_ge(*when(("sb", "ln", i)))
                nc.vector.scalar_tensor_tensor(s[:, 0:n], r[:, 0:n], 0.0, s[:, 0:n], ALU.max, ALU.add).then_inc(*up(dve))
                dve.wait_ge(*latest(dve))
                nc.vector.tensor_tensor(s[:, d], s[:, d], cst("strict"), ALU.mult).then_inc(*up(dve))
                dve.wait_ge(*latest(dve))
                v = s[:, 0:n][:, ::-1]
                nc.vector.tensor_tensor_scan(v, v, v, 0.0, ALU.add, ALU.max).then_inc(*up(dve))
                dve.wait_ge(*latest(dve))
                nc.vector.tensor_tensor(s[:, 0:n], r[:, 0:n], s[:, 0:n], ALU.subtract).then_inc(*up(dve))
                dve.wait_ge(*latest(dve))
                nc.vector.tensor_tensor(s[:, d], s[:, d], cst("strict_add"), ALU.add).then_inc(*up(dve, ("sb", "exponent", i)))
                dve.wait_ge(*latest(dve))

            for step, i in unit_tick(16, scaled, exponent):
                step(i)

        cq = area(0, 2, 512)
        ckv = area(1024, 2, 288)
        cqT = area(1600, 4, 256)
        ckvT = area(2624, 2, 256)
        mq = area(3136, 2, 16, 96)
        mkv = area(6208, 2, 16, 128)
        mk = area(10304, 2, 16, 96)
        mqT = area(13376, 16, 256)
        mkT = area(17472, 16, 256)
        msq = area(21568, 16, 96)
        pos_i = sb("pos_i", [P, 2], I32)
        rot = area(23104, 6, 32)

        def mla_pool(pool):
            stage(pool, "mla")
            nc.gpsimd.dma_start(pos_i[:, :], a["positions_2"][0].rearrange("(t p) -> p t", p=P), allow_slow_non_contiguous=True)\
                .then_inc(landing("positions"), 16)

        def rstd_pool(pool, v, width, before, event):
            pool.wait_ge(*when(before))
            nc.gpsimd.tensor_scalar(v, v, 1.0 / width, EPS, ALU.mult, ALU.add).then_inc(*up(pool))
            pool.wait_ge(*latest(pool))
            nc.gpsimd.tensor_tensor(v, v, half[:, 0:v.shape[1]], ALU.pow).then_inc(*up(pool, event))
            pool.wait_ge(*latest(pool))

        def mla_pool_rstd(pool):
            stage(pool, "mla")
            rstd_pool(pool, stat[:, 134:136], 512, "cq squares", "cq rstd")
            rstd_pool(pool, stat[:, 136:138], 256, "ckv squares", "ckv rstd")
            for y in range(2):
                for t in range(2):
                    at = 144 + 16 * (2 * y + t)
                    rstd_pool(pool, stat[:, at:at + 16], 96, ("mla squares", y, t), ("mla rstd", y, t))

        def angles_dve(dve):
            stage(dve, "angles")
            dve.wait_ge(*when(("dma", "positions")))
            C1, C2 = 6.28125, 0.0019353071795864769
            posf = stat[:, 138:140]
            ang, n, r, c = (rot[:, j, :] for j in range(4))
            nc.vector.tensor_copy(posf, pos_i[:, :]).then_inc(*up(dve))
            dve.wait_ge(*latest(dve))
            for t in range(2):
                nc.vector.tensor_scalar(ang[:, 16 * t:16 * t + 16], cst("inv_freq"), posf[:, t:t + 1], None,
                                               ALU.mult).then_inc(*up(dve))
                dve.wait_ge(*latest(dve))
            nc.vector.tensor_scalar(n, ang, float(1 / (2 * np.pi)), 12582912.0, ALU.mult, ALU.add).then_inc(*up(dve))
            dve.wait_ge(*latest(dve))
            nc.vector.tensor_scalar(n, n, 12582912.0, None, ALU.subtract).then_inc(*up(dve))
            dve.wait_ge(*latest(dve))
            nc.vector.scalar_tensor_tensor(r, n, -C1, ang, ALU.mult, ALU.add).then_inc(*up(dve))
            dve.wait_ge(*latest(dve))
            nc.vector.scalar_tensor_tensor(r, n, -C2, r, ALU.mult, ALU.add).then_inc(*up(dve))
            dve.wait_ge(*latest(dve))
            nc.vector.tensor_scalar(c, r, float(np.pi / 2), float(-2 * np.pi), ALU.is_gt, ALU.mult).then_inc(*up(dve))
            dve.wait_ge(*latest(dve))
            nc.vector.scalar_tensor_tensor(c, r, float(np.pi / 2), c, ALU.add, ALU.add).then_inc(*up(dve))
            dve.wait_ge(*latest(dve))
            for v in (r, c):
                nc.vector.tensor_scalar(v, v, 3.1415925, -3.1415925, ALU.min, ALU.max).then_inc(*up(dve, "angles"))
                dve.wait_ge(*latest(dve))

        def angles_act(act):
            stage(act, "angles")
            act.wait_ge(*when("angles"))
            nc.scalar.activation(rot[:, 4, :], rot[:, 2, :], ACT.Sin).then_inc(*up(act))
            act.wait_ge(*latest(act))
            nc.scalar.activation(rot[:, 5, :], rot[:, 3, :], ACT.Sin).then_inc(*up(act, "sines"))
            act.wait_ge(*latest(act))

        def mla_pe(pe):
            rows_pe(pe, "mla_in", lambda k, t: hT[:, k, P * t:P * t + P], range(2), KT, 800, [0, 1, 2, 3],
                    [("read", ("mix1", b)) for b in range(4)])
            stage(pe, "mla")
            for i, (src, nf) in enumerate(((cq, 4), (ckv, 2))):
                for t in range(2):
                    b = 4 + 2 * i + t
                    pe.wait_ge(*when(("latent normed", i, t)))
                    pe.wait_ge(*bank(b, ("latT", i, t)))
                    for f in range(nf):
                        ins = nc.tensor.transpose(psum[:, b, P * f:P * f + P], src[:, t, P * f:P * f + P], ident)
                    ins.then_inc(*up(pe, ("latT", "full", i, t)))
            rows_pe(pe, "mla_uq", lambda k, t: cqT[:, k, P * t:P * t + P], range(2), 4, 1536, [0, 1, 2, 3],
                    [("read", ("latT", 0, 1))])
            rows_pe(pe, "mla_ukv", lambda k, t: ckvT[:, k, P * t:P * t + P], range(2), 2, 2048, [4, 5, 6, 7],
                    [("read", ("latT", 1, 1))])
            stage(pe, "mla")
            for i, (y, t, g) in enumerate(mla_turns):
                pe.wait_ge(*when(("mla roped", y, t)))
                b = i % 4
                pe.wait_ge(*bank(b, ("mlaT", i)))
                for j in range(4):
                    ins = nc.tensor.transpose(psum[0:96, b, P * j:P * j + P], (mq, mk)[y][:, t, 4 * g + j, :], ident)
                ins.then_inc(*up(pe, ("mlaT", "full", i)))

        mla_turns = [(y, t, g) for y in range(2) for t in range(2) for g in range(4)]

        def mla_act(act):
            stage(act, "mla")
            act.wait_ge(*when(("pre1_down", "full", 1, 1)))
            for n in range(2):
                for t in range(2):
                    act.wait_ge(*when(("mla_in", "full", n, t)))
                    w = 512 if n == 0 else 288
                    nc.scalar.copy((cq, ckv)[n][:, t, :], psum[:, 2 * n + t, 0:w]).then_inc(*up(act, ("read", ("mla_in", n, t))))
            for n in range(3):
                for t in range(2):
                    act.wait_ge(*when(("mla_uq", "full", n, t)))
                    nc.scalar.copy(mq[:, t].rearrange("p h d -> p (h d)")[:, 512 * n:512 * n + 512],
                                          psum[:, (2 * n + t) % 4, :]).then_inc(*up(act, ("read", ("mla_uq", n, t))))
            for n in range(4):
                for t in range(2):
                    act.wait_ge(*when(("mla_ukv", "full", n, t)))
                    nc.scalar.copy(mkv[:, t].rearrange("p h d -> p (h d)")[:, 512 * n:512 * n + 512],
                                          psum[:, 4 + (2 * n + t) % 4, :]).then_inc(*up(act, ("read", ("mla_ukv", n, t))))
            for i, (y, t, g) in enumerate(mla_turns):
                act.wait_ge(*when(("mlaT", "full", i)))
                nc.scalar.copy((mqT, mkT)[y][0:96, 4 * g:4 * g + 4, P * t:P * t + P],
                                      psum[0:96, i % 4, :].rearrange("p (h t) -> p h t", h=4)).then_inc(*up(act, ("read", ("mlaT", i))))

        def mla_dve(dve):
            stage(dve, "mla")
            for i, (y, w, at, name) in enumerate(((cq, 512, 134, "cq"), (ckv, 256, 136, "ckv"))):
                for t in range(2):
                    dve.wait_ge(*when(("read", ("mla_in", i, t))))
                    nc.vector.tensor_tensor(msq.rearrange("p a b -> p (a b)")[:, 0:w], y[:, t, 0:w], y[:, t, 0:w],
                                                   ALU.mult).then_inc(*up(dve))
                    dve.wait_ge(*latest(dve))
                    nc.vector.tensor_reduce(stat[:, at + t:at + t + 1], msq.rearrange("p a b -> p (a b)")[:, 0:w],
                                                   AX.X, ALU.add).then_inc(*up(dve, name + " squares"))
                    dve.wait_ge(*latest(dve))
            for i, (y, w, at, name) in enumerate(((cq, 512, 134, "cq"), (ckv, 256, 136, "ckv"))):
                dve.wait_ge(*when(name + " rstd"))
                for t in range(2):
                    nc.vector.tensor_scalar(y[:, t, 0:w], y[:, t, 0:w], stat[:, at + t:at + t + 1], None, ALU.mult).then_inc(*up(dve, ("latent normed", i, t)))
                    dve.wait_ge(*latest(dve))
            for i, (nf, dst, name) in enumerate(((4, cqT, "q_lora"), (2, ckvT, "kv_lora"))):
                for t in range(2):
                    b = 4 + 2 * i + t
                    dve.wait_ge(*when(("latT", "full", i, t)))
                    for f in range(nf):
                        at = ROWS_B[name] + f
                        nc.vector.tensor_scalar(dst[:, f, P * t:P * t + P], psum[:, b, P * f:P * f + P],
                                                       colB[:, at:at + 1], None, ALU.mult).then_inc(*up(dve, ("read", ("latT", i, t))))
            for y in range(2):
                v = (mq, mk)[y]
                for t in range(2):
                    if y == 0:
                        for event in [("read", ("mla_uq", n, t)) for n in range(3)]:
                            dve.wait_ge(*when(event))
                    else:
                        for event in [("read", ("mla_ukv", n, t)) for n in range(4)]:
                            dve.wait_ge(*when(event))
                        nc.vector.tensor_copy(mk[:, t, :, 0:64], mkv[:, t, :, 0:64]).then_inc(*up(dve))
                        dve.wait_ge(*latest(dve))
                        nc.vector.tensor_copy(mk[:, t, :, 64:96],
                                                     ckv[:, t, 256:288].unsqueeze(1).to_broadcast([P, 16, 32])).then_inc(*up(dve))
                        dve.wait_ge(*latest(dve))
                    at = 144 + 16 * (2 * y + t)
                    nc.vector.tensor_tensor(msq, v[:, t], v[:, t], ALU.mult).then_inc(*up(dve))
                    dve.wait_ge(*latest(dve))
                    nc.vector.tensor_reduce(stat[:, at:at + 16], msq, AX.X, ALU.add).then_inc(*up(dve, ("mla squares", y, t)))
                    dve.wait_ge(*latest(dve))
            dve.wait_ge(*when("sines"))
            dve.wait_ge(*when(("dma", "q_gain")))
            dve.wait_ge(*when(("dma", "k_gain")))
            for y in range(2):
                for t in range(2):
                    v = (mq, mk)[y][:, t]
                    at = 144 + 16 * (2 * y + t)
                    dve.wait_ge(*when(("mla rstd", y, t)))
                    nc.vector.tensor_tensor(v, v, stat[:, at:at + 16].unsqueeze(2).to_broadcast([P, 16, 96]),
                                                   ALU.mult).then_inc(*up(dve))
                    dve.wait_ge(*latest(dve))
                    nc.vector.tensor_tensor(v, v, gbc[:, 96 * y:96 * y + 96].unsqueeze(1).to_broadcast([P, 16, 96]),
                                                   ALU.mult).then_inc(*up(dve))
                    dve.wait_ge(*latest(dve))
                    s = rot[:, 4, 16 * t:16 * t + 16].unsqueeze(1).to_broadcast([P, 16, 16])
                    c = rot[:, 5, 16 * t:16 * t + 16].unsqueeze(1).to_broadcast([P, 16, 16])
                    tmp = [sc2[:, 0, 256 * (j % 2):256 * (j % 2) + 256].rearrange("p (h d) -> p h d", h=16) if j < 2 else
                           sc2[:, 1, 256 * (j % 2):256 * (j % 2) + 256].rearrange("p (h d) -> p h d", h=16)
                           for j in range(4)]
                    x1, x2 = v[:, :, 64:80], v[:, :, 80:96]
                    for j, (u, w) in enumerate(((x1, c), (x2, s), (x1, s), (x2, c))):
                        nc.vector.tensor_tensor(tmp[j], u, w, ALU.mult).then_inc(*up(dve))
                        dve.wait_ge(*latest(dve))
                    nc.vector.tensor_tensor(x1, tmp[0], tmp[1], ALU.subtract).then_inc(*up(dve))
                    dve.wait_ge(*latest(dve))
                    nc.vector.tensor_tensor(x2, tmp[2], tmp[3], ALU.add).then_inc(*up(dve, ("mla roped", y, t)))
                    dve.wait_ge(*latest(dve))

        mla_units = []
        for h in range(16):
            for qt in range(2):
                r, f = head_rows(h), h // 2
                mla_units.append(dict(keys=P * (qt + 1),
                                      qk=[(mqT[0:96, h, P * qt:P * qt + P], mkT[0:96, h, 0:P * (qt + 1)])],
                                      bias=[(P, None)] * qt + [(P, cst("causal_add"))],
                                      v=[(lambda k, h=h: mkv[:, k, h, 64:128], r.start)],
                                      dst=[hT[r, f, P * qt:P * qt + P]]))

        xkm = area(0, 2, 4, 256)
        xvm = area(2048, 2, 4, 256)
        xqr = area(4096, 2, 4, 256)
        xkT = area(6144, 8, 256)
        xqT = area(8192, 8, 256)
        xsq = area(10240, 2, 4, 256)

        def mem_load(pool, layer):
            if layer == 0:
                pool.wait_ge(*when("y normed"))
                pool.wait_ge(*when(("chains", 7)))
                nc.gpsimd.dma_start(cx[:, :, :], a["mem_2"][0].rearrange("(t p) d -> p t d", p=P))\
                    .then_inc(landing("mem"), 16)

        def xmem_pe(pe, l):
            rows_pe(pe, f"xkv{l}", lambda k, t: hT[:, k, P * t:P * t + P], (2, 3), KT, 2 * D, [0, 1, 2, 3],
                    [("read", (f"xm{l}", b)) for b in range(4)])
            rows_pe(pe, f"xq{l}", lambda k, t: hT[:, k, P * t:P * t + P], (0, 1), KT, D, [4, 5, 6, 7],
                    [("read", (f"xx{l}", b)) for b in range(4)])
            stage(pe, "xmem")
            for i in range(8):
                y, t, b2 = i // 4, (i // 2) % 2, i % 2
                pe.wait_ge(*when((f"x normed {l}", y, t)))
                pe.wait_ge(*bank(i % 4, (f"xT{l}", i)))
                for j in range(4):
                    src = (xkm, xqr)[y][:, t].rearrange("p h d -> p (h d)")
                    at = 512 * b2 + P * j
                    ins = nc.tensor.transpose(psum[:, i % 4, P * j:P * j + P], src[:, at:at + P], ident)
                ins.then_inc(*up(pe, (f"xT{l}", "full", i)))

        def xmem_act(act, l):
            stage(act, "xmem")
            act.wait_ge(*when(("sbg_out" if l == 0 else "mla_out", "full", 1, 1)))
            for n in range(4):
                for i, t in enumerate((2, 3)):
                    act.wait_ge(*when((f"xkv{l}", "full", n, t)))
                    b = (2 * n + i) % 4
                    nc.scalar.copy(xkm[:, i, n, :], psum[:, b, 0:256]).then_inc(*up(act))
                    nc.scalar.copy(xvm[:, i, n, :], psum[:, b, 256:512]).then_inc(*up(act, ("read", (f"xkv{l}", n, t))))
            for n in range(2):
                for t in range(2):
                    act.wait_ge(*when((f"xq{l}", "full", n, t)))
                    nc.scalar.copy(xqr[:, t, 2 * n:2 * n + 2, :].rearrange("p a b -> p (a b)"),
                                          psum[:, 4 + (2 * n + t) % 4, :]).then_inc(*up(act, ("read", (f"xq{l}", n, t))))

        def xmem_dve(dve, l):
            stage(dve, "xmem")
            for y in range(2):
                dve.wait_ge(*when(("read", (f"xkv{l}", 3, 3)) if y == 0 else ("read", (f"xq{l}", 1, 1))))
                v = (xkm, xqr)[y]
                at = 176 + 8 * y
                nc.vector.tensor_tensor(xsq, v, v, ALU.mult).then_inc(*up(dve))
                dve.wait_ge(*latest(dve))
                nc.vector.tensor_reduce(stat[:, at:at + 8], xsq.rearrange("p a b c -> p (a b) c"), AX.X, ALU.add).then_inc(*up(dve, (f"x squares {l}", y)))
                dve.wait_ge(*latest(dve))
                dve.wait_ge(*when((f"x rstd {l}", y)))
                for t in range(2):
                    nc.vector.tensor_tensor(v[:, t], v[:, t], stat[:, at + 4 * t:at + 4 * t + 4].unsqueeze(2)
                                                   .to_broadcast([P, 4, 256]), ALU.mult).then_inc(*up(dve, (f"x normed {l}", y, t)))
                    dve.wait_ge(*latest(dve))
            for i in range(8):
                y, t, b2 = i // 4, (i // 2) % 2, i % 2
                dve.wait_ge(*when((f"xT{l}", "full", i)))
                for j in range(2):
                    at = ROWS_B["xk" if y == 0 else "xq"] + 2 * l + j
                    dst = (xkT, xqT)[y].rearrange("p (h j) n -> p h j n", j=2)[:, 2 * b2:2 * b2 + 2, j, P * t:P * t + P]
                    src = psum[:, i % 4, :].rearrange("p (h j n) -> p h j n", h=2, j=2)[:, :, j, :]
                    nc.vector.tensor_scalar(dst, src, colB[:, at:at + 1], None, ALU.mult).then_inc(*up(dve, ("read", (f"xT{l}", i))))

        def xmem_pool(pool, l):
            stage(pool, "xmem")
            for y in range(2):
                rstd_pool(pool, stat[:, 176 + 8 * y:184 + 8 * y], 256, (f"x squares {l}", y), (f"x rstd {l}", y))

        x_units = []
        for h in range(4):
            for qt in range(2):
                x_units.append(dict(keys=256, bias=None,
                                    qk=[(xqT[:, 2 * h + j, P * qt:P * qt + P], xkT[:, 2 * h + j, :]) for j in range(2)],
                                    v=[(lambda k, h=h, j=j: xvm[:, k, h, P * j:P * j + P], 0) for j in range(2)],
                                    dst=[hT[:, 2 * h + j, P * qt:P * qt + P] for j in range(2)]))

        def cat(k, t):
            return hT[:, k, P * t:P * t + P]


        block = ctx.enter_context(nc.Block())

        @block.sync
        def _(eng):
            sp = Side(eng, "sp")
            stage(sp, "setup")
            setup_sp(sp)
            for i, (name, pieces) in enumerate(slabs):
                if 0 <= i - slab_at[("rw_o", 0, 0)] < RING:
                    sp.wait_ge(*when(("chains", 6)))
                if i >= RING:
                    sp.wait_ge(*when(("used", i - RING)))
                view = ring[:, i % RING, :].rearrange("p (k n) -> p k n", k=8)
                for nk, at, nn, src in pieces:
                    nc.sync.dma_start(view[:, 0:nk, at:at + nn], src)\
                        .then_inc(add(f"slab_landed_{i % RING}", 16, ("slab", i)), 16)
            sp.wait_ge(*when(("post1_down", "added", 1, 1)))
            nc.sync.dma_start(out[0].rearrange("(t p) d -> p t d", p=P), x[:, :, :])\
                .then_inc(landing("out"), 16)
            eng.wait_ge(sem("landed_out"), 16)

        @block.tensor
        def _(eng):
            pe = Side(eng, "pe")
            stage(pe, "setup")
            setup_pe(pe)
            ada_pe(pe)
            norm_pe(pe, "L0a")
            norm_pe(pe, "C0a")
            ab_in_pe(pe)
            qk_norm_pe(pe)
            att_pe(pe, "na", na, [("read", ("qkT", i)) for i in range(8)])
            att_pe(pe, "cx", cxa)
            decay_pe(pe)
            mlT_pe(pe)
            ml_pe(pe)
            merge_pe(pe)
            rows_pe(pe, "ab_out", lambda k, t: hT[:, k, P * t:P * t + P], range(4), KT, D, [0, 1, 2, 3], [("read", ("merge", 3)), ("read", ("cx", "o", 15))])
            norm_pe(pe, "L0m")
            norm_pe(pe, "C0m")
            up_pe(pe, "mlp0_up", 512, [("read", (k, b)) for k in ("L0m", "C0m") for b in range(4)])
            rows_pe(pe, "mlp0_down", lambda k, t: hid[:, k, P * t:P * t + P], range(4), 32, D, [0, 1, 2, 3], [("mlp0_up", "hidden", 31)])
            norm_pe(pe, "L1a")
            norm_pe(pe, "C1a")
            proj_pe(pe)
            for part in range(4):
                prep_pe(pe, 0, part)
            for f in range(8):
                gram_pe(pe, f)
                inv_pe(pe, f)
            for hop in range(HOPS):
                walk_pe(pe, 7, hop)
            readout_pe(pe)
            rows_pe(pe, "rw_o", lambda k, t: hT[:, k, P * t:P * t + P], range(2), KT, D, [4, 5, 6, 7], [("rw gated", 7)])
            norm_pe(pe, "L1m")
            up_pe(pe, "mlp1_up", 256, [("read", ("L1m", b)) for b in range(4)])
            rows_pe(pe, "mlp1_down", lambda k, t: hid[:, k, P * t:P * t + P], range(2), 32, D, [4, 5, 6, 7], [("mlp1_up", "hidden", 31)])
            norm_pe(pe, "pre0")
            swiglu_pe(pe, "pre0")
            norm_pe(pe, "mix0")
            even_in_pe(pe)
            even_gate_pe(pe)
            att_pe(pe, "sb", sb_units)
            rows_pe(pe, "sbg_out", cat, range(2), KT, D, [4, 5, 6, 7], [("read", ("sb", "o", 15)), ("read", ("gatedT", 1))])
            norm_pe(pe, "xm0")
            norm_pe(pe, "xx0")
            xmem_pe(pe, 0)
            att_pe(pe, "xa0", x_units, [("read", ("xT0", i)) for i in range(8)])
            rows_pe(pe, "xo0", cat, range(2), KT, D, [4, 5, 6, 7], [("read", ("xa0", "o", 7))])
            norm_pe(pe, "post0")
            swiglu_pe(pe, "post0")
            norm_pe(pe, "pre1")
            swiglu_pe(pe, "pre1")
            norm_pe(pe, "mix1")
            mla_pe(pe)
            att_pe(pe, "mla", mla_units, [("read", ("mlaT", 15))])
            rows_pe(pe, "mla_out", cat, range(2), KT, D, [4, 5, 6, 7], [("read", ("mla", "o", 31))])
            norm_pe(pe, "xm1")
            norm_pe(pe, "xx1")
            xmem_pe(pe, 1)
            att_pe(pe, "xa1", x_units, [("read", ("xT1", i)) for i in range(8)])
            rows_pe(pe, "xo1", cat, range(2), KT, D, [4, 5, 6, 7], [("read", ("xa1", "o", 7))])
            norm_pe(pe, "post1")
            swiglu_pe(pe, "post1")

        @block.scalar
        def _(eng):
            act = Side(eng, "act")
            stage(act, "setup")
            setup_act(act)
            norm_act(act, "L0a", x, [("dma", "x")])
            norm_act(act, "C0a", cx, [("dma", "ctx")])
            ab_in_act(act)
            gates_act(act)
            att_act(act, "na", na, 0.125, [("gates", "full", 3)])
            att_act(act, "cx", cxa, 0.125)
            softplus_act(act)
            decay_act(act)
            mlT_act(act)
            ml_act(act)
            norm_act(act, "L0m", x, [("ab_out", "added", 1, 1)])
            norm_act(act, "C0m", cx, [("ab_out", "added", 1, 3)])
            up_act(act, "mlp0_up", 512)
            norm_act(act, "L1a", x, [("mlp0_down", "added", 1, 1)])
            norm_act(act, "C1a", cx, [("mlp0_down", "added", 1, 3)])
            proj_act(act)
            for f in range(8):
                prep_act(act, f)
                if f:
                    for hop in range(HOPS):
                        walk_act(act, f - 1, hop)
            for hop in range(HOPS):
                walk_act(act, 7, hop)
            norm_act(act, "L1m", x, [("rw_o", "added", 1, 1)])
            up_act(act, "mlp1_up", 256)
            norm_act(act, "pre0", x, [("mlp1_down", "added", 1, 1)])
            swiglu_act(act, "pre0")
            norm_act(act, "mix0", x, [("pre0_down", "added", 1, 1)])
            even_in_act(act)
            stick_act(act)
            norm_act(act, "xm0", cx, [("dma", "mem"), ("sbg_out", "added", 1, 1)])
            norm_act(act, "xx0", x, [("sbg_out", "added", 1, 1)])
            xmem_act(act, 0)
            att_act(act, "xa0", x_units, 0.0625, [("xq0", "full", 1, 1)])
            norm_act(act, "post0", x, [("xo0", "added", 1, 1)])
            swiglu_act(act, "post0")
            norm_act(act, "pre1", x, [("post0_down", "added", 1, 1)])
            swiglu_act(act, "pre1")
            norm_act(act, "mix1", x, [("pre1_down", "added", 1, 1)])
            angles_act(act)
            mla_act(act)
            att_act(act, "mla", mla_units, 96 ** -0.5)
            norm_act(act, "xm1", cx, [("dma", "mem"), ("mla_out", "added", 1, 1)])
            norm_act(act, "xx1", x, [("mla_out", "added", 1, 1)])
            xmem_act(act, 1)
            att_act(act, "xa1", x_units, 0.0625, [("xq1", "full", 1, 1)])
            norm_act(act, "post1", x, [("xo1", "added", 1, 1)])
            swiglu_act(act, "post1")

        @block.vector
        def _(eng):
            dve = Side(eng, "dve")
            stage(dve, "setup")
            setup_dve(dve)
            ada_dve(dve)
            norm_dve(dve, "L0a", x, 0, mcol(0, 0, 1), mcol(0, 0, 0), True)
            norm_dve(dve, "C0a", cx, 256, mcol(0, 1, 1), mcol(0, 1, 0), True)
            gates_dve(dve)
            qk_norm_dve(dve)
            att_dve(dve, "na", na, 0.125, after_first=["bias ready"])
            att_dve(dve, "cx", cxa, 0.125)
            decay_dve(dve)
            decay_out_dve(dve)
            ml_dve(dve)
            merge_dve(dve)
            gated_rows_dve(dve, "ab_out", range(4), [0, 1, 2, 3], gates_a, ("gate a0", "gate a1"))
            norm_dve(dve, "L0m", x, 0, mcol(0, 0, 4), mcol(0, 0, 3), True)
            norm_dve(dve, "C0m", cx, 256, mcol(0, 1, 4), mcol(0, 1, 3), True)
            up_dve(dve, "mlp0_up", 512)
            gated_rows_dve(dve, "mlp0_down", range(4), [0, 1, 2, 3], gates_m, ("gate m0", "gate m1"))
            norm_dve(dve, "L1a", x, 0, mcol(1, 0, 1), mcol(1, 0, 0), True)
            norm_dve(dve, "C1a", cx, 256, mcol(1, 1, 1), mcol(1, 1, 0), True)
            mix_dve(dve)
            for part in range(PREP_PARTS):
                prep_dve(dve, 0, part)
            for f in range(8):
                gram_dve(dve, f)
                inv_dve(dve, f)
                walk_start(dve, f)
            for y in range(4, 8):
                walk_y(dve, 7, y)
            readout_dve(dve)
            gated_rows_dve(dve, "rw_o", range(2), [4, 5, 6, 7], gates_r, ("gate r",))
            norm_dve(dve, "L1m", x, 0, mcol(1, 0, 4), mcol(1, 0, 3), True)
            up_dve(dve, "mlp1_up", 256)
            gated_rows_dve(dve, "mlp1_down", range(2), [4, 5, 6, 7], gates_m, ("gate n",))
            norm_dve(dve, "pre0", x, 0, gain("ffn_pre", 0), split=("pre0_gu", 0, 0))
            swiglu_dve(dve, "pre0")
            norm_dve(dve, "mix0", x, 0, gain("mix", 0))
            even_gate_dve(dve)
            stick_dve(dve)
            add_rows_dve(dve, "sbg_out", [4, 5, 6, 7], 1.0)
            norm_dve(dve, "xm0", cx, 256, gain("xmem_mem", 0))
            norm_dve(dve, "xx0", x, 0, gain("xmem", 0))
            xmem_dve(dve, 0)
            att_dve(dve, "xa0", x_units, 0.0625)
            add_rows_dve(dve, "xo0", [4, 5, 6, 7], 1.0)
            norm_dve(dve, "post0", x, 0, gain("ffn_post", 0), split=("post0_gu", 0, 0))
            swiglu_dve(dve, "post0")
            norm_dve(dve, "pre1", x, 0, gain("ffn_pre", 1), split=("pre1_gu", 0, 0))
            swiglu_dve(dve, "pre1")
            angles_dve(dve)
            norm_dve(dve, "mix1", x, 0, gain("mix", 1))
            mla_dve(dve)
            att_dve(dve, "mla", mla_units, 96 ** -0.5)
            add_rows_dve(dve, "mla_out", [4, 5, 6, 7], 1.0)
            norm_dve(dve, "xm1", cx, 256, gain("xmem_mem", 1))
            norm_dve(dve, "xx1", x, 0, gain("xmem", 1))
            xmem_dve(dve, 1)
            att_dve(dve, "xa1", x_units, 0.0625)
            add_rows_dve(dve, "xo1", [4, 5, 6, 7], 1.0)
            norm_dve(dve, "post1", x, 0, gain("ffn_post", 1), split=("post1_gu", 0, 0))
            swiglu_dve(dve, "post1")

        @block.gpsimd
        def _(eng):
            pool = Side(eng, "pool")
            stage(pool, "setup")
            setup_pool(pool)
            ada_pool(pool)
            norm_pool(pool, "L0a")
            norm_pool(pool, "C0a")
            qk_norm_pool(pool)
            rope_pool(pool)
            ml_pool(pool)
            merge_pool(pool)
            pool.wait_ge(*when(("merge", "turned", 3)))
            gate_load(pool, "gate a0", gates_a[0], 0, 0, 2)
            gate_load(pool, "gate a1", gates_a[1], 0, 1, 2)
            pool.wait_ge(*when(("merge", "turned", 3)))
            gate_load(pool, "gate m0", gates_m[0], 0, 0, 5)
            gate_load(pool, "gate m1", gates_m[1], 0, 1, 5)
            norm_pool(pool, "L0m")
            norm_pool(pool, "C0m")
            norm_pool(pool, "L1a")
            norm_pool(pool, "C1a")
            rw_pool(pool)
            readout_pool(pool)
            norm_pool(pool, "L1m")
            pool.wait_ge(*when(("L1m", "normed", 0)))
            gate_load(pool, "gate n", gates_m[0], 1, 0, 5)
            norm_pool(pool, "pre0")
            norm_pool(pool, "mix0")
            even_pool(pool)
            even_pool_rstd(pool)
            mem_load(pool, 0)
            norm_pool(pool, "xm0")
            norm_pool(pool, "xx0")
            xmem_pool(pool, 0)
            norm_pool(pool, "post0")
            norm_pool(pool, "pre1")
            norm_pool(pool, "mix1")
            mla_pool(pool)
            mla_pool_rstd(pool)
            mem_load(pool, 1)
            norm_pool(pool, "xm1")
            norm_pool(pool, "xx1")
            xmem_pool(pool, 1)
            norm_pool(pool, "post1")
    return now


_DIRECT = ["x", "ctx", "ada_w", "ada_b", "ab_w_in", "ab_gate_b", "na_rpb", "ab_w_out", "rw_w_rkv", "rw_w1", "rw_w2",
           "rw_a1", "rw_a2", "rw_g1", "rw_g2", "rw_w_o", "mlp_w1", "mlp_w2", "mem_2", "positions_2",
           "ffn_pre_w_gu_2", "ffn_pre_w_down_2", "sbg_w_in_2", "sgu_w_2", "sgu_ln_gain_2", "sgu_ln_bias_2", "sbg_w_out_2", "mla_w_in_2", "mla_w_uq_2",
           "mla_w_ukv_2", "mla_q_gain_2", "mla_k_gain_2", "mla_w_out_2", "xmem_wq_2", "xmem_wkv_2", "xmem_wo_2",
           "ffn_post_w_gu_2", "ffn_post_w_down_2"]
_VEC_A = ["rw_mu", "rw_w0", "rw_a0", "rw_k_k", "rw_k_a", "rw_r_k", "rw_lnx_w", "rw_lnx_b", "ml_head_norm",
          "na_q_norm", "na_q_norm", "na_k_norm", "na_k_norm"]
_VEC_B = ["ffn_pre_norm_2", "mix_norm_2", "xmem_norm_2", "xmem_mem_norm_2", "ffn_post_norm_2", "sgu_ln_gain_2",
          "sgu_ln_bias_2", "mla_q_lora_gain_2", "mla_kv_lora_gain_2", "xmem_q_gain_2", "xmem_k_gain_2", "sgu_b_2",
          "c", "c_ctx"]


def kernel(**inputs):
    import concourse.bacc as _bacc
    from concourse.bass_utils import run_bass_kernel_spmd as _run

    arrays = {name: np.ascontiguousarray(inputs[name]) for name in _DIRECT}
    arrays["vec_a"] = np.concatenate([np.asarray(inputs[n]).reshape(-1) for n in _VEC_A]).reshape(-1, P)
    arrays["vec_b"] = np.concatenate([np.asarray(inputs[n]).reshape(-1) for n in _VEC_B]).reshape(-1, P)
    arrays["const"] = np.ascontiguousarray(np.concatenate(list(constant_blocks().values()), axis=1))

    noted = None
    for _ in range(2):
        nc = _bacc.Bacc("TRN2", target_bir_lowering=False, num_devices=1)
        a = {name: nc.dram_tensor(f"in_{name}", v.shape, mybir.dt.from_np(v.dtype), kind="ExternalInput").ap()
             for name, v in arrays.items()}
        out = nc.dram_tensor("out", (1, T, D), F32, kind="ExternalOutput").ap()
        scratch_mod = nc.dram_tensor("modulation", (2, 2, 6 * D), F32, kind="Internal").ap()
        scratch_rpb = nc.dram_tensor("bias_rows", (56, 64, 127), F32, kind="Internal").ap()
        noted = bidir_dual_stack(nc, a, out, scratch_mod, scratch_rpb, noted)
    r = _run(nc, [{f"in_{name}": v for name, v in arrays.items()}], core_ids=[0])
    return r.results[0]["out"]
```

```python
from contextlib import ExitStack

import numpy as np

import concourse.bass as bass
from concourse import mybir

ALU = mybir.AluOpType
ACT = mybir.ActivationFunctionType
F32 = mybir.dt.float32
F32R = mybir.dt.float32r
I32 = mybir.dt.int32
AX = mybir.AxisListType

P = 128
T = 256
D = 1024
KT = D // P
RING = 3
SLAB = 8 * 512
EPS = 1e-6
NEG = -1e30
GRID_W = 64
D_FF = 4096
D_FF2 = 2816
C = 64
NCH = 2 * T // C


def constant_blocks():
    p = np.arange(P)[:, None]
    f = np.arange(P)[None, :]
    s64, t64 = np.arange(P)[:, None] % C, np.arange(C)[None, :]
    col, key = np.arange(P)[:, None] % GRID_W, np.arange(GRID_W)[None, :]
    start = np.clip(col - 8, 0, GRID_W - 16)
    blocks = {
        "ident": p == f,
        "headones": (p // 64) == (f // 64),
        "causal_add": np.where(f <= p, 0.0, NEG),
        "strict": f < p,
        "strict_add": np.where(f < p, 0.0, NEG),
        "window_add": np.where((key >= start) & (key < start + 16), 0.0, NEG),
        "st_fwd": p <= f,
        "st_bwd": p >= f,
        "eye64": s64 == t64,
        "diag16": s64 // 16 == t64 // 16,
        "off32": (s64 // 32 == t64 // 32) & (s64 // 16 != t64 // 16),
        "off64": s64 // 32 != t64 // 32,
        "ones": np.ones((P, 64)),
        "chunk_start": np.broadcast_to(np.arange(512) % C != 0, (P, 512)),
    }
    one = np.ones((P, C))
    for z, (lt, le, gt) in enumerate([(s64 < t64, s64 <= t64, s64 > t64), (s64 > t64, s64 >= t64, s64 < t64)]):
        blocks[f"gram{z}"] = np.concatenate([lt, one, le, lt, one, le, gt], axis=1)
    sel = np.zeros((P, 4, P))
    for h in range(4):
        sel[h, h] = 1.0
    blocks["select4"] = sel.reshape(P, -1)
    tok = np.arange(T)
    inv = (10000.0 ** (-np.arange(32, dtype=np.float32) / 32)).astype(np.float32)
    ang = np.stack([(tok // GRID_W).astype(np.float32)[:, None] * inv,
                    (tok % GRID_W).astype(np.float32)[:, None] * inv], axis=1)
    for name, fn in (("cos2d", np.cos), ("sin2d", np.sin)):
        blocks[name] = fn(ang).reshape(2, P, 64).transpose(1, 0, 2).reshape(P, P)
    blocks["inv_freq"] = np.broadcast_to(
        (10000.0 ** (-np.arange(16, dtype=np.float32) / 16)).astype(np.float32), (P, 16))
    return {k: np.asarray(v, np.float32) for k, v in blocks.items()}


def constant_columns():
    at, out = 0, {}
    for name, b in constant_blocks().items():
        out[name] = (at, b.shape[1])
        at += b.shape[1]
    return out, at


ROWS_A, ROWS_B = {}, {}
for _rows, _list in ((ROWS_A, [("mu", 48), ("w0", 16), ("a0", 16), ("k_k", 8), ("k_a", 8), ("r_k", 8),
                               ("lnx_w", 8), ("lnx_b", 8), ("head_norm", 4), ("na_q", 1), ("na_k", 1)]),
                     (ROWS_B, [("ffn_pre", 16), ("mix", 16), ("xmem", 16), ("xmem_mem", 16), ("ffn_post", 16),
                               ("ln_gain", 4), ("ln_bias", 4), ("q_lora", 4), ("kv_lora", 2), ("xq", 4),
                               ("xk", 4), ("sgu_b", 8), ("c", 8), ("c_ctx", 8)])):
    _at = 0
    for _name, _n in _list:
        _rows[_name] = _at
        _at += _n
    _rows["rows"] = _at


class Side:

    def __init__(self, eng, name):
        self.eng, self.name, self.passed = eng, name, {}

    def wait_ge(self, sem, value):
        if self.passed.get(sem.name, 0) < value:
            self.eng.wait_ge(sem, value)
            self.passed[sem.name] = value


def bidir_dual_stack(nc, a, out, scratch_mod, scratch_rpb, noted):
    const_at, n_const = constant_columns()

    with ExitStack() as ctx:
        def sb(name, shape, dt=F32):
            return ctx.enter_context(nc.sbuf_tensor(name, shape, dt))

        sems, count, now, stages, own, tiles = {}, {}, {}, {}, {}, {}

        def sem(name):
            if name not in sems:
                sems[name] = ctx.enter_context(nc.semaphore(name))
            return sems[name]

        def stage(side, name):
            stages[side.name] = name

        def add(name, by, event):
            count[name] = count.get(name, 0) + by
            if event is not None:
                now[event] = (name, count[name])
            return sem(name)

        def up(side, event=None):
            name = f"{stages[side.name]}_by_{side.name}"
            own[side.name] = (add(name, 1, event), count[name])
            return own[side.name][0], 1

        def landing(event):
            return add("landed_" + str(event).replace(" ", "_"), 16, ("dma", event))

        def latest(side):
            return own[side.name]

        def when(event):
            if noted is None:
                return sem("uncounted"), 1
            name, value = noted[event]
            return sem(name), value

        def also(event, same):
            now[event] = now[same]

        def bank(b, tile):
            last, tiles[b] = tiles.get(b), tile
            return (sem("setup_by_pe"), 0) if last is None else when(("read", last))

        x = sb("x", [P, 2, D])
        cx = sb("cx", [P, 2, D])
        sc = sb("sc", [P, 6, 512])
        sc2 = sb("sc2", [P, 3, 512])
        const = sb("const", [P, n_const])
        colA = sb("colA", [P, P])
        colB = sb("colB", [P, P])
        modcol = sb("modcol", [P, 2, 96])
        csil = sb("csil", [P, KT, 2])
        stat = sb("stat", [P, 256])
        half = sb("half", [P, 64])
        gbc = sb("gbc", [P, 192])
        epsc = sb("epsc", [P, 2])
        ARENA = 23588
        with ExitStack() as same_place:
            hT = same_place.enter_context(nc.sbuf_tensor("hT", [P, KT, 2 * T], F32))
            ring = same_place.enter_context(nc.sbuf_tensor("ring", [P, RING, SLAB], F32))
            arena = same_place.enter_context(nc.sbuf_tensor("arena", [P, ARENA], F32))
        hT_parts = sb("hT_parts", [P, KT, 2 * T], F32R)
        ring_parts = sb("ring_parts", [P, RING, SLAB], F32R)
        arena_parts = sb("arena_parts", [P, ARENA], F32R)
        psum = ctx.enter_context(nc.psum_tensor("psum", [P, 8, 512], F32))

        def cst(name, n=P):
            at, w = const_at[name]
            return const[0:n, at:at + w]

        def area(at, *shape, rounded=False):
            n = int(np.prod(shape))
            v = (arena_parts if rounded else arena)[:, at:at + n]
            if len(shape) == 1:
                return v
            names = "abcde"[:len(shape)]
            return v.rearrange(f"p ({' '.join(names)}) -> p {' '.join(names)}",
                               **{k: s for k, s in zip(names[1:], shape[1:])})

        ident = cst("ident")

        slabs = []

        def plan(name, w, nk, n0, nn, k0=0, at=0):
            src = w[k0 * P:(k0 + nk) * P, n0:n0 + nn].rearrange("(k p) n -> p k n", p=P)
            if slabs and slabs[-1][0] == name:
                slabs[-1][1].append((nk, at, nn, src))
            else:
                slabs.append((name, [(nk, at, nn, src)]))

        def plan_rows(name, w, nk_total, n_total):
            for n in range(0, n_total, 512):
                for k in range(0, nk_total, 8):
                    plan((name, n // 512, k // 8), w, min(8, nk_total - k), n, min(512, n_total - n), k)

        def plan_ffn(name, gu, down):
            for n in range(0, D_FF2, 256):
                plan((name + "_gu", n // 256, 0), gu, KT, n, 256)
                plan((name + "_gu", n // 256, 0), gu, KT, D_FF2 + n, 256, at=256)
            plan_rows(name + "_down", down, D_FF2 // P, D)

        MLP_ORDER = (("up", 0, 0), ("up", 1, 0), ("up", 2, 0), ("down", 0, 0), ("down", 1, 0),
                     ("up", 3, 0), ("up", 4, 0), ("down", 0, 1), ("down", 1, 1),
                     ("up", 5, 0), ("up", 6, 0), ("down", 0, 2), ("down", 1, 2),
                     ("up", 7, 0), ("down", 0, 3), ("down", 1, 3))

        def plan_mlp(name, layer):
            for kind, n, g in MLP_ORDER:
                if kind == "up":
                    plan((name + "_up", n, 0), a["mlp_w1"][layer], KT, 512 * n, 512)
                else:
                    plan((name + "_down", n, g), a["mlp_w2"][layer], 8, 512 * n, 512, k0=8 * g)

        for layer in range(2):
            plan_rows(f"ada{layer}", a["ada_w"][layer], KT, 6 * D)
        plan_rows("ab_in", a["ab_w_in"][0], KT, 3600)
        plan_rows("ab_out", a["ab_w_out"][0], KT, D)
        plan_mlp("mlp0", 0)
        plan_mlp("mlp0c", 0)
        for w in ("w1", "a1"):
            for z in range(2):
                plan((w, 0, 0), a["rw_" + w][0, z], KT, 0, 64, at=64 * z)
        plan_rows("g1", a["rw_g1"][0], KT, 160)
        for i, w in enumerate("rkv"):
            plan_rows("rw_" + w, a["rw_w_rkv"][0, i], KT, D)
        plan_rows("rw_o", a["rw_w_o"][0], KT, D)
        plan_mlp("mlp1", 1)
        for layer in range(2):
            plan_ffn(f"pre{layer}", a["ffn_pre_w_gu_2"][layer], a["ffn_pre_w_down_2"][layer])
            if layer == 0:
                plan_rows("sbg_in", a["sbg_w_in_2"][0], KT, 2560)
                plan_rows("sbg_out", a["sbg_w_out_2"][0], KT, D)
            else:
                plan_rows("mla_in", a["mla_w_in_2"][0], KT, 800)
                plan_rows("mla_uq", a["mla_w_uq_2"][0], 4, 1536)
                plan_rows("mla_ukv", a["mla_w_ukv_2"][0], 2, 2048)
                plan_rows("mla_out", a["mla_w_out_2"][0], KT, D)
            plan_rows(f"xkv{layer}", a["xmem_wkv_2"][layer], KT, 2 * D)
            plan_rows(f"xq{layer}", a["xmem_wq_2"][layer], KT, D)
            plan_rows(f"xo{layer}", a["xmem_wo_2"][layer], KT, D)
            plan_ffn(f"post{layer}", a["ffn_post_w_gu_2"][layer], a["ffn_post_w_down_2"][layer])
        slab_at = {name: i for i, (name, _) in enumerate(slabs)}

        def slab(pe, name):
            i = slab_at[name]
            pe.wait_ge(*when(("slab", i)))
            return ring[:, i % RING, :].rearrange("p (k n) -> p k n", k=8)

        x_parts = [area(at, 8, 256, rounded=True) for at in (11264, 13312)]
        split_at = {}
        highs = area(15360, 2, 8, 512, rounded=True)

        def ffn_slabs(key):
            return [(key + "_gu", n, 0) for n in range(11)] + [(key + "_down", n, k) for n in range(2) for k in range(3)]

        def mlp_slabs(name):
            return [(f"{name}_{kind}", n, g) for kind, n, g in MLP_ORDER]

        sbg_slabs = [("sbg_in", n, 0) for n in range(5)]

        def mem_slabs(layer):
            return [(f"xkv{layer}", n, 0) for n in range(4)] + [(f"xq{layer}", n, 0) for n in range(2)]

        for names in (mlp_slabs("mlp0"), mlp_slabs("mlp0c"), mlp_slabs("mlp1"), ffn_slabs("pre0"), sbg_slabs, mem_slabs(0), ffn_slabs("post0"),
                      ffn_slabs("pre1"), mem_slabs(1), ffn_slabs("post1")):
            for name in names:
                split_at[name] = len(split_at)
        split_names = list(split_at)
        AHEAD = {}
        for key, names, n in (("mlp0", mlp_slabs("mlp0"), 1), ("mlp0c", mlp_slabs("mlp0c"), 1),
                              ("mlp1", mlp_slabs("mlp1"), 1), ("pre0", ffn_slabs("pre0"), 1), ("sbg", sbg_slabs, 1),
                              ("mem0", mem_slabs(0), 1), ("post0", ffn_slabs("post0"), 1),
                              ("pre1", ffn_slabs("pre1"), 1), ("mem1", mem_slabs(1), 1),
                              ("post1", ffn_slabs("post1"), 1)):
            AHEAD[key] = names[0:n]

        def slab_rows(name):
            return sum(piece[0] for piece in slabs[slab_at[name]][1]) if name[0].endswith("_down") else KT

        def raw_view(name):
            return ring[:, slab_at[name] % RING, :].rearrange("p (k n) -> p k n", k=8)

        def low_view(name):
            return ring_parts[:, slab_at[name] % RING, :].rearrange("p (k n) -> p k n", k=8)

        def high_view(name):
            return highs[:, split_at[name] % 2]

        def high_act(act, name):
            stage(act, "split")
            act.wait_ge(*when(("slab", slab_at[name])))
            if split_at[name] >= 2:
                act.wait_ge(*when(("used", slab_at[split_names[split_at[name] - 2]])))
            rows = slab_rows(name)
            for h in range(2):
                k = slice(4 * h, min(4 * h + 4, rows))
                nc.scalar.copy(high_view(name)[:, k, :], raw_view(name)[:, k, :])\
                    .then_inc(*up(act, ("high", name, h)))

        def low_dve(dve, name, h):
            stage(dve, "split")
            k = slice(4 * h, min(4 * h + 4, slab_rows(name)))
            dve.wait_ge(*when(("high", name, h)))
            nc.vector.tensor_tensor(low_view(name)[:, k, :], raw_view(name)[:, k, :],
                                    high_view(name).bitcast(F32)[:, k, :], ALU.subtract)\
                .then_inc(*up(dve, ("low", name, h)))

        def high_ahead(act, key):
            for name in AHEAD[key]:
                high_act(act, name)

        def low_slabs(dve, names):
            for name in names:
                for h in range(2):
                    low_dve(dve, name, h)

        def parts(name):
            high, low = high_view(name), low_view(name)
            return ((high, 0), (high, 1), (low, 0))

        def rows3_pe(pe, name, lhs, kt, n_total, banks, tiles=(0, 1), needs=(), first=0, key=None):
            stage(pe, "rows")
            for event in needs:
                pe.wait_ge(*when(event))
            for n in range(first, n_total // 512):
                for k0 in range(0, kt, 8):
                    w = (name, n, k0 // 8)
                    nk = min(8, kt - k0)
                    for t in range(2):
                        b = banks[(2 * (n - first) + t) % 4]
                        if k0 == 0:
                            pe.wait_ge(*bank(b, (name, n, tiles[t])))
                        for k in range(nk):
                            if key is not None:
                                pe.wait_ge(*when(("read", (key, k // 2))))
                            if k % 4 == 0:
                                pe.wait_ge(*when(("low", w, k // 4)))
                            for i, (s, q) in enumerate(parts(w)):
                                ins = nc.tensor.matmul(psum[:, b, :], lhs[q][:, k0 + k, P * t:P * t + P], s[:, k, :],
                                                       start=(k0 + k == 0 and i == 0), stop=(k0 + k == kt - 1 and i == 2))
                        if k0 + nk == kt and t == 0:
                            ins.then_inc(*up(pe, (name, "full", n, tiles[t])))
                    if k0 + nk == kt:
                        ins.then_inc(*up(pe, (name, "full", n, tiles[1])))
                        also(("used", slab_at[w]), (name, "full", n, tiles[1]))
                    else:
                        ins.then_inc(*up(pe, ("used", slab_at[w])))

        norms = []

        def norm_stat(who, key):
            if key not in norms:
                norms.append(key)
            i = norms.index(key)
            if who is not None and i >= 2:
                who.wait_ge(*when((norms[i - 2], "normed", 1)))
            return stat[:, 208 + 8 * (i % 2):216 + 8 * (i % 2)]

        def norm_act(act, key, src, needs=()):
            stage(act, "norm")
            for event in needs:
                act.wait_ge(*when(event))
            s = norm_stat(act, key)
            for t in range(2):
                nc.scalar.activation(sc[:, 4:6, :].rearrange("p a b -> p (a b)"), src[:, t, :], ACT.Square,
                                            accum_out=s[:, t:t + 1]).then_inc(*up(act, (key, "squares", t)))
                act.wait_ge(*latest(act))

        def norm_pool(pool, key):
            stage(pool, "norm")
            pool.wait_ge(*when((key, "squares", 1)))
            s = norm_stat(pool, key)
            nc.gpsimd.tensor_scalar(s[:, 2:4], s[:, 0:2], 1.0 / D, EPS, ALU.mult, ALU.add).then_inc(*up(pool))
            pool.wait_ge(*latest(pool))
            nc.gpsimd.tensor_tensor(s[:, 4:6], s[:, 2:4], half[:, 0:2], ALU.pow)\
                .then_inc(*up(pool, (key, "rstd")))
            pool.wait_ge(*latest(pool))

        def norm_dve(dve, key, src, off, scale, shift=None, plus1=False, dest=None):
            stage(dve, "norm")
            dve.wait_ge(*when((key, "rstd")))
            s = norm_stat(None, key)
            for t in range(2):
                xn = sc[:, 2 * t:2 * t + 2, :].rearrange("p a b -> p (a b)")
                nc.vector.tensor_scalar(xn, src[:, t, :], s[:, 4 + t:5 + t], None, ALU.mult)\
                    .then_inc(*up(dve, (key, "normed", t)))
                dve.wait_ge(*latest(dve))
            if plus1:
                nc.vector.tensor_scalar(stat[:, 8:16], scale, 1.0, None, ALU.add)\
                    .then_inc(*up(dve, (key, "scale")))
                dve.wait_ge(*latest(dve))
                scale = stat[:, 8:16]
            for b in range(4):
                dve.wait_ge(*when((key, "turned", b)))
                for k in (2 * b, 2 * b + 1):
                    src_ = psum[:, b + 4, 256 * (k % 2):256 * (k % 2) + 256]
                    dst = hT[:, k, off:off + 256]
                    if dest is not None and shift is not None:
                        full = sc2[:, k % 2, 0:256]
                        nc.vector.tensor_scalar(full, src_, scale[:, k:k + 1], shift[:, k:k + 1],
                                                ALU.mult, ALU.add).then_inc(*up(dve))
                        dve.wait_ge(*latest(dve))
                        nc.vector.tensor_copy(dest[0][:, k, :], full).then_inc(*up(dve))
                        dve.wait_ge(*latest(dve))
                        ins = nc.vector.tensor_tensor(dest[1][:, k, :], full, dest[0].bitcast(F32)[:, k, :],
                                                      ALU.subtract)
                    elif dest is not None:
                        nc.vector.tensor_scalar(dest[0][:, k, :], src_, scale[:, k:k + 1], None, ALU.mult)\
                            .then_inc(*up(dve))
                        dve.wait_ge(*latest(dve))
                        ins = nc.vector.scalar_tensor_tensor(dest[1][:, k, :], src_, scale[:, k:k + 1],
                                                             dest[0].bitcast(F32)[:, k, :],
                                                             ALU.mult, ALU.subtract)
                    elif shift is None:
                        ins = nc.vector.tensor_scalar(dst, src_, scale[:, k:k + 1], None, ALU.mult)
                    else:
                        ins = nc.vector.tensor_scalar(dst, src_, scale[:, k:k + 1], shift[:, k:k + 1],
                                                      ALU.mult, ALU.add)
                    ins.then_inc(*up(dve, ("read", (key, b)) if k % 2 else None))

        def norm_pe(pe, key):
            stage(pe, "norm")
            norm_stat(None, key)
            for b in range(4):
                pe.wait_ge(*bank(b + 4, (key, b)))
                for k in (2 * b, 2 * b + 1):
                    for t in range(2):
                        pe.wait_ge(*when((key, "normed", t)))
                        at = 256 * (k % 2) + 128 * t
                        ins = nc.tensor.transpose(psum[:, b + 4, at:at + 128],
                                                  sc[:, 2 * t + k // 4, 128 * (k % 4):128 * (k % 4) + 128], ident)
                ins.then_inc(*up(pe, (key, "turned", b)))

        def rows_pe(pe, name, lhs, tiles, kt, n_total, banks, needs=(), only=None):
            stage(pe, "rows")
            for event in needs:
                pe.wait_ge(*when(event))
            i = 0
            for n in range(0, n_total, 512):
                if only is not None and n // 512 not in only:
                    continue
                w = min(512, n_total - n)
                where = [banks[(i + t) % len(banks)] for t in range(len(tiles))]
                i += len(tiles)
                for k0 in range(0, kt, 8):
                    s = slab(pe, (name, n // 512, k0 // 8))
                    nk = min(8, kt - k0)
                    for t, tile in enumerate(tiles):
                        if k0 == 0:
                            pe.wait_ge(*bank(where[t], (name, n // 512, tile)))
                        for k in range(nk):
                            ins = nc.tensor.matmul(psum[:, where[t], 0:w], lhs(k0 + k, tile), s[:, k, 0:w],
                                                   start=(k0 + k == 0), stop=(k0 + k == kt - 1))
                        if k0 + nk == kt and t < len(tiles) - 1:
                            ins.then_inc(*up(pe, (name, "full", n // 512, tile)))
                    if k0 + nk == kt:
                        ins.then_inc(*up(pe, (name, "full", n // 512, tiles[-1])))
                        also(("used", slab_at[(name, n // 512, k0 // 8)]), (name, "full", n // 512, tiles[-1]))
                    else:
                        ins.then_inc(*up(pe, ("used", slab_at[(name, n // 512, k0 // 8)])))

        def rows_bank(name, n, i, tiles, banks):
            return banks[(n * len(tiles) + i) % len(banks)]

        modrow = area(0, 2, 6 * D)
        pad = arena[0:56, 23000:23127]
        nab = area(18448, 2, 4, 8, 64)

        def setup_sp(sp):
            nc.sync.dma_start(const[:, :], a["const"])\
                .then_inc(landing("const"), 16)
            nc.sync.dma_start(sc[0:ROWS_A["rows"], 0, 0:P], a["vec_a"])\
                .then_inc(landing("vec_a"), 16)
            nc.sync.dma_start(sc[0:ROWS_B["rows"], 1, 0:P], a["vec_b"])\
                .then_inc(landing("vec_b"), 16)

        def setup_pool(pool):
            nc.gpsimd.memset(half[:, :], -0.5).then_inc(*up(pool))
            pool.wait_ge(*latest(pool))
            nc.gpsimd.memset(pad, 0.0).then_inc(*up(pool, "pad zero"))
            pool.wait_ge(*latest(pool))
            nc.gpsimd.memset(epsc[:, 0:1], EPS).then_inc(*up(pool))
            pool.wait_ge(*latest(pool))
            pool.wait_ge(*when("pad zero"))
            nc.gpsimd.dma_start(pad.rearrange("p (a c) -> p a c", a=1)[:, :, 48:79], bass.AP(tensor=a["na_rpb"].tensor, offset=4 * 31,
                              ap=[[31, 7], [15 * 31, 8], [1, 31]]))\
                .then_inc(landing("rpb"), 16)
            nc.gpsimd.dma_start(modrow[0:2, :, :], a["ada_b"].partition_broadcast(2))\
                .then_inc(landing("ada_b"), 16)
            nc.gpsimd.dma_start(x[:, :, :], a["x"][0].rearrange("(t p) d -> p t d", p=P))\
                .then_inc(landing("x"), 16)
            nc.gpsimd.dma_start(cx[:, :, :], a["ctx"][0].rearrange("(t p) d -> p t d", p=P))\
                .then_inc(landing("ctx"), 16)
            nc.gpsimd.dma_start(gbc[:, 0:96], a["mla_q_gain_2"][0].partition_broadcast(P))\
                .then_inc(landing("q_gain"), 16)
            nc.gpsimd.dma_start(gbc[:, 96:192], a["mla_k_gain_2"][0].partition_broadcast(P))\
                .then_inc(landing("k_gain"), 16)
            nc.gpsimd.dma_start(stat[0:4, 200:204], a["ab_gate_b"][0].rearrange("(a b) -> b a", b=4), allow_slow_non_contiguous=True)\
                .then_inc(landing("gate_b"), 16)
            pool.wait_ge(*when(("dma", "rpb")))
            nc.gpsimd.dma_start(scratch_rpb, pad.unsqueeze(1).to_broadcast([56, 64, 127]))\
                .then_inc(landing("rpb rows"), 16)
            pool.wait_ge(*when(("dma", "rpb rows")))
            for r in range(4):
                qt, r2 = divmod(r, 2)
                nc.gpsimd.dma_start(nab[64 * r2:64 * r2 + 64, qt, :, :, :].rearrange("p a b c -> p (a b) c"), bass.AP(tensor=scratch_rpb.tensor, offset=(3 - r) * 8 * 64 * 127 + 63,
                                  ap=[[126, 64], [64 * 127, 32], [1, 64]]))\
                    .then_inc(landing("bias"), 16)
            pool.wait_ge(*when(("dma", "bias")))
            pool.wait_ge(*when(("dma", "const")))
            nc.gpsimd.tensor_tensor(
                nab.rearrange("p a b c d -> p (a b c) d"),
                nab.rearrange("p a b c d -> p (a b c) d"),
                cst("window_add").unsqueeze(1).to_broadcast([P, 64, 64]), ALU.add)\
                .then_inc(*up(pool, "bias ready"))
            pool.wait_ge(*latest(pool))

        def setup_pe(pe):
            pe.wait_ge(*when(("dma", "const")))
            for i, (rows, ev) in enumerate(((ROWS_A, "vec_a"), (ROWS_B, "vec_b"))):
                pe.wait_ge(*when(("dma", ev)))
                pe.wait_ge(*bank(i, ("vec", i)))
                n = rows["rows"]
                nc.tensor.transpose(psum[:, i, 0:n], sc[0:n, i, 0:P], ident[0:n, 0:n])\
                    .then_inc(*up(pe, ("vec", "turned", i)))

        def setup_dve(dve):
            for i, (col, rows) in enumerate(((colA, ROWS_A), (colB, ROWS_B))):
                dve.wait_ge(*when(("vec", "turned", i)))
                n = rows["rows"]
                nc.vector.tensor_copy(col[:, 0:n], psum[:, i, 0:n]).then_inc(*up(dve, ("read", ("vec", i))))
                dve.wait_ge(*latest(dve))

        def setup_act(act):
            act.wait_ge(*when(("read", ("vec", 1))))
            for i, name in enumerate(("c", "c_ctx")):
                nc.scalar.activation(csil[:, :, i], colB[:, ROWS_B[name]:ROWS_B[name] + 8], ACT.Silu)\
                    .then_inc(*up(act, "silu c"))
                act.wait_ge(*latest(act))

        def ada_pe(pe):
            stage(pe, "ada")
            pe.wait_ge(*when("silu c"))
            for i in range(24):
                s = slab(pe, (f"ada{i // 12}", i % 12, 0))
                pe.wait_ge(*bank(i % 4, ("ada", i)))
                for k in range(KT):
                    ins = nc.tensor.matmul(psum[0:2, i % 4, :], csil[:, k, :], s[:, k, :], start=(k == 0), stop=(k == 7))
                ins.then_inc(*up(pe, ("ada", "full", i)))
                also(("used", slab_at[(f"ada{i // 12}", i % 12, 0)]), ("ada", "full", i))
            for layer in range(2):
                pe.wait_ge(*when(("dma", f"mod back {layer}")))
                pe.wait_ge(*bank(layer, ("mod", layer)))
                nc.tensor.transpose(psum[:, layer, 0:96], sc[0:96, layer, 0:P], ident[0:96, 0:96])\
                    .then_inc(*up(pe, ("mod", "turned", layer)))

        def ada_dve(dve):
            stage(dve, "ada")
            dve.wait_ge(*when(("dma", "ada_b")))
            for i in range(24):
                dve.wait_ge(*when(("ada", "full", i)))
                row = modrow[0:2, i // 12, 512 * (i % 12):512 * (i % 12) + 512]
                nc.vector.tensor_tensor(row, psum[0:2, i % 4, :], row, ALU.add)\
                    .then_inc(*up(dve, ("read", ("ada", i))))
            for layer in range(2):
                dve.wait_ge(*when(("mod", "turned", layer)))
                nc.vector.tensor_copy(modcol[:, layer, :], psum[:, layer, 0:96])\
                    .then_inc(*up(dve, ("read", ("mod", layer))))
                dve.wait_ge(*latest(dve))

        def ada_pool(pool):
            stage(pool, "ada")
            for layer in range(2):
                pool.wait_ge(*when(("read", ("ada", 12 * layer + 11))))
                nc.gpsimd.dma_start(scratch_mod[layer], modrow[0:2, layer, :])\
                    .then_inc(landing(f"mod {layer}"), 16)
                pool.wait_ge(*when(("dma", f"mod {layer}")))
                pool.wait_ge(*when(("read", ("vec", 1))))
                nc.gpsimd.dma_start(sc[0:96, layer, 0:P], scratch_mod[layer].rearrange("v (r p) -> (v r) p", p=P))\
                    .then_inc(landing(f"mod back {layer}"), 16)

        def mcol(layer, vec, kind):
            at = 48 * vec + 8 * kind
            return modcol[:, layer, at:at + 8]

        def gate_load(pool, tag, dst, layer, vec, kind):
            nc.gpsimd.dma_start(dst, scratch_mod[layer, vec, kind * D:(kind + 1) * D].partition_broadcast(P))\
                .then_inc(landing(tag), 16)

        qa = area(0, 4, 512)
        ka = area(2048, 4, 512)
        va = area(4096, 4, 512)
        qb = area(6144, 4, 512)
        kb = area(8192, 4, 512)
        vb = area(10240, 4, 4, 129)
        so = area(12304, 4, 512)
        qaT = area(14352, 4, 512)
        kaT = area(16400, 4, 512)
        gates_a = (area(10240, 1024), area(11264, 1024))
        AB = ("qa", "ka", "va", "qb", "kb", "vb", "so")

        def ab_in_pe(pe):
            for event in [("read", (k, b)) for k in ("L0a", "C0a") for b in range(4)]:
                pe.wait_ge(*when(event))
            rows_pe(pe, "ab_in", lambda k, t: hT[:, k, P * t:P * t + P], range(4), KT, 3584, [0, 1, 2, 3])
            stage(pe, "ab")
            s = slab(pe, ("ab_in", 7, 0))
            for g in range(4):
                pe.wait_ge(*bank(4 + g, ("gates", g)))
                for k in range(KT):
                    ins = nc.tensor.matmul(psum[0:4, 4 + g, :], s[:, k, 4 * g:4 * g + 4], hT[:, k, :],
                                           start=(k == 0), stop=(k == 7))
                ins.then_inc(*up(pe, ("gates", "full", g)))
            also(("used", slab_at[("ab_in", 7, 0)]), ("gates", "full", 3))

        def ab_in_act(act):
            stage(act, "ab_in")
            act.wait_ge(*when(("dma", "mod 1")))
            for n, name in enumerate(AB):
                for t in range(4):
                    act.wait_ge(*when(("ab_in", "full", n, t)))
                    src = psum[:, t, :]
                    event = ("read", ("ab_in", n, t))
                    if name == "so":
                        ins = nc.scalar.activation(so[:, t, :], src, ACT.Sigmoid)
                    elif name == "kb":
                        ins = nc.scalar.activation(kb[:, t, :], src, ACT.Copy, scale=128 ** -0.5)
                    elif name == "vb":
                        ins = nc.scalar.copy(vb[:, t, :, 0:128], src.rearrange("p (h d) -> p h d", h=4))
                    else:
                        ins = nc.scalar.copy({"qa": qa, "ka": ka, "va": va, "qb": qb}[name][:, t, :], src)
                    ins.then_inc(*up(act, event))

        def qk_norm_dve(dve):
            stage(dve, "qk")
            for i in range(8):
                y = (qa, ka)[i % 2][:, i // 2, :].rearrange("p (h d) -> p h d", h=8)
                sq = sc[:, i % 2, :].rearrange("p (h d) -> p h d", h=8)
                dve.wait_ge(*when(("read", ("ab_in", i % 2, i // 2))))
                if i < 2:
                    dve.wait_ge(*when(("C0a", "turned", 3)))
                nc.vector.tensor_tensor(sq, y, y, ALU.mult).then_inc(*up(dve))
                dve.wait_ge(*latest(dve))
                nc.vector.tensor_reduce(stat[:, 16 + 8 * i:24 + 8 * i], sq, AX.X, ALU.add)\
                    .then_inc(*up(dve, ("qk", "squares", i)))
                dve.wait_ge(*latest(dve))
            for i in range(8):
                y = (qa, ka)[i % 2][:, i // 2, :].rearrange("p (h d) -> p h d", h=8)
                dve.wait_ge(*when(("qk", "rstd", i)))
                nc.vector.tensor_tensor(y, y, stat[:, 16 + 8 * i:24 + 8 * i].unsqueeze(2).to_broadcast([P, 8, 64]),
                                               ALU.mult).then_inc(*up(dve, ("qk", "normed", i)))
                dve.wait_ge(*latest(dve))
                if i >= 2:
                    qk_turn_out(dve, i - 2)
            qk_turn_out(dve, 6)
            qk_turn_out(dve, 7)

        def qk_turn_out(dve, i):
            dve.wait_ge(*when(("qk", "turned", i)))
            at = ROWS_A["na_q"] + i % 2
            nc.vector.tensor_scalar((qaT, kaT)[i % 2][:, :, P * (i // 2):P * (i // 2) + P],
                                           psum[:, 4 + i % 4, :].rearrange("p (f t) -> p f t", f=4),
                                           colA[:, at:at + 1], None, ALU.mult)\
                .then_inc(*up(dve, ("read", ("qkT", i))))
            dve.wait_ge(*latest(dve))

        def qk_norm_pool(pool):
            stage(pool, "qk")
            for i in range(8):
                pool.wait_ge(*when(("qk", "squares", i)))
                r = stat[:, 16 + 8 * i:24 + 8 * i]
                nc.gpsimd.tensor_scalar(r, r, 1.0 / 64, EPS, ALU.mult, ALU.add).then_inc(*up(pool))
                pool.wait_ge(*latest(pool))
                nc.gpsimd.tensor_tensor(r, r, half[:, 0:8], ALU.pow).then_inc(*up(pool, ("qk", "rstd", i)))
                pool.wait_ge(*latest(pool))

        def qk_norm_pe(pe):
            stage(pe, "qk")
            for i in range(8):
                pe.wait_ge(*when(("qk", "normed", i)))
                pe.wait_ge(*bank(4 + i % 4, ("qkT", i)))
                for f in range(4):
                    ins = nc.tensor.transpose(psum[:, 4 + i % 4, P * f:P * f + P],
                                              (qa, ka)[i % 2][:, i // 2, P * f:P * f + P], ident)
                ins.then_inc(*up(pe, ("qk", "turned", i)))

        def unit_tick(n, *steps):
            for i in range(n + len(steps) - 1):
                for j, step in enumerate(steps):
                    if step is not None and 0 <= i - j < n:
                        yield step, i - j

        def att_pe(pe, key, units, needs=()):
            stage(pe, "att")
            for event in needs:
                pe.wait_ge(*when(event))

            def scores(i):
                u = units[i]
                pe.wait_ge(*bank(i % 2, (key, "s", i)))
                n = len(u["qk"])
                for j, (l, r) in enumerate(u["qk"]):
                    ins = nc.tensor.matmul(psum[:, i % 2, 0:u["keys"]], l, r, start=(j == 0), stop=(j == n - 1))
                ins.then_inc(*up(pe, (key, "scores", i)))

            def turn(i):
                u = units[i]
                pe.wait_ge(*when((key, "probs", i)))
                pe.wait_ge(*bank(2 + i % 2, (key, "t", i)))
                for k in range(u["keys"] // P):
                    ins = nc.tensor.transpose(psum[:, 2 + i % 2, P * k:P * k + P], sc2[:, i % 2, P * k:P * k + P], ident)
                ins.then_inc(*up(pe, (key, "turned", i)))

            def values(i):
                u = units[i]
                pe.wait_ge(*when((key, "probsT", i)))
                pe.wait_ge(*bank(4 + i % 2, (key, "o", i)))
                nk = u["keys"] // P
                for j, (vs, part) in enumerate(u["v"]):
                    for k in range(nk):
                        v = vs(k)
                        w = v.shape[-1]
                        ins = nc.tensor.matmul(psum[part:part + w, 4 + i % 2, P * j:P * j + P], v,
                                               sc[:, 4 + i % 2, P * k:P * k + P], start=(k == 0), stop=(k == nk - 1))
                ins.then_inc(*up(pe, (key, "out", i)))

            for step, i in unit_tick(len(units), scores, None, turn, values):
                step(i)

        def att_dve(dve, key, units, scale, probs=True, after_first=()):
            stage(dve, "att")

            def maximum(i):
                u = units[i]
                n, s, b = u["keys"], sc[:, i % 2, :], psum[:, i % 2, :]
                dve.wait_ge(*when((key, "scores", i)))
                if i == 0:
                    for event in after_first:
                        dve.wait_ge(*when(event))
                m = stat[:, 96 + 2 * (i % 4):97 + 2 * (i % 4)]
                nm = stat[:, 97 + 2 * (i % 4):98 + 2 * (i % 4)]
                if u["bias"] is None:
                    nc.vector.tensor_reduce(m, b[:, 0:n], AX.X, ALU.max, negate=True).then_inc(*up(dve))
                    dve.wait_ge(*latest(dve))
                    nc.vector.tensor_scalar(nm, m, scale, None, ALU.mult).then_inc(*up(dve, (key, "max", i)))
                    dve.wait_ge(*latest(dve))
                else:
                    at = 0
                    if i >= 2:
                        dve.wait_ge(*when((key, "exp", i - 2)))
                    for w, bias in u["bias"]:
                        if bias is None:
                            ins = nc.vector.tensor_scalar(s[:, at:at + w], b[:, at:at + w], scale, None, ALU.mult)
                        else:
                            o, y = s[:, at:at + w], b[:, at:at + w]
                            if len(bias.shape) == 3:
                                o, y = (v.rearrange("p (a b) -> p a b", b=bias.shape[2]) for v in (o, y))
                            ins = nc.vector.scalar_tensor_tensor(o, y, scale, bias, ALU.mult, ALU.add)
                        at += w
                        ins.then_inc(*up(dve, ("read", (key, "s", i)) if at == n else None))
                        dve.wait_ge(*latest(dve))
                    nc.vector.tensor_reduce(nm, s[:, 0:n], AX.X, ALU.max, negate=True)\
                        .then_inc(*up(dve, (key, "max", i)))
                    dve.wait_ge(*latest(dve))

            def normalise(i):
                u = units[i]
                n = u["keys"]
                dve.wait_ge(*when((key, "exp", i)))
                rs, ri = stat[:, 104 + i % 4:105 + i % 4], stat[:, 108 + i % 4:109 + i % 4]
                nc.vector.reciprocal(ri, rs).then_inc(*up(dve))
                dve.wait_ge(*latest(dve))
                if i >= 2:
                    dve.wait_ge(*when((key, "turned", i - 2)))
                nc.vector.tensor_scalar(sc2[:, i % 2, 0:n], sc[:, 2 + i % 2, 0:n], ri, None, ALU.mult)\
                    .then_inc(*up(dve, (key, "probs", i)))
                dve.wait_ge(*latest(dve))

            for step, i in unit_tick(len(units), maximum, normalise):
                step(i)

        def att_act(act, key, units, scale, needs=()):
            stage(act, "att")
            for event in needs:
                act.wait_ge(*when(event))

            def exponent(i):
                u = units[i]
                n = u["keys"]
                act.wait_ge(*when((key, "max", i)))
                nm = stat[:, 97 + 2 * (i % 4):98 + 2 * (i % 4)]
                if i >= 2:
                    act.wait_ge(*when((key, "probs", i - 2)))
                src = psum[:, i % 2, 0:n] if u["bias"] is None else sc[:, i % 2, 0:n]
                nc.scalar.activation(sc[:, 2 + i % 2, 0:n], src, ACT.Exp, bias=nm,
                                            scale=scale if u["bias"] is None else 1.0,
                                            accum_out=stat[:, 104 + i % 4:105 + i % 4])\
                    .then_inc(*up(act, (key, "exp", i)))
                if u["bias"] is None:
                    also(("read", (key, "s", i)), (key, "exp", i))

            for step, i in unit_tick(len(units), exponent, None, lambda i: att_probsT(act, key, units, i),
                                     lambda i: att_out(act, key, units, i)):
                step(i)

        def att_probsT(act, key, units, i):
            n = units[i]["keys"]
            act.wait_ge(*when((key, "turned", i)))
            if i >= 2:
                act.wait_ge(*when((key, "out", i - 2)))
            nc.scalar.copy(sc[:, 4 + i % 2, 0:n], psum[:, 2 + i % 2, 0:n])\
                .then_inc(*up(act, (key, "probsT", i)))
            also(("read", (key, "t", i)), (key, "probsT", i))

        def att_out(act, key, units, i):
            u = units[i]
            act.wait_ge(*when((key, "out", i)))
            for j, ((vs, part), dst) in enumerate(zip(u["v"], u["dst"])):
                w = dst.shape[0]
                nc.scalar.copy(dst, psum[part:part + w, 4 + i % 2, P * j:P * j + P])\
                    .then_inc(*up(act, ("read", (key, "o", i)) if j == len(u["v"]) - 1 else None))

        def head_rows(h):
            return slice(64 * (h % 2), 64 * (h % 2) + 64)

        def na_units():
            us = []
            for h in range(8):
                for qt in range(2):
                    r, f = head_rows(h), h // 2
                    us.append(dict(keys=512, qk=[(qaT[r, f, P * qt:P * qt + P], kaT[r, f, :])],
                                   bias=[(256, nab[:, qt, :, h, :]), (256, None)],
                                   v=[(lambda k, h=h: va[:, k, 64 * h:64 * h + 64], r.start)],
                                   dst=[hT[r, f, P * qt:P * qt + P]]))
            return us

        def ctx_units():
            us = []
            for h in range(8):
                for qt in range(2):
                    r, f = head_rows(h), h // 2
                    us.append(dict(keys=256, qk=[(qaT[r, f, 256 + P * qt:256 + P * qt + P], kaT[r, f, 256:512])],
                                   bias=None, v=[(lambda k, h=h: va[:, 2 + k, 64 * h:64 * h + 64], r.start)],
                                   dst=[hT[r, f, 256 + P * qt:256 + P * qt + P]]))
            return us

        na, cxa = na_units(), ctx_units()

        R0 = 14352
        gi = area(R0, 2, 512)
        gl = area(R0 + 1024, 2, 512)
        gb = area(R0 + 2048, 2, 512)
        gm = area(R0 + 3072, 2, 512)
        gw = area(R0 + 4096, 2, 512)
        gv = area(R0 + 5120, 2, 512)
        ge = area(R0 + 6144, 2, 512)
        mlD = area(R0 + 7168, 2, 512)
        capped = [v[p:p + 4] for v in (area(22544, 512), sc2[:, 2, :]) for p in (0, 32)]
        mst = stat[:, 112:128].rearrange("p (z s) -> p z s", z=2)
        qbT = area(0, 4, 512)
        kbT = area(2048, 4, 512)
        mlc = sc2[:, 2, 0:128].rearrange("p (q z t h) -> p q z t h", q=4, z=2, t=4)
        dec = sc2[:, 2, 128:160].rearrange("p (h z t) -> p h z t", h=4, z=2)
        hs = area(4096, 4, 4, 128)
        mlW = sc[:, 0:2, :]
        mlK = sc[:, 2:4, :]
        mlC = sc2[:, 0:2, 0:129]
        mlY = sc2[:, 0:2, 256:385]
        ORDER = ((2, 3, 0, 1), (3, 2, 1, 0))

        def gates_act(act):
            stage(act, "gates")
            act.wait_ge(*when("gatecol"))
            act.wait_ge(*when(("dma", "rpb rows")))
            for g in range(4):
                act.wait_ge(*when(("gates", "full", g)))
                nc.scalar.activation(capped[g], psum[0:4, 4 + g, :], ACT.Tanh, bias=stat[0:4, 204 + g:205 + g],
                                            scale=1 / 15.0).then_inc(*up(act, ("read", ("gates", g))))
                act.wait_ge(*latest(act))

        def softplus_act(act):
            stage(act, "softplus")
            act.wait_ge(*when(("na", "probs", 15)))
            act.wait_ge(*when(("cx", "probs", 15)))
            act.wait_ge(*when(("cx", "out", 15)))
            for z in range(2):
                nc.scalar.activation(gl[0:4, z, :], capped[2 * z + 1], ACT.Exp, scale=-15.0).then_inc(*up(act))
                act.wait_ge(*latest(act))
            nc.scalar.activation(gl[0:4], gl[0:4], ACT.Ln, bias=1.0).then_inc(*up(act, "softplus f"))
            act.wait_ge(*latest(act))

        def gates_dve(dve):
            stage(dve, "gates")
            dve.wait_ge(*when(("dma", "gate_b")))
            nc.vector.tensor_scalar(stat[0:4, 204:208], stat[0:4, 200:204], 1 / 15.0, None, ALU.mult)\
                .then_inc(*up(dve, "gatecol"))
            dve.wait_ge(*latest(dve))

        def scan_view(a_, z):
            return a_ if z == 0 else a_[:, ::-1]

        def decay_dve(dve):
            stage(dve, "decay")
            dve.wait_ge(*when("softplus f"))
            nc.vector.memset(mlD[0:4, 0, 0:128], 0.0).then_inc(*up(dve))
            dve.wait_ge(*latest(dve))
            nc.vector.memset(mst[0:4, :, 0:1], 0.0).then_inc(*up(dve))
            dve.wait_ge(*latest(dve))
            for z in range(2):
                for t in range(4):
                    s = slice(P * t, P * t + P)
                    nc.vector.tensor_tensor_scan(scan_view(gb[0:4, z, s], z), mlD[0:4, 0, 0:128],
                                                        scan_view(gl[0:4, z, s], z), 0.0, ALU.add, ALU.subtract)\
                        .then_inc(*up(dve))
                    dve.wait_ge(*latest(dve))
            for z in range(2):
                nc.vector.scalar_tensor_tensor(gi[0:4, z, :], capped[2 * z], 15.0, gb[0:4, z, :],
                                                      ALU.mult, ALU.subtract).then_inc(*up(dve))
                dve.wait_ge(*latest(dve))
            for j in range(4):
                for z in range(2):
                    t = ORDER[z][j]
                    s = slice(P * t, P * t + P)
                    last = P * t + (127 if z == 0 else 0)
                    g = scan_view(gi[0:4, z, s], z)
                    m0 = mst[0:4, z, j:j + 1]
                    nc.vector.tensor_tensor_scan(scan_view(gm[0:4, z, s], z), g, g, m0, ALU.max, ALU.max)\
                        .then_inc(*up(dve))
                    dve.wait_ge(*latest(dve))
                    nc.vector.tensor_tensor(mst[0:4, z, j + 1:j + 2], gb[0:4, z, last:last + 1],
                                                   gm[0:4, z, last:last + 1], ALU.add).then_inc(*up(dve))
                    dve.wait_ge(*latest(dve))
                    nc.vector.tensor_scalar(gw[0:4, z, s], gi[0:4, z, s], gm[0:4, z, last:last + 1], None,
                                                   ALU.subtract).then_inc(*up(dve))
                    dve.wait_ge(*latest(dve))
                    nc.vector.tensor_scalar(gv[0:4, z, s], gm[0:4, z, s], m0, None, ALU.subtract)\
                        .then_inc(*up(dve))
                    dve.wait_ge(*latest(dve))
            nc.vector.tensor_tensor(ge[0:4], gb[0:4], gm[0:4], ALU.add).then_inc(*up(dve, "exponents"))
            dve.wait_ge(*latest(dve))

        def decay_act(act):
            stage(act, "decay")
            act.wait_ge(*when("exponents"))
            nc.scalar.activation(gw[0:4], gw[0:4], ACT.Exp).then_inc(*up(act))
            act.wait_ge(*latest(act))
            nc.scalar.activation(gv[0:4], gv[0:4], ACT.Exp, scale=-1.0).then_inc(*up(act))
            act.wait_ge(*latest(act))
            nc.scalar.activation(ge[0:4], ge[0:4], ACT.Exp, scale=-1.0).then_inc(*up(act, "gate rows"))
            act.wait_ge(*latest(act))

        def decay_pe(pe):
            stage(pe, "decay")
            pe.wait_ge(*when("gate rows"))
            pe.wait_ge(*bank(0, "gate columns"))
            for q, src in enumerate((gi, gw, gv, ge)):
                for z in range(2):
                    for t in range(4):
                        at = 32 * q + 16 * z + 4 * t
                        nc.tensor.transpose(psum[:, 0, at:at + 4], src[0:4, z, P * t:P * t + P], ident[0:4, 0:4])
            sel = cst("select4").rearrange("p (h m) -> p h m", h=4)
            for h in range(4):
                for z in range(2):
                    rows = gv[0:4, z, :].rearrange("p (t s) -> p t s", s=P)[:, :, (127 if z == 0 else 0)]
                    at = 128 + 8 * h + 4 * z
                    ins = nc.tensor.matmul(psum[:, 0, at:at + 4], sel[0:4, h, :], rows, start=True, stop=True)
            ins.then_inc(*up(pe, "gate columns full"))

        def decay_out_dve(dve):
            dve.wait_ge(*when("gate columns full"))
            nc.vector.tensor_copy(sc2[:, 2, 0:160], psum[:, 0, 0:160])\
                .then_inc(*up(dve, ("read", "gate columns")))
            dve.wait_ge(*latest(dve))

        def rope_pool(pool):
            stage(pool, "rope")
            for event in [("read", ("ab_in", n, t)) for n in (3, 4) for t in range(2)]:
                pool.wait_ge(*when(event))
            for t in range(4):
                pool.wait_ge(*when(("ab_in", "full", 6, t)))
            pool.wait_ge(*when(("gates", "full", 3)))
            for y in (qb, kb):
                for t in range(2):
                    v = y[:, t, :].rearrange("p (h c u f) -> p h c u f", h=4, c=2, u=2)
                    c = cst("cos2d")[:, 64 * t:64 * t + 64].rearrange("p (c f) -> p c f", c=2)
                    s = cst("sin2d")[:, 64 * t:64 * t + 64].rearrange("p (c f) -> p c f", c=2)
                    tmp = [hT[:, 4 + j, 0:256].rearrange("p (h c f) -> p h c f", h=4, c=2) for j in range(4)]
                    for c_ in range(2):
                        for j, (half_, w) in enumerate(((0, c), (1, s), (0, s), (1, c))):
                            nc.gpsimd.tensor_tensor(tmp[j][:, :, c_, :], v[:, :, c_, half_, :],
                                                           w[:, c_, :].unsqueeze(1).to_broadcast([P, 4, 32]), ALU.mult)\
                                .then_inc(*up(pool))
                            pool.wait_ge(*latest(pool))
                        nc.gpsimd.tensor_tensor(v[:, :, c_, 0, :], tmp[0][:, :, c_, :], tmp[1][:, :, c_, :],
                                                       ALU.subtract).then_inc(*up(pool))
                        pool.wait_ge(*latest(pool))
                        nc.gpsimd.tensor_tensor(v[:, :, c_, 1, :], tmp[2][:, :, c_, :], tmp[3][:, :, c_, :],
                                                       ALU.add).then_inc(*up(pool, ("roped", t)))
                        pool.wait_ge(*latest(pool))
            nc.gpsimd.memset(vb[:, :, :, 128:129], 1.0).then_inc(*up(pool, "v ones"))
            pool.wait_ge(*latest(pool))

        def mlT_pe(pe):
            stage(pe, "mlT")
            pe.wait_ge(*when(("roped", 1)))
            for event in [("read", ("ab_in", n, t)) for n in (3, 4) for t in range(4)]:
                pe.wait_ge(*when(event))
            for i in range(8):
                pe.wait_ge(*bank(4 + i % 4, ("mlT", i)))
                for h in range(4):
                    ins = nc.tensor.transpose(psum[:, 4 + i % 4, P * h:P * h + P],
                                              (qb, kb)[i % 2][:, i // 2, P * h:P * h + P], ident)
                ins.then_inc(*up(pe, ("mlT", "full", i)))

        def mlT_act(act):
            stage(act, "mlT")
            act.wait_ge(*when(("qk", "turned", 7)))
            for i in range(8):
                act.wait_ge(*when(("mlT", "full", i)))
                nc.scalar.copy((qbT, kbT)[i % 2][:, :, P * (i // 2):P * (i // 2) + P],
                                      psum[:, 4 + i % 4, :].rearrange("p (f t) -> p f t", f=4))\
                    .then_inc(*up(act, ("read", ("mlT", i))))

        def ml_pe(pe):
            stage(pe, "ml")
            pe.wait_ge(*when(("read", ("mlT", 7))))
            pe.wait_ge(*when("v ones"))
            sel = cst("select4").rearrange("p (h m) -> p h m", h=4)
            for h in range(4):
                pe.wait_ge(*bank(1, ("ml", "S", h)))
                for t in range(4):
                    ins = nc.tensor.matmul(psum[:, 1, P * t:P * t + P], kbT[:, h, P * t:P * t + P],
                                           qbT[:, h, P * t:P * t + P], start=True, stop=True)
                ins.then_inc(*up(pe, ("ml", "S full", h)))
                for z in range(2):
                    pe.wait_ge(*bank(2 + z, ("ml", "M", h, z)))
                    nc.tensor.matmul(psum[:, 2 + z, :], sel[0:4, h, :], gm[0:4, z, :], start=True, stop=True)\
                        .then_inc(*up(pe, ("ml", "M full", h, z)))
                for j in range(4):
                    for z in range(2):
                        t = ORDER[z][j]
                        i = 4 * h + j
                        b = 4 + z + 2 * (j % 2)
                        s = slice(P * t, P * t + P)
                        pe.wait_ge(*bank(b, ("ml", "P", i, z)))
                        if j == 0:
                            pe.wait_ge(*when(("ml", "W", h, z)))
                            pe.wait_ge(*when(("ml", "K", h, z)))
                        nc.tensor.matmul(psum[:, b, 0:129], mlW[:, z, s], vb[:, t, h, :], start=True, stop=True)
                        nc.tensor.matmul(psum[:, b, 258:387], mlK[:, z, s], vb[:, t, h, :], start=True, stop=True)
                        pe.wait_ge(*when(("ml", "state", i, z)))
                        nc.tensor.matmul(psum[:, b, 129:258], qbT[:, h, s], mlC[:, z, :], start=True, stop=True)\
                            .then_inc(*up(pe, ("ml", "P full", i, z)))

        def ml_act(act):
            stage(act, "ml")
            for h in range(4):
                for z in range(2):
                    act.wait_ge(*when(("ml", "D", h, z)))
                    nc.scalar.activation(mlD[:, z, :], mlD[:, z, :], ACT.Exp, scale=-1.0)\
                        .then_inc(*up(act, ("ml", "E", h, z)))
                    act.wait_ge(*latest(act))

        def ml_pool(pool):
            stage(pool, "ml")
            pool.wait_ge(*when("v ones"))
            pool.wait_ge(*when(("read", "gate columns")))
            pool.wait_ge(*when(("roped", 1)))
            for h in range(4):
                for z in range(2):
                    if h:
                        pool.wait_ge(*when(("ml", "P full", 4 * h - 1, z)))
                    for t in range(4):
                        nc.gpsimd.tensor_scalar(mlK[:, z, P * t:P * t + P], kb[:, t, P * h:P * h + P],
                                                        mlc[:, 1, z, t, h:h + 1], None, ALU.mult)\
                            .then_inc(*up(pool, ("ml", "K", h, z)))
                        pool.wait_ge(*latest(pool))

        def ml_dve(dve):
            stage(dve, "ml")
            mask = (cst("st_fwd"), cst("st_bwd"))
            for h in range(4):
                for z in range(2):
                    dve.wait_ge(*when(("ml", "M full", h, z)))
                    for t in range(4):
                        nc.vector.tensor_scalar(mlD[:, z, P * t:P * t + P], psum[:, 2 + z, P * t:P * t + P],
                                                       mlc[:, 0, z, t, h:h + 1], 0.0, ALU.subtract, ALU.max)\
                            .then_inc(*up(dve, ("ml", "D", h, z)))
                    also(("read", ("ml", "M", h, z)), ("ml", "D", h, z))
                for z in range(2):
                    dve.wait_ge(*when(("ml", "E", h, z)))
                    dve.wait_ge(*when(("ml", "S full", h)))
                    if h:
                        dve.wait_ge(*when(("ml", "P full", 4 * h - 1, z)))
                    nc.vector.tensor_tensor(mlD[:, z, :].rearrange("p (t s) -> p t s", t=4),
                                                   mlD[:, z, :].rearrange("p (t s) -> p t s", t=4),
                                                   mask[z].unsqueeze(1).to_broadcast([P, 4, P]), ALU.mult)\
                        .then_inc(*up(dve))
                    dve.wait_ge(*latest(dve))
                    nc.vector.tensor_tensor(mlW[:, z, :], psum[:, 1, :], mlD[:, z, :], ALU.mult)\
                        .then_inc(*up(dve, ("ml", "W", h, z)))
                    dve.wait_ge(*latest(dve))
                    nc.vector.memset(mlC[:, z, :], 0.0).then_inc(*up(dve, ("ml", "state", 4 * h, z)))
                    dve.wait_ge(*latest(dve))
                also(("read", ("ml", "S", h)), ("ml", "W", h, 1))
                for j in range(4):
                    for z in range(2):
                        t = ORDER[z][j]
                        i = 4 * h + j
                        b = 4 + z + 2 * (j % 2)
                        y, den = mlY[:, z, :], stat[:, 128 + z:129 + z]
                        dve.wait_ge(*when(("ml", "P full", i, z)))
                        if j < 3:
                            nc.vector.scalar_tensor_tensor(mlC[:, z, :], mlC[:, z, :], dec[:, h, z, t:t + 1],
                                                                  psum[:, b, 258:387], ALU.mult, ALU.add)\
                                .then_inc(*up(dve, ("ml", "state", i + 1, z)))
                            dve.wait_ge(*latest(dve))
                        nc.vector.tensor_scalar(y, psum[:, b, 129:258], mlc[:, 2, z, t, h:h + 1], None, ALU.mult)\
                            .then_inc(*up(dve))
                        dve.wait_ge(*latest(dve))
                        nc.vector.tensor_tensor(y, psum[:, b, 0:129], y, ALU.add)\
                            .then_inc(*up(dve, ("read", ("ml", "P", i, z))))
                        dve.wait_ge(*latest(dve))
                        nc.vector.tensor_scalar(den, y[:, 128:129], -1.0, mlc[:, 3, z, t, h:h + 1],
                                                       ALU.mult, ALU.max).then_inc(*up(dve))
                        dve.wait_ge(*latest(dve))
                        nc.vector.tensor_tensor(den, den, y[:, 128:129], ALU.max).then_inc(*up(dve))
                        dve.wait_ge(*latest(dve))
                        nc.vector.reciprocal(den, den).then_inc(*up(dve))
                        dve.wait_ge(*latest(dve))
                        seen_first = ORDER[0].index(t) < ORDER[1].index(t) or (ORDER[0].index(t) == ORDER[1].index(t))
                        first = (z == 0) if seen_first else (z == 1)
                        if first:
                            nc.vector.tensor_scalar(hs[:, t, h, :], y[:, 0:128], den, None, ALU.mult)\
                                .then_inc(*up(dve))
                            dve.wait_ge(*latest(dve))
                        else:
                            nc.vector.scalar_tensor_tensor(hs[:, t, h, :], y[:, 0:128], den, hs[:, t, h, :],
                                                                  ALU.mult, ALU.add)\
                                .then_inc(*up(dve, ("ml", "h", i, z)))
                            dve.wait_ge(*latest(dve))

        def merge_dve(dve):
            stage(dve, "merge")
            for t in range(4):
                nc.vector.tensor_tensor(sc[:, t % 2, :].rearrange("p (h d) -> p h d", h=4), hs[:, t], hs[:, t],
                                               ALU.mult).then_inc(*up(dve))
                dve.wait_ge(*latest(dve))
                nc.vector.tensor_reduce(stat[:, 16 + 4 * t:20 + 4 * t],
                                               sc[:, t % 2, :].rearrange("p (h d) -> p h d", h=4), AX.X, ALU.add)\
                    .then_inc(*up(dve, ("merge", "squares")))
                dve.wait_ge(*latest(dve))
            dve.wait_ge(*when(("merge", "rstd")))
            for t in range(4):
                nc.vector.tensor_tensor(hs[:, t], hs[:, t],
                                               stat[:, 16 + 4 * t:20 + 4 * t].unsqueeze(2).to_broadcast([P, 4, P]), ALU.mult)\
                    .then_inc(*up(dve))
                dve.wait_ge(*latest(dve))
                nc.vector.tensor_tensor(hs[:, t], hs[:, t], so[:, t, :].rearrange("p (h d) -> p h d", h=4),
                                               ALU.mult).then_inc(*up(dve, ("merge", "gated", t)))
                dve.wait_ge(*latest(dve))
            for t in range(4):
                dve.wait_ge(*when(("merge", "turned", t)))
                for h in range(4):
                    at = ROWS_A["head_norm"] + h
                    nc.vector.tensor_scalar(hT[:, 4 + h, P * t:P * t + P], psum[:, 4 + t, P * h:P * h + P],
                                                   colA[:, at:at + 1], None, ALU.mult)\
                        .then_inc(*up(dve, ("read", ("merge", t))))

        def merge_pool(pool):
            stage(pool, "merge")
            pool.wait_ge(*when(("merge", "squares")))
            nc.gpsimd.tensor_scalar(stat[:, 16:32], stat[:, 16:32], 1.0 / 128, EPS, ALU.mult, ALU.add)\
                .then_inc(*up(pool))
            pool.wait_ge(*latest(pool))
            nc.gpsimd.tensor_tensor(stat[:, 16:32], stat[:, 16:32], half[:, 0:16], ALU.pow)\
                .then_inc(*up(pool, ("merge", "rstd")))
            pool.wait_ge(*latest(pool))

        def merge_pe(pe):
            stage(pe, "merge")
            for t in range(4):
                pe.wait_ge(*when(("merge", "gated", t)))
                pe.wait_ge(*bank(4 + t, ("merge", t)))
                for h in range(4):
                    ins = nc.tensor.transpose(psum[:, 4 + t, P * h:P * h + P], hs[:, t, h, :], ident)
                ins.then_inc(*up(pe, ("merge", "turned", t)))

        def gated_rows_dve(dve, name, tiles, banks, gates, tags):
            stage(dve, "gated")
            for event in [("dma", tag) for tag in tags]:
                dve.wait_ge(*when(event))
            for n in range(2):
                for i, t in enumerate(tiles):
                    dve.wait_ge(*when((name, "full", n, t)))
                    b = rows_bank(name, n, i, tiles, banks)
                    dst = (x if t < 2 else cx)[:, t % 2, 512 * n:512 * n + 512]
                    tmp = sc2[:, 0, :]
                    nc.vector.tensor_tensor(tmp, psum[:, b, :], gates[t // 2][:, 512 * n:512 * n + 512], ALU.mult)\
                        .then_inc(*up(dve, ("read", (name, n, t))))
                    dve.wait_ge(*latest(dve))
                    nc.vector.tensor_tensor(dst, dst, tmp, ALU.add).then_inc(*up(dve, (name, "added", n, t)))
                    dve.wait_ge(*latest(dve))

        hid_groups = [[area(4096 * g + 2048 * q, 8, 256, rounded=True) for q in range(2)] for g in range(2)]
        gates_m = (area(8192, 1024), area(9216, 1024))
        c_parts = [hT_parts[:, :, 256 * q:256 * q + 256] for q in range(2)]

        def mlp_pe(pe, name, src, tiles, key):
            stage(pe, "mlp")
            for kind, n, g in MLP_ORDER:
                w = (f"{name}_{kind}", n, g)
                if kind == "up":
                    for unit in (2 * n, 2 * n + 1):
                        b = unit % 4
                        pe.wait_ge(*bank(b, (name, unit)))
                        for j in range(2):
                            at = 256 * (unit % 2) + P * j
                            for k in range(KT):
                                pe.wait_ge(*when(("read", (key, k // 2))))
                                if k % 4 == 0:
                                    pe.wait_ge(*when(("low", w, k // 4)))
                                for i, (s, q) in enumerate(parts(w)):
                                    ins = nc.tensor.matmul(psum[:, b, 256 * j:256 * j + 256], s[:, k, at:at + P],
                                                           src[q][:, k, :], start=(k == 0 and i == 0),
                                                           stop=(k == 7 and i == 2))
                        ins.then_inc(*up(pe, (name, "full", unit)))
                    also(("used", slab_at[w]), (name, "full", 2 * n + 1))
                else:
                    pe.wait_ge(*when((name, "hidden", 4 * g + 3)))
                    for t in range(2):
                        b = 4 + 2 * n + t
                        if g == 0:
                            pe.wait_ge(*bank(b, (name + "_down", n, tiles[t])))
                        for k in range(8):
                            if k % 4 == 0:
                                pe.wait_ge(*when(("low", w, k // 4)))
                            for i, (s, q) in enumerate(parts(w)):
                                ins = nc.tensor.matmul(psum[:, b, :], hid_groups[g % 2][q][:, k, P * t:P * t + P],
                                                       s[:, k, :], start=(g == 0 and k == 0 and i == 0),
                                                       stop=(g == 3 and k == 7 and i == 2))
                        if g == 3 and t == 0:
                            ins.then_inc(*up(pe, (name + "_down", "full", n, tiles[0])))
                    if g == 3:
                        ins.then_inc(*up(pe, (name + "_down", "full", n, tiles[1])))
                        also(("used", slab_at[w]), (name + "_down", "full", n, tiles[1]))
                    else:
                        ins.then_inc(*up(pe, ("used", slab_at[w])))

        def mlp_act(act, name):
            names = mlp_slabs(name)
            for slab_name in names[len(AHEAD[name]):2]:
                high_act(act, slab_name)
            for m, (kind, n, g) in enumerate(MLP_ORDER):
                if kind == "up":
                    stage(act, "mlp")
                    for unit in (2 * n, 2 * n + 1):
                        act.wait_ge(*when((name, "full", unit)))
                        if unit >= 2:
                            act.wait_ge(*when((name, "hidden", unit - 2)))
                        nc.scalar.activation(sc[:, unit % 2, :], psum[:, unit % 4, :], ACT.Relu)\
                            .then_inc(*up(act, (name, "relu", unit)))
                if m + 2 < len(names):
                    high_act(act, names[m + 2])

        def mlp_dve(dve, name, following=()):
            names = mlp_slabs(name)
            low_slabs(dve, names[len(AHEAD[name]):2])
            for m, (kind, n, g) in enumerate(MLP_ORDER):
                if kind == "up":
                    stage(dve, "mlp")
                    for unit in (2 * n, 2 * n + 1):
                        g_, at = unit // 4, 2 * (unit % 4)
                        t = sc[:, unit % 2, :]
                        high, low = [v[:, at:at + 2, :].rearrange("p a b -> p (a b)") for v in hid_groups[g_ % 2]]
                        dve.wait_ge(*when((name, "relu", unit)))
                        nc.vector.scalar_tensor_tensor(t, psum[:, unit % 4, :], 0.0, t, ALU.max, ALU.mult)\
                            .then_inc(*up(dve, ("read", (name, unit))))
                        dve.wait_ge(*latest(dve))
                        if g_ >= 2:
                            dve.wait_ge(*when(("used", slab_at[(name + "_down", 1, g_ - 2)])))
                        nc.vector.tensor_copy(high, t).then_inc(*up(dve))
                        dve.wait_ge(*latest(dve))
                        nc.vector.tensor_tensor(low, t, high.bitcast(F32), ALU.subtract)\
                            .then_inc(*up(dve, (name, "hidden", unit)))
                if m + 2 < len(names):
                    for h in range(2):
                        low_dve(dve, names[m + 2], h)
            low_slabs(dve, following)

        KAPPA = float(np.exp(-0.5))
        LNS = 65536.0
        shifted = area(0, 16, 256)
        mixed = (area(4096, 8, 512), area(14336, 8, 512))
        v_rows = area(0, 4, 1024)
        rT = area(8192, 8, 256)
        kT = area(10240, 8, 512)
        VS = area(14336, 8, 8, 64)
        gT = area(18432, 8, 256)
        g2_sb = area(20480, 2, 1024)
        Y = area(20480, 4, 8, 64)
        w2_sb = area(22528, 1024)
        cxf = cx[:, :, :].rearrange("p a b -> p (a b)")
        a2_sb, t_w, t_a = cxf[:, 0:1024], cxf[:, 1024:1536], cxf[:, 1536:2048]
        hTf = hT[:, :, :].rearrange("p a b -> p (a b)")
        scf = sc[:, :, :].rearrange("p a b -> p (a b)")
        sc2f = sc2[:, :, :].rearrange("p a b -> p (a b)")

        def chunks(v):
            return v.rearrange("p (c t) -> p c t", c=8)

        ringf = ring[:, :, :].rearrange("p a b -> p (a b)")
        small = sc2f[:, 1024:1536]
        SETS = ((ringf[:, 0:7168], ringf[:, 7168:10240], ringf[:, 10240:11264], ringf[:, 11264:12288]),
                (area(0, 7168), hTf[:, 0:3072], hTf[:, 3072:4096], area(7168, 1024)))
        G, ARI, Bh, Kh, INV, PC, tmp_ = [], [], [], [], [], [], []
        for e, (g_, ari_, bk0, bk1) in enumerate(SETS):
            G.append([g_[:, 3584 * z:3584 * z + 3584].rearrange("p (c n) -> p c n", c=8) for z in range(2)])
            tmp_.append([[g_[:, 3584 * z + 512 * j:3584 * z + 512 * j + 512] for j in range(7)] for z in range(2)])
            ARI.append([ari_[:, 1536 * z:1536 * z + 1536].rearrange("p (c n) -> p c n", c=8) for z in range(2)])
            Bh.append([b_[:, 0:512] for b_ in (bk0, bk1)])
            Kh.append([b_[:, 512:1024] for b_ in (bk0, bk1)])
            INV.append([[chunks(Bh[e][0]), chunks(Kh[e][0])] + [chunks(scf[:, 512 * j:512 * j + 512]) for j in range(4)],
                        [chunks(Bh[e][1]), chunks(Kh[e][1])] + [chunks(v) for v in (scf[:, 2048:2560], scf[:, 2560:3072],
                                                                                  sc2f[:, 0:512], sc2f[:, 512:1024])]])
            PC.append([stat[:, 120 + 16 * e:128 + 16 * e], stat[:, 128 + 16 * e:136 + 16 * e]])
        St = [[small[:, 128 * z + 64 * j:128 * z + 64 * j + 64] for j in range(2)] for z in range(2)]
        Wt = [small[:, 256 + 64 * z:320 + 64 * z] for z in range(2)]
        Ut = [small[:, 384 + 64 * z:448 + 64 * z] for z in range(2)]
        coef = stat[:, 16:48].rearrange("p (c f) -> p c f", c=4)
        one_ka = stat[:, 48:56]
        neg0 = stat[:, 56:88]
        WALK = ((4, 5, 6, 7, 0, 1, 2, 3), (7, 6, 5, 4, 3, 2, 1, 0))
        MIXES = ("w", "a", "g", "r", "k", "v")
        MU = dict(r=0, w=1, k=2, v=3, a=4, g=5)
        HH = (slice(0, 64), slice(64, 128))

        def colr(name, i):
            at = ROWS_A[name] + i
            return colA[:, at:at + 1]

        def mix_width(m):
            return 256 if m in "rg" else 512

        def rw_pool(pool):
            stage(pool, "rw")
            pool.wait_ge(*when(("mlp0c_down", "added", 1, 3)))
            nc.gpsimd.dma_start(w2_sb, a["rw_w2"][0].rearrange("z r d -> (z r) d"))\
                .then_inc(landing("w2"), 16)
            pool.wait_ge(*when(("C1a", "normed", 1)))
            nc.gpsimd.dma_start(a2_sb, a["rw_a2"][0].rearrange("z r d -> (z r) d"))\
                .then_inc(landing("a2"), 16)
            nc.gpsimd.dma_start(g2_sb[:, 0, :], a["rw_g2"][0, 0:128])\
                .then_inc(landing("g2a"), 16)
            nc.gpsimd.dma_start(g2_sb[0:32, 1, :], a["rw_g2"][0, 128:160])\
                .then_inc(landing("g2b"), 16)
            for t in range(4):
                pool.wait_ge(*when(("rw", "mix used", 5)))
                pool.wait_ge(*when(("rw_v", "rows", 1, t)))
                for hh in range(2):
                    for par in range(2):
                        nc.gpsimd.dma_start(VS[HH[hh], 2 * t + par, :, :], v_rows[HH[par], t, :].rearrange("p (f h d) -> p f h d", f=8, h=2)[:, :, hh, :])\
                            .then_inc(landing("VS"), 16)

        def mix_dve(dve):
            dve.wait_ge(*latest(dve))
            stage(dve, "mix")
            h = hTf.rearrange("p (g t) -> p g t", t=256)
            nc.vector.tensor_tensor(shifted[:, :, 1:255], h[:, :, 0:254], h[:, :, 2:256], ALU.add)\
                .then_inc(*up(dve))
            dve.wait_ge(*latest(dve))
            nc.vector.tensor_copy(shifted[:, :, 0:1], h[:, :, 1:2]).then_inc(*up(dve))
            dve.wait_ge(*latest(dve))
            nc.vector.tensor_copy(shifted[:, :, 255:256], h[:, :, 254:255]).then_inc(*up(dve))
            dve.wait_ge(*latest(dve))
            nc.vector.scalar_tensor_tensor(area(0, 4096), area(0, 4096), 0.5, hTf, ALU.mult, ALU.subtract)\
                .then_inc(*up(dve))
            dve.wait_ge(*latest(dve))
            for i, m in enumerate(MIXES):
                if i >= 2:
                    dve.wait_ge(*when(("rw", "mix used", i - 2)))
                w = mix_width(m)
                for k in range(KT):
                    s = shifted[:, 2 * k:2 * k + 2, :].rearrange("p a b -> p (a b)")
                    nc.vector.scalar_tensor_tensor(mixed[i % 2][:, k, 0:w], s[:, 0:w], colr("mu", 8 * MU[m] + k),
                                                          hT[:, k, 0:w], ALU.mult, ALU.add)\
                        .then_inc(*up(dve, ("rw", "mixed", i)))
            nc.vector.tensor_scalar(one_ka, colA[:, ROWS_A["k_a"]:ROWS_A["k_a"] + 8], -1.0, 1.0,
                                           ALU.mult, ALU.add).then_inc(*up(dve))
            dve.wait_ge(*latest(dve))
            nc.vector.tensor_scalar(neg0, colA[:, ROWS_A["w0"]:ROWS_A["w0"] + 32], -1.0, None, ALU.mult)\
                .then_inc(*up(dve))
            dve.wait_ge(*latest(dve))
            nc.vector.memset(epsc[:, 1:2], 0.5 * float(np.log(LNS))).then_inc(*up(dve, "rw columns"))
            dve.wait_ge(*latest(dve))

        def proj_pe(pe):
            stage(pe, "proj")
            for i, m in enumerate(MIXES):
                pe.wait_ge(*when(("rw", "mixed", i)))
                x_, w = mixed[i % 2], mix_width(m)
                if m in "wag":
                    name = (m + "1", 0, 0)
                    s = slab(pe, name)
                    for j, n in enumerate((128,) if m != "g" else (128, 32)):
                        pe.wait_ge(*bank(j, (name, j)))
                        for k in range(KT):
                            ins = nc.tensor.matmul(psum[0:n, j, 0:w], s[:, k, P * j:P * j + n], x_[:, k, 0:w],
                                                   start=(k == 0), stop=(k == 7))
                        ins.then_inc(*up(pe, (name, "full", j)))
                    also(("used", slab_at[name]), (name, "full", j))
                    also(("rw", "mix used", i), (name, "full", j))
                    if m == "g":
                        pe.wait_ge(*when(("sig g", 1)))
                        pe.wait_ge(*when(("dma", "g2a")))
                        pe.wait_ge(*when(("dma", "g2b")))
                        for f in range(8):
                            b = 2 + f // 2
                            if f % 2 == 0:
                                pe.wait_ge(*bank(b, ("g2", b)))
                            o = psum[:, b, 256 * (f % 2):256 * (f % 2) + 256]
                            nc.tensor.matmul(o, g2_sb[:, 0, P * f:P * f + P], sc2[:, 0, 0:256], start=True, stop=False)
                            ins = nc.tensor.matmul(o, g2_sb[0:32, 1, P * f:P * f + P], sc2[0:32, 0, 256:512],
                                                   start=False, stop=True)
                            if f % 2:
                                ins.then_inc(*up(pe, ("g2", "full", b)))
                elif m in "rk":
                    for n in range(2):
                        s = slab(pe, ("rw_" + m, n, 0))
                        for j in range(4):
                            pe.wait_ge(*bank(j, ("rw_" + m, n, j)))
                            for k in range(KT):
                                ins = nc.tensor.matmul(psum[:, j, 0:w], s[:, k, P * j:P * j + P], x_[:, k, 0:w],
                                                       start=(k == 0), stop=(k == 7))
                            ins.then_inc(*up(pe, ("rw_" + m, "full", n, j)))
                        also(("used", slab_at[("rw_" + m, n, 0)]), ("rw_" + m, "full", n, 3))
                    also(("rw", "mix used", i), ("rw_" + m, "full", 1, 3))
                else:
                    rows_pe(pe, "rw_v", lambda k, t: mixed[1][:, k, P * t:P * t + P], range(4), KT, D, [0, 1, 2, 3])
                    stage(pe, "proj")
                    also(("rw", "mix used", i), ("rw_v", "full", 1, 3))

        def proj_act(act):
            stage(act, "proj")
            for i, m in enumerate(MIXES):
                if m in "wa":
                    act.wait_ge(*when(((m + "1", 0, 0), "full", 0)))
                    act.wait_ge(*when(("C1a", "normed", 1)))
                    nc.scalar.activation({"w": t_w, "a": t_a}[m], psum[:, 0, :],
                                                ACT.Tanh if m == "w" else ACT.Copy)\
                        .then_inc(*up(act, ("read", ((m + "1", 0, 0), 0))))
                    act.wait_ge(*latest(act))
                elif m == "g":
                    name = ("g1", 0, 0)
                    for j, n in enumerate((128, 32)):
                        act.wait_ge(*when((name, "full", j)))
                        nc.scalar.activation(sc2[0:n, 0, 256 * j:256 * j + 256], psum[0:n, j, 0:256],
                                                    ACT.Sigmoid).then_inc(*up(act, ("read", (name, j))))
                        act.wait_ge(*latest(act))
                        also(("sig g", j), ("read", (name, j)))
                    for b in range(2, 6):
                        act.wait_ge(*when(("g2", "full", b)))
                        nc.scalar.copy(gT[:, 2 * b - 4:2 * b - 2, :].rearrange("p a b -> p (a b)"), psum[:, b, :])\
                            .then_inc(*up(act, ("read", ("g2", b))))
                elif m in "rk":
                    w = mix_width(m)
                    for n in range(2):
                        for j in range(4):
                            act.wait_ge(*when(("rw_" + m, "full", n, j)))
                            nc.scalar.copy({"r": rT, "k": kT}[m][:, 4 * n + j, :], psum[:, j, 0:w])\
                                .then_inc(*up(act, ("read", ("rw_" + m, n, j))))
                else:
                    act.wait_ge(*when(("rw", "mixed", 5)))
                    for n in range(2):
                        for t in range(4):
                            act.wait_ge(*when(("rw_v", "full", n, t)))
                            nc.scalar.copy(v_rows[:, t, 512 * n:512 * n + 512], psum[:, t, :])\
                                .then_inc(*up(act, ("read", ("rw_v", n, t))))
                            also(("rw_v", "rows", n, t), ("read", ("rw_v", n, t)))

        PREP_PE = {0: 0, 1: 1, 3: 2, 13: 3}
        PREP_PARTS = 17

        def prep_pe(pe, f, part):
            if f > 7:
                return
            stage(pe, "prep")
            if f == 0 and part == 0:
                pe.wait_ge(*when(("dma", "w2")))
                pe.wait_ge(*when(("dma", "a2")))
                pe.wait_ge(*when(("read", (("w1", 0, 0), 0))))
                pe.wait_ge(*when(("read", (("a1", 0, 0), 0))))
            if f >= 2 and part == 0:
                pe.wait_ge(*when(("chains", f - 2)))
            c = slice(P * f, P * f + P)
            if part == 0:
                pe.wait_ge(*bank(5, ("wl", f, 0)))
                nc.tensor.matmul(psum[:, 5, :], w2_sb[HH[0], c], t_w[HH[0], :], start=True, stop=True)\
                    .then_inc(*up(pe, ("wl", "full", f, 0)))
                pe.wait_ge(*bank(6, ("al", f, 0)))
                nc.tensor.matmul(psum[:, 6, :], a2_sb[HH[0], c], t_a[HH[0], :], start=True, stop=True)\
                    .then_inc(*up(pe, ("al", "full", f, 0)))
                pe.wait_ge(*bank(7, ("wl", f, 1)))
                nc.tensor.matmul(psum[:, 7, :], w2_sb[HH[1], c], t_w[HH[1], :], start=True, stop=True)\
                    .then_inc(*up(pe, ("wl", "full", f, 1)))
            if part == 1:
                pe.wait_ge(*bank(5, ("al", f, 1)))
                nc.tensor.matmul(psum[:, 5, :], a2_sb[HH[1], c], t_a[HH[1], :], start=True, stop=True)\
                    .then_inc(*up(pe, ("al", "full", f, 1)))
            if part == 2:
                pe.wait_ge(*when(("kk squared", f)))
                pe.wait_ge(*bank(6, ("kk", f)))
                nc.tensor.matmul(psum[:, 6, :], cst("headones"), tmp_[f % 2][1][6], start=True, stop=True)\
                    .then_inc(*up(pe, ("kk", "full", f)))
            if part == 3:
                pe.wait_ge(*when(("coef product", f)))
                pe.wait_ge(*bank(7, ("coef", f)))
                for hh in range(2):
                    for c_ in range(4):
                        ins = nc.tensor.matmul(psum[HH[hh], 7, c_:c_ + 1],
                                               tmp_[f % 2][0][4][HH[hh], 64 * c_:64 * c_ + 64],
                                               cst("ones")[HH[hh], 0:1], start=True, stop=True)
                ins.then_inc(*up(pe, ("coef", "full", f)))

        def prep_act(act, f):
            stage(act, "prep")
            act.wait_ge(*when("rw columns"))
            if f == 0:
                act.wait_ge(*when(("dma", "VS")))
                act.wait_ge(*when(("used", slab_at[("rw_o", 0, 0)] - 1)))
            elif f >= 2:
                act.wait_ge(*when(("chains", f - 2)))
            for z in range(2):
                t = tmp_[f % 2][z]
                act.wait_ge(*when(("wl", "full", f, z)))
                nc.scalar.activation(t[0], psum[:, (5, 7)[z], :], ACT.Exp, bias=neg0[:, 8 * z + f:8 * z + f + 1],
                                     scale=-1.0).then_inc(*up(act, ("read", ("wl", f, z))))
                act.wait_ge(*when(("al", "full", f, z)))
                nc.scalar.activation(t[1], psum[:, (6, 5)[z], :], ACT.Exp,
                                     bias=neg0[:, 16 + 8 * z + f:16 + 8 * z + f + 1], scale=-1.0)\
                    .then_inc(*up(act, ("read", ("al", f, z))))
            for z in range(2):
                t = tmp_[f % 2][z]
                act.wait_ge(*latest(act))
                for v in (t[0], t[1]):
                    nc.scalar.activation(v, v, ACT.Ln, bias=cst("ones")[:, 0:1]).then_inc(*up(act))
                act.wait_ge(*latest(act))
                nc.scalar.activation(t[0], t[0], ACT.Exp, scale=-1.0).then_inc(*up(act))
                nc.scalar.activation(t[1], t[1], ACT.Exp, scale=-1.0).then_inc(*up(act, ("sigmoids", f, z)))
            for z in range(2):
                t = tmp_[f % 2][z]
                act.wait_ge(*when(("decay sums", f, z)))
                nc.scalar.activation(t[2], t[2], ACT.Exp, scale=-KAPPA).then_inc(*up(act))
                nc.scalar.activation(t[0], t[3], ACT.Exp, scale=-KAPPA).then_inc(*up(act))
                nc.scalar.activation(t[3], t[3], ACT.Exp, scale=KAPPA).then_inc(*up(act, ("decays", f, z)))
            act.wait_ge(*when(("kk", "full", f)))
            act.wait_ge(*when(("kk bounded", f)))
            sq = tmp_[f % 2][1][6]
            nc.scalar.activation(sq, sq, ACT.Ln, scale=LNS).then_inc(*up(act))
            act.wait_ge(*latest(act))
            nc.scalar.activation(sq, sq, ACT.Exp, scale=-0.5, bias=epsc[:, 1:2])\
                .then_inc(*up(act, ("kk rnorm", f)))

        def prep_dve(dve, f, part):
            if f > 7 or part >= PREP_PARTS:
                return
            stage(dve, "prep")
            kk, sq = tmp_[f % 2][0][6], tmp_[f % 2][1][6]
            if part == 0:
                if f == 0:
                    dve.wait_ge(*when(("dma", "VS")))
                    dve.wait_ge(*when(("rw", "mix used", 5)))
                    dve.wait_ge(*when(("used", slab_at[("rw_o", 0, 0)] - 1)))
                    for e, z in ((0, 0), (0, 1), (1, 0), (1, 1)):
                        nc.vector.tensor_copy(ARI[e][z][:, :, 64:128],
                                              cst("eye64").unsqueeze(1).to_broadcast([P, 8, 64]))\
                            .then_inc(*up(dve, "eyes"))
                elif f >= 2:
                    dve.wait_ge(*when(("chains", f - 2)))
                nc.vector.tensor_scalar(kk, kT[:, f, :], colr("k_k", f), None, ALU.mult).then_inc(*up(dve))
                dve.wait_ge(*latest(dve))
                nc.vector.tensor_tensor(sq, kk, kk, ALU.mult).then_inc(*up(dve, ("kk squared", f)))
            z, quarter = divmod(part - 3, 3)
            if 3 <= part <= 8:
                t = tmp_[f % 2][z]
                v = (lambda q: q) if z == 0 else (lambda q: q[:, ::-1])
                if quarter == 0:
                    dve.wait_ge(*when(("sigmoids", f, z)))
                    nc.vector.tensor_tensor_scan(v(t[3]), cst("chunk_start"), v(t[0]), 0.0, ALU.mult, ALU.add)\
                        .then_inc(*up(dve))
                    nc.vector.tensor_scalar(t[4], t[1], colr("k_a", f), one_ka[:, f:f + 1], ALU.mult, ALU.add)\
                        .then_inc(*up(dve))
                if quarter == 1:
                    dve.wait_ge(*latest(dve))
                    nc.vector.tensor_tensor(t[2], t[3], t[0], ALU.subtract)\
                        .then_inc(*up(dve, ("decay sums", f, z)))
                    nc.vector.tensor_tensor(t[5], t[4], kT[:, f, :], ALU.mult).then_inc(*up(dve))
            c4 = tmp_[f % 2][0][4][:, 0:256]
            if part == 9:
                dve.wait_ge(*when(("kk", "full", f)))
                nc.vector.tensor_scalar(sq, psum[:, 6, :], 1e-24, None, ALU.max)\
                    .then_inc(*up(dve, ("kk bounded", f)))
                also(("read", ("kk", f)), ("kk bounded", f))
                dve.wait_ge(*latest(dve))
                nc.vector.tensor_tensor(c4, tmp_[f % 2][0][5][:, 0:256], tmp_[f % 2][1][5][:, 0:256], ALU.add)\
                    .then_inc(*up(dve))
            if part == 10:
                dve.wait_ge(*latest(dve))
                nc.vector.scalar_tensor_tensor(c4, c4, colr("r_k", f), rT[:, f, :], ALU.mult, ALU.mult)\
                    .then_inc(*up(dve, ("coef product", f)))
            if part == 11:
                dve.wait_ge(*when(("kk rnorm", f)))
                nc.vector.tensor_tensor(kk, kk, sq, ALU.mult).then_inc(*up(dve))
            z, half_ = divmod(part - 12, 2)
            if 12 <= part <= 15:
                t = tmp_[f % 2][z]
                ari = ARI[f % 2][z]
                last = 63 if z == 0 else 0
                if half_ == 0:
                    dve.wait_ge(*when(("decays", f, z)))
                    nc.vector.tensor_copy(PC[f % 2][z].unsqueeze(2), chunks(t[0])[:, :, last:last + 1])\
                        .then_inc(*up(dve))
                    dve.wait_ge(*latest(dve))
                    nc.vector.scalar_tensor_tensor(ari[:, :, 0:64], chunks(kk), -1.0, chunks(t[2]),
                                                   ALU.mult, ALU.mult).then_inc(*up(dve))
                    nc.vector.tensor_tensor(t[1], t[1], kk, ALU.mult).then_inc(*up(dve))
                if half_ == 1:
                    nc.vector.tensor_tensor(ari[:, 0:4, 128:192], rT[:, f, :].rearrange("p (c t) -> p c t", c=4),
                                            chunks(t[0])[:, 0:4, :], ALU.mult).then_inc(*up(dve))
                    dve.wait_ge(*latest(dve))
                    nc.vector.tensor_tensor(Bh[f % 2][z], t[1], t[3], ALU.mult).then_inc(*up(dve))
                    nc.vector.tensor_tensor(Kh[f % 2][z], t[5], t[3], ALU.mult)\
                        .then_inc(*up(dve, ("scaled", f, z)))
            if part == 16:
                dve.wait_ge(*when(("coef", "full", f)))
                nc.vector.tensor_copy(coef[:, :, f:f + 1], psum[:, 7, 0:4].unsqueeze(2))\
                    .then_inc(*up(dve, ("read", ("coef", f))))

        Y_AT = (9, 11, 13, 15)
        GRAM_BANKS = (0, 1, 2, 3, 4)

        def gram_list(f):
            return [(z, c) for z in range(2) for c in range(8)]

        def gram_pe(pe, f):
            stage(pe, "gram")
            pe.wait_ge(*when("eyes"))
            pe.wait_ge(*when(("scaled", f, 1)))
            pe.wait_ge(*when(("decays", f, 1)))
            for i, (z, c) in enumerate(gram_list(f)):
                b = GRAM_BANKS[i % 5]
                w = 192 if c < 4 else 128
                s = slice(64 * c, 64 * c + 64)
                pe.wait_ge(*bank(b, ("gram", f, z, c)))
                for n, r in enumerate(HH):
                    nc.tensor.matmul(psum[r, b, 0:w], Bh[f % 2][z][r, s], ARI[f % 2][z][r, c, 0:w], start=True, stop=True)
                    nc.tensor.matmul(psum[r, b, 192:192 + w], Kh[f % 2][z][r, s], ARI[f % 2][z][r, c, 0:w], start=True, stop=True)
                    ins = nc.tensor.matmul(psum[r, b, 384:448], ARI[f % 2][z][r, c, 0:64], Bh[f % 2][z][r, s],
                                           start=True, stop=True)
                    if n == 1:
                        ins.then_inc(*up(pe, ("gram", "full", f, z, c)))
                    at = 2 * i + n
                    for hop in range(HOPS * at // 32, HOPS * (at + 1) // 32):
                        walk_pe(pe, f - 1, hop)
                    stage(pe, "gram")

        def gram_dve(dve, f):
            stage(dve, "gram")
            for i, (z, c) in enumerate(gram_list(f)):
                b = GRAM_BANKS[i % 5]
                m = cst(f"gram{z}")
                dve.wait_ge(*when(("gram", "full", f, z, c)))
                if i == 0:
                    dve.wait_ge(*when(("coef", "full", f)))
                if c < 4:
                    ins = nc.vector.tensor_tensor(G[f % 2][z][:, c, :], psum[:, b, 0:448], m, ALU.mult)
                else:
                    two = lambda q: q.rearrange("p (a n) -> p a n", a=2)[:, :, 0:128]
                    nc.vector.tensor_tensor(two(G[f % 2][z][:, c, 0:384]), two(psum[:, b, 0:384]), two(m[:, 0:384]),
                                                   ALU.mult).then_inc(*up(dve))
                    ins = nc.vector.tensor_tensor(G[f % 2][z][:, c, 384:448], psum[:, b, 384:448], m[:, 384:448], ALU.mult)
                ins.then_inc(*up(dve, ("read", ("gram", f, z, c))))
                dve.wait_ge(*latest(dve))
                for y in range(4, 8):
                    if i == Y_AT[y - 4]:
                        walk_y(dve, f - 1, y)
                        stage(dve, "gram")
                if i in (9, 15):
                    inv_start(dve, f, i // 15)
                    stage(dve, "gram")

        INV_STEPS = (
            ((1, 0, 2, None), (0, 1, 3, None)),
            ((3, 4, 4, 4), (3, 2, 0, None), (2, 3, 1, None)),
            ((1, 4, 4, 4), (0, 1, 2, None)),
            ((2, 4, 4, 4),),
            ((4, "eye", 5, None),),
            (("off32", 4, 3, None),),
            ((5, 3, 4, 4), (3, 5, 5, 5)),
            (("off64", 4, 3, None),),
            ((5, 3, 0, 4),),
        )

        def inv_tiles(f):
            n = 0
            for r, steps in enumerate(INV_STEPS):
                for z in range(2):
                    for j, step in enumerate(steps):
                        yield r, z, j, step, n % 5
                        n += 1

        def inv_pe(pe, f):
            stage(pe, "inv")
            for r, z, j, (left, right, dst, add), b in inv_tiles(f):
                if j == 0 and 2 * r + z in PREP_PE:
                    prep_pe(pe, f + 1, PREP_PE[2 * r + z])
                    stage(pe, "inv")
                pe.wait_ge(*when(("inv ready", f, r, z)))
                pe.wait_ge(*bank(b, ("inv", f, r, z, j)))
                for c in range(8):
                    for h in HH:
                        l = INV[f % 2][z][2 if left in ("off32", "off64") else left][h, c, :]
                        rr = cst("eye64")[h, :] if right == "eye" else INV[f % 2][z][right][h, c, :]
                        ins = nc.tensor.matmul(psum[h, b, 64 * c:64 * c + 64], l, rr, start=True, stop=True)
                ins.then_inc(*up(pe, ("inv", "full", f, r, z, j)))

        def blocks_of(name):
            return cst(name).unsqueeze(1).to_broadcast([P, 8, 64])

        def inv_start(dve, f, z):
            stage(dve, "inv")
            B = INV[f % 2][z]
            dve.wait_ge(*when(("gram", "full", f, z, 7)))
            dve.wait_ge(*latest(dve))
            nc.vector.tensor_tensor(B[0], G[f % 2][z][:, :, 0:64], blocks_of("diag16"), ALU.mult)\
                .then_inc(*up(dve))
            nc.vector.tensor_tensor(B[1], G[f % 2][z][:, :, 384:448], blocks_of("diag16"), ALU.mult)\
                .then_inc(*up(dve))
            dve.wait_ge(*latest(dve))
            nc.vector.tensor_tensor(B[4], B[0], blocks_of("eye64"), ALU.add)\
                .then_inc(*up(dve, ("inv ready", f, 0, z)))

        def inv_dve(dve, f):
            stage(dve, "inv")
            for r, z, j, (left, right, dst, add), b in inv_tiles(f):
                B = INV[f % 2][z]
                dve.wait_ge(*when(("inv", "full", f, r, z, len(INV_STEPS[r]) - 1)))
                src = chunks(psum[:, b, :])
                if add is None:
                    ins = nc.vector.tensor_copy(B[dst], src)
                else:
                    ins = nc.vector.tensor_tensor(B[dst], src, B[add], ALU.add)
                ins.then_inc(*up(dve, ("read", ("inv", f, r, z, j))))
                if j == len(INV_STEPS[r]) - 1:
                    if r == 4:
                        ins = nc.vector.tensor_tensor(B[2], G[f % 2][z][:, :, 384:448], blocks_of("off32"), ALU.mult)
                        ins.then_inc(*up(dve, ("inv ready", f, 5, z)))
                        dve.wait_ge(*latest(dve))
                    elif r == 6:
                        ins = nc.vector.tensor_tensor(B[2], G[f % 2][z][:, :, 384:448], blocks_of("off64"), ALU.mult)
                        ins.then_inc(*up(dve, ("inv ready", f, 7, z)))
                        dve.wait_ge(*latest(dve))
                    else:
                        also(("inv ready", f, r + 1, z), ("read", ("inv", f, r, z, j)))
                    prep_dve(dve, f + 1, 2 * r + z)
                    stage(dve, "inv")

        HOPS = 24

        def walk_tile(z, j):
            return psum[:, 5, 64 * z:64 * z + 64] if j == 3 else psum[:, 6 + z, 64 * j:64 * j + 64]

        def walk_pe(pe, f, hop):
            if f < 0 or hop >= HOPS:
                return
            stage(pe, "walk")
            i, part = divmod(hop, 3)
            if hop == 0:
                if f < 7:
                    pe.wait_ge(*when(("read", ("coef", f + 1))))
                pe.wait_ge(*when(("inv ready", f, len(INV_STEPS), 0)))
                pe.wait_ge(*when(("inv ready", f, len(INV_STEPS), 1)))
                pe.wait_ge(*when(("walk zero", f)))
            for z in range(2):
                c, S = WALK[z][i], St[z][i % 2]
                ari, g = ARI[f % 2][z], G[f % 2][z]
                if part == 0:
                    t = walk_tile(z, 0)
                    pe.wait_ge(*bank(("W", z), ("W", f, i, z)))
                    pe.wait_ge(*when(("S", f, i, z)))
                    for r in HH:
                        nc.tensor.matmul(t[r], ari[r, c, 0:64], S[r, :], start=True, stop=False)
                        ins = nc.tensor.matmul(t[r], g[r, c, 192:256], VS[r, c, f, :], start=False, stop=True)
                    ins.then_inc(*up(pe, ("W", "full", f, i, z)))
                if part == 1:
                    t = walk_tile(z, 1)
                    pe.wait_ge(*bank(("U", z), ("U", f, i, z)))
                    pe.wait_ge(*when(("W", "out", f, i, z)))
                    for r in HH:
                        ins = nc.tensor.matmul(t[r], INV[f % 2][z][0][r, c, :], Wt[z][r, :], start=True, stop=True)
                    ins.then_inc(*up(pe, ("U", "full", f, i, z)))
                if part == 2:
                    pe.wait_ge(*when(("U", "out", f, i, z)))
                    if i < 7:
                        t = walk_tile(z, 2)
                        pe.wait_ge(*bank(("S", z), ("S psum", f, i, z)))
                        for r in HH:
                            nc.tensor.matmul(t[r], cst("eye64")[r, :], S[r, :], start=True, stop=False)
                            nc.tensor.matmul(t[r], g[r, c, 256:320], VS[r, c, f, :], start=False, stop=False)
                            ins = nc.tensor.matmul(t[r], g[r, c, 64:128], Ut[z][r, :], start=False, stop=True)
                        ins.then_inc(*up(pe, ("S", "full", f, i, z)))
            for z in range(2):
                c, S = WALK[z][i], St[z][i % 2]
                ari, g = ARI[f % 2][z], G[f % 2][z]
                if part == 2 and c < 4:
                    t = walk_tile(z, 3)
                    if z == 0:
                        pe.wait_ge(*bank(5, ("Y", f, i, 1)))
                    for r in HH:
                        nc.tensor.matmul(t[r], ari[r, c, 128:192], S[r, :], start=True, stop=False)
                        nc.tensor.matmul(t[r], g[r, c, 320:384], VS[r, c, f, :], start=False, stop=False)
                        ins = nc.tensor.matmul(t[r], g[r, c, 128:192], Ut[z][r, :], start=False, stop=True)
                    ins.then_inc(*up(pe, ("Y", "full", f, i, z)))

        def walk_act(act, f, hop):
            if f < 0 or hop >= HOPS:
                return
            stage(act, "walk")
            i, part = divmod(hop, 3)
            for z in range(2):
                if part == 0:
                    act.wait_ge(*when(("W", "full", f, i, z)))
                    nc.scalar.copy(Wt[z], walk_tile(z, 0)).then_inc(*up(act, ("W", "out", f, i, z)))
                    also(("read", ("W", f, i, z)), ("W", "out", f, i, z))
                if part == 1:
                    act.wait_ge(*when(("U", "full", f, i, z)))
                    if i:
                        act.wait_ge(*when(("Y", "full", f, i - 1, z) if WALK[z][i - 1] < 4
                                          else ("S", "full", f, i - 1, z)))
                    nc.scalar.copy(Ut[z], walk_tile(z, 1)).then_inc(*up(act, ("U", "out", f, i, z)))
                    also(("read", ("U", f, i, z)), ("U", "out", f, i, z))
                if part == 2 and i < 7:
                    act.wait_ge(*when(("S", "full", f, i, z)))
                    c = WALK[z][i]
                    nc.scalar.activation(St[z][(i + 1) % 2], walk_tile(z, 2), ACT.Copy,
                                         scale=PC[f % 2][z][:, c:c + 1]).then_inc(*up(act, ("S", f, i + 1, z)))
                    also(("read", ("S psum", f, i, z)), ("S", f, i + 1, z))

        def walk_start(dve, f):
            stage(dve, "walk")
            if f:
                dve.wait_ge(*when(("chains", f - 1)))
            for z in range(2):
                nc.vector.memset(St[z][0], 0.0).then_inc(*up(dve, ("S", f, 0, z)))
            also(("walk zero", f), ("S", f, 0, 1))

        def walk_y(dve, f, i):
            if f < 0:
                return
            stage(dve, "walk")
            for z in range(2):
                c = WALK[z][i]
                first = (z == 0) == (c < 2)
                dve.wait_ge(*when(("Y", "full", f, i, 1)))
                src = walk_tile(z, 3)
                if first:
                    ins = nc.vector.tensor_copy(Y[:, c, f, :], src)
                else:
                    ins = nc.vector.tensor_tensor(Y[:, c, f, :], src, Y[:, c, f, :], ALU.add)
                ins.then_inc(*up(dve, ("read", ("Y", f, i, z))))
                dve.wait_ge(*latest(dve))
            if i == 7:
                also(("chains", f), ("read", ("Y", f, 7, 1)))

        bonus = area(0, 4, 8, 64)
        ysq = area(2048, 32, 64)
        ystat = stat[:, 88:120]
        gates_r = (area(4096, 1024),)

        def readout_dve(dve):
            stage(dve, "readout")
            Yf = Y.rearrange("p c f d -> p (c f) d")
            bc = lambda v: v.unsqueeze(2).to_broadcast([P, 32, 64])
            nc.vector.tensor_reduce(ystat, Yf, AX.X, ALU.add).then_inc(*up(dve))
            dve.wait_ge(*latest(dve))
            nc.vector.tensor_scalar(ystat, ystat, 1.0 / 64, None, ALU.mult).then_inc(*up(dve))
            dve.wait_ge(*latest(dve))
            nc.vector.tensor_tensor(Yf, Yf, bc(ystat), ALU.subtract).then_inc(*up(dve))
            dve.wait_ge(*latest(dve))
            nc.vector.tensor_tensor(ysq, Yf, Yf, ALU.mult).then_inc(*up(dve))
            dve.wait_ge(*latest(dve))
            nc.vector.tensor_reduce(ystat, ysq, AX.X, ALU.add).then_inc(*up(dve, "y squares"))
            dve.wait_ge(*latest(dve))
            nc.vector.tensor_tensor(bonus.rearrange("p c f d -> p (c f) d"),
                                           VS[:, 0:4, :, :].rearrange("p c f d -> p (c f) d"),
                                           coef.rearrange("p c f -> p (c f)").unsqueeze(2).to_broadcast([P, 32, 64]),
                                           ALU.mult).then_inc(*up(dve))
            dve.wait_ge(*latest(dve))
            dve.wait_ge(*when("y rstd"))
            nc.vector.tensor_tensor(Yf, Yf, bc(ystat), ALU.mult).then_inc(*up(dve, "y normed"))
            dve.wait_ge(*latest(dve))
            for f in range(8):
                dve.wait_ge(*when(("y turned", f)))
                t = sc[:, f % 2, 0:256]
                nc.vector.tensor_scalar(t, psum[:, f % 4, 0:256], colr("lnx_w", f), colr("lnx_b", f),
                                               ALU.mult, ALU.add).then_inc(*up(dve))
                dve.wait_ge(*latest(dve))
                nc.vector.tensor_tensor(t, t, psum[:, f % 4, 256:512], ALU.add)\
                    .then_inc(*up(dve, ("read", ("y", f))))
                dve.wait_ge(*latest(dve))
                nc.vector.tensor_tensor(hT[:, f, 0:256], t, gT[:, f, :], ALU.mult)\
                    .then_inc(*up(dve, ("rw gated", f)))
                dve.wait_ge(*latest(dve))

        def readout_pool(pool):
            stage(pool, "readout")
            pool.wait_ge(*when("y squares"))
            nc.gpsimd.tensor_scalar(ystat, ystat, 1.0 / 64, 64e-5, ALU.mult, ALU.add).then_inc(*up(pool))
            pool.wait_ge(*latest(pool))
            nc.gpsimd.tensor_tensor(ystat, ystat, half[:, 0:32], ALU.pow).then_inc(*up(pool, "y rstd"))
            pool.wait_ge(*latest(pool))
            gate_load(pool, "gate r", gates_r[0], 1, 0, 2)

        def readout_pe(pe):
            stage(pe, "readout")
            pe.wait_ge(*when("y normed"))
            for f in range(8):
                pe.wait_ge(*bank(f % 4, ("y", f)))
                for h in HH:
                    for c in range(4):
                        s = slice(64 * c, 64 * c + 64)
                        nc.tensor.matmul(psum[h, f % 4, 64 * c:64 * c + 64], Y[h, c, f, :], cst("eye64")[h, :],
                                         start=True, stop=True)
                        ins = nc.tensor.matmul(psum[h, f % 4, 256 + 64 * c:320 + 64 * c], bonus[h, c, f, :],
                                               cst("eye64")[h, :], start=True, stop=True)
                ins.then_inc(*up(pe, ("y turned", f)))
        def gain(name, layer=0, n=8):
            at = ROWS_B[name] + n * layer
            return colB[:, at:at + n]

        def add_rows_dve(dve, name, banks, scale, split=()):
            stage(dve, "add")
            for n in range(2):
                for i in range(2):
                    dve.wait_ge(*when((name, "full", n, i)))
                    b = rows_bank(name, n, i, range(2), banks)
                    dst = x[:, i, 512 * n:512 * n + 512]
                    nc.vector.scalar_tensor_tensor(dst, psum[:, b, :], scale, dst, ALU.mult, ALU.add)\
                        .then_inc(*up(dve, (name, "added", n, i)))
                    also(("read", (name, n, i)), (name, "added", n, i))
                if n == 0:
                    for slab_name in split:
                        for h in range(2):
                            low_dve(dve, slab_name, h)
                    stage(dve, "add")
            dve.wait_ge(*latest(dve))

        UP_BANKS = [4, 5, 6, 7]

        hid_parts = [area(at, 22, 256, rounded=True) for at in (0, 5632)]

        def swiglu_pe(pe, key):
            stage(pe, "swiglu")
            for n in range(11):
                w = (key + "_gu", n, 0)
                for part in range(2):
                    b = 2 * (n % 2) + part
                    pe.wait_ge(*bank(b, (key, "gu", n, part)))
                    for j in range(2):
                        at = 256 * part + P * j
                        for k in range(KT):
                            pe.wait_ge(*when(("read", (key, k // 2))))
                            if k % 4 == 0:
                                pe.wait_ge(*when(("low", w, k // 4)))
                            for i, (s, q) in enumerate(parts(w)):
                                ins = nc.tensor.matmul(psum[:, b, 256 * j:256 * j + 256], s[:, k, at:at + P],
                                                       x_parts[q][:, k, :], start=(k == 0 and i == 0),
                                                       stop=(k == 7 and i == 2))
                    ins.then_inc(*up(pe, (key, "gu full", n, part)))
                also(("used", slab_at[w]), (key, "gu full", n, 1))
            rows3_pe(pe, key + "_down", hid_parts, 22, D, UP_BANKS, needs=[(key, "hidden", 10)])

        def swiglu_act(act, key):
            names = ffn_slabs(key)
            for name in names[len(AHEAD[key]):2]:
                high_act(act, name)
            for n in range(11):
                stage(act, "swiglu")
                act.wait_ge(*when((key, "gu full", n, 0)))
                if n >= 2:
                    act.wait_ge(*when((key, "hidden", n - 2)))
                nc.scalar.activation(sc[:, n % 2, :], psum[:, 2 * (n % 2), :], ACT.Silu)\
                    .then_inc(*up(act, ("read", (key, "gu", n, 0))))
                high_act(act, names[n + 2])
            for name in names[13:]:
                high_act(act, name)

        def swiglu_dve(dve, key, following=()):
            names = ffn_slabs(key)
            low_slabs(dve, names[len(AHEAD[key]):2])
            for n in range(11):
                stage(dve, "swiglu")
                dve.wait_ge(*when(("read", (key, "gu", n, 0))))
                dve.wait_ge(*when((key, "gu full", n, 1)))
                t = sc[:, n % 2, :]
                high, low = [v[:, 2 * n:2 * n + 2, :].rearrange("p a b -> p (a b)") for v in hid_parts]
                nc.vector.tensor_tensor(t, t, psum[:, 2 * (n % 2) + 1, :], ALU.mult)\
                    .then_inc(*up(dve, ("read", (key, "gu", n, 1))))
                dve.wait_ge(*latest(dve))
                nc.vector.tensor_copy(high, t).then_inc(*up(dve))
                dve.wait_ge(*latest(dve))
                nc.vector.tensor_tensor(low, t, high.bitcast(F32), ALU.subtract)\
                    .then_inc(*up(dve, (key, "hidden", n)))
                for h in range(2):
                    low_dve(dve, names[n + 2], h)
            for name in names[13:15]:
                for h in range(2):
                    low_dve(dve, name, h)
            stage(dve, "swiglu")
            add_rows_dve(dve, key + "_down", UP_BANKS, 0.5, names[15:] + list(following))

        eq = area(0, 4, 256)
        ek = area(1024, 4, 256)
        ev = area(2048, 2, 512)
        eu = area(3072, 2, 512)
        eg = area(4096, 2, 512)
        e_gain, e_bias = area(6144, 512), area(6656, 512)
        ew = area(7168, 8, P)
        ewT = area(8192, 8, P)
        esq = area(9216, 2, 512)

        def even_pool(pool):
            stage(pool, "even")
            pool.wait_ge(*when(("pre0_down", "added", 1, 1)))
            nc.gpsimd.dma_start(e_gain, a["sgu_ln_gain_2"][0].partition_broadcast(P))\
                .then_inc(landing("ln gain"), 16)
            nc.gpsimd.dma_start(e_bias, a["sgu_ln_bias_2"][0].partition_broadcast(P))\
                .then_inc(landing("ln bias"), 16)
            nc.gpsimd.dma_start(ew, a["sgu_w_2"][0].rearrange("g t s -> t g s"))\
                .then_inc(landing("sgu w"), 16)

        def even_pool_rstd(pool):
            stage(pool, "even")
            pool.wait_ge(*when("g squares"))
            nc.gpsimd.tensor_scalar(stat[:, 132:134], stat[:, 132:134], 1.0 / 512, EPS, ALU.mult, ALU.add)\
                .then_inc(*up(pool))
            pool.wait_ge(*latest(pool))
            nc.gpsimd.tensor_tensor(stat[:, 132:134], stat[:, 132:134], half[:, 0:2], ALU.pow)\
                .then_inc(*up(pool, "g rstd"))
            pool.wait_ge(*latest(pool))

        def even_in_pe(pe):
            stage(pe, "even")
            for n in range(2):
                w = ("sbg_in", n, 0)
                for j in range(4):
                    pe.wait_ge(*bank(j, ("sbg", n, j)))
                    for k in range(KT):
                        pe.wait_ge(*when(("read", ("mix0", k // 2))))
                        if k % 4 == 0:
                            pe.wait_ge(*when(("low", w, k // 4)))
                        for i, (s, q) in enumerate(parts(w)):
                            ins = nc.tensor.matmul(psum[:, j, 0:256], s[:, k, P * j:P * j + P], x_parts[q][:, k, :],
                                                   start=(k == 0 and i == 0), stop=(k == 7 and i == 2))
                    ins.then_inc(*up(pe, ("sbg", "full", n, j)))
                also(("used", slab_at[("sbg_in", n, 0)]), ("sbg", "full", n, 3))
            rows3_pe(pe, "sbg_in", x_parts, KT, 2560, [4, 5, 6, 7], first=2)
            stage(pe, "even")
            pe.wait_ge(*when(("dma", "sgu w")))
            for b in range(2):
                pe.wait_ge(*bank(b, ("ewT", b)))
                for g in range(4):
                    ins = nc.tensor.transpose(psum[:, b, P * g:P * g + P], ew[:, 4 * b + g, :], ident)
                ins.then_inc(*up(pe, ("ewT", "full", b)))

        def even_in_act(act):
            act.wait_ge(*when(("pre0_down", "full", 1, 1)))
            high_act(act, sbg_slabs[1])
            for n in range(2):
                stage(act, "even")
                for j in range(4):
                    act.wait_ge(*when(("sbg", "full", n, j)))
                    nc.scalar.copy((eq, ek)[n][:, j, :], psum[:, j, 0:256])\
                        .then_inc(*up(act, ("read", ("sbg", n, j))))
                high_act(act, sbg_slabs[n + 2])
            for i, n in enumerate((2, 3, 4)):
                stage(act, "even")
                for t in range(2):
                    act.wait_ge(*when(("sbg_in", "full", n, t)))
                    nc.scalar.activation((ev, eu, eg)[i][:, t, :], psum[:, 4 + (2 * i + t) % 4, :],
                                                ACT.Copy if n == 2 else ACT.Gelu_apprx_tanh)\
                        .then_inc(*up(act, ("read", ("sbg_in", n, t))))
                if n == 2:
                    high_act(act, sbg_slabs[4])

        def even_gate_dve(dve):
            low_slabs(dve, sbg_slabs[1:])
            stage(dve, "even")
            for b in range(2):
                dve.wait_ge(*when(("ewT", "full", b)))
                nc.vector.tensor_tensor(ewT[:, 4 * b:4 * b + 4, :],
                                               psum[:, b, :].rearrange("p (g t) -> p g t", g=4),
                                               cst("st_fwd").unsqueeze(1).to_broadcast([P, 4, P]), ALU.mult)\
                    .then_inc(*up(dve, ("read", ("ewT", b))))
                dve.wait_ge(*latest(dve))
            dve.wait_ge(*when(("read", ("sbg_in", 4, 0))))
            dve.wait_ge(*when(("read", ("sbg_in", 4, 1))))
            dve.wait_ge(*when(("dma", "ln gain")))
            dve.wait_ge(*when(("dma", "ln bias")))
            m = stat[:, 130:132]
            nc.vector.tensor_reduce(m, eg, AX.X, ALU.add).then_inc(*up(dve))
            dve.wait_ge(*latest(dve))
            nc.vector.tensor_scalar(m, m, 1.0 / 512, None, ALU.mult).then_inc(*up(dve))
            dve.wait_ge(*latest(dve))
            for t in range(2):
                nc.vector.tensor_scalar(eg[:, t, :], eg[:, t, :], m[:, t:t + 1], None, ALU.subtract)\
                    .then_inc(*up(dve))
                dve.wait_ge(*latest(dve))
            nc.vector.tensor_tensor(esq, eg, eg, ALU.mult).then_inc(*up(dve))
            dve.wait_ge(*latest(dve))
            nc.vector.tensor_reduce(stat[:, 132:134], esq, AX.X, ALU.add).then_inc(*up(dve, "g squares"))
            dve.wait_ge(*latest(dve))
            dve.wait_ge(*when("g rstd"))
            for t in range(2):
                nc.vector.scalar_tensor_tensor(eg[:, t, :], eg[:, t, :], stat[:, 132 + t:133 + t], e_gain,
                                                      ALU.mult, ALU.mult).then_inc(*up(dve))
                dve.wait_ge(*latest(dve))
                nc.vector.tensor_tensor(eg[:, t, :], eg[:, t, :], e_bias, ALU.add)\
                    .then_inc(*up(dve, "g normed"))
                dve.wait_ge(*latest(dve))
            for t in range(2):
                dve.wait_ge(*when(("mixed", "full", t)))
                for g in range(8):
                    c = slice(64 * g, 64 * g + 64)
                    at = ROWS_B["sgu_b"] + g
                    nc.vector.scalar_tensor_tensor(eu[:, t, c], psum[:, 2 + t, c], colB[:, at:at + 1],
                                                          eu[:, t, c], ALU.add, ALU.mult)\
                        .then_inc(*up(dve, ("gated", t)))
                also(("read", ("mixed", t)), ("gated", t))
            for t in range(2):
                dve.wait_ge(*when(("gated", "turned", t)))
                nc.vector.tensor_copy(hT[:, 4:8, P * t:P * t + P],
                                             psum[:, 6 + t, :].rearrange("p (f t) -> p f t", f=4))\
                    .then_inc(*up(dve, ("read", ("gatedT", t))))

        def even_gate_pe(pe):
            stage(pe, "even")
            pe.wait_ge(*when("g normed"))
            pe.wait_ge(*when(("read", ("ewT", 1))))
            for t in range(2):
                pe.wait_ge(*bank(2 + t, ("mixed", t)))
                for g in range(8):
                    c = slice(64 * g, 64 * g + 64)
                    ins = nc.tensor.matmul(psum[:, 2 + t, c], ewT[:, g, :], eg[:, t, c], start=True, stop=True)
                ins.then_inc(*up(pe, ("mixed", "full", t)))
            for t in range(2):
                pe.wait_ge(*when(("gated", t)))
                pe.wait_ge(*bank(6 + t, ("gatedT", t)))
                for f in range(4):
                    ins = nc.tensor.transpose(psum[:, 6 + t, P * f:P * f + P], eu[:, t, P * f:P * f + P], ident)
                ins.then_inc(*up(pe, ("gated", "turned", t)))

        sb_units = []
        for h in range(8):
            for qt in range(2):
                r, f = head_rows(h), h // 2
                sb_units.append(dict(keys=P * (qt + 1), qk=[(eq[r, f, P * qt:P * qt + P], ek[r, f, 0:P * (qt + 1)])],
                                     v=[(lambda k, h=h: ev[:, k, 64 * h:64 * h + 64], r.start)],
                                     dst=[hT[r, f, P * qt:P * qt + P]]))

        def stick_act(act):
            stage(act, "stick")
            act.wait_ge(*when(("sbg_in", "full", 4, 1)))

            def softplus(i):
                n, s = sb_units[i]["keys"], sc[:, i % 2, :]
                act.wait_ge(*when(("sb", "z", i)))
                if i >= 2:
                    act.wait_ge(*when(("sb", "probs", i - 2)))
                nc.scalar.activation(s[:, 0:n], sc[:, 2 + i % 2, 0:n], ACT.Abs).then_inc(*up(act))
                act.wait_ge(*latest(act))
                nc.scalar.activation(s[:, 0:n], s[:, 0:n], ACT.Exp, scale=-1.0).then_inc(*up(act))
                act.wait_ge(*latest(act))
                nc.scalar.activation(s[:, 0:n], s[:, 0:n], ACT.Ln, bias=1.0).then_inc(*up(act, ("sb", "ln", i)))
                act.wait_ge(*latest(act))

            def weights(i):
                n = sb_units[i]["keys"]
                act.wait_ge(*when(("sb", "exponent", i)))
                if i >= 2:
                    act.wait_ge(*when(("sb", "turned", i - 2)))
                nc.scalar.activation(sc2[:, i % 2, 0:n], sc[:, i % 2, 0:n], ACT.Exp)\
                    .then_inc(*up(act, ("sb", "probs", i)))

            for step, i in unit_tick(16, softplus, weights, lambda i: att_probsT(act, "sb", sb_units, i),
                                     lambda i: att_out(act, "sb", sb_units, i)):
                step(i)

        def stick_dve(dve):
            stage(dve, "stick")

            def scaled(i):
                n, r = sb_units[i]["keys"], sc[:, 2 + i % 2, :]
                dve.wait_ge(*when(("sb", "scores", i)))
                nc.vector.tensor_scalar(r[:, 0:n], psum[:, i % 2, 0:n], 0.125, None, ALU.mult)\
                    .then_inc(*up(dve, ("sb", "z", i)))
                dve.wait_ge(*latest(dve))
                also(("read", ("sb", "s", i)), ("sb", "z", i))

            def exponent(i):
                n, s, r = sb_units[i]["keys"], sc[:, i % 2, :], sc[:, 2 + i % 2, :]
                d = slice(n - P, n)
                dve.wait_ge(*when(("sb", "ln", i)))
                nc.vector.scalar_tensor_tensor(s[:, 0:n], r[:, 0:n], 0.0, s[:, 0:n], ALU.max, ALU.add)\
                    .then_inc(*up(dve))
                dve.wait_ge(*latest(dve))
                nc.vector.tensor_tensor(s[:, d], s[:, d], cst("strict"), ALU.mult).then_inc(*up(dve))
                dve.wait_ge(*latest(dve))
                v = s[:, 0:n][:, ::-1]
                nc.vector.tensor_tensor_scan(v, v, v, 0.0, ALU.add, ALU.max).then_inc(*up(dve))
                dve.wait_ge(*latest(dve))
                nc.vector.tensor_tensor(s[:, 0:n], r[:, 0:n], s[:, 0:n], ALU.subtract).then_inc(*up(dve))
                dve.wait_ge(*latest(dve))
                nc.vector.tensor_tensor(s[:, d], s[:, d], cst("strict_add"), ALU.add)\
                    .then_inc(*up(dve, ("sb", "exponent", i)))
                dve.wait_ge(*latest(dve))

            for step, i in unit_tick(16, scaled, exponent):
                step(i)

        cq = area(0, 2, 512)
        ckv = area(1024, 2, 288)
        cqT = area(1600, 4, 256)
        ckvT = area(2624, 2, 256)
        mq = area(3136, 2, 16, 96)
        mkv = area(6208, 2, 16, 128)
        mk = area(10304, 2, 16, 96)
        mqT = area(13376, 16, 256)
        mkT = area(17472, 16, 256)
        msq = area(21568, 16, 96)
        pos_i = sb("pos_i", [P, 2], I32)
        rot = area(23104, 6, 32)

        def mla_pool(pool):
            stage(pool, "mla")
            nc.gpsimd.dma_start(pos_i[:, :], a["positions_2"][0].rearrange("(t p) -> p t", p=P), allow_slow_non_contiguous=True)\
                .then_inc(landing("positions"), 16)

        def rstd_pool(pool, v, width, before, event):
            pool.wait_ge(*when(before))
            nc.gpsimd.tensor_scalar(v, v, 1.0 / width, EPS, ALU.mult, ALU.add).then_inc(*up(pool))
            pool.wait_ge(*latest(pool))
            nc.gpsimd.tensor_tensor(v, v, half[:, 0:v.shape[1]], ALU.pow).then_inc(*up(pool, event))
            pool.wait_ge(*latest(pool))

        def mla_pool_rstd(pool):
            stage(pool, "mla")
            rstd_pool(pool, stat[:, 134:136], 512, "cq squares", "cq rstd")
            rstd_pool(pool, stat[:, 136:138], 256, "ckv squares", "ckv rstd")
            for y in range(2):
                for t in range(2):
                    at = 144 + 16 * (2 * y + t)
                    rstd_pool(pool, stat[:, at:at + 16], 96, ("mla squares", y, t), ("mla rstd", y, t))

        def angles_dve(dve):
            stage(dve, "angles")
            dve.wait_ge(*when(("dma", "positions")))
            C1, C2 = 6.28125, 0.0019353071795864769
            posf = stat[:, 138:140]
            ang, n, r, c = (rot[:, j, :] for j in range(4))
            nc.vector.tensor_copy(posf, pos_i[:, :]).then_inc(*up(dve))
            dve.wait_ge(*latest(dve))
            for t in range(2):
                nc.vector.tensor_scalar(ang[:, 16 * t:16 * t + 16], cst("inv_freq"), posf[:, t:t + 1], None,
                                               ALU.mult).then_inc(*up(dve))
                dve.wait_ge(*latest(dve))
            nc.vector.tensor_scalar(n, ang, float(1 / (2 * np.pi)), 12582912.0, ALU.mult, ALU.add)\
                .then_inc(*up(dve))
            dve.wait_ge(*latest(dve))
            nc.vector.tensor_scalar(n, n, 12582912.0, None, ALU.subtract).then_inc(*up(dve))
            dve.wait_ge(*latest(dve))
            nc.vector.scalar_tensor_tensor(r, n, -C1, ang, ALU.mult, ALU.add).then_inc(*up(dve))
            dve.wait_ge(*latest(dve))
            nc.vector.scalar_tensor_tensor(r, n, -C2, r, ALU.mult, ALU.add).then_inc(*up(dve))
            dve.wait_ge(*latest(dve))
            nc.vector.tensor_scalar(c, r, float(np.pi / 2), float(-2 * np.pi), ALU.is_gt, ALU.mult)\
                .then_inc(*up(dve))
            dve.wait_ge(*latest(dve))
            nc.vector.scalar_tensor_tensor(c, r, float(np.pi / 2), c, ALU.add, ALU.add).then_inc(*up(dve))
            dve.wait_ge(*latest(dve))
            for v in (r, c):
                nc.vector.tensor_scalar(v, v, 3.1415925, -3.1415925, ALU.min, ALU.max)\
                    .then_inc(*up(dve, "angles"))
                dve.wait_ge(*latest(dve))

        def angles_act(act):
            stage(act, "angles")
            act.wait_ge(*when("angles"))
            nc.scalar.activation(rot[:, 4, :], rot[:, 2, :], ACT.Sin).then_inc(*up(act))
            act.wait_ge(*latest(act))
            nc.scalar.activation(rot[:, 5, :], rot[:, 3, :], ACT.Sin).then_inc(*up(act, "sines"))
            act.wait_ge(*latest(act))

        def mla_pe(pe):
            rows_pe(pe, "mla_in", lambda k, t: hT[:, k, P * t:P * t + P], range(2), KT, 800, [0, 1, 2, 3],
                    [("read", ("mix1", b)) for b in range(4)])
            stage(pe, "mla")
            for i, (src, nf) in enumerate(((cq, 4), (ckv, 2))):
                for t in range(2):
                    b = 4 + 2 * i + t
                    pe.wait_ge(*when(("latent normed", i, t)))
                    pe.wait_ge(*bank(b, ("latT", i, t)))
                    for f in range(nf):
                        ins = nc.tensor.transpose(psum[:, b, P * f:P * f + P], src[:, t, P * f:P * f + P], ident)
                    ins.then_inc(*up(pe, ("latT", "full", i, t)))
            rows_pe(pe, "mla_uq", lambda k, t: cqT[:, k, P * t:P * t + P], range(2), 4, 1536, [0, 1, 2, 3],
                    [("read", ("latT", 0, 1))])
            rows_pe(pe, "mla_ukv", lambda k, t: ckvT[:, k, P * t:P * t + P], range(2), 2, 2048, [4, 5, 6, 7],
                    [("read", ("latT", 1, 1))])
            stage(pe, "mla")
            for i, (y, t, g) in enumerate(mla_turns):
                pe.wait_ge(*when(("mla roped", y, t)))
                b = i % 4
                pe.wait_ge(*bank(b, ("mlaT", i)))
                for j in range(4):
                    ins = nc.tensor.transpose(psum[0:96, b, P * j:P * j + P], (mq, mk)[y][:, t, 4 * g + j, :], ident)
                ins.then_inc(*up(pe, ("mlaT", "full", i)))

        mla_turns = [(y, t, g) for y in range(2) for t in range(2) for g in range(4)]

        def mla_act(act):
            stage(act, "mla")
            act.wait_ge(*when(("pre1_down", "full", 1, 1)))
            for n in range(2):
                for t in range(2):
                    act.wait_ge(*when(("mla_in", "full", n, t)))
                    w = 512 if n == 0 else 288
                    nc.scalar.copy((cq, ckv)[n][:, t, :], psum[:, 2 * n + t, 0:w])\
                        .then_inc(*up(act, ("read", ("mla_in", n, t))))
            for n in range(3):
                for t in range(2):
                    act.wait_ge(*when(("mla_uq", "full", n, t)))
                    nc.scalar.copy(mq[:, t].rearrange("p h d -> p (h d)")[:, 512 * n:512 * n + 512],
                                          psum[:, (2 * n + t) % 4, :])\
                        .then_inc(*up(act, ("read", ("mla_uq", n, t))))
            for n in range(4):
                for t in range(2):
                    act.wait_ge(*when(("mla_ukv", "full", n, t)))
                    nc.scalar.copy(mkv[:, t].rearrange("p h d -> p (h d)")[:, 512 * n:512 * n + 512],
                                          psum[:, 4 + (2 * n + t) % 4, :])\
                        .then_inc(*up(act, ("read", ("mla_ukv", n, t))))
            for i, (y, t, g) in enumerate(mla_turns):
                act.wait_ge(*when(("mlaT", "full", i)))
                nc.scalar.copy((mqT, mkT)[y][0:96, 4 * g:4 * g + 4, P * t:P * t + P],
                                      psum[0:96, i % 4, :].rearrange("p (h t) -> p h t", h=4))\
                    .then_inc(*up(act, ("read", ("mlaT", i))))

        def mla_dve(dve):
            stage(dve, "mla")
            for i, (y, w, at, name) in enumerate(((cq, 512, 134, "cq"), (ckv, 256, 136, "ckv"))):
                for t in range(2):
                    dve.wait_ge(*when(("read", ("mla_in", i, t))))
                    nc.vector.tensor_tensor(msq.rearrange("p a b -> p (a b)")[:, 0:w], y[:, t, 0:w], y[:, t, 0:w],
                                                   ALU.mult).then_inc(*up(dve))
                    dve.wait_ge(*latest(dve))
                    nc.vector.tensor_reduce(stat[:, at + t:at + t + 1], msq.rearrange("p a b -> p (a b)")[:, 0:w],
                                                   AX.X, ALU.add).then_inc(*up(dve, name + " squares"))
                    dve.wait_ge(*latest(dve))
            for i, (y, w, at, name) in enumerate(((cq, 512, 134, "cq"), (ckv, 256, 136, "ckv"))):
                dve.wait_ge(*when(name + " rstd"))
                for t in range(2):
                    nc.vector.tensor_scalar(y[:, t, 0:w], y[:, t, 0:w], stat[:, at + t:at + t + 1], None, ALU.mult)\
                        .then_inc(*up(dve, ("latent normed", i, t)))
                    dve.wait_ge(*latest(dve))
            for i, (nf, dst, name) in enumerate(((4, cqT, "q_lora"), (2, ckvT, "kv_lora"))):
                for t in range(2):
                    b = 4 + 2 * i + t
                    dve.wait_ge(*when(("latT", "full", i, t)))
                    for f in range(nf):
                        at = ROWS_B[name] + f
                        nc.vector.tensor_scalar(dst[:, f, P * t:P * t + P], psum[:, b, P * f:P * f + P],
                                                       colB[:, at:at + 1], None, ALU.mult)\
                            .then_inc(*up(dve, ("read", ("latT", i, t))))
            for y in range(2):
                v = (mq, mk)[y]
                for t in range(2):
                    if y == 0:
                        for event in [("read", ("mla_uq", n, t)) for n in range(3)]:
                            dve.wait_ge(*when(event))
                    else:
                        for event in [("read", ("mla_ukv", n, t)) for n in range(4)]:
                            dve.wait_ge(*when(event))
                        nc.vector.tensor_copy(mk[:, t, :, 0:64], mkv[:, t, :, 0:64]).then_inc(*up(dve))
                        dve.wait_ge(*latest(dve))
                        nc.vector.tensor_copy(mk[:, t, :, 64:96],
                                                     ckv[:, t, 256:288].unsqueeze(1).to_broadcast([P, 16, 32]))\
                            .then_inc(*up(dve))
                        dve.wait_ge(*latest(dve))
                    at = 144 + 16 * (2 * y + t)
                    nc.vector.tensor_tensor(msq, v[:, t], v[:, t], ALU.mult).then_inc(*up(dve))
                    dve.wait_ge(*latest(dve))
                    nc.vector.tensor_reduce(stat[:, at:at + 16], msq, AX.X, ALU.add)\
                        .then_inc(*up(dve, ("mla squares", y, t)))
                    dve.wait_ge(*latest(dve))
            dve.wait_ge(*when("sines"))
            dve.wait_ge(*when(("dma", "q_gain")))
            dve.wait_ge(*when(("dma", "k_gain")))
            for y in range(2):
                for t in range(2):
                    v = (mq, mk)[y][:, t]
                    at = 144 + 16 * (2 * y + t)
                    dve.wait_ge(*when(("mla rstd", y, t)))
                    nc.vector.tensor_tensor(v, v, stat[:, at:at + 16].unsqueeze(2).to_broadcast([P, 16, 96]),
                                                   ALU.mult).then_inc(*up(dve))
                    dve.wait_ge(*latest(dve))
                    nc.vector.tensor_tensor(v, v, gbc[:, 96 * y:96 * y + 96].unsqueeze(1).to_broadcast([P, 16, 96]),
                                                   ALU.mult).then_inc(*up(dve))
                    dve.wait_ge(*latest(dve))
                    s = rot[:, 4, 16 * t:16 * t + 16].unsqueeze(1).to_broadcast([P, 16, 16])
                    c = rot[:, 5, 16 * t:16 * t + 16].unsqueeze(1).to_broadcast([P, 16, 16])
                    tmp = [sc2[:, 0, 256 * (j % 2):256 * (j % 2) + 256].rearrange("p (h d) -> p h d", h=16) if j < 2 else
                           sc2[:, 1, 256 * (j % 2):256 * (j % 2) + 256].rearrange("p (h d) -> p h d", h=16)
                           for j in range(4)]
                    x1, x2 = v[:, :, 64:80], v[:, :, 80:96]
                    for j, (u, w) in enumerate(((x1, c), (x2, s), (x1, s), (x2, c))):
                        nc.vector.tensor_tensor(tmp[j], u, w, ALU.mult).then_inc(*up(dve))
                        dve.wait_ge(*latest(dve))
                    nc.vector.tensor_tensor(x1, tmp[0], tmp[1], ALU.subtract).then_inc(*up(dve))
                    dve.wait_ge(*latest(dve))
                    nc.vector.tensor_tensor(x2, tmp[2], tmp[3], ALU.add).then_inc(*up(dve, ("mla roped", y, t)))
                    dve.wait_ge(*latest(dve))

        mla_units = []
        for h in range(16):
            for qt in range(2):
                r, f = head_rows(h), h // 2
                mla_units.append(dict(keys=P * (qt + 1),
                                      qk=[(mqT[0:96, h, P * qt:P * qt + P], mkT[0:96, h, 0:P * (qt + 1)])],
                                      bias=[(P, None)] * qt + [(P, cst("causal_add"))],
                                      v=[(lambda k, h=h: mkv[:, k, h, 64:128], r.start)],
                                      dst=[hT[r, f, P * qt:P * qt + P]]))

        xkm = area(0, 2, 4, 256)
        xvm = area(2048, 2, 4, 256)
        xqr = area(4096, 2, 4, 256)
        xkT = area(6144, 8, 256)
        xqT = area(8192, 8, 256)
        xsq = hT[:, 0:4, :].rearrange("p t (h d) -> p (t h) d", h=2).rearrange("p (t h) d -> p t h d", t=2)
        mem_parts = [area(at, 8, 256, rounded=True) for at in (6144, 8192)]

        def mem_load(pool, layer):
            if layer == 0:
                pool.wait_ge(*when("y normed"))
                pool.wait_ge(*when(("chains", 7)))
                nc.gpsimd.dma_start(cx[:, :, :], a["mem_2"][0].rearrange("(t p) d -> p t d", p=P))\
                    .then_inc(landing("mem"), 16)

        def xmem_pe(pe, l):
            rows3_pe(pe, f"xkv{l}", mem_parts, KT, 2 * D, [0, 1, 2, 3], tiles=(2, 3), key=f"xm{l}")
            rows3_pe(pe, f"xq{l}", x_parts, KT, D, [4, 5, 6, 7], key=f"xx{l}")
            stage(pe, "xmem")
            for i in range(8):
                y, t, b2 = i // 4, (i // 2) % 2, i % 2
                pe.wait_ge(*when((f"x normed {l}", y, t)))
                pe.wait_ge(*bank(i % 4, (f"xT{l}", i)))
                for j in range(4):
                    src = (xkm, xqr)[y][:, t].rearrange("p h d -> p (h d)")
                    at = 512 * b2 + P * j
                    ins = nc.tensor.transpose(psum[:, i % 4, P * j:P * j + P], src[:, at:at + P], ident)
                ins.then_inc(*up(pe, (f"xT{l}", "full", i)))

        def xmem_act(act, l):
            names = mem_slabs(l)
            high_act(act, names[1])
            act.wait_ge(*when(("sbg_out" if l == 0 else "mla_out", "full", 1, 1)))
            for n in range(4):
                stage(act, "xmem")
                for i, t in enumerate((2, 3)):
                    act.wait_ge(*when((f"xkv{l}", "full", n, t)))
                    b = (2 * n + i) % 4
                    nc.scalar.copy(xkm[:, i, n, :], psum[:, b, 0:256]).then_inc(*up(act))
                    nc.scalar.copy(xvm[:, i, n, :], psum[:, b, 256:512])\
                        .then_inc(*up(act, ("read", (f"xkv{l}", n, t))))
                high_act(act, names[n + 2])
            stage(act, "xmem")
            for n in range(2):
                for t in range(2):
                    act.wait_ge(*when((f"xq{l}", "full", n, t)))
                    nc.scalar.copy(xqr[:, t, 2 * n:2 * n + 2, :].rearrange("p a b -> p (a b)"),
                                          psum[:, 4 + (2 * n + t) % 4, :])\
                        .then_inc(*up(act, ("read", (f"xq{l}", n, t))))

        def xmem_dve(dve, l):
            names = mem_slabs(l)
            low_slabs(dve, names[1:])
            stage(dve, "xmem")
            for y in range(2):
                dve.wait_ge(*when(("read", (f"xkv{l}", 3, 3)) if y == 0 else ("read", (f"xq{l}", 1, 1))))
                v = (xkm, xqr)[y]
                at = 176 + 8 * y
                nc.vector.tensor_tensor(xsq, v, v, ALU.mult).then_inc(*up(dve))
                dve.wait_ge(*latest(dve))
                nc.vector.tensor_reduce(stat[:, at:at + 8], xsq.rearrange("p a b c -> p (a b) c"), AX.X, ALU.add)\
                    .then_inc(*up(dve, (f"x squares {l}", y)))
                dve.wait_ge(*latest(dve))
                dve.wait_ge(*when((f"x rstd {l}", y)))
                for t in range(2):
                    nc.vector.tensor_tensor(v[:, t], v[:, t], stat[:, at + 4 * t:at + 4 * t + 4].unsqueeze(2)
                                                   .to_broadcast([P, 4, 256]), ALU.mult)\
                        .then_inc(*up(dve, (f"x normed {l}", y, t)))
                    dve.wait_ge(*latest(dve))
            for i in range(8):
                y, t, b2 = i // 4, (i // 2) % 2, i % 2
                dve.wait_ge(*when((f"xT{l}", "full", i)))
                for j in range(2):
                    at = ROWS_B["xk" if y == 0 else "xq"] + 2 * l + j
                    dst = (xkT, xqT)[y].rearrange("p (h j) n -> p h j n", j=2)[:, 2 * b2:2 * b2 + 2, j, P * t:P * t + P]
                    src = psum[:, i % 4, :].rearrange("p (h j n) -> p h j n", h=2, j=2)[:, :, j, :]
                    nc.vector.tensor_scalar(dst, src, colB[:, at:at + 1], None, ALU.mult)\
                        .then_inc(*up(dve, ("read", (f"xT{l}", i))))

        def xmem_pool(pool, l):
            stage(pool, "xmem")
            for y in range(2):
                rstd_pool(pool, stat[:, 176 + 8 * y:184 + 8 * y], 256, (f"x squares {l}", y), (f"x rstd {l}", y))

        x_units = []
        for h in range(4):
            for qt in range(2):
                x_units.append(dict(keys=256, bias=None,
                                    qk=[(xqT[:, 2 * h + j, P * qt:P * qt + P], xkT[:, 2 * h + j, :]) for j in range(2)],
                                    v=[(lambda k, h=h, j=j: xvm[:, k, h, P * j:P * j + P], 0) for j in range(2)],
                                    dst=[hT[:, 2 * h + j, P * qt:P * qt + P] for j in range(2)]))

        def cat(k, t):
            return hT[:, k, P * t:P * t + P]


        block = ctx.enter_context(nc.Block())

        @block.sync
        def _(eng):
            sp = Side(eng, "sp")
            stage(sp, "setup")
            setup_sp(sp)
            for i, (name, pieces) in enumerate(slabs):
                if 0 <= i - slab_at[("rw_o", 0, 0)] < RING:
                    sp.wait_ge(*when(("chains", 6)))
                if i >= RING:
                    sp.wait_ge(*when(("used", i - RING)))
                view = ring[:, i % RING, :].rearrange("p (k n) -> p k n", k=8)
                for nk, at, nn, src in pieces:
                    nc.sync.dma_start(view[:, 0:nk, at:at + nn], src)\
                        .then_inc(add(f"slab_landed_{i % RING}", 16, ("slab", i)), 16)
            sp.wait_ge(*when(("post1_down", "added", 1, 1)))
            nc.sync.dma_start(out[0].rearrange("(t p) d -> p t d", p=P), x[:, :, :])\
                .then_inc(landing("out"), 16)
            eng.wait_ge(sem("landed_out"), 16)

        @block.tensor
        def _(eng):
            pe = Side(eng, "pe")
            stage(pe, "setup")
            setup_pe(pe)
            ada_pe(pe)
            norm_pe(pe, "L0a")
            norm_pe(pe, "C0a")
            ab_in_pe(pe)
            qk_norm_pe(pe)
            att_pe(pe, "na", na, [("read", ("qkT", i)) for i in range(8)])
            att_pe(pe, "cx", cxa)
            decay_pe(pe)
            mlT_pe(pe)
            ml_pe(pe)
            merge_pe(pe)
            rows_pe(pe, "ab_out", lambda k, t: hT[:, k, P * t:P * t + P], range(4), KT, D, [0, 1, 2, 3], [("read", ("merge", 3)), ("read", ("cx", "o", 15))])
            norm_pe(pe, "L0m")
            norm_pe(pe, "C0m")
            mlp_pe(pe, "mlp0", x_parts, (0, 1), "L0m")
            mlp_pe(pe, "mlp0c", c_parts, (2, 3), "C0m")
            norm_pe(pe, "L1a")
            norm_pe(pe, "C1a")
            proj_pe(pe)
            for part in range(4):
                prep_pe(pe, 0, part)
            for f in range(8):
                gram_pe(pe, f)
                inv_pe(pe, f)
            for hop in range(HOPS):
                walk_pe(pe, 7, hop)
            readout_pe(pe)
            rows_pe(pe, "rw_o", lambda k, t: hT[:, k, P * t:P * t + P], range(2), KT, D, [4, 5, 6, 7], [("rw gated", 7)])
            norm_pe(pe, "L1m")
            mlp_pe(pe, "mlp1", x_parts, (0, 1), "L1m")
            norm_pe(pe, "pre0")
            swiglu_pe(pe, "pre0")
            norm_pe(pe, "mix0")
            even_in_pe(pe)
            even_gate_pe(pe)
            att_pe(pe, "sb", sb_units)
            rows_pe(pe, "sbg_out", cat, range(2), KT, D, [4, 5, 6, 7], [("read", ("sb", "o", 15)), ("read", ("gatedT", 1))])
            norm_pe(pe, "xm0")
            norm_pe(pe, "xx0")
            xmem_pe(pe, 0)
            att_pe(pe, "xa0", x_units, [("read", ("xT0", i)) for i in range(8)])
            rows_pe(pe, "xo0", cat, range(2), KT, D, [4, 5, 6, 7], [("read", ("xa0", "o", 7))])
            norm_pe(pe, "post0")
            swiglu_pe(pe, "post0")
            norm_pe(pe, "pre1")
            swiglu_pe(pe, "pre1")
            norm_pe(pe, "mix1")
            mla_pe(pe)
            att_pe(pe, "mla", mla_units, [("read", ("mlaT", 15))])
            rows_pe(pe, "mla_out", cat, range(2), KT, D, [4, 5, 6, 7], [("read", ("mla", "o", 31))])
            norm_pe(pe, "xm1")
            norm_pe(pe, "xx1")
            xmem_pe(pe, 1)
            att_pe(pe, "xa1", x_units, [("read", ("xT1", i)) for i in range(8)])
            rows_pe(pe, "xo1", cat, range(2), KT, D, [4, 5, 6, 7], [("read", ("xa1", "o", 7))])
            norm_pe(pe, "post1")
            swiglu_pe(pe, "post1")

        @block.scalar
        def _(eng):
            act = Side(eng, "act")
            stage(act, "setup")
            setup_act(act)
            norm_act(act, "L0a", x, [("dma", "x")])
            norm_act(act, "C0a", cx, [("dma", "ctx")])
            ab_in_act(act)
            gates_act(act)
            att_act(act, "na", na, 0.125, [("gates", "full", 3)])
            att_act(act, "cx", cxa, 0.125)
            softplus_act(act)
            decay_act(act)
            mlT_act(act)
            ml_act(act)
            act.wait_ge(*when(("read", ("merge", 3))))
            high_ahead(act, "mlp0")
            norm_act(act, "L0m", x, [("ab_out", "added", 1, 1)])
            norm_act(act, "C0m", cx, [("ab_out", "added", 1, 3)])
            mlp_act(act, "mlp0")
            high_ahead(act, "mlp0c")
            mlp_act(act, "mlp0c")
            norm_act(act, "L1a", x, [("mlp0_down", "added", 1, 1)])
            norm_act(act, "C1a", cx, [("mlp0c_down", "added", 1, 3)])
            proj_act(act)
            for f in range(8):
                prep_act(act, f)
                if f:
                    for hop in range(HOPS):
                        walk_act(act, f - 1, hop)
            for hop in range(HOPS):
                walk_act(act, 7, hop)
            act.wait_ge(*when(("rw gated", 7)))
            high_ahead(act, "mlp1")
            norm_act(act, "L1m", x, [("rw_o", "added", 1, 1)])
            mlp_act(act, "mlp1")
            high_ahead(act, "pre0")
            norm_act(act, "pre0", x, [("mlp1_down", "added", 1, 1)])
            swiglu_act(act, "pre0")
            high_ahead(act, "sbg")
            norm_act(act, "mix0", x, [("pre0_down", "added", 1, 1)])
            even_in_act(act)
            stick_act(act)
            high_ahead(act, "mem0")
            norm_act(act, "xm0", cx, [("dma", "mem"), ("sbg_out", "added", 1, 1)])
            norm_act(act, "xx0", x, [("sbg_out", "added", 1, 1)])
            xmem_act(act, 0)
            att_act(act, "xa0", x_units, 0.0625, [("xq0", "full", 1, 1)])
            high_ahead(act, "post0")
            norm_act(act, "post0", x, [("xo0", "added", 1, 1)])
            swiglu_act(act, "post0")
            high_ahead(act, "pre1")
            norm_act(act, "pre1", x, [("post0_down", "added", 1, 1)])
            swiglu_act(act, "pre1")
            norm_act(act, "mix1", x, [("pre1_down", "added", 1, 1)])
            angles_act(act)
            mla_act(act)
            att_act(act, "mla", mla_units, 96 ** -0.5)
            high_ahead(act, "mem1")
            norm_act(act, "xm1", cx, [("dma", "mem"), ("mla_out", "added", 1, 1)])
            norm_act(act, "xx1", x, [("mla_out", "added", 1, 1)])
            xmem_act(act, 1)
            att_act(act, "xa1", x_units, 0.0625, [("xq1", "full", 1, 1)])
            high_ahead(act, "post1")
            norm_act(act, "post1", x, [("xo1", "added", 1, 1)])
            swiglu_act(act, "post1")

        @block.vector
        def _(eng):
            dve = Side(eng, "dve")
            stage(dve, "setup")
            setup_dve(dve)
            ada_dve(dve)
            norm_dve(dve, "L0a", x, 0, mcol(0, 0, 1), mcol(0, 0, 0), True)
            norm_dve(dve, "C0a", cx, 256, mcol(0, 1, 1), mcol(0, 1, 0), True)
            gates_dve(dve)
            qk_norm_dve(dve)
            att_dve(dve, "na", na, 0.125, after_first=["bias ready"])
            att_dve(dve, "cx", cxa, 0.125)
            decay_dve(dve)
            decay_out_dve(dve)
            ml_dve(dve)
            merge_dve(dve)
            gated_rows_dve(dve, "ab_out", range(4), [0, 1, 2, 3], gates_a, ("gate a0", "gate a1"))
            norm_dve(dve, "L0m", x, 0, mcol(0, 0, 4), mcol(0, 0, 3), True, dest=x_parts)
            low_slabs(dve, AHEAD["mlp0"])
            norm_dve(dve, "C0m", cx, 256, mcol(0, 1, 4), mcol(0, 1, 3), True, dest=c_parts)
            mlp_dve(dve, "mlp0", AHEAD["mlp0c"])
            gated_rows_dve(dve, "mlp0_down", (0, 1), UP_BANKS, gates_m, ("gate m0", "gate m1"))
            mlp_dve(dve, "mlp0c")
            gated_rows_dve(dve, "mlp0c_down", (2, 3), UP_BANKS, gates_m, ())
            norm_dve(dve, "L1a", x, 0, mcol(1, 0, 1), mcol(1, 0, 0), True)
            norm_dve(dve, "C1a", cx, 256, mcol(1, 1, 1), mcol(1, 1, 0), True)
            mix_dve(dve)
            for part in range(PREP_PARTS):
                prep_dve(dve, 0, part)
            for f in range(8):
                gram_dve(dve, f)
                inv_dve(dve, f)
                walk_start(dve, f)
            for y in range(4, 8):
                walk_y(dve, 7, y)
            readout_dve(dve)
            low_slabs(dve, AHEAD["mlp1"])
            gated_rows_dve(dve, "rw_o", range(2), [4, 5, 6, 7], gates_r, ("gate r",))
            norm_dve(dve, "L1m", x, 0, mcol(1, 0, 4), mcol(1, 0, 3), True, dest=x_parts)
            mlp_dve(dve, "mlp1", AHEAD["pre0"])
            gated_rows_dve(dve, "mlp1_down", range(2), [4, 5, 6, 7], gates_m, ("gate n",))
            norm_dve(dve, "pre0", x, 0, gain("ffn_pre", 0), dest=x_parts)
            swiglu_dve(dve, "pre0", AHEAD["sbg"])
            norm_dve(dve, "mix0", x, 0, gain("mix", 0), dest=x_parts)
            even_gate_dve(dve)
            stick_dve(dve)
            low_slabs(dve, AHEAD["mem0"])
            add_rows_dve(dve, "sbg_out", [4, 5, 6, 7], 1.0)
            norm_dve(dve, "xm0", cx, 256, gain("xmem_mem", 0), dest=mem_parts)
            norm_dve(dve, "xx0", x, 0, gain("xmem", 0), dest=x_parts)
            xmem_dve(dve, 0)
            att_dve(dve, "xa0", x_units, 0.0625)
            low_slabs(dve, AHEAD["post0"])
            add_rows_dve(dve, "xo0", [4, 5, 6, 7], 1.0)
            norm_dve(dve, "post0", x, 0, gain("ffn_post", 0), dest=x_parts)
            swiglu_dve(dve, "post0", AHEAD["pre1"])
            norm_dve(dve, "pre1", x, 0, gain("ffn_pre", 1), dest=x_parts)
            swiglu_dve(dve, "pre1")
            angles_dve(dve)
            norm_dve(dve, "mix1", x, 0, gain("mix", 1))
            mla_dve(dve)
            att_dve(dve, "mla", mla_units, 96 ** -0.5)
            low_slabs(dve, AHEAD["mem1"])
            add_rows_dve(dve, "mla_out", [4, 5, 6, 7], 1.0)
            norm_dve(dve, "xm1", cx, 256, gain("xmem_mem", 1), dest=mem_parts)
            norm_dve(dve, "xx1", x, 0, gain("xmem", 1), dest=x_parts)
            xmem_dve(dve, 1)
            att_dve(dve, "xa1", x_units, 0.0625)
            low_slabs(dve, AHEAD["post1"])
            add_rows_dve(dve, "xo1", [4, 5, 6, 7], 1.0)
            norm_dve(dve, "post1", x, 0, gain("ffn_post", 1), dest=x_parts)
            swiglu_dve(dve, "post1")

        @block.gpsimd
        def _(eng):
            pool = Side(eng, "pool")
            stage(pool, "setup")
            setup_pool(pool)
            ada_pool(pool)
            norm_pool(pool, "L0a")
            norm_pool(pool, "C0a")
            qk_norm_pool(pool)
            rope_pool(pool)
            ml_pool(pool)
            merge_pool(pool)
            pool.wait_ge(*when(("merge", "turned", 3)))
            gate_load(pool, "gate a0", gates_a[0], 0, 0, 2)
            gate_load(pool, "gate a1", gates_a[1], 0, 1, 2)
            pool.wait_ge(*when(("merge", "turned", 3)))
            gate_load(pool, "gate m0", gates_m[0], 0, 0, 5)
            gate_load(pool, "gate m1", gates_m[1], 0, 1, 5)
            norm_pool(pool, "L0m")
            norm_pool(pool, "C0m")
            norm_pool(pool, "L1a")
            norm_pool(pool, "C1a")
            rw_pool(pool)
            readout_pool(pool)
            norm_pool(pool, "L1m")
            pool.wait_ge(*when(("L1m", "normed", 0)))
            gate_load(pool, "gate n", gates_m[0], 1, 0, 5)
            norm_pool(pool, "pre0")
            norm_pool(pool, "mix0")
            even_pool(pool)
            even_pool_rstd(pool)
            mem_load(pool, 0)
            norm_pool(pool, "xm0")
            norm_pool(pool, "xx0")
            xmem_pool(pool, 0)
            norm_pool(pool, "post0")
            norm_pool(pool, "pre1")
            norm_pool(pool, "mix1")
            mla_pool(pool)
            mla_pool_rstd(pool)
            mem_load(pool, 1)
            norm_pool(pool, "xm1")
            norm_pool(pool, "xx1")
            xmem_pool(pool, 1)
            norm_pool(pool, "post1")
    return now


_DIRECT = ["x", "ctx", "ada_w", "ada_b", "ab_w_in", "ab_gate_b", "na_rpb", "ab_w_out", "rw_w_rkv", "rw_w1", "rw_w2",
           "rw_a1", "rw_a2", "rw_g1", "rw_g2", "rw_w_o", "mlp_w1", "mlp_w2", "mem_2", "positions_2",
           "ffn_pre_w_gu_2", "ffn_pre_w_down_2", "sbg_w_in_2", "sgu_w_2", "sgu_ln_gain_2", "sgu_ln_bias_2", "sbg_w_out_2", "mla_w_in_2", "mla_w_uq_2",
           "mla_w_ukv_2", "mla_q_gain_2", "mla_k_gain_2", "mla_w_out_2", "xmem_wq_2", "xmem_wkv_2", "xmem_wo_2",
           "ffn_post_w_gu_2", "ffn_post_w_down_2"]
_VEC_A = ["rw_mu", "rw_w0", "rw_a0", "rw_k_k", "rw_k_a", "rw_r_k", "rw_lnx_w", "rw_lnx_b", "ml_head_norm",
          "na_q_norm", "na_q_norm", "na_k_norm", "na_k_norm"]
_VEC_B = ["ffn_pre_norm_2", "mix_norm_2", "xmem_norm_2", "xmem_mem_norm_2", "ffn_post_norm_2", "sgu_ln_gain_2",
          "sgu_ln_bias_2", "mla_q_lora_gain_2", "mla_kv_lora_gain_2", "xmem_q_gain_2", "xmem_k_gain_2", "sgu_b_2",
          "c", "c_ctx"]


def kernel(**inputs):
    import concourse.bacc as _bacc
    from concourse.bass_utils import run_bass_kernel_spmd as _run

    arrays = {name: np.ascontiguousarray(inputs[name]) for name in _DIRECT}
    arrays["vec_a"] = np.concatenate([np.asarray(inputs[n]).reshape(-1) for n in _VEC_A]).reshape(-1, P)
    arrays["vec_b"] = np.concatenate([np.asarray(inputs[n]).reshape(-1) for n in _VEC_B]).reshape(-1, P)
    arrays["const"] = np.ascontiguousarray(np.concatenate(list(constant_blocks().values()), axis=1))

    noted = None
    for _ in range(2):
        nc = _bacc.Bacc("TRN2", target_bir_lowering=False, num_devices=1)
        a = {name: nc.dram_tensor(f"in_{name}", v.shape, mybir.dt.from_np(v.dtype), kind="ExternalInput").ap()
             for name, v in arrays.items()}
        out = nc.dram_tensor("out", (1, T, D), F32, kind="ExternalOutput").ap()
        scratch_mod = nc.dram_tensor("modulation", (2, 2, 6 * D), F32, kind="Internal").ap()
        scratch_rpb = nc.dram_tensor("bias_rows", (56, 64, 127), F32, kind="Internal").ap()
        noted = bidir_dual_stack(nc, a, out, scratch_mod, scratch_rpb, noted)
    r = _run(nc, [{f"in_{name}": v for name, v in arrays.items()}], core_ids=[0])
    return r.results[0]["out"]
```
